# Optimizing a Trainium2 kernel written in Bass

```python
import math
import jax, jax.numpy as jnp
from jax import lax
import numpy as np

D_MODEL = 1024
BATCH = 1
SEQ = 2048
DEPTH = 1

MIX_WIDTH = D_MODEL
SSM_WIDTH = MIX_WIDTH // 2
CONV_WIDTH = MIX_WIDTH - SSM_WIDTH
SSM_GROUP = 16
SSM_N_GROUPS = SSM_WIDTH // SSM_GROUP
SSM_STATE = 64
CONV_HEAD_DIM = 64
CONV_N_HEADS = CONV_WIDTH // CONV_HEAD_DIM
CONV_K = 3
DT_MIN = 0.001
DT_MAX = 0.1
EPS = 1e-6
IN_COLS = 2 * SSM_WIDTH + 4 * CONV_WIDTH


def rmsnorm(x, g):
    x32 = x.astype(jnp.float32)
    y = x32 * lax.rsqrt(jnp.mean(x32 * x32, axis=-1, keepdims=True) + EPS)
    return (y * g.astype(jnp.float32)).astype(x.dtype)

def _scan_combine(c1, c2):
    a1r, a1i, b1r, b1i = c1
    a2r, a2i, b2r, b2i = c2
    ar = a2r * a1r - a2i * a1i
    ai = a2r * a1i + a2i * a1r
    br = a2r * b1r - a2i * b1i + b2r
    bi = a2r * b1i + a2i * b1r + b2i
    return (ar, ai, br, bi)

def s5_mixer(u, a_re, a_im, log_dt, b_re, b_im, c_re, c_im, d_skip, w_glu, b_glu):
    bsz, seq, _ = u.shape
    f32 = jnp.float32
    u32 = u.astype(f32).reshape(bsz, seq, SSM_N_GROUPS, SSM_GROUP)
    a_re = a_re.astype(f32); a_im = a_im.astype(f32)
    dt = jnp.exp(log_dt.astype(f32))[:, None]
    mag = jnp.exp(a_re * dt)
    ab_re = mag * jnp.cos(a_im * dt)
    ab_im = mag * jnp.sin(a_im * dt)
    den = a_re * a_re + a_im * a_im
    p_re = ab_re - 1.0
    p_im = ab_im
    q_re = (p_re * a_re + p_im * a_im) / den
    q_im = (p_im * a_re - p_re * a_im) / den
    b_re = b_re.astype(f32); b_im = b_im.astype(f32)
    bb_re = q_re[..., None] * b_re - q_im[..., None] * b_im
    bb_im = q_re[..., None] * b_im + q_im[..., None] * b_re
    bu_re = jnp.einsum('blgh,gph->blgp', u32, bb_re)
    bu_im = jnp.einsum('blgh,gph->blgp', u32, bb_im)
    a_seq_re = jnp.broadcast_to(ab_re[None, None], (1, seq, SSM_N_GROUPS, SSM_STATE))
    a_seq_im = jnp.broadcast_to(ab_im[None, None], (1, seq, SSM_N_GROUPS, SSM_STATE))
    _, _, s_re, s_im = lax.associative_scan(
        _scan_combine, (a_seq_re, a_seq_im, bu_re, bu_im), axis=1)
    y = (jnp.einsum('blgp,ghp->blgh', s_re, c_re.astype(f32))
         - jnp.einsum('blgp,ghp->blgh', s_im, c_im.astype(f32))
         + d_skip.astype(f32) * u32)
    y = y.reshape(bsz, seq, SSM_WIDTH)
    y = jax.nn.gelu(y)
    y = y * jax.nn.sigmoid(jnp.einsum('bld,de->ble', y, w_glu.astype(f32)) + b_glu.astype(f32))
    return y.astype(u.dtype)

def short_conv_mixer(h, gate_b, gate_c, conv_w):
    v = gate_c * h
    vp = jnp.pad(v, ((0, 0), (CONV_K - 1, 0), (0, 0)))
    seq = h.shape[1]
    y = sum(conv_w[k] * vp[:, k:k + seq] for k in range(CONV_K))
    return gate_b * y

def first_inputs(seed: int = 0) -> dict:
    key = jax.random.key(seed)
    ks = jax.random.split(key, 20)
    f32 = jnp.float32
    x = jax.random.normal(ks[0], (BATCH, SEQ, D_MODEL), f32)
    norm_gain = 1.0 + 0.02 * jax.random.normal(ks[1], (DEPTH, D_MODEL), f32)
    w_in = jax.random.normal(ks[2], (DEPTH, D_MODEL, IN_COLS), f32) * D_MODEL ** -0.5
    n = jnp.arange(SSM_STATE, dtype=f32)
    ssm_a_re = -0.5 + 0.01 * jax.random.normal(ks[3], (DEPTH, SSM_N_GROUPS, SSM_STATE), f32)
    ssm_a_im = math.pi * n + 0.01 * jax.random.normal(ks[4], (DEPTH, SSM_N_GROUPS, SSM_STATE), f32)
    ssm_log_dt = jax.random.uniform(ks[5], (DEPTH, SSM_N_GROUPS), f32,
                                    math.log(DT_MIN), math.log(DT_MAX))
    bscale = (2.0 * SSM_GROUP) ** -0.5
    ssm_b_re = jax.random.normal(ks[6], (DEPTH, SSM_N_GROUPS, SSM_STATE, SSM_GROUP), f32) * bscale
    ssm_b_im = jax.random.normal(ks[7], (DEPTH, SSM_N_GROUPS, SSM_STATE, SSM_GROUP), f32) * bscale
    cscale = (2.0 * SSM_STATE) ** -0.5
    ssm_c_re = jax.random.normal(ks[8], (DEPTH, SSM_N_GROUPS, SSM_GROUP, SSM_STATE), f32) * cscale
    ssm_c_im = jax.random.normal(ks[9], (DEPTH, SSM_N_GROUPS, SSM_GROUP, SSM_STATE), f32) * cscale
    ssm_d = 1.0 + 0.1 * jax.random.normal(ks[10], (DEPTH, SSM_N_GROUPS, SSM_GROUP), f32)
    w_glu = jax.random.normal(ks[11], (DEPTH, SSM_WIDTH, SSM_WIDTH), f32) * SSM_WIDTH ** -0.5
    b_glu = 0.01 * jax.random.normal(ks[12], (DEPTH, SSM_WIDTH), f32)
    conv_w = jax.random.normal(ks[13], (DEPTH, CONV_K, CONV_WIDTH), f32) * CONV_K ** -0.5
    w_out = jax.random.normal(ks[14], (DEPTH, MIX_WIDTH, D_MODEL), f32) * MIX_WIDTH ** -0.5
    final_norm_gain = 1.0 + 0.02 * jax.random.normal(ks[15], (D_MODEL,), f32)
    return {"x": x, "norm_gain": norm_gain, "w_in": w_in,
            "ssm_a_re": ssm_a_re, "ssm_a_im": ssm_a_im, "ssm_log_dt": ssm_log_dt,
            "ssm_b_re": ssm_b_re, "ssm_b_im": ssm_b_im,
            "ssm_c_re": ssm_c_re, "ssm_c_im": ssm_c_im, "ssm_d": ssm_d,
            "w_glu": w_glu, "b_glu": b_glu, "conv_w": conv_w, "w_out": w_out,
            "final_norm_gain": final_norm_gain}

def first_block(x, norm_gain, w_in, ssm_a_re, ssm_a_im, ssm_log_dt, ssm_b_re, ssm_b_im,
              ssm_c_re, ssm_c_im, ssm_d, w_glu, b_glu, conv_w, w_out, final_norm_gain):
    h = x
    for l in range(DEPTH):
        xn = rmsnorm(h, norm_gain[l])
        proj = jnp.einsum('bld,dc->blc', xn, w_in[l])
        s0 = SSM_WIDTH
        u_ssm = proj[..., :s0]
        z_ssm = proj[..., s0:2 * s0]
        c0 = 2 * s0
        h_conv = proj[..., c0:c0 + CONV_WIDTH]
        b_conv = proj[..., c0 + CONV_WIDTH:c0 + 2 * CONV_WIDTH]
        c_conv = proj[..., c0 + 2 * CONV_WIDTH:c0 + 3 * CONV_WIDTH]
        z_conv = proj[..., c0 + 3 * CONV_WIDTH:c0 + 4 * CONV_WIDTH]
        y_ssm = s5_mixer(u_ssm, ssm_a_re[l], ssm_a_im[l], ssm_log_dt[l],
                         ssm_b_re[l], ssm_b_im[l], ssm_c_re[l], ssm_c_im[l],
                         ssm_d[l], w_glu[l], b_glu[l]) * jax.nn.silu(z_ssm)
        y_conv = short_conv_mixer(h_conv, b_conv, c_conv, conv_w[l]) * jax.nn.silu(z_conv)
        y = jnp.concatenate([y_ssm, y_conv], axis=-1)
        h = h + jnp.einsum('blc,cd->bld', y, w_out[l])
    return rmsnorm(h, final_norm_gain)


GRID_W = 64
CTX_LEN = 256
D_MIX = D_MODEL
F_WIDTH = D_MIX // 4
N_FGROUPS = 4
FGROUP_DIM = F_WIDTH // N_FGROUPS
SSD_WIDTH = D_MIX - F_WIDTH
SSD_HEAD_DIM = 64
SSD_HEADS = SSD_WIDTH // SSD_HEAD_DIM
SSD_GROUPS = 4
HEADS_PER_GROUP = SSD_HEADS // SSD_GROUPS
D_STATE = 128
BC_WIDTH = SSD_GROUPS * D_STATE
CONV_DIM = SSD_WIDTH + 2 * BC_WIDTH
D_CONV = 7
CHUNK = 128
XBC_OFF = F_WIDTH + SSD_WIDTH
IN_WIDTH = XBC_OFF + CONV_DIM + 2 * SSD_HEADS
D_FF = -(-8 * D_MODEL // (3 * 256)) * 256
N_MOD = 6


def rms_norm(x, g):
    xf = x.astype(jnp.float32)
    y = xf * lax.rsqrt(jnp.mean(xf * xf, axis=-1, keepdims=True) + EPS)
    return (y * g.astype(jnp.float32)).astype(x.dtype)

def modulate(h, shift, scale):
    return h * (1 + scale) + shift

def conv_rows(u, w, bias, rows, row_len):
    b, L, ch = u.shape
    half = D_CONV // 2
    up = jnp.pad(u.reshape(b, rows, row_len, ch), ((0, 0), (0, 0), (half, half), (0, 0)))
    out = bias
    for k in range(D_CONV):
        out = out + up[:, :, k:k + row_len, :] * w[:, k]
    return out.reshape(b, L, ch)

def fourier_mix(u):
    b, L, _ = u.shape
    ug = u.reshape(b, L, N_FGROUPS, FGROUP_DIM).astype(jnp.float32)
    yf = jnp.fft.fft2(ug, axes=(1, 3), norm='ortho').real
    return yf.reshape(b, L, F_WIDTH).astype(u.dtype)

def ssd_scan(xdt, dA, Bm, Cm, h0, with_output):
    b, L = xdt.shape[:2]
    nc = L // CHUNK
    xq = xdt.reshape(b, nc, CHUNK, SSD_GROUPS, HEADS_PER_GROUP, SSD_HEAD_DIM)
    aq = dA.reshape(b, nc, CHUNK, SSD_GROUPS, HEADS_PER_GROUP)
    Bq = Bm.reshape(b, nc, CHUNK, SSD_GROUPS, D_STATE)
    Cq = Cm.reshape(b, nc, CHUNK, SSD_GROUPS, D_STATE)
    a_cs = jnp.cumsum(aq, axis=2)
    a_end = a_cs[:, :, -1]
    st = jnp.einsum('bcsgn,bcsgr,bcsgrp->bcgrpn', Bq, jnp.exp(a_end[:, :, None] - a_cs), xq)

    def step(h, inp):
        s_c, a_c = inp
        return jnp.exp(a_c)[..., None, None] * h + s_c, h

    h_fin, h_in = lax.scan(step, h0, (jnp.moveaxis(st, 1, 0), jnp.moveaxis(a_end, 1, 0)))
    if not with_output:
        return None, h_fin
    h_in = jnp.moveaxis(h_in, 0, 1)
    seg = a_cs[:, :, :, None] - a_cs[:, :, None]
    lower = jnp.tril(jnp.ones((CHUNK, CHUNK), dtype=bool))[:, :, None, None]
    decay = jnp.exp(jnp.where(lower, seg, -jnp.inf))
    scores = jnp.einsum('bcqgn,bcsgn->bcqsg', Cq, Bq)
    y_diag = jnp.einsum('bcqsg,bcqsgr,bcsgrp->bcqgrp', scores, decay, xq)
    y_off = jnp.einsum('bcqgn,bcgrpn,bcqgr->bcqgrp', Cq, h_in, jnp.exp(a_cs))
    return (y_diag + y_off).reshape(b, L, SSD_HEADS, SSD_HEAD_DIM), h_fin

def ssd_direction(xs, Bm, Cm, dt_raw, dt_bias, a_log, h0, with_output):
    b, L, _ = xs.shape
    dt = jax.nn.softplus(dt_raw.astype(jnp.float32) + dt_bias.astype(jnp.float32))
    dA = dt * -jnp.exp(a_log.astype(jnp.float32))
    xdt = xs.reshape(b, L, SSD_HEADS, SSD_HEAD_DIM) * dt[..., None]
    return ssd_scan(xdt, dA, Bm.reshape(b, L, SSD_GROUPS, D_STATE),
                    Cm.reshape(b, L, SSD_GROUPS, D_STATE), h0, with_output)

def ssd_bidir(xs, Bm, Cm, dt_raw, dt_bias, a_log, h0_fwd, h0_bwd, with_output):
    flip = lambda t: jnp.flip(t, axis=1)
    y_f, h_f = ssd_direction(xs, Bm, Cm, dt_raw[..., :SSD_HEADS], dt_bias[0], a_log[0], h0_fwd, with_output)
    y_b, h_b = ssd_direction(flip(xs), flip(Bm), flip(Cm), flip(dt_raw[..., SSD_HEADS:]),
                             dt_bias[1], a_log[1], h0_bwd, with_output)
    y = y_f + flip(y_b) if with_output else None
    return y, h_f, h_b

def mixer_inputs(h, w_in, conv_w, conv_b, rows, row_len, full):
    p = h @ (w_in if full else w_in[:, XBC_OFF:])
    if full:
        u_f, z, rest = p[..., :F_WIDTH], p[..., F_WIDTH:XBC_OFF], p[..., XBC_OFF:]
    else:
        u_f, z, rest = None, None, p
    xbc = jax.nn.silu(conv_rows(rest[..., :CONV_DIM], conv_w, conv_b, rows, row_len))
    dt_raw = rest[..., CONV_DIM:]
    xs = xbc[..., :SSD_WIDTH]
    Bm = xbc[..., SSD_WIDTH:SSD_WIDTH + BC_WIDTH]
    Cm = xbc[..., SSD_WIDTH + BC_WIDTH:]
    return u_f, z, xs, Bm, Cm, dt_raw

def mixer_output(u_f, z, xs, y, d_skip, g_ssd, w_out):
    b, L, _ = xs.shape
    y = y + xs.reshape(b, L, SSD_HEADS, SSD_HEAD_DIM) * d_skip[:, None]
    y = y.reshape(b, L, SSD_WIDTH).astype(xs.dtype)
    y = rms_norm(y * jax.nn.silu(z), g_ssd)
    return jnp.concatenate([fourier_mix(u_f), y], axis=-1) @ w_out

def swiglu(h, w_gate, w_up, w_down):
    return (jax.nn.silu(h @ w_gate) * (h @ w_up)) @ w_down

def second_inputs(seed: int = 0) -> dict:
    key = jax.random.key(seed)
    ks = jax.random.split(key, 24)
    nrm = lambda k, shape, fan_in: jax.random.normal(k, shape, jnp.float32) * fan_in ** -0.5
    gain = lambda k, n: 1.0 + 0.05 * jax.random.normal(k, (DEPTH, n), jnp.float32)
    dt0 = jnp.exp(jax.random.uniform(ks[10], (DEPTH, 2, SSD_HEADS), jnp.float32)
                  * (math.log(0.1) - math.log(0.001)) + math.log(0.001))
    return {
        'x': jax.random.normal(ks[0], (BATCH, SEQ, D_MODEL), jnp.float32),
        'c': jax.random.normal(ks[1], (BATCH, D_MODEL), jnp.float32),
        'ctx': jax.random.normal(ks[2], (BATCH, CTX_LEN, D_MODEL), jnp.float32),
        'c_ctx': jax.random.normal(ks[3], (D_MODEL,), jnp.float32),
        'w_ada': nrm(ks[4], (DEPTH, D_MODEL, N_MOD * D_MODEL), D_MODEL),
        'b_ada': 0.01 * jax.random.normal(ks[5], (DEPTH, N_MOD * D_MODEL), jnp.float32),
        'g_pre_mix': gain(ks[6], D_MODEL),
        'g_post_mix': gain(ks[7], D_MODEL),
        'g_pre_ffn': gain(ks[8], D_MODEL),
        'g_post_ffn': gain(ks[9], D_MODEL),
        'w_in': nrm(ks[11], (DEPTH, D_MODEL, IN_WIDTH), D_MODEL),
        'conv_w': nrm(ks[12], (DEPTH, CONV_DIM, D_CONV), D_CONV),
        'conv_b': 0.01 * jax.random.normal(ks[13], (DEPTH, CONV_DIM), jnp.float32),
        'dt_bias': dt0 + jnp.log(-jnp.expm1(-dt0)),
        'a_log': jnp.log(jax.random.uniform(ks[14], (DEPTH, 2, SSD_HEADS), jnp.float32, 1.0, 16.0)),
        'd_skip': 1.0 + 0.1 * jax.random.normal(ks[15], (DEPTH, SSD_HEADS), jnp.float32),
        'g_ssd': gain(ks[16], SSD_WIDTH),
        'w_out': nrm(ks[17], (DEPTH, D_MIX, D_MODEL), D_MIX),
        'w_gate': nrm(ks[18], (DEPTH, D_MODEL, D_FF), D_MODEL),
        'w_up': nrm(ks[19], (DEPTH, D_MODEL, D_FF), D_MODEL),
        'w_down': nrm(ks[20], (DEPTH, D_FF, D_MODEL), D_FF),
    }

def second_block(x, c, ctx, c_ctx, w_ada, b_ada, g_pre_mix, g_post_mix, g_pre_ffn, g_post_ffn,
              w_in, conv_w, conv_b, dt_bias, a_log, d_skip, g_ssd, w_out, w_gate, w_up, w_down):
    b = x.shape[0]
    rows = x.shape[1] // GRID_W
    ctx_len = ctx.shape[1]
    h0 = jnp.zeros((b, SSD_GROUPS, HEADS_PER_GROUP, SSD_HEAD_DIM, D_STATE), jnp.float32)
    for l in range(DEPTH):
        keep_ctx = l + 1 < DEPTH
        mx = (jax.nn.silu(c) @ w_ada[l] + b_ada[l])[:, None, :]
        sm_x, cm_x, gm_x, sf_x, cf_x, gf_x = jnp.split(mx, N_MOD, axis=-1)
        mc = jax.nn.silu(c_ctx) @ w_ada[l] + b_ada[l]
        sm_c, cm_c, gm_c, sf_c, cf_c, gf_c = jnp.split(mc, N_MOD, axis=-1)

        hc = modulate(rms_norm(ctx, g_pre_mix[l]), sm_c, cm_c)
        uf_c, z_c, xs_c, B_c, C_c, dt_c = mixer_inputs(hc, w_in[l], conv_w[l], conv_b[l], 1, ctx_len, keep_ctx)
        y_c, hf_c, hb_c = ssd_bidir(xs_c, B_c, C_c, dt_c, dt_bias[l], a_log[l], h0, h0, keep_ctx)

        hx = modulate(rms_norm(x, g_pre_mix[l]), sm_x, cm_x)
        uf_x, z_x, xs_x, B_x, C_x, dt_x = mixer_inputs(hx, w_in[l], conv_w[l], conv_b[l], rows, GRID_W, True)
        y_x, _, _ = ssd_bidir(xs_x, B_x, C_x, dt_x, dt_bias[l], a_log[l], hf_c, hb_c, True)
        x = x + gm_x * rms_norm(mixer_output(uf_x, z_x, xs_x, y_x, d_skip[l], g_ssd[l], w_out[l]), g_post_mix[l])

        hx2 = modulate(rms_norm(x, g_pre_ffn[l]), sf_x, cf_x)
        x = x + gf_x * rms_norm(swiglu(hx2, w_gate[l], w_up[l], w_down[l]), g_post_ffn[l])

        if keep_ctx:
            out_c = mixer_output(uf_c, z_c, xs_c, y_c, d_skip[l], g_ssd[l], w_out[l])
            ctx = ctx + gm_c * rms_norm(out_c, g_post_mix[l])
            hc2 = modulate(rms_norm(ctx, g_pre_ffn[l]), sf_c, cf_c)
            ctx = ctx + gf_c * rms_norm(swiglu(hc2, w_gate[l], w_up[l], w_down[l]), g_post_ffn[l])
    return x


def setup_inputs(seed=0):
    out = dict(first_inputs(seed))
    for name, value in second_inputs(seed + 1).items():
        if name != "x":
            out[name + "_2"] = value
    return out


def reference(
    x, norm_gain, w_in, ssm_a_re, ssm_a_im, ssm_log_dt, ssm_b_re, ssm_b_im, ssm_c_re, ssm_c_im,
    ssm_d, w_glu, b_glu, conv_w, w_out, final_norm_gain, c_2, ctx_2, c_ctx_2, w_ada_2, b_ada_2,
    g_pre_mix_2, g_post_mix_2, g_pre_ffn_2, g_post_ffn_2, w_in_2, conv_w_2, conv_b_2, dt_bias_2,
    a_log_2, d_skip_2, g_ssd_2, w_out_2, w_gate_2, w_up_2, w_down_2,
):
    x = first_block(
        x, norm_gain, w_in, ssm_a_re, ssm_a_im, ssm_log_dt, ssm_b_re, ssm_b_im, ssm_c_re,
        ssm_c_im, ssm_d, w_glu, b_glu, conv_w, w_out, final_norm_gain,
    )
    return second_block(
        x, c_2, ctx_2, c_ctx_2, w_ada_2, b_ada_2, g_pre_mix_2, g_post_mix_2, g_pre_ffn_2,
        g_post_ffn_2, w_in_2, conv_w_2, conv_b_2, dt_bias_2, a_log_2, d_skip_2, g_ssd_2,
        w_out_2, w_gate_2, w_up_2, w_down_2,
    )


_drawn_inputs = setup_inputs


def setup_inputs(seed=0):
    import zlib

    import numpy as np

    out = dict(_drawn_inputs(seed))
    spreads = {}
    factors = {'norm_gain': 2.893,
     'ssm_a_re': 64.0,
     'ssm_a_im': 41.312,
     'ssm_log_dt': 42.488,
     'ssm_b_re': 57.32,
     'ssm_b_im': 58.176,
     'ssm_c_re': 57.928,
     'ssm_c_im': 58.424,
     'ssm_d': 3.008,
     'b_glu': 187.088,
     'ctx_2': 43.432,
     'b_ada_2': 3.463,
     'conv_b_2': 8.0,
     'd_skip_2': 5.24,
     'c_ctx_2': 4.621}
    for name, (base, spread) in spreads.items():
        noise = np.random.default_rng([zlib.crc32(name.encode()), seed]).standard_normal(out[name].shape)
        drawn = base * np.exp(spread * noise) if base else spread * noise
        out[name] = __import__('jax').numpy.asarray(drawn.astype(out[name].dtype))
    for name, factor in factors.items():
        out[name] = (out[name] * factor).astype(out[name].dtype)
    return out
```

```python
from contextlib import ExitStack
import math

import numpy as np
import concourse.bass as bass
from concourse import mybir

F32 = mybir.dt.float32
F32R = mybir.dt.float32r
ALU = mybir.AluOpType
ACT = mybir.ActivationFunctionType

P = 128
D = 1024
KD = D // P
L = 2048
LC = 256
LT = L + LC
TILES = L // P
NB = 512
LB = L // NB
EPS = 1e-6

SSM_W = 512
CW = 512
G1, H1, S1 = 32, 16, 64
T8 = 8
NC8 = L // T8
QP = G1 // 2
HALF = NC8 // P
SB = 16
NSB = NC8 // SB

FW = 256
FG = 64
SW = 768
HEADS, HD, SG, ST = 12, 64, 4, 128
HR = HEADS // SG
CONV_DIM = SW + 2 * SG * ST
XT_ = CONV_DIM // P
KC = 7
ROWLEN = 64
XBC = FW + SW
NCH = L // P
CCH = LC // P
FF = 2816
FT = FF // P


class Mem:

    def __init__(self, nc, stage):
        self.nc, self.stage, self.stack, self.sems = nc, stage, ExitStack(), []

    def sb(self, name, *shape):
        return self.stack.enter_context(self.nc.sbuf_tensor(f"{self.stage}_{name}", list(shape), F32))

    def sb_r(self, name, *shape):
        return self.stack.enter_context(self.nc.sbuf_tensor(f"{self.stage}_{name}", list(shape), F32R))

    def ps(self, name, *shape):
        return self.stack.enter_context(self.nc.psum_tensor(f"{self.stage}_{name}", list(shape), F32))

    def sem(self, name):
        self.sems.append(self.nc.alloc_semaphore(f"{self.stage}_{name}"))
        return self.sems[-1]

    def block(self):
        return self.stack.enter_context(self.nc.Block())

    def __enter__(self):
        self.stack.__enter__()
        return self

    def __exit__(self, *e):
        self.stack.__exit__(*e)
        if self.sems and e[0] is None:
            self.nc.clear_and_free_semaphores(self.sems)
            self.nc.all_engine_barrier()


def over(ap, shape):
    return ap.broadcast_to(list(shape))


def columns(vec, tiles):
    return vec.rearrange("(k p) -> p k", p=P)


def every_partition(vec, n=P):
    return vec.partition_broadcast(n)


def make_constants(nc, ident, ones):
    with Mem(nc, "const") as m:
        zeroed, made = m.sem("zeroed"), m.sem("made")
        block = m.block()

        @block.gpsimd
        def _(pool):
            nc.gpsimd.memset(ident[:, :], 0.0).then_inc(zeroed, 1)
            nc.gpsimd.memset(ones[:, :], 1.0).then_inc(made, 1)
            pool.wait_ge(zeroed, 1)
            nc.gpsimd.affine_select(out=ident[:, :], in_=ident[:, :], compare_op=ALU.not_equal, fill=1.0,
                                    base=0, pattern=[[-1, P]], channel_multiplier=1).then_inc(made, 1)
            pool.wait_ge(made, 2)


def norm_to_columns(nc, stage, src, tiles, dst, col0, ident, gain, modulation=None):
    with Mem(nc, stage) as m:
        x = m.sb("x", P, 2, D)
        xn = m.sb("xn", P, 2, D)
        junk = m.sb("junk", P, D)
        stat = m.sb("stat", P, 2, 4)
        a = m.sb("a", P, KD)
        b = m.sb("b", P, KD)
        s = m.sb("s", P, KD)
        eps = m.sb("eps", P, 1)
        ps = [m.ps(f"ps{i}", P, KD, P) for i in range(2)]
        vec = m.sem("vec")
        loaded = [m.sem(f"loaded{i}") for i in range(2)]
        squared, rooted, inverted, scaled = m.sem("squared"), m.sem("rooted"), m.sem("inverted"), m.sem("scaled")
        turned, placed, mul_done = m.sem("turned"), m.sem("placed"), m.sem("mul_done")
        ab, eps_set = m.sem("ab"), m.sem("eps_set")
        block = m.block()
        rows = src.rearrange("(t p) d -> t p d", p=P)

        @block.sync
        def _(sp):
            sp.dma_start(a[:, :], columns(gain, KD), allow_slow_non_contiguous=True).then_inc(vec, 16)
            if modulation:
                sp.dma_start(b[:, :], columns(modulation[0], KD), allow_slow_non_contiguous=True).then_inc(vec, 16)
                sp.dma_start(s[:, :], columns(modulation[1], KD), allow_slow_non_contiguous=True).then_inc(vec, 16)
            with sp.Fori(0, tiles // 2) as i:
                for j in range(2):
                    sp.wait_ge(scaled, 2 * i + j + 1)
                    sp.dma_start(x[:, j, :], rows[bass.ds(2 * i + j, 1), :, :].rearrange("t p d -> p (t d)"))\
                      .then_inc(loaded[j], 16)

        @block.scalar
        def _(act):
            act.wait_ge(eps_set, 1)
            nc.scalar.preload_act_table(ACT.Sqrt)
            with act.Fori(0, tiles // 2) as i:
                for j in range(2):
                    act.wait_ge(loaded[j], 16 * i + 16)
                    nc.scalar.activation(junk[:, :], x[:, j, :], ACT.Square, accum_out=stat[:, j, 0:1])\
                      .then_inc(squared, 1)
                    act.wait_ge(squared, 2 * i + j + 1)
                    nc.scalar.activation(stat[:, j, 1:2], stat[:, j, 0:1], ACT.Sqrt, scale=1.0 / D, bias=eps[:, :])\
                      .then_inc(rooted, 1)

        @block.vector
        def _(dve):
            nc.vector.memset(eps[:, :], EPS).then_inc(eps_set, 1)
            dve.wait_ge(vec, 48 if modulation else 16)
            if modulation:
                nc.vector.scalar_tensor_tensor(out=a[:, :], in0=s[:, :], scalar=1.0, in1=a[:, :],
                                               op0=ALU.add, op1=ALU.mult).then_inc(ab, 1)
                dve.wait_ge(ab, 1)
            dve.sem_inc(scaled, 2)
            dve.sem_inc(placed, 2)

            with dve.Fori(0, tiles // 2) as i:
                for j in range(2):
                    dve.wait_ge(rooted, 2 * i + j + 1)
                    nc.vector.reciprocal(stat[:, j, 2:3], stat[:, j, 1:2]).then_inc(inverted, 1)
                    dve.wait_ge(inverted, 2 * i + j + 1)
                    nc.vector.tensor_scalar(xn[:, j, :], x[:, j, :], stat[:, j, 2:3], None, ALU.mult)\
                      .then_inc(scaled, 1)
                    dve.wait_ge(turned, 2 * i + j + 1)
                    to = dst[:, :, bass.ds(col0 + (2 * i + j) * P, P)]
                    w = nc.vector.tensor_tensor(to, ps[j][:, :, :], over(a[:, :, None], (P, KD, P)), ALU.mult)
                    if modulation:
                        w.then_inc(mul_done, 1)
                        dve.wait_ge(mul_done, 2 * i + j + 1)
                        w = nc.vector.tensor_tensor(to, to, over(b[:, :, None], (P, KD, P)), ALU.add)
                    w.then_inc(placed, 1)

        @block.tensor
        def _(pe):
            with pe.Fori(0, tiles // 2) as i:
                for j in range(2):
                    pe.wait_ge(scaled, 2 * i + j + 3)
                    pe.wait_ge(placed, 2 * i + j + 1)
                    for k in range(KD):
                        t = nc.tensor.transpose(ps[j][:, k, :], xn[:, j, k * P:(k + 1) * P], ident[:, :])
                    t.then_inc(turned, 1)


def short_convolution(nc, xn, w_in, conv_w, out_t):
    with Mem(nc, "sc") as m:
        w = m.sb("w", P, 2, KD, 4, P)
        taps = m.sb("taps", P, 3, CW // P)
        v = m.sb("v", P, 2 + L)
        hs = m.sb("hs", P, NB)
        sz = m.sb("sz", P, 2, NB)
        y = m.sb("y", P, 2, L)
        ps = [[m.ps(f"ps{i}{s}", P, NB) for s in range(4)] for i in range(2)]
        taps_in, v_pad = m.sem("taps_in"), m.sem("v_pad")
        loaded = [m.sem(f"loaded{i}") for i in range(2)]
        stored, free = m.sem("stored"), m.sem("free")
        proj, h_out, z_out, drained, step, whole = (m.sem(n) for n in ("proj", "h_out", "z_out", "drained", "step", "whole"))
        block = m.block()
        H, B, C, Z = range(4)
        wv = w_in[:, 2 * SSM_W:].rearrange("(k p) (s c) -> p k s c", p=P, s=4)
        STEPS = 7

        @block.sync
        def _(sp):
            for k in range(3):
                sp.dma_start(taps[:, k, :], columns(conv_w[k, :], CW // P), allow_slow_non_contiguous=True)\
                  .then_inc(taps_in, 16)
            with sp.Fori(0, CW // P // 2) as i:
                for b in range(2):
                    sp.wait_ge(proj, (2 * i + b + 1) * LB)
                    for s in range(4):
                        sp.dma_start(w[:, b, :, s, :], wv[:, :, s, bass.ds((2 * i + b) * P, P)])\
                          .then_inc(loaded[b], 16)

        @block.tensor
        def _(pe):
            pe.sem_inc(proj, 2 * LB)
            with pe.Fori(0, CW // P // 2) as i:
                for b in range(2):
                    pe.wait_ge(loaded[b], 64 * i + 64)
                    for n in range(LB):
                        pe.wait_ge(drained, (2 * i + b) * LB + n + 1)
                        for s in range(4):
                            for k in range(KD):
                                mm = nc.tensor.matmul(ps[n % 2][s][:, :], w[:, b, k, s, :], xn[:, k, n * NB:(n + 1) * NB],
                                                      start=(k == 0), stop=(k == KD - 1))
                        mm.then_inc(proj, 1)

        @block.scalar
        def _(act):
            nc.scalar.preload_act_table(ACT.Sigmoid)
            with act.Fori(0, CW // P // 2) as i:
                for b in range(2):
                    for n in range(LB):
                        t = (2 * i + b) * LB + n
                        act.wait_ge(proj, t + 2 * LB + 1)
                        act.wait_ge(drained, t + 2)
                        nc.scalar.activation(hs[:, :], ps[n % 2][H][:, :], ACT.Copy).then_inc(h_out, 1)
                        nc.scalar.activation(sz[:, n % 2, :], ps[n % 2][Z][:, :], ACT.Sigmoid).then_inc(z_out, 1)

        @block.vector
        def _(dve):
            nc.vector.memset(v[:, 0:2], 0.0).then_inc(v_pad, 1)
            dve.wait_ge(taps_in, 48)
            dve.wait_ge(v_pad, 1)
            dve.sem_inc(drained, 2)
            with dve.Fori(0, CW // P // 2) as i:
                for b in range(2):
                    dve.wait_ge(free, 2 * i + b + 1)
                    for n in range(LB):
                        t = (2 * i + b) * LB + n
                        bank = ps[n % 2]
                        yn = y[:, b, n * NB:(n + 1) * NB]
                        tap = [taps[:, k, bass.ds(2 * i + b, 1)] for k in range(3)]
                        dve.wait_ge(h_out, t + 1)
                        nc.vector.tensor_tensor(v[:, 2 + n * NB:2 + (n + 1) * NB], bank[C][:, :], hs[:, :], ALU.mult)\
                          .then_inc(step, 1)
                        dve.wait_ge(step, STEPS * t + 1)
                        nc.vector.tensor_scalar(yn, v[:, n * NB:(n + 1) * NB], tap[0], None, ALU.mult).then_inc(step, 1)
                        for k in (1, 2):
                            dve.wait_ge(step, STEPS * t + 1 + k)
                            nc.vector.scalar_tensor_tensor(out=yn, in0=v[:, k + n * NB:k + (n + 1) * NB], scalar=tap[k],
                                                           in1=yn, op0=ALU.mult, op1=ALU.add).then_inc(step, 1)
                        dve.wait_ge(step, STEPS * t + 4)
                        nc.vector.tensor_tensor(yn, bank[B][:, :], yn, ALU.mult).then_inc(step, 1)
                        dve.wait_ge(step, STEPS * t + 5)
                        dve.wait_ge(z_out, t + 1)
                        nc.vector.tensor_tensor(yn, yn, sz[:, n % 2, :], ALU.mult).then_inc(step, 1)
                        dve.wait_ge(step, STEPS * t + 6)
                        nc.vector.tensor_tensor(yn, bank[Z][:, :], yn, ALU.mult).then_inc(step, 1)
                        dve.wait_ge(step, STEPS * t + 7)
                        dve.sem_inc(drained, 1)
                    dve.sem_inc(whole, 1)

        @block.gpsimd
        def _(pool):
            pool.sem_inc(free, 2)
            with pool.Fori(0, CW // P // 2) as i:
                for b in range(2):
                    pool.wait_ge(whole, 2 * i + b + 1)
                    pool.dma_start(out_t[bass.ds(SSM_W // P + 2 * i + b, 1), :, :].rearrange("k p l -> p (k l)"),
                                   y[:, b, :]).then_inc(stored, 16)
                    pool.wait_ge(stored, 16 * (2 * i + b) + 16)
                    pool.sem_inc(free, 1)


def silu_projection(nc, stage, xn, w, tiles, out_t):
    with Mem(nc, stage) as m:
        wt = m.sb("wt", P, 2, KD, P)
        sg = m.sb("sg", P, 2, NB)
        y = m.sb("y", P, 2, L)
        ps = [m.ps(f"ps{i}", P, NB) for i in range(2)]
        loaded = [m.sem(f"loaded{i}") for i in range(2)]
        stored, free = m.sem("stored"), m.sem("free")
        proj, gated, done = m.sem("proj"), m.sem("gated"), m.sem("done")
        block = m.block()
        wv = w.rearrange("(k p) c -> p k c", p=P)

        @block.sync
        def _(sp):
            with sp.Fori(0, tiles // 2) as i:
                for b in range(2):
                    sp.wait_ge(proj, (2 * i + b + 1) * LB)
                    sp.dma_start(wt[:, b, :, :], wv[:, :, bass.ds((2 * i + b) * P, P)]).then_inc(loaded[b], 16)

        @block.tensor
        def _(pe):
            pe.sem_inc(proj, 2 * LB)
            with pe.Fori(0, tiles // 2) as i:
                for b in range(2):
                    pe.wait_ge(loaded[b], 16 * i + 16)
                    for n in range(LB):
                        pe.wait_ge(done, (2 * i + b) * LB + n + 1)
                        for k in range(KD):
                            mm = nc.tensor.matmul(ps[n % 2][:, :], wt[:, b, k, :], xn[:, k, n * NB:(n + 1) * NB],
                                                  start=(k == 0), stop=(k == KD - 1))
                        mm.then_inc(proj, 1)

        @block.scalar
        def _(act):
            nc.scalar.preload_act_table(ACT.Sigmoid)
            with act.Fori(0, tiles // 2) as i:
                for b in range(2):
                    for n in range(LB):
                        t = (2 * i + b) * LB + n
                        act.wait_ge(proj, t + 2 * LB + 1)
                        act.wait_ge(done, t + 1)
                        nc.scalar.activation(sg[:, n % 2, :], ps[n % 2][:, :], ACT.Sigmoid).then_inc(gated, 1)

        @block.vector
        def _(dve):
            dve.sem_inc(done, 2)
            with dve.Fori(0, tiles // 2) as i:
                for b in range(2):
                    dve.wait_ge(free, 2 * i + b + 1)
                    for n in range(LB):
                        dve.wait_ge(gated, (2 * i + b) * LB + n + 1)
                        nc.vector.tensor_tensor(y[:, b, n * NB:(n + 1) * NB], ps[n % 2][:, :], sg[:, n % 2, :], ALU.mult)\
                          .then_inc(done, 1)

        @block.gpsimd
        def _(pool):
            pool.sem_inc(free, 2)
            with pool.Fori(0, tiles // 2) as i:
                for b in range(2):
                    pool.wait_ge(done, (2 * i + b + 1) * LB + 2)
                    pool.dma_start(out_t[bass.ds(2 * i + b, 1), :, :].rearrange("k p l -> p (k l)"),
                                   y[:, b, :]).then_inc(stored, 16)
                    pool.wait_ge(stored, 16 * (2 * i + b) + 16)
                    pool.sem_inc(free, 1)


def group_in(r, x):
    return 8 * (r // 2) + 2 * x + r % 2


def s5_weights(nc, d, vw, q, toeplitz, a8, ident, kernel_rows):
    TWO_PI = 2.0 * math.pi
    C1 = 6.28125
    C2 = float(np.float32(np.round((TWO_PI - C1) * 2.0 ** 22) / 2.0 ** 22))
    C3 = float(np.float32(TWO_PI - C1 - C2))
    ROUND = 1.5 * 2.0 ** 23
    HPI = float(np.float32(math.pi / 2))
    PI = float(np.nextafter(np.float32(math.pi), np.float32(0)))
    with Mem(nc, "s5w") as m:
        are, aim, dt = m.sb("are", P, QP), m.sb("aim", P, QP), m.sb("dt", P, QP)
        sc = m.sb("sc", P, 12, QP)
        pw = m.sb("pw", P, 2, T8 + 1, QP)
        rev = m.sb("rev", P, 2, T8, QP)
        tmp = m.sb("tmp", P, QP * (T8 + 1) * H1)
        tmp2 = m.sb("tmp2", P, QP * (T8 + 1) * H1)
        bin_ = m.sb("bin", P, 2, QP, H1)
        bb = m.sb("bb", P, 2, QP, H1)
        cc = m.sb("cc", P, 2, QP, H1)
        crow = m.sb("crow", P, 2, 4, 2, S1)
        w = m.sb("w", P, 2, QP, T8, H1)
        kp = m.sb("kp", H1, G1, 7 * H1 + P)
        dcol = m.sb("dcol", P, G1)
        pst = [m.ps(f"pst{i}", P, 4, P) for i in range(4)]
        psk = [m.ps(f"psk{i}", H1, 4, P) for i in range(4)]
        par, bld, cld, dld, chain_, act_done = (m.sem(n) for n in ("par", "bld", "cld", "dld", "chain", "act_done"))
        c_turned, w_turned, k_made, pe_free, w_ready, k_stored, t_loaded, k_pad = (
            m.sem(n) for n in ("c_turned", "w_turned", "k_made", "pe_free", "w_ready", "k_stored", "t_loaded", "k_pad"))
        b_ready, q_ready, k_ready, for_act = (m.sem(n) for n in ("b_ready", "q_ready", "k_ready", "for_act"))
        block = m.block()
        (DT, X, MAG, TH, N, R, SIN, COS, DEN, QR, QI, T) = range(12)

        @block.sync
        def _(sp):
            for g in range(2):
                half = slice(S1 * g, S1 * g + S1)
                for to, of in ((are, d["ssm_a_re"]), (aim, d["ssm_a_im"])):
                    sp.dma_start(to[half, :], of[0, g::2, :].rearrange("q p -> p q"), allow_slow_non_contiguous=True)\
                      .then_inc(par, 16)
                sp.dma_start(dt[half, :], d["ssm_log_dt"][0, g::2].partition_broadcast(S1), allow_slow_non_contiguous=True)\
                  .then_inc(par, 16)
            for g in range(2):
                half = slice(S1 * g, S1 * g + S1)
                for ri, of in ((0, d["ssm_b_re"]), (1, d["ssm_b_im"])):
                    sp.dma_start(bin_[half, ri, :, :], of[0, g::2, :, :].rearrange("q p h -> p q h")).then_inc(bld, 16)
            for ri, of in ((0, d["ssm_c_re"]), (1, d["ssm_c_im"])):
                for dup in range(2):
                    sp.dma_start(crow[:, ri, :, dup, :], of[0].rearrange("(r g) h p -> (g h) r p", r=4)).then_inc(cld, 16)
            for j in range(T8):
                sp.dma_start(dcol[j * H1:(j + 1) * H1, :], d["ssm_d"][0].rearrange("g h -> h g"),
                             allow_slow_non_contiguous=True).then_inc(dld, 16)
            sp.wait_ge(k_ready, 1)
            sp.dma_start(kernel_rows, kp[:, :, :]).then_inc(k_stored, 16)
            sp.wait_ge(k_stored, 16)
            for j in range(T8):
                at = (T8 - 1 - j) * H1
                sp.dma_start(toeplitz[j * H1:(j + 1) * H1, :, :], kernel_rows[:, :, at:at + P]).then_inc(t_loaded, 16)

        @block.scalar
        def _(act):
            act.wait_ge(par, 96)
            nc.scalar.activation(sc[:, DT, :], dt[:, :], ACT.Exp).then_inc(act_done, 1)
            act.wait_ge(for_act, 1)
            nc.scalar.activation(sc[:, MAG, :], sc[:, X, :], ACT.Exp).then_inc(act_done, 1)
            act.wait_ge(for_act, 2)
            nc.scalar.activation(sc[:, SIN, :], sc[:, R, :], ACT.Sin).then_inc(act_done, 1)
            nc.scalar.activation(sc[:, COS, :], sc[:, N, :], ACT.Sin).then_inc(act_done, 1)

        @block.gpsimd
        def _(pool):
            nc.gpsimd.memset(kp[:, :, :], 0.0).then_inc(k_pad, 1)

        @block.vector
        def _(dve):
            n = [0]

            def then(ins):
                n[0] += 1
                ins.then_inc(chain_, 1)
                dve.wait_ge(chain_, n[0])

            def s(i):
                return sc[:, i, :]

            def tt(o, a, b, op):
                then(nc.vector.tensor_tensor(o, a, b, op))

            def ts(o, a, s1, op1, s2=None, op2=None):
                if op2 is None:
                    then(nc.vector.tensor_scalar(o, a, s1, None, op1))
                else:
                    then(nc.vector.tensor_scalar(o, a, s1, s2, op1, op2))

            def complex_product(o, a, b, t, conj=False):
                tt(o[0], a[0], b[0], ALU.mult)
                tt(t, a[1], b[1], ALU.mult)
                tt(o[0], o[0], t, ALU.subtract)
                tt(o[1], a[0], b[1], ALU.mult)
                tt(t, a[1], b[0], ALU.mult)
                if conj:
                    ts(o[1], o[1], -1.0, ALU.mult)
                    tt(o[1], o[1], t, ALU.subtract)
                else:
                    tt(o[1], o[1], t, ALU.add)

            dve.wait_ge(act_done, 1)
            tt(s(X), are[:, :], s(DT), ALU.mult)
            dve.sem_inc(for_act, 1)
            tt(s(TH), aim[:, :], s(DT), ALU.mult)
            ts(s(N), s(TH), 1.0 / TWO_PI, ALU.mult, ROUND, ALU.add)
            ts(s(N), s(N), ROUND, ALU.subtract)
            then(nc.vector.scalar_tensor_tensor(out=s(R), in0=s(N), scalar=-C1, in1=s(TH), op0=ALU.mult, op1=ALU.add))
            then(nc.vector.scalar_tensor_tensor(out=s(R), in0=s(N), scalar=-C2, in1=s(R), op0=ALU.mult, op1=ALU.add))
            then(nc.vector.scalar_tensor_tensor(out=s(R), in0=s(N), scalar=-C3, in1=s(R), op0=ALU.mult, op1=ALU.add))
            ts(s(R), s(R), PI, ALU.min, -PI, ALU.max)
            ts(s(N), s(R), -1.0, ALU.mult)
            tt(s(N), s(N), s(R), ALU.max)
            ts(s(N), s(N), -1.0, ALU.mult, HPI, ALU.add)
            dve.sem_inc(for_act, 1)
            dve.wait_ge(act_done, 4)
            tt(pw[:, 0, 1, :], s(MAG), s(COS), ALU.mult)
            tt(pw[:, 1, 1, :], s(MAG), s(SIN), ALU.mult)
            then(nc.vector.memset(pw[:, 0, 0, :], 1.0))
            then(nc.vector.memset(pw[:, 1, 0, :], 0.0))
            tt(s(DEN), are[:, :], are[:, :], ALU.mult)
            tt(s(T), aim[:, :], aim[:, :], ALU.mult)
            tt(s(DEN), s(DEN), s(T), ALU.add)
            then(nc.vector.reciprocal(s(DEN), s(DEN)))
            ts(s(X), pw[:, 0, 1, :], 1.0, ALU.subtract)
            tt(s(QR), s(X), are[:, :], ALU.mult)
            tt(s(T), pw[:, 1, 1, :], aim[:, :], ALU.mult)
            tt(s(QR), s(QR), s(T), ALU.add)
            tt(s(QR), s(QR), s(DEN), ALU.mult)
            tt(s(QI), pw[:, 1, 1, :], are[:, :], ALU.mult)
            tt(s(T), s(X), aim[:, :], ALU.mult)
            tt(s(QI), s(QI), s(T), ALU.subtract)
            tt(s(QI), s(QI), s(DEN), ALU.mult)
            for have in (1, 2, 4):
                by = [over(pw[:, ri, have:have + 1, :], (P, have, QP)) for ri in range(2)]
                complex_product([pw[:, ri, have + 1:2 * have + 1, :] for ri in range(2)],
                                [pw[:, ri, 1:have + 1, :] for ri in range(2)], by,
                                tmp[:, 0:have * QP].rearrange("p (a b) -> p a b", a=have))
            for ri in range(2):
                then(nc.vector.tensor_copy(a8[:, ri, :], pw[:, ri, T8, :]))
                for j in range(T8):
                    then(nc.vector.tensor_copy(rev[:, ri, j, :], pw[:, ri, T8 - 1 - j, :]))
            dve.wait_ge(bld, 64)
            shape = (P, QP, H1)
            complex_product([bb[:, ri, :, :] for ri in range(2)], [over(s(x)[:, :, None], shape) for x in (QR, QI)],
                            [bin_[:, ri, :, :] for ri in range(2)],
                            tmp[:, 0:QP * H1].rearrange("p (a b) -> p a b", a=QP))
            shape = (P, QP, T8, H1)
            complex_product([w[:, ri, :, :, :] for ri in range(2)],
                            [over(rev[:, ri, :, :].rearrange("p j q -> p q j")[:, :, :, None], shape) for ri in range(2)],
                            [over(bb[:, ri, :, None, :], shape) for ri in range(2)],
                            tmp[:, 0:QP * T8 * H1].rearrange("p (a b c) -> p a b c", a=QP, b=T8))
            dve.sem_inc(w_ready, 1)
            for ri in range(2):
                dve.wait_ge(c_turned, ri + 1)
                for r in range(4):
                    for g in range(2):
                        half = slice(S1 * g, S1 * g + S1)
                        then(nc.vector.tensor_copy(
                            cc[half, ri, 4 * r:4 * r + 4, :],
                            pst[ri][half, r, :].rearrange("p (q g h) -> p q g h", g=2, h=H1)[:, :, g, :]))
            dve.sem_inc(pe_free, 1)
            shape = (P, QP, T8 + 1, H1)
            complex_product([q[:, ri, :, :, :] for ri in range(2)],
                            [over(pw[:, ri, :, :].rearrange("p t q -> p q t")[:, :, :, None], shape) for ri in range(2)],
                            [over(cc[:, ri, :, None, :], shape) for ri in range(2)],
                            tmp[:, :].rearrange("p (a b c) -> p a b c", a=QP, b=T8 + 1), conj=True)
            dve.sem_inc(q_ready, 1)
            for n8 in range(8):
                ri, r = n8 // 4, n8 % 4
                dve.wait_ge(w_turned, n8 + 1)
                then(nc.vector.tensor_copy(vw[:, ri, 4 * r:4 * r + 4, :], pst[2 + n8 % 2][:, :, :]))
                dve.sem_inc(pe_free, 1)
            dve.wait_ge(k_pad, 1)
            for r in range(8):
                dve.wait_ge(k_made, r + 1)
                g = group_in(r, 0)
                then(nc.vector.tensor_copy(kp[:, g:g + 7:2, 7 * H1:], psk[r % 4][:, :, :]))
                dve.sem_inc(pe_free, 1)
            dve.sem_inc(k_ready, 1)
            dve.wait_ge(t_loaded, 16 * T8)
            dve.wait_ge(dld, 16 * T8)
            diag = tmp[:, 0:8 * P].rearrange("p (g x) -> p g x", g=8)
            for r in range(4):
                gs = slice(8 * r, 8 * r + 8)
                tt(diag, over(ident[:, None, :], (P, 8, P)), over(dcol[:, gs, None], (P, 8, P)), ALU.mult)
                tt(toeplitz[:, gs, :], toeplitz[:, gs, :], diag, ALU.add)

        @block.tensor
        def _(pe):
            pe.wait_ge(cld, 64)
            for ri in range(2):
                for r in range(4):
                    t = nc.tensor.transpose(pst[ri][:, r, :], crow[:, ri, r, :, :].rearrange("p a b -> p (a b)"), ident[:, :])
                t.then_inc(c_turned, 1)
            pe.wait_ge(w_ready, 1)
            for n8 in range(8):
                ri, r = n8 // 4, n8 % 4
                if n8 >= 2:
                    pe.wait_ge(pe_free, n8)
                for x in range(4):
                    t = nc.tensor.transpose(pst[2 + n8 % 2][:, x, :],
                                            w[:, ri, 4 * r + x, :, :].rearrange("p a b -> p (a b)"), ident[:, :])
                t.then_inc(w_turned, 1)
            pe.wait_ge(q_ready, 1)
            for r in range(8):
                if r >= 4:
                    pe.wait_ge(pe_free, 9 + r - 3)
                for x in range(4):
                    g = group_in(r, x)
                    half = slice(S1 * (g % 2), S1 * (g % 2) + S1)
                    for ri in range(2):
                        mm = nc.tensor.matmul(psk[r % 4][:, x, :], bb[half, ri, g // 2, :],
                                              q[half, ri, g // 2, 0:T8, :].rearrange("p a b -> p (a b)"),
                                              start=(ri == 0), stop=(ri == 1))
                mm.then_inc(k_made, 1)


def s5_inputs(nc, xn, w_u, uc, ident):
    with Mem(nc, "s5u") as m:
        w = m.sb("w", P, KD, SSM_W)
        u = m.sb("u", P, G1, T8, H1)
        slab = m.sb("slab", P, 2, KD, P)
        ps = [m.ps(f"ps{i}", P, NB) for i in range(2)]
        pst = [m.ps(f"pst{i}", P, 4, P) for i in range(2)]
        loaded, cut, proj, kept, turned, placed = (m.sem(n) for n in ("loaded", "cut", "proj", "kept", "turned", "placed"))
        block = m.block()
        N = T8 // 2

        @block.sync
        def _(sp):
            sp.dma_start(w[:, :, :], w_u.rearrange("(k p) c -> p k c", p=P)).then_inc(loaded, 16)

        @block.vector
        def _(dve):
            dve.sem_inc(cut, 2)
            for half in range(HALF):
                with dve.Fori(0, N) as i:
                    for b in range(2):
                        dve.wait_ge(proj, half * T8 + 2 * i + b + 1)
                        src = xn[:, :, half * P * T8:(half + 1) * P * T8].rearrange("p k (c j) -> p k j c", j=T8)
                        nc.vector.tensor_copy(slab[:, b, :, :], src[:, :, bass.ds(2 * i + b, 1), :]
                                              .rearrange("p k j c -> p k (j c)")).then_inc(cut, 1)
                for r in range(8):
                    dve.wait_ge(turned, half * 8 + r + 1)
                    nc.vector.tensor_copy(uc[:, 4 * r:4 * r + 4, half * P:(half + 1) * P], pst[r % 2][:, :, :])\
                      .then_inc(placed, 1)

        @block.scalar
        def _(act):
            act.sem_inc(kept, 2)
            for half in range(HALF):
                if half:
                    act.wait_ge(turned, 8 * half)
                with act.Fori(0, N) as i:
                    for b in range(2):
                        act.wait_ge(proj, half * T8 + 2 * i + b + 3)
                        nc.scalar.activation(u[:, :, bass.ds(2 * i + b, 1), :].rearrange("p g j h -> p g (j h)"),
                                             ps[b][:, :].rearrange("p (g h) -> p g h", h=H1), ACT.Copy).then_inc(kept, 1)

        @block.tensor
        def _(pe):
            pe.sem_inc(proj, 2)
            pe.wait_ge(loaded, 16)
            for half in range(HALF):
                with pe.Fori(0, N) as i:
                    for b in range(2):
                        pe.wait_ge(cut, half * T8 + 2 * i + b + 3)
                        pe.wait_ge(kept, half * T8 + 2 * i + b + 1)
                        for k in range(KD):
                            mm = nc.tensor.matmul(ps[b][:, :], slab[:, b, k, :], w[:, k, :], start=(k == 0), stop=(k == KD - 1))
                        mm.then_inc(proj, 1)
                pe.wait_ge(kept, (half + 1) * T8 + 2)
                for r in range(8):
                    n = half * 8 + r
                    if n >= 2:
                        pe.wait_ge(placed, n - 1)
                    for x in range(4):
                        g = 4 * r + x
                        t = nc.tensor.transpose(pst[r % 2][:, x, :], u[:, g, :, :].rearrange("p j h -> p (j h)"), ident[:, :])
                    t.then_inc(turned, 1)


def s5_scan(nc, uc, vw, a8, st):
    with Mem(nc, "s5s") as m:
        ps = [m.ps(f"ps{i}", P, 2, NC8) for i in range(4)]
        a128 = m.sb("a128", P, 2, QP)
        carry = m.sb("carry", P, 2, QP, NSB)
        t1 = m.sb("t1", P, 2, QP, NSB)
        t2 = m.sb("t2", P, 2, QP, NSB)
        made, kept, link, zero = (m.sem(n) for n in ("made", "kept", "link", "zero"))
        block = m.block()

        @block.tensor
        def _(pe):
            for r in range(QP):
                if r >= 4:
                    pe.wait_ge(kept, r - 3)
                for ri in range(2):
                    for g in range(2):
                        mm = nc.tensor.matmul(ps[r % 4][S1 * g:S1 * g + S1, ri, :], vw[:, ri, r, S1 * g:S1 * g + S1],
                                              uc[:, 2 * r + g, :], start=True, stop=True)
                mm.then_inc(made, 1)

        @block.scalar
        def _(act):
            for r in range(QP):
                act.wait_ge(made, r + 1)
                nc.scalar.activation(st[:, :, r, 1:NC8], ps[r % 4][:, :, 0:NC8 - 1], ACT.Copy).then_inc(kept, 1)

        @block.vector
        def _(dve):
            n = [0]

            def then(ins):
                n[0] += 1
                ins.then_inc(link, 1)
                dve.wait_ge(link, n[0])

            def times(o, s, a, shape):
                x1, x2 = ([t[:, ri, :, 0:shape[2]] for ri in range(2)] for t in (t1, t2))
                for ri in range(2):
                    then(nc.vector.tensor_tensor(x1[ri], s[ri], over(a[:, 0, :, None], shape), ALU.mult))
                    then(nc.vector.tensor_tensor(x2[ri], s[ri], over(a[:, 1, :, None], shape), ALU.mult))
                then(nc.vector.tensor_tensor(o[0], x1[0], x2[1], ALU.subtract))
                then(nc.vector.tensor_tensor(o[1], x1[1], x2[0], ALU.add))

            then(nc.vector.memset(st[:, :, :, 0:1], 0.0))
            dve.wait_ge(kept, QP)
            blocks = [st[:, ri, :, :].rearrange("p q (b k) -> p q b k", k=SB) for ri in range(2)]
            shape = (P, QP, NSB)
            then(nc.vector.tensor_copy(a128[:, :, :], a8[:, :, :]))
            for _i in range(int(math.log2(SB))):
                x = [a128[:, ri, :] for ri in range(2)]
                then(nc.vector.tensor_tensor(t1[:, 0, :, 0], x[0], x[0], ALU.mult))
                then(nc.vector.tensor_tensor(t1[:, 1, :, 0], x[1], x[1], ALU.mult))
                then(nc.vector.tensor_tensor(t2[:, 0, :, 0], x[0], x[1], ALU.mult))
                then(nc.vector.tensor_tensor(x[0], t1[:, 0, :, 0], t1[:, 1, :, 0], ALU.subtract))
                then(nc.vector.tensor_scalar(x[1], t2[:, 0, :, 0], 2.0, None, ALU.mult))
            for k in range(1, SB):
                times([carry[:, ri, :, :] for ri in range(2)], [b[:, :, :, k - 1] for b in blocks], a8, shape)
                for ri in range(2):
                    then(nc.vector.tensor_tensor(blocks[ri][:, :, :, k], blocks[ri][:, :, :, k], carry[:, ri, :, :], ALU.add))
            for b in range(1, NSB):
                times([carry[:, ri, :, 0:1] for ri in range(2)], [x[:, :, b - 1:b, SB - 1] for x in blocks], a128, (P, QP, 1))
                for ri in range(2):
                    end = blocks[ri][:, :, b:b + 1, SB - 1]
                    then(nc.vector.tensor_tensor(end, end, carry[:, ri, :, 0:1], ALU.add))
            shape = (P, QP, NSB - 1)
            now = [carry[:, ri, :, 0:NSB - 1] for ri in range(2)]
            for k in range(SB - 1):
                times(now, [x[:, :, 0:NSB - 1, SB - 1] for x in blocks] if k == 0 else now, a8, shape)
                for ri in range(2):
                    to = blocks[ri][:, :, 1:NSB, k]
                    then(nc.vector.tensor_tensor(to, to, now[ri], ALU.add))


def s5_outputs(nc, uc, st, q, toeplitz, yt, ident):
    with Mem(nc, "s5y") as m:
        y = m.sb("y", P, T8, SSM_W)
        ps = [m.ps(f"ps{i}", P, 4, P) for i in range(2)]
        pst = [m.ps(f"pst{i}", P, 4, P) for i in range(2)]
        made, kept, turned, placed = (m.sem(n) for n in ("made", "kept", "turned", "placed"))
        block = m.block()

        @block.tensor
        def _(pe):
            for half in range(HALF):
                cs = slice(half * P, (half + 1) * P)
                for r in range(8):
                    n = half * 8 + r
                    if n >= 2:
                        pe.wait_ge(kept, n - 1)
                    for x in range(4):
                        g = group_in(r, x)
                        part = slice(S1 * (g % 2), S1 * (g % 2) + S1)
                        nc.tensor.matmul(ps[r % 2][:, x, :], uc[:, g, cs], toeplitz[:, g, :], start=True, stop=False)
                        for ri in range(2):
                            mm = nc.tensor.matmul(ps[r % 2][:, x, :], st[part, ri, g // 2, cs],
                                                  q[part, ri, g // 2, 1:, :].rearrange("p a b -> p (a b)"),
                                                  start=False, stop=(ri == 1))
                    mm.then_inc(made, 1)
                pe.wait_ge(kept, 8 * (half + 1))
                for j in range(T8):
                    n = half * T8 + j
                    if n >= 2:
                        pe.wait_ge(placed, n - 1)
                    for t in range(4):
                        tr = nc.tensor.transpose(pst[j % 2][:, t, :], y[:, j, t * P:(t + 1) * P], ident[:, :])
                    tr.then_inc(turned, 1)

        @block.scalar
        def _(act):
            nc.scalar.preload_act_table(ACT.Gelu_apprx_tanh)
            for half in range(HALF):
                if half:
                    act.wait_ge(turned, T8 * half)
                for r in range(8):
                    act.wait_ge(made, half * 8 + r + 1)
                    for x in range(4):
                        g = group_in(r, x)
                        a = nc.scalar.activation(y[:, :, g * H1:(g + 1) * H1],
                                                 ps[r % 2][:, x, :].rearrange("p (i h) -> p i h", h=H1), ACT.Gelu_apprx_tanh)
                    a.then_inc(kept, 1)

        @block.vector
        def _(dve):
            for half in range(HALF):
                to = yt[:, :, half * P * T8:(half + 1) * P * T8].rearrange("p t (c j) -> p t j c", j=T8)
                for j in range(T8):
                    dve.wait_ge(turned, half * T8 + j + 1)
                    nc.vector.tensor_copy(to[:, :, j, :], pst[j % 2][:, :, :]).then_inc(placed, 1)


def s5_gate(nc, yt, w_glu, b_glu, silu_z, out_t):
    KS = SSM_W // P
    with Mem(nc, "glu") as m:
        w = m.sb("w", P, KS, SSM_W)
        bias = m.sb("bias", P, KS)
        z = m.sb("z", P, 2, L)
        o = m.sb("o", P, 2, L)
        sg = m.sb("sg", P, 2, NB)
        ps = [m.ps(f"ps{i}", P, NB) for i in range(2)]
        loaded, biased = m.sem("loaded"), m.sem("biased")
        z_in = [m.sem(f"z_in{i}") for i in range(2)]
        stored = [m.sem(f"stored{i}") for i in range(2)]
        proj, gated, half_done, done = (m.sem(n) for n in ("proj", "gated", "half_done", "done"))
        block = m.block()

        @block.sync
        def _(sp):
            sp.dma_start(w[:, :, :], w_glu.rearrange("(k p) c -> p k c", p=P)).then_inc(loaded, 16)
            sp.dma_start(bias[:, :], columns(b_glu, KS), allow_slow_non_contiguous=True).then_inc(biased, 16)
            for e in range(KS):
                if e >= 2:
                    sp.wait_ge(done, LB * (e - 1))
                sp.dma_start(z[:, e % 2, :], silu_z[e, :, :]).then_inc(z_in[e % 2], 16)
            for e in range(KS):
                sp.wait_ge(done, LB * (e + 1))
                sp.dma_start(out_t[e, :, :], o[:, e % 2, :]).then_inc(stored[e % 2], 16)
            for b in range(2):
                sp.wait_ge(stored[b], 16 * KS // 2)

        @block.tensor
        def _(pe):
            pe.wait_ge(loaded, 16)
            for e in range(KS):
                for n in range(LB):
                    t = e * LB + n
                    if t >= 2:
                        pe.wait_ge(gated, t - 1)
                    for k in range(KS):
                        mm = nc.tensor.matmul(ps[n % 2][:, :], w[:, k, e * P:(e + 1) * P], yt[:, k, n * NB:(n + 1) * NB],
                                              start=(k == 0), stop=(k == KS - 1))
                    mm.then_inc(proj, 1)

        @block.scalar
        def _(act):
            act.wait_ge(biased, 16)
            for e in range(KS):
                for n in range(LB):
                    t = e * LB + n
                    act.wait_ge(proj, t + 1)
                    if t >= 2:
                        act.wait_ge(done, t - 1)
                    nc.scalar.activation(sg[:, n % 2, :], ps[n % 2][:, :], ACT.Sigmoid, bias=bias[:, e:e + 1]).then_inc(gated, 1)

        @block.vector
        def _(dve):
            for e in range(KS):
                dve.wait_ge(z_in[e % 2], 16 * (e // 2 + 1))
                if e >= 2:
                    dve.wait_ge(stored[e % 2], 16 * (e // 2))
                for n in range(LB):
                    t = e * LB + n
                    cols = slice(n * NB, (n + 1) * NB)
                    dve.wait_ge(gated, t + 1)
                    nc.vector.tensor_tensor(o[:, e % 2, cols], sg[:, n % 2, :], yt[:, e, cols], ALU.mult).then_inc(half_done, 1)
                    dve.wait_ge(half_done, t + 1)
                    nc.vector.tensor_tensor(o[:, e % 2, cols], o[:, e % 2, cols], z[:, e % 2, cols], ALU.mult).then_inc(done, 1)


def output_rows_1(nc, y_t, w_out, x, gain, x2):
    with Mem(nc, "or1") as m:
        w = m.sb("w", P, KD, D)
        g = m.sb("g", P, D)
        y = m.sb("y", P, 2, KD, P)
        xr = m.sb("xr", P, 2, D)
        h = m.sb("h", P, 2, D)
        o = m.sb("o", P, 2, D)
        junk = m.sb("junk", P, D)
        stat = m.sb("stat", P, 2, 4)
        eps = m.sb("eps", P, 1)
        ps = [m.ps(f"ps{i}", P, D) for i in range(2)]
        w_in, eps_set = m.sem("w_in"), m.sem("eps_set")
        y_in = [m.sem(f"y_in{i}") for i in range(2)]
        x_in = [m.sem(f"x_in{i}") for i in range(2)]
        proj, added, squared, rooted, inverted, normed, stored, free = (
            m.sem(n) for n in ("proj", "added", "squared", "rooted", "inverted", "normed", "stored", "free"))
        block = m.block()
        rows_in = x.rearrange("(t p) d -> t p d", p=P)
        rows_out = x2.rearrange("(t p) d -> t p d", p=P)

        @block.sync
        def _(sp):
            sp.dma_start(w[:, :, :], w_out.rearrange("(k p) d -> p k d", p=P)).then_inc(w_in, 16)
            sp.dma_start(g[:, :], every_partition(gain)).then_inc(w_in, 16)
            with sp.Fori(0, TILES // 2) as i:
                for b in range(2):
                    t = 2 * i + b
                    sp.wait_ge(proj, t + 1)
                    sp.dma_start(y[:, b, :, :], y_t[:, :, bass.ds(t * P, P)].rearrange("k p l -> p k l")).then_inc(y_in[b], 16)
                    sp.wait_ge(added, t + 1)
                    sp.dma_start(xr[:, b, :], rows_in[bass.ds(t, 1), :, :].rearrange("t p d -> p (t d)")).then_inc(x_in[b], 16)

        @block.tensor
        def _(pe):
            pe.sem_inc(proj, 2)
            pe.wait_ge(w_in, 32)
            with pe.Fori(0, TILES // 2) as i:
                for b in range(2):
                    pe.wait_ge(y_in[b], 16 * i + 16)
                    pe.wait_ge(added, 2 * i + b + 1)
                    for n in range(2):
                        for k in range(KD):
                            mm = nc.tensor.matmul(ps[b][:, n * NB:(n + 1) * NB], y[:, b, k, :], w[:, k, n * NB:(n + 1) * NB],
                                                  start=(k == 0), stop=(k == KD - 1))
                    mm.then_inc(proj, 1)

        @block.scalar
        def _(act):
            act.wait_ge(eps_set, 1)
            nc.scalar.preload_act_table(ACT.Sqrt)
            with act.Fori(0, TILES // 2) as i:
                for b in range(2):
                    t = 2 * i + b
                    act.wait_ge(added, t + 3)
                    nc.scalar.activation(junk[:, :], h[:, b, :], ACT.Square, accum_out=stat[:, b, 0:1]).then_inc(squared, 1)
                    act.wait_ge(squared, t + 1)
                    nc.scalar.activation(stat[:, b, 1:2], stat[:, b, 0:1], ACT.Sqrt, scale=1.0 / D, bias=eps[:, :])\
                      .then_inc(rooted, 1)

        @block.vector
        def _(dve):
            nc.vector.memset(eps[:, :], EPS).then_inc(eps_set, 1)
            dve.sem_inc(added, 2)
            with dve.Fori(0, TILES // 2) as i:
                for b in range(2):
                    t = 2 * i + b
                    dve.wait_ge(x_in[b], 16 * i + 16)
                    dve.wait_ge(proj, t + 3)
                    nc.vector.tensor_tensor(h[:, b, :], ps[b][:, :], xr[:, b, :], ALU.add).then_inc(added, 1)
                    dve.wait_ge(rooted, t + 1)
                    nc.vector.reciprocal(stat[:, b, 2:3], stat[:, b, 1:2]).then_inc(inverted, 1)
                    dve.wait_ge(inverted, t + 1)
                    dve.wait_ge(free, t + 1)
                    nc.vector.scalar_tensor_tensor(out=o[:, b, :], in0=h[:, b, :], scalar=stat[:, b, 2:3], in1=g[:, :],
                                                   op0=ALU.mult, op1=ALU.mult).then_inc(normed, 1)

        @block.gpsimd
        def _(pool):
            pool.sem_inc(free, 2)
            with pool.Fori(0, TILES // 2) as i:
                for b in range(2):
                    t = 2 * i + b
                    pool.wait_ge(normed, t + 1)
                    pool.dma_start(rows_out[bass.ds(t, 1), :, :].rearrange("t p d -> p (t d)"), o[:, b, :]).then_inc(stored, 16)
                    pool.wait_ge(stored, 16 * t + 16)
                    pool.sem_inc(free, 1)


def modulations(nc, c, c_ctx, w_ada, b_ada, mod):
    NM = 6 * D
    with Mem(nc, "ada") as m:
        w = m.sb("w", P, 2, KD, NB)
        cc = m.sb("cc", P, KD, 2)
        sg = m.sb("sg", P, KD, 2)
        row = m.sb("row", 2, NM)
        bias = m.sb("bias", 2, NM)
        ps = [m.ps(f"ps{i}", 2, NB) for i in range(2)]
        c_in, b_in, gated, ready = (m.sem(n) for n in ("c_in", "b_in", "gated", "ready"))
        loaded = [m.sem(f"loaded{i}") for i in range(2)]
        proj, added, stored = m.sem("proj"), m.sem("added"), m.sem("stored")
        block = m.block()
        wv = w_ada.rearrange("(k p) n -> p k n", p=P)

        @block.sync
        def _(sp):
            for j, v in enumerate((c, c_ctx)):
                sp.dma_start(cc[:, :, j], columns(v, KD), allow_slow_non_contiguous=True).then_inc(c_in, 16)
            sp.dma_start(bias[:, :], every_partition(b_ada, 2)).then_inc(b_in, 16)
            with sp.Fori(0, NM // NB // 2) as i:
                for b in range(2):
                    sp.wait_ge(proj, 2 * i + b + 1)
                    sp.dma_start(w[:, b, :, :], wv[:, :, bass.ds((2 * i + b) * NB, NB)]).then_inc(loaded[b], 16)
            sp.wait_ge(added, NM // NB + 2)
            sp.dma_start(mod, row[:, :]).then_inc(stored, 16)
            sp.wait_ge(stored, 16)

        @block.scalar
        def _(act):
            act.wait_ge(c_in, 32)
            nc.scalar.activation(sg[:, :, :], cc[:, :, :], ACT.Sigmoid).then_inc(gated, 1)

        @block.vector
        def _(dve):
            dve.wait_ge(gated, 1)
            nc.vector.tensor_tensor(cc[:, :, :], cc[:, :, :], sg[:, :, :], ALU.mult).then_inc(ready, 1)
            dve.wait_ge(b_in, 16)
            dve.sem_inc(added, 2)
            with dve.Fori(0, NM // NB // 2) as i:
                for b in range(2):
                    dve.wait_ge(proj, 2 * i + b + 3)
                    cols = bass.ds((2 * i + b) * NB, NB)
                    nc.vector.tensor_tensor(row[:, cols], ps[b][:, :], bias[:, cols], ALU.add).then_inc(added, 1)

        @block.tensor
        def _(pe):
            pe.sem_inc(proj, 2)
            pe.wait_ge(ready, 1)
            with pe.Fori(0, NM // NB // 2) as i:
                for b in range(2):
                    pe.wait_ge(loaded[b], 16 * i + 16)
                    pe.wait_ge(added, 2 * i + b + 1)
                    for k in range(KD):
                        mm = nc.tensor.matmul(ps[b][:, :], cc[:, k, :], w[:, b, k, :], start=(k == 0), stop=(k == KD - 1))
                    mm.then_inc(proj, 1)


def convolved_projection(nc, h_t, w, conv_w, conv_b, xbc):
    with Mem(nc, "cp") as m:
        wt = m.sb("wt", P, 2, KD, P)
        taps = m.sb("taps", P, XT_, KC)
        bias = m.sb("bias", P, XT_)
        rows, half = L // ROWLEN, KC // 2
        pitch = ROWLEN + 2 * half
        XP = rows * pitch
        CP = LC + 2 * half
        pad = m.sb("pad", P, 2, XP + CP)
        acc = m.sb("acc", P, 2, LT)
        y = m.sb("y", P, 2, LT)
        blocks = [(n * NB, NB) for n in range(LB)] + [(L, LC)]
        ps = [m.ps(f"ps{n}", P, NB) for n in range(len(blocks))]
        taps_in, padded = m.sem("taps_in"), m.sem("padded")
        loaded = [m.sem(f"loaded{i}") for i in range(2)]
        proj, kept, tap, silu, stored, free = (m.sem(n) for n in ("proj", "kept", "tap", "silu", "stored", "free"))
        block = m.block()
        wv = w.rearrange("(k p) c -> p k c", p=P)
        NBL = len(blocks)

        @block.sync
        def _(sp):
            sp.dma_start(taps[:, :, :], conv_w.rearrange("(t p) k -> p t k", p=P)).then_inc(taps_in, 16)
            sp.dma_start(bias[:, :], columns(conv_b, XT_), allow_slow_non_contiguous=True).then_inc(taps_in, 16)
            with sp.Fori(0, XT_ // 2) as i:
                for b in range(2):
                    sp.wait_ge(proj, (2 * i + b + 1) * NBL)
                    sp.dma_start(wt[:, b, :, :], wv[:, :, bass.ds((2 * i + b) * P, P)]).then_inc(loaded[b], 16)

        @block.tensor
        def _(pe):
            pe.sem_inc(proj, 2 * NBL)
            with pe.Fori(0, XT_ // 2) as i:
                for b in range(2):
                    pe.wait_ge(loaded[b], 16 * i + 16)
                    for n, (at, size) in enumerate(blocks):
                        pe.wait_ge(kept, (2 * i + b) * NBL + n + 1)
                        for k in range(KD):
                            mm = nc.tensor.matmul(ps[n][:, 0:size], wt[:, b, k, :], h_t[:, k, at:at + size],
                                                  start=(k == 0), stop=(k == KD - 1))
                        mm.then_inc(proj, 1)

        @block.scalar
        def _(act):
            nc.scalar.preload_act_table(ACT.Silu)
            act.wait_ge(padded, 1)
            act.sem_inc(kept, NBL)
            act.sem_inc(silu, 2)

            def activate(t, b):
                act.wait_ge(tap, 2 * KC * (t + 1) + 2)
                act.wait_ge(free, t + 1)
                nc.scalar.activation(y[:, b, :], acc[:, b, :], ACT.Silu).then_inc(silu, 1)

            with act.Fori(0, XT_ // 2) as i:
                for b in range(2):
                    t = 2 * i + b
                    act.wait_ge(silu, t + 1)
                    for n, (at, size) in enumerate(blocks):
                        act.wait_ge(proj, t * NBL + n + 2 * NBL + 1)
                        if n < LB:
                            r = NB // ROWLEN
                            to = pad[:, b, n * r * pitch:(n + 1) * r * pitch].rearrange("p (r c) -> p r c", c=pitch)
                            nc.scalar.activation(to[:, :, half:half + ROWLEN], ps[n][:, :].rearrange("p (r c) -> p r c", c=ROWLEN),
                                                 ACT.Copy).then_inc(kept, 1)
                        else:
                            nc.scalar.activation(pad[:, b, XP + half:XP + half + LC], ps[n][:, 0:LC], ACT.Copy).then_inc(kept, 1)
                    activate(t, b)

        @block.vector
        def _(dve):
            nc.vector.memset(pad[:, :, :], 0.0).then_inc(padded, 1)
            dve.wait_ge(taps_in, 32)
            dve.sem_inc(tap, 2)
            with dve.Fori(0, XT_ // 2) as i:
                for b in range(2):
                    t = 2 * i + b
                    grid = pad[:, b, 0:XP].rearrange("p (r c) -> p r c", c=pitch)
                    parts = [(acc[:, b, 0:L].rearrange("p (r c) -> p r c", c=ROWLEN), lambda k: grid[:, :, k:k + ROWLEN]),
                             (acc[:, b, L:LT], lambda k: pad[:, b, XP + k:XP + k + LC])]
                    dve.wait_ge(kept, (t + 2) * NBL)
                    dve.wait_ge(silu, t + 1)
                    for k in range(KC):
                        for x, (to, src) in enumerate(parts):
                            one = taps[:, bass.ds(t, 1), k]
                            if k == 0:
                                nc.vector.tensor_scalar(to, src(0), one, bias[:, bass.ds(t, 1)], ALU.mult, ALU.add).then_inc(tap, 1)
                            else:
                                dve.wait_ge(tap, 2 * KC * t + 2 * (k - 1) + x + 3)
                                nc.vector.scalar_tensor_tensor(out=to, in0=src(k), scalar=one, in1=to, op0=ALU.mult,
                                                               op1=ALU.add).then_inc(tap, 1)

        @block.gpsimd
        def _(pool):
            pool.sem_inc(free, 2)
            with pool.Fori(0, XT_ // 2) as i:
                for b in range(2):
                    t = 2 * i + b
                    pool.wait_ge(silu, t + 3)
                    pool.dma_start(xbc[bass.ds(t, 1), :, :].rearrange("k p l -> p (k l)"), y[:, b, :]).then_inc(stored, 16)
                    pool.wait_ge(stored, 16 * t + 16)
                    pool.sem_inc(free, 1)


def decays(nc, h_t, w_dt, dt_bias, a_log, decay_rows, totals, decay_cols, ident):
    R2 = 64
    CH = LT // P
    with Mem(nc, "dec") as m:
        w = m.sb("w", P, KD, R2)
        bias, al = m.sb("bias", R2, 1), m.sb("al", R2, 1)
        v, n_, e, z, a, reset = (m.sb(n, R2, LT) for n in ("v", "n", "e", "z", "a", "reset"))
        dt_, wgt = m.sb("dt", R2, LT), m.sb("wgt", R2, LT)
        tot, etot = m.sb("tot", R2, CH), m.sb("etot", R2, CH)
        cols = m.sb("cols", P, CH, 3, R2)
        blocks = [(n * NB, NB) for n in range(LB)] + [(L, LC)]
        ps = [m.ps(f"ps{n}", R2, NB) for n in range(len(blocks))]
        pst = [m.ps(f"pst{n}", P, 3, R2) for n in range(2)]
        zeroed, loaded, proj, kept, link, exped, ready, turned, placed, stored = (
            m.sem(n) for n in ("zeroed", "loaded", "proj", "kept", "link", "exped", "ready", "turned", "placed", "stored"))
        block = m.block()
        halves = (slice(0, HEADS), slice(32, 32 + HEADS))

        @block.sync
        def _(sp):
            sp.wait_ge(zeroed, 3)
            for x in range(2):
                sp.dma_start(w[:, :, halves[x]], w_dt[:, x * HEADS:(x + 1) * HEADS].rearrange("(k p) h -> p k h", p=P))\
                  .then_inc(loaded, 16)
                sp.dma_start(bias[halves[x], :], dt_bias[x].rearrange("(h o) -> h o", o=1)).then_inc(loaded, 16)
                sp.dma_start(al[halves[x], :], a_log[x].rearrange("(h o) -> h o", o=1)).then_inc(loaded, 16)
            sp.wait_ge(ready, 1)
            for x in range(2):
                hs = slice(x * HEADS, (x + 1) * HEADS)
                sp.dma_start(decay_rows[:, hs, :].rearrange("c h l -> h c l"),
                             a[halves[x], :].rearrange("h (c l) -> h c l", l=P)).then_inc(stored, 16)
            sp.wait_ge(exped, 5)
            for x in range(2):
                hs = slice(x * HEADS, (x + 1) * HEADS)
                sp.dma_start(totals[:, hs].rearrange("c h -> h c"), etot[halves[x], :], allow_slow_non_contiguous=True)\
                  .then_inc(stored, 16)
            sp.wait_ge(placed, CH)
            sp.dma_start(decay_cols.rearrange("c p x -> p c x"), cols[:, :, :, :].rearrange("p c a b -> p c (a b)"))\
              .then_inc(stored, 16)
            sp.wait_ge(stored, 80)

        @block.gpsimd
        def _(pool):
            nc.gpsimd.memset(w[:, :, :], 0.0).then_inc(zeroed, 1)
            nc.gpsimd.memset(bias[:, :], 0.0).then_inc(zeroed, 1)
            nc.gpsimd.memset(al[:, :], 0.0).then_inc(zeroed, 1)

        @block.tensor
        def _(pe):
            pe.wait_ge(loaded, 96)
            for n, (at, size) in enumerate(blocks):
                for k in range(KD):
                    mm = nc.tensor.matmul(ps[n][:, 0:size], w[:, k, :], h_t[:, k, at:at + size], start=(k == 0), stop=(k == KD - 1))
                mm.then_inc(proj, 1)
            pe.wait_ge(ready, 2)
            for c in range(CH):
                if c >= 2:
                    pe.wait_ge(placed, c - 1)
                for x, of in enumerate((dt_, a, wgt)):
                    t = nc.tensor.transpose(pst[c % 2][:, x, :], of[:, c * P:(c + 1) * P], ident[0:R2, 0:R2])
                t.then_inc(turned, 1)

        @block.scalar
        def _(act):
            act.wait_ge(loaded, 96)
            nc.scalar.activation(al[:, :], al[:, :], ACT.Exp).then_inc(exped, 1)
            act.wait_ge(kept, 1)
            nc.scalar.activation(e[:, :], n_[:, :], ACT.Exp).then_inc(exped, 1)
            act.wait_ge(kept, 2)
            nc.scalar.activation(wgt[:, :], wgt[:, :], ACT.Exp).then_inc(exped, 1)
            nc.scalar.activation(etot[:, :], tot[:, :], ACT.Exp).then_inc(exped, 2)

        @block.vector
        def _(dve):
            n = [0]

            def then(ins):
                n[0] += 1
                ins.then_inc(link, 1)
                dve.wait_ge(link, n[0])

            chunks = [t[:, :].rearrange("h (c l) -> h c l", l=P) for t in (a, wgt, dt_, z)]
            then(nc.vector.memset(reset[:, :], 1.0))
            then(nc.vector.memset(reset[:, 0:LT:P], 0.0))
            dve.wait_ge(loaded, 96)
            for k, (at, size) in enumerate(blocks):
                dve.wait_ge(proj, k + 1)
                then(nc.vector.tensor_scalar(v[:, at:at + size], ps[k][:, 0:size], bias[:, :], None, ALU.add))
            then(nc.vector.tensor_scalar(n_[:, :], v[:, :], -1.0, None, ALU.mult))
            then(nc.vector.tensor_tensor(n_[:, :], n_[:, :], v[:, :], ALU.min))
            dve.sem_inc(kept, 1)
            then(nc.vector.tensor_scalar(v[:, :], v[:, :], 0.0, None, ALU.max))
            dve.wait_ge(exped, 2)
            then(nc.vector.tensor_scalar(n_[:, :], e[:, :], 2.0, None, ALU.add))
            then(nc.vector.reciprocal(n_[:, :], n_[:, :]))
            then(nc.vector.tensor_tensor(z[:, :], e[:, :], n_[:, :], ALU.mult))
            then(nc.vector.tensor_tensor(n_[:, :], z[:, :], z[:, :], ALU.mult))
            then(nc.vector.tensor_scalar(e[:, :], n_[:, :], 1.0 / 15, None, ALU.mult))
            for k in range(13, 1, -2):
                then(nc.vector.scalar_tensor_tensor(out=e[:, :], in0=e[:, :], scalar=1.0 / k, in1=n_[:, :], op0=ALU.add, op1=ALU.mult))
            then(nc.vector.scalar_tensor_tensor(out=e[:, :], in0=e[:, :], scalar=1.0, in1=z[:, :], op0=ALU.add, op1=ALU.mult))
            then(nc.vector.scalar_tensor_tensor(out=dt_[:, :], in0=e[:, :], scalar=2.0, in1=v[:, :], op0=ALU.mult, op1=ALU.add))
            then(nc.vector.tensor_scalar(al[:, :], al[:, :], -1.0, None, ALU.mult))
            then(nc.vector.tensor_scalar(z[:, :], dt_[:, :], al[:, :], None, ALU.mult))
            then(nc.vector.tensor_tensor_scan(out=a[:, :], data0=reset[:, :], data1=z[:, :], initial=0.0, op0=ALU.mult, op1=ALU.add))
            then(nc.vector.tensor_copy(tot[:, :], a[:, P - 1:LT:P]))
            b = slice(32, R2)
            whole = over(tot[:, :, None], (R2, CH, P))
            then(nc.vector.tensor_tensor(chunks[0][b], whole[b], chunks[0][b], ALU.subtract))
            then(nc.vector.tensor_tensor(chunks[0][b], chunks[0][b], chunks[3][b], ALU.add))
            then(nc.vector.tensor_tensor(chunks[1], whole, chunks[0], ALU.subtract))
            dve.sem_inc(ready, 1)
            dve.sem_inc(kept, 1)
            dve.wait_ge(exped, 5)
            then(nc.vector.tensor_tensor(wgt[:, :], wgt[:, :], dt_[:, :], ALU.mult))
            dve.sem_inc(ready, 1)
            for c in range(CH):
                dve.wait_ge(turned, c + 1)
                nc.vector.tensor_copy(cols[:, c, :, :], pst[c % 2][:, :, :]).then_inc(placed, 1)


def turn_chunk(nc, xc, pst, tiles, ident):
    for k in range(tiles):
        t = nc.tensor.transpose(pst[:, k, :], xc[:, k, :], ident[:, :])
    return t


def chunk_states(nc, rows, xw, pss):
    XR = SW // P
    for g in range(SG):
        mm = nc.tensor.matmul(pss[:, g // 2, (g % 2) * HR * HD:(g % 2 + 1) * HR * HD], rows[:, XR + g, :],
                              xw[:, g * HR:(g + 1) * HR, :].rearrange("p h d -> p (h d)"), start=True, stop=True)
    return mm


def states_view(h):
    return h.rearrange("p (b x) d -> p b (x d)", b=2)


def context_states(nc, xbc, totals, decay_cols, hf, hb, ident):
    XR, TS = SW // P, SW // P + SG
    with Mem(nc, "cst") as m:
        xc = m.sb("xc", P, CCH, TS, P)
        dc = m.sb("dc", P, CCH, 3, 64)
        dec = m.sb("dec", P, LT // P, 2 * HEADS)
        rows = m.sb("rows", P, TS, P)
        xw = m.sb("xw", P, HEADS, HD)
        pst = m.ps("pst", P, 12, P)
        pss = m.ps("pss", P, 2, NB)
        loaded, turned, kept, weighted, made, link = (m.sem(n) for n in ("loaded", "turned", "kept", "weighted", "made", "link"))
        block = m.block()
        work = [(0, 0, hf, True), (0, 1, hb, True), (1, 0, hf, False), (1, 1, hb, False)]

        @block.sync
        def _(sp):
            for c in range(CCH):
                sp.dma_start(xc[:, c, :, :], xbc[0:TS, :, L + c * P:L + (c + 1) * P].rearrange("k p l -> p k l")).then_inc(loaded, 16)
                sp.dma_start(dc[:, c, :, :].rearrange("p a b -> p (a b)"), decay_cols[NCH + c, :, :]).then_inc(loaded, 16)
            sp.dma_start(dec[:, :, :].rearrange("p c h -> p (c h)"), every_partition(totals.rearrange("c h -> (c h)")))\
              .then_inc(loaded, 16)

        @block.tensor
        def _(pe):
            pe.wait_ge(loaded, 80)
            for c in range(CCH):
                if c:
                    pe.wait_ge(kept, c)
                turn_chunk(nc, xc[:, c, :, :], pst, TS, ident).then_inc(turned, 1)
                for x in range(2):
                    pe.wait_ge(weighted, 2 * c + x + 1)
                    chunk_states(nc, rows, xw, pss).then_inc(made, 1)

        @block.scalar
        def _(act):
            for c in range(CCH):
                act.wait_ge(turned, c + 1)
                if c:
                    act.wait_ge(made, 2 * c)
                nc.scalar.activation(rows[:, :, :], pst[:, 0:TS, :], ACT.Copy).then_inc(kept, 1)

        @block.vector
        def _(dve):
            n = [0]

            def then(ins):
                n[0] += 1
                ins.then_inc(link, 1)
                dve.wait_ge(link, n[0])

            dve.wait_ge(loaded, 80)
            for w, (c, x, h, first) in enumerate(work):
                dve.wait_ge(kept, c + 1)
                if w:
                    dve.wait_ge(made, w)
                nc.vector.tensor_tensor(xw[:, :, :], rows[:, 0:XR, :].rearrange("p k (h d) -> p (k h) d", d=HD),
                                        over(dc[:, c, 2, 32 * x:32 * x + HEADS, None], (P, HEADS, HD)), ALU.mult).then_inc(weighted, 1)
                dve.wait_ge(made, w + 1)
                sts = pss[:, :, 0:2 * HR * HD]
                if first:
                    then(nc.vector.tensor_copy(states_view(h), sts))
                elif x == 0:
                    then(nc.vector.tensor_tensor(h, h, over(dec[:, NCH + 1, 0:HEADS, None], (P, HEADS, HD)), ALU.mult))
                    then(nc.vector.tensor_tensor(states_view(h), states_view(h), sts, ALU.add))
                else:
                    t = xw[:, :, :]
                    then(nc.vector.tensor_copy(states_view(t), sts))
                    then(nc.vector.tensor_tensor(t, t, over(dec[:, NCH, HEADS:2 * HEADS, None], (P, HEADS, HD)), ALU.mult))
                    then(nc.vector.tensor_tensor(h, h, t, ALU.add))


def backward_states(nc, xbc, totals, decay_cols, hb, hb_in, ident):
    XR, TS = SW // P, SW // P + SG
    with Mem(nc, "bst") as m:
        xc = m.sb("xc", P, 2, TS, P)
        dc = m.sb("dc", P, 2, 3 * 64)
        dec = m.sb("dec", P, LT // P, 2 * HEADS)
        rows = m.sb("rows", P, 2, TS, P)
        xw = m.sb("xw", P, 2, HEADS, HD)
        h = m.sb("h", P, 2, HEADS, HD)
        pst = [m.ps(f"pst{i}", P, 12, P) for i in range(2)]
        pss = m.ps("pss", P, 2, NB)
        start, turned, kept, weighted, made, decayed, ahead, stored, free, begun = (
            m.sem(n) for n in ("start", "turned", "kept", "weighted", "made", "decayed", "ahead", "stored", "free", "begun"))
        loaded = [m.sem(f"loaded{i}") for i in range(2)]
        block = m.block()

        @block.sync
        def _(sp):
            sp.dma_start(dec[:, :, :].rearrange("p c h -> p (c h)"), every_partition(totals.rearrange("c h -> (c h)")))\
              .then_inc(start, 16)
            chunk = sp.alloc_register("back_sp")
            sp.reg_mov(chunk, NCH + 1)
            with sp.Fori(0, NCH // 2) as i:
                sp.reg_sub(chunk, chunk, 2)
                last = sp.snap(chunk, min_val=1, max_val=NCH - 1)
                for b in range(2):
                    t = 2 * i + b
                    sp.wait_ge(turned, t + 1)
                    sp.wait_ge(weighted, t + 1)
                    c = last - b
                    sp.dma_start(xc[:, b, :, :], xbc[0:TS, :, bass.ds(c * P, P)].rearrange("k p l -> p k l")).then_inc(loaded[b], 16)
                    sp.dma_start(dc[:, b, :], decay_cols[bass.ds(c, 1), :, :].rearrange("c p x -> p (c x)")).then_inc(loaded[b], 16)

        @block.tensor
        def _(pe):
            pe.sem_inc(turned, 2)
            pe.sem_inc(made, 2)
            with pe.Fori(0, NCH // 2) as i:
                for b in range(2):
                    t = 2 * i + b
                    pe.wait_ge(loaded[b], 32 * i + 32)
                    pe.wait_ge(kept, t + 1)
                    turn_chunk(nc, xc[:, b, :, :], pst[b], TS, ident).then_inc(turned, 1)
                    pe.wait_ge(weighted, t + 3)
                    pe.wait_ge(ahead, t + 1)
                    chunk_states(nc, rows[:, b, :, :], xw[:, b, :, :], pss).then_inc(made, 1)

        @block.scalar
        def _(act):
            act.sem_inc(kept, 2)
            with act.Fori(0, NCH // 2) as i:
                for b in range(2):
                    t = 2 * i + b
                    act.wait_ge(turned, t + 3)
                    act.wait_ge(made, t + 1)
                    nc.scalar.activation(rows[:, b, :, :], pst[b][:, 0:TS, :], ACT.Copy).then_inc(kept, 1)

        @block.vector
        def _(dve):
            dve.sem_inc(weighted, 2)
            dve.sem_inc(ahead, 1)
            dve.wait_ge(start, 16)
            nc.vector.tensor_copy(h[:, 0, :, :], hb[:, :, :]).then_inc(begun, 1)
            dve.wait_ge(begun, 1)
            chunk = dve.alloc_register("back_dve")
            dve.reg_mov(chunk, NCH + 1)
            with dve.Fori(0, NCH // 2) as i:
                dve.reg_sub(chunk, chunk, 2)
                last = dve.snap(chunk, min_val=1, max_val=NCH - 1)
                for b in range(2):
                    t = 2 * i + b
                    dve.wait_ge(kept, t + 3)
                    nc.vector.tensor_tensor(xw[:, b, :, :], rows[:, b, 0:XR, :].rearrange("p k (h d) -> p (k h) d", d=HD),
                                            over(dc[:, b, 128 + 32:128 + 32 + HEADS, None], (P, HEADS, HD)), ALU.mult)\
                      .then_inc(weighted, 1)
                    dve.wait_ge(free, t + 1)
                    nc.vector.tensor_tensor(h[:, 1 - b, :, :], h[:, b, :, :],
                                            over(dec[:, bass.ds(last - b, 1), HEADS:2 * HEADS].rearrange("p c h -> p (c h)")[:, :, None],
                                                 (P, HEADS, HD)), ALU.mult).then_inc(decayed, 1)
                    dve.wait_ge(decayed, t + 1)
                    dve.wait_ge(made, t + 3)
                    nc.vector.tensor_tensor(states_view(h[:, 1 - b, :, :]), states_view(h[:, 1 - b, :, :]),
                                            pss[:, :, 0:2 * HR * HD], ALU.add).then_inc(ahead, 1)
                    dve.wait_ge(ahead, t + 2)

        @block.gpsimd
        def _(pool):
            pool.sem_inc(free, 1)
            pool.wait_ge(begun, 1)
            chunk = pool.alloc_register("back_pool")
            pool.reg_mov(chunk, NCH + 1)
            with pool.Fori(0, NCH // 2) as i:
                pool.reg_sub(chunk, chunk, 2)
                last = pool.snap(chunk, min_val=1, max_val=NCH - 1)
                for b in range(2):
                    t = 2 * i + b
                    pool.wait_ge(ahead, t + 1)
                    pool.dma_start(hb_in[bass.ds(last - b, 1), :, :].rearrange("c p x -> p (c x)"),
                                   h[:, b, :, :].rearrange("p h d -> p (h d)")).then_inc(stored, 16)
                    pool.wait_ge(stored, 16 * t + 16)
                    pool.sem_inc(free, 1)


def ssd_outputs(nc, xbc, silu_z, decay_rows, totals, decay_cols, d_skip, hf, hb_in, y_t, ident, ones):
    XR = SW // P
    TS = XR + SG
    H2 = 2 * HEADS
    with Mem(nc, "so") as m:
        xc = m.sb("xc", P, 2, XT_, P)
        dc = m.sb("dc", P, 2, 3 * 64)
        decay = m.sb("decay", P, 2, H2, P)
        z = m.sb("z", P, 2, XR, P)
        hb = m.sb("hb", P, 2, HEADS, HD)
        h = m.sb("h", P, 2, HEADS, HD)
        dec = m.sb("dec", P, LT // P, H2)
        skip = m.sb("skip", P, XR)
        mask = m.sb("mask", P, 2, P)
        seg = m.sb("seg", P, H2, P)
        grown = m.sb("grown", P, H2, P)
        cs = m.sb("cs", P, H2, P)
        sm = m.sb("sm", P, 2, SG, P)
        mix = m.sb("mix", P, H2, P)
        rows = m.sb("rows", P, 2, TS, P)
        xw = m.sb("xw", P, HEADS, HD)
        y = m.sb("y", P, 2, XR, P)
        pst = m.ps("pst", P, 12, P)
        psc = m.ps("psc", P, SG, P)
        psy = m.ps("psy", P, 8, P)
        pss = m.ps("pss", P, 2, NB)
        start, masks, begun = m.sem("start"), m.sem("masks"), m.sem("begun")
        loaded = [m.sem(f"loaded{i}") for i in range(2)]
        stored = [m.sem(f"stored{i}") for i in range(2)]
        (turned, scored, made_s, made_y, kept, seg_exp, grown_s, seg_f, seg_b, weighted, masked, cs_f, cs_b, mixed, summed,
         skipped, gated, decayed, ahead, seg_free) = (m.sem(n) for n in (
            "turned", "scored", "made_s", "made_y", "kept", "seg_exp", "grown", "seg_f", "seg_b", "weighted", "masked", "cs_f",
            "cs_b", "mixed", "summed", "skipped", "gated", "decayed", "ahead", "seg_free"))
        block = m.block()
        A, DT, W = 64, 0, 128
        heads = [(x, hh, x * HEADS + hh) for x in range(2) for hh in range(HEADS)]

        def load(sp, c, b):
            at = bass.ds(c * P, P)
            one = bass.ds(c, 1)
            sp.dma_start(xc[:, b, :, :], xbc[:, :, at].rearrange("k p l -> p k l")).then_inc(loaded[b], 16)
            sp.dma_start(dc[:, b, :], decay_cols[one, :, :].rearrange("c p x -> p (c x)")).then_inc(loaded[b], 16)
            sp.dma_start(decay[:, b, :, :].rearrange("p h l -> p (h l)"),
                         decay_rows[one, :, :].rearrange("c h l -> (c h l)").partition_broadcast(P)).then_inc(loaded[b], 16)
            sp.dma_start(z[:, b, :, :], silu_z[:, :, at].rearrange("k p l -> p k l")).then_inc(loaded[b], 16)
            sp.dma_start(hb[:, b, :, :].rearrange("p h d -> p (h d)"), hb_in[one, :, :].rearrange("c p x -> p (c x)"))\
              .then_inc(loaded[b], 16)

        def store(sp, c, b):
            sp.dma_start(y_t[FW // P:, :, bass.ds(c * P, P)].rearrange("k p l -> p k l"), y[:, b, :, :]).then_inc(stored[b], 16)

        @block.sync
        def _(sp):
            sp.dma_start(dec[:, :, :].rearrange("p c h -> p (c h)"), every_partition(totals.rearrange("c h -> (c h)")))\
              .then_inc(start, 16)
            for g in range(2):
                sp.dma_start(skip[HD * g:HD * g + HD, :], d_skip[g::2].partition_broadcast(HD),
                             allow_slow_non_contiguous=True).then_inc(start, 16)
            for b in range(2):
                load(sp, b, b)
            with sp.Fori(0, NCH // 2 - 1) as i:
                for b in range(2):
                    sp.wait_ge(gated, 2 * i + b + 1)
                    store(sp, 2 * i + b, b)
                    load(sp, 2 * i + b + 2, b)
            for b in range(2):
                sp.wait_ge(gated, NCH - 2 + b + 1)
                store(sp, NCH - 2 + b, b)
            for b in range(2):
                sp.wait_ge(stored[b], 16 * (NCH // 2) + 16)

        @block.tensor
        def _(pe):
            with pe.Fori(0, NCH // 2) as i:
                for b in range(2):
                    t = 2 * i + b
                    pe.wait_ge(loaded[b], 80 * i + 80)
                    pe.wait_ge(kept, t + 1)
                    turn_chunk(nc, xc[:, b, :, :], pst, TS, ident).then_inc(turned, 1)
                    pe.wait_ge(masked, t + 1)
                    for g in range(SG):
                        mm = nc.tensor.matmul(psc[:, g, :], xc[:, b, XR + g, :], xc[:, b, TS + g, :], start=True, stop=True)
                    mm.then_inc(scored, 1)
                    pe.wait_ge(weighted, t + 1)
                    pe.wait_ge(ahead, t + 1)
                    chunk_states(nc, rows[:, b, :, :], xw, pss).then_inc(made_s, 1)
                    pe.wait_ge(cs_f, t + 1)
                    pe.wait_ge(cs_b, t + 1)
                    pe.wait_ge(summed, t + 1)
                    pe.wait_ge(skipped, t + 1)
                    for hh in range(HEADS):
                        to = psy[HD * (hh % 2):HD * (hh % 2) + HD, hh // 2, :]
                        x = rows[:, b, hh // 2, HD * (hh % 2):HD * (hh % 2) + HD]
                        nc.tensor.matmul(to, x, mix[:, hh, :], start=True, stop=False)
                        nc.tensor.matmul(to, h[:, b, hh, :], cs[:, hh, :], start=False, stop=False)
                        mm = nc.tensor.matmul(to, hb[:, b, hh, :], cs[:, HEADS + hh, :], start=False, stop=True)
                    mm.then_inc(made_y, 1)

        @block.scalar
        def _(act):
            nc.scalar.preload_act_table(ACT.Exp)
            act.sem_inc(kept, 1)
            with act.Fori(0, NCH // 2) as i:
                for b in range(2):
                    t = 2 * i + b
                    act.wait_ge(turned, t + 1)
                    act.wait_ge(made_y, t + 1)
                    nc.scalar.activation(rows[:, b, :, :], pst[:, 0:TS, :], ACT.Copy).then_inc(kept, 1)
                    act.wait_ge(seg_f, t + 1)
                    act.wait_ge(seg_b, t + 1)
                    nc.scalar.activation(seg[:, :, :], seg[:, :, :], ACT.Exp).then_inc(seg_exp, 1)
                    act.wait_ge(made_y, t + 2)
                    nc.scalar.activation(grown[:, :, :], decay[:, b, :, :], ACT.Exp).then_inc(grown_s, 1)

        @block.vector
        def _(dve):
            dve.wait_ge(start, 48)
            dve.sem_inc(masked, 1)
            dve.sem_inc(ahead, 1)
            dve.sem_inc(skipped, 1)
            for b in range(2):
                dve.sem_inc(stored[b], 16)
            dve.sem_inc(made_y, 2)
            nc.vector.tensor_copy(h[:, 0, :, :], hf[:, :, :]).then_inc(begun, 1)
            dve.wait_ge(begun, 1)
            dve.wait_ge(masks, 4)
            with dve.Fori(0, NCH // 2) as i:
                for b in range(2):
                    t = 2 * i + b
                    dve.wait_ge(loaded[b], 80 * i + 80)
                    for x, hh, n in heads[:HEADS]:
                        last = nc.vector.tensor_scalar(seg[:, n, :], decay[:, b, n, :], dc[:, b, A + 32 * x + hh:A + 32 * x + hh + 1],
                                                       0.0, ALU.subtract, ALU.min)
                    last.then_inc(seg_f, 1)
                    dve.wait_ge(scored, t + 1)
                    for x in range(2):
                        last = nc.vector.tensor_tensor(sm[:, x, :, :], psc[:, :, :], over(mask[:, x, None, :], (P, SG, P)), ALU.mult)
                    last.then_inc(masked, 1)
                    dve.wait_ge(kept, t + 2)
                    nc.vector.tensor_tensor(xw[:, :, :], rows[:, b, 0:XR, :].rearrange("p k (h d) -> p (k h) d", d=HD),
                                            over(dc[:, b, W:W + HEADS, None], (P, HEADS, HD)), ALU.mult).then_inc(weighted, 1)
                    dve.wait_ge(grown_s, t + 1)
                    nc.vector.tensor_tensor(cs[:, 0:HEADS, :].rearrange("p (g r) q -> p g r q", r=HR),
                                            grown[:, 0:HEADS, :].rearrange("p (g r) q -> p g r q", r=HR),
                                            over(xc[:, b, TS:, None, :], (P, SG, HR, P)), ALU.mult).then_inc(cs_f, 1)
                    dve.wait_ge(seg_exp, t + 1)
                    dve.wait_ge(masked, t + 2)
                    for x, hh, n in heads:
                        last = nc.vector.scalar_tensor_tensor(out=mix[:, n, :], in0=seg[:, n, :],
                                                              scalar=dc[:, b, DT + 32 * x + hh:DT + 32 * x + hh + 1],
                                                              in1=sm[:, x, hh // HR, :], op0=ALU.mult, op1=ALU.mult)
                    last.then_inc(mixed, 1)
                    nc.vector.tensor_tensor(h[:, 1 - b, :, :], h[:, b, :, :],
                                            over(dec[:, bass.ds(t, 1), 0:HEADS].rearrange("p c h -> p (c h)")[:, :, None],
                                                 (P, HEADS, HD)), ALU.mult).then_inc(decayed, 1)
                    dve.wait_ge(decayed, t + 1)
                    dve.wait_ge(made_s, t + 1)
                    nc.vector.tensor_tensor(states_view(h[:, 1 - b, :, :]), states_view(h[:, 1 - b, :, :]),
                                            pss[:, :, 0:2 * HR * HD], ALU.add).then_inc(ahead, 1)
                    dve.wait_ge(stored[b], 16 * i + 16)
                    dve.wait_ge(made_y, t + 3)
                    for k in range(XR):
                        last = nc.vector.scalar_tensor_tensor(out=y[:, b, k, :], in0=xc[:, b, k, :], scalar=skip[:, k:k + 1],
                                                              in1=psy[:, k, :], op0=ALU.mult, op1=ALU.add)
                    last.then_inc(skipped, 1)
                    dve.wait_ge(skipped, t + 2)
                    nc.vector.tensor_tensor(y[:, b, :, :], y[:, b, :, :], z[:, b, :, :], ALU.mult).then_inc(gated, 1)

        @block.gpsimd
        def _(pool):
            nc.gpsimd.memset(mask[:, :, :], 1.0).then_inc(masks, 1)
            pool.wait_ge(masks, 1)
            for x, sign in ((0, 1), (1, -1)):
                nc.gpsimd.affine_select(out=mask[:, x, :], in_=mask[:, x, :], compare_op=ALU.is_ge, fill=0.0, base=0,
                                        pattern=[[sign, P]], channel_multiplier=-sign).then_inc(masks, 1)
            pool.sem_inc(masks, 1)
            pool.wait_ge(masks, 4)
            with pool.Fori(0, NCH // 2) as i:
                for b in range(2):
                    t = 2 * i + b
                    pool.wait_ge(loaded[b], 80 * i + 80)
                    pool.wait_ge(made_y, t + 2)
                    pool.sem_inc(seg_free, 1)
                    for x, hh, n in heads[HEADS:]:
                        last = nc.gpsimd.tensor_scalar(seg[:, n, :], decay[:, b, n, :], dc[:, b, A + 32 * x + hh:A + 32 * x + hh + 1],
                                                       0.0, ALU.subtract, ALU.min)
                    last.then_inc(seg_b, 1)
                    pool.wait_ge(grown_s, t + 1)
                    nc.gpsimd.tensor_tensor(cs[:, HEADS:, :].rearrange("p (g r) q -> p g r q", r=HR),
                                            grown[:, HEADS:, :].rearrange("p (g r) q -> p g r q", r=HR),
                                            over(xc[:, b, TS:, None, :], (P, SG, HR, P)), ALU.mult).then_inc(cs_b, 1)
                    pool.wait_ge(mixed, t + 1)
                    nc.gpsimd.tensor_tensor(mix[:, 0:HEADS, :], mix[:, 0:HEADS, :], mix[:, HEADS:, :], ALU.add).then_inc(summed, 1)


def fourier_tables():
    B, A8 = L // P, 8
    kb = np.outer(np.arange(B), np.arange(B)) * (2 * np.pi / B)
    eye = np.eye(A8)
    over_b = np.stack([np.kron(np.cos(kb), eye), -np.kron(np.sin(kb), eye)], 1)
    kc = np.outer(np.arange(FG), np.arange(FG)) * (2 * np.pi / FG)
    two = np.eye(P // FG)
    c, s = np.kron(two, np.cos(kc)), np.kron(two, np.sin(kc))
    over_c = np.stack([np.concatenate([c, -s], 1), np.concatenate([s, c], 1)], 1)
    k = (B * np.arange(P)[None, :] + np.arange(B)[:, None]).reshape(-1)
    ka = (np.arange(P)[:, None] * k[None, :] % L) * (2 * np.pi / L)
    over_a = np.stack([np.cos(ka), np.sin(ka)], 1)
    return [np.ascontiguousarray(t, np.float32) for t in (over_b, over_c, over_a)]


def fourier_mix(nc, h_t, w_u, over_b, over_c, over_a, y_t):
    B, A8 = L // P, 8
    NA = P // A8
    FT2 = FW // P
    SCALE = 1.0 / math.sqrt(L * FG)
    with Mem(nc, "fo") as m:
        w = m.sb("w", P, KD, FW)
        tb = m.sb("tb", P, 2 * P)
        tc = m.sb("tc", P, 2, 2 * P)
        ta = m.sb("ta", P, 2, L)
        slab = m.sb("slab", P, 2, KD, P)
        u = m.sb("u", P, 2, FW)
        g = m.sb("g", P, FT2, 2 * B, P)
        gs = m.sb("gs", P, 2, FT2 * 2, P)
        hs = m.sb("hs", P, 2, FT2, 2, P)
        y = m.sb("y", P, FT2, L)
        psu = [m.ps(f"psu{i}", P, FW) for i in range(2)]
        psg = [m.ps(f"psg{i}", P, FT2, 2 * P) for i in range(2)]
        psh = [m.ps(f"psh{i}", P, FT2, 2 * P) for i in range(2)]
        psy = [m.ps(f"psy{i}", P, FT2, P) for i in range(2)]
        (loaded, cut, proj, kept_u, made_g, kept_g, cut_g, made_h, kept_h, made_y, kept_y, stored) = (m.sem(n) for n in (
            "loaded", "cut", "proj", "kept_u", "made_g", "kept_g", "cut_g", "made_h", "kept_h", "made_y", "kept_y", "stored"))
        block = m.block()

        @block.sync
        def _(sp):
            sp.dma_start(w[:, :, :], w_u.rearrange("(k p) c -> p k c", p=P)).then_inc(loaded, 16)
            sp.dma_start(tb[:, :], over_b.rearrange("p r c -> p (r c)")).then_inc(loaded, 16)
            sp.dma_start(tc[:, :, :], over_c).then_inc(loaded, 16)
            sp.dma_start(ta[:, :, :], over_a).then_inc(loaded, 16)
            sp.wait_ge(kept_y, B + 2)
            for k in range(FT2):
                sp.dma_start(y_t[k, :, :], y[:, k, :]).then_inc(stored, 16)
            sp.wait_ge(stored, 16 * FT2)

        @block.scalar
        def _(act):
            act.sem_inc(cut, 2)
            with act.Fori(0, NA // 2) as i:
                for b in range(2):
                    t = 2 * i + b
                    act.wait_ge(proj, t + 1)
                    src = h_t[:, :, 0:L].rearrange("p k (b a) -> p k b a", b=B)[:, :, :, bass.ds(t * A8, A8)]
                    nc.scalar.activation(slab[:, b, :, :].rearrange("p k (b a) -> p k b a", b=B), src, ACT.Copy).then_inc(cut, 1)
            act.wait_ge(kept_g, NA + 2)
            with act.Fori(0, B // 2) as i:
                for b in range(2):
                    t = 2 * i + b
                    act.wait_ge(made_h, t + 1)
                    nc.scalar.activation(gs[:, b, :, :].rearrange("p (t r) a -> p t r a", r=2),
                                         g[:, :, :, :].rearrange("p t (r k) a -> p t r k a", r=2)[:, :, :, bass.ds(t, 1), :]
                                         .rearrange("p t r k a -> p t r (k a)"), ACT.Copy).then_inc(cut_g, 1)

        @block.vector
        def _(dve):
            dve.sem_inc(kept_u, 2)
            dve.sem_inc(kept_g, 2)
            dve.sem_inc(kept_h, 2)
            dve.sem_inc(kept_y, 2)
            with dve.Fori(0, NA // 2) as i:
                for b in range(2):
                    t = 2 * i + b
                    dve.wait_ge(proj, t + 3)
                    nc.vector.tensor_copy(u[:, b, :], psu[b][:, :]).then_inc(kept_u, 1)
                    dve.wait_ge(made_g, t + 3)
                    nc.vector.tensor_copy(g[:, :, :, bass.ds(t * A8, A8)], psg[b][:, :, :].rearrange("p t (k a) -> p t k a", a=A8))\
                      .then_inc(kept_g, 1)
            with dve.Fori(0, B // 2) as i:
                for b in range(2):
                    t = 2 * i + b
                    dve.wait_ge(made_h, t + 3)
                    nc.vector.tensor_copy(hs[:, b, :, :, :].rearrange("p t r c -> p t (r c)"), psh[b][:, :, :]).then_inc(kept_h, 1)
                    dve.wait_ge(made_y, t + 1)
                    to = y[:, :, :].rearrange("p t (k1 k2) -> p t k1 k2", k2=B)[:, :, :, bass.ds(t, 1)].rearrange("p t a b -> p t (a b)")
                    nc.vector.tensor_scalar(to, psy[b][:, :, :], SCALE, None, ALU.mult).then_inc(kept_y, 1)

        @block.tensor
        def _(pe):
            pe.sem_inc(proj, 2)
            pe.sem_inc(made_g, 2)
            pe.sem_inc(made_h, 2)
            pe.wait_ge(loaded, 64)
            with pe.Fori(0, NA // 2) as i:
                for b in range(2):
                    t = 2 * i + b
                    pe.wait_ge(cut, t + 3)
                    pe.wait_ge(kept_u, t + 1)
                    for k in range(KD):
                        mm = nc.tensor.matmul(psu[b][:, :], slab[:, b, k, :], w[:, k, :], start=(k == 0), stop=(k == KD - 1))
                    mm.then_inc(proj, 1)
                    pe.wait_ge(kept_u, t + 3)
                    pe.wait_ge(kept_g, t + 1)
                    for x in range(FT2):
                        mm = nc.tensor.matmul(psg[b][:, x, :], u[:, b, x * P:(x + 1) * P], tb[:, :], start=True, stop=True)
                    mm.then_inc(made_g, 1)
            with pe.Fori(0, B // 2) as i:
                for b in range(2):
                    t = 2 * i + b
                    pe.wait_ge(cut_g, t + 1)
                    pe.wait_ge(kept_h, t + 1)
                    for x in range(FT2):
                        for ri in range(2):
                            mm = nc.tensor.matmul(psh[b][:, x, :], gs[:, b, 2 * x + ri, :], tc[:, ri, :], start=(ri == 0), stop=(ri == 1))
                    mm.then_inc(made_h, 1)
                    pe.wait_ge(kept_h, t + 3)
                    pe.wait_ge(kept_y, t + 1)
                    for x in range(FT2):
                        for ri in range(2):
                            mm = nc.tensor.matmul(psy[b][:, x, :], hs[:, b, x, ri, :], ta[:, ri, bass.ds(t * P, P)],
                                                  start=(ri == 0), stop=(ri == 1))
                    mm.then_inc(made_y, 1)


def output_rows_2(nc, y_t, w_out, g_ssd, g_post, gate, x2, x3, ones):
    KF = FW // P
    KS = SW // P
    with Mem(nc, "or2") as m:
        w = m.sb("w", P, KD, D)
        gs = m.sb("gs", P, KS)
        gg = m.sb("gg", P, 2, D)
        y = m.sb("y", P, 2, KD, P)
        sq = m.sb("sq", P, 2, KS, P)
        xr = m.sb("xr", P, 2, D)
        h = m.sb("h", P, 2, D)
        o = m.sb("o", P, 2, D)
        junk = m.sb("junk", P, D)
        stat = m.sb("stat", P, 2, 8)
        eps = m.sb("eps", P, 1)
        psf = m.ps("psf", P, D)
        pss = [m.ps(f"pss{i}", P, D) for i in range(2)]
        psq = [m.ps(f"psq{i}", P, 1) for i in range(2)]
        w_in, eps_set, scaled_w = m.sem("w_in"), m.sem("eps_set"), m.sem("scaled_w")
        y_in = [m.sem(f"y_in{i}") for i in range(2)]
        x_in = [m.sem(f"x_in{i}") for i in range(2)]
        (squared_y, summed, root_y, f_out, proj_f, proj, inv, mixed, squared, rooted, normed, added, stored, free) = (
            m.sem(n) for n in ("squared_y", "summed", "root_y", "f_out", "proj_f", "proj", "inv", "mixed", "squared", "rooted",
                               "normed", "added", "stored", "free"))
        block = m.block()
        rows_in = x2.rearrange("(t p) d -> t p d", p=P)
        rows_out = x3.rearrange("(t p) d -> t p d", p=P)

        @block.sync
        def _(sp):
            sp.dma_start(w[:, :, :], w_out.rearrange("(k p) d -> p k d", p=P)).then_inc(w_in, 16)
            sp.dma_start(gs[:, :], columns(g_ssd, KS), allow_slow_non_contiguous=True).then_inc(w_in, 16)
            sp.dma_start(gg[:, 0, :], every_partition(g_post)).then_inc(w_in, 16)
            sp.dma_start(gg[:, 1, :], every_partition(gate)).then_inc(w_in, 16)
            with sp.Fori(0, TILES // 2) as i:
                for b in range(2):
                    t = 2 * i + b
                    sp.wait_ge(proj, t + 1)
                    sp.dma_start(y[:, b, :, :], y_t[:, :, bass.ds(t * P, P)].rearrange("k p l -> p k l")).then_inc(y_in[b], 16)
                    sp.wait_ge(added, t + 1)
                    sp.dma_start(xr[:, b, :], rows_in[bass.ds(t, 1), :, :].rearrange("t p d -> p (t d)")).then_inc(x_in[b], 16)

        @block.tensor
        def _(pe):
            pe.sem_inc(proj, 2)
            pe.wait_ge(w_in, 64)
            pe.wait_ge(scaled_w, KS)
            with pe.Fori(0, TILES // 2) as i:
                for b in range(2):
                    t = 2 * i + b
                    pe.wait_ge(y_in[b], 16 * i + 16)
                    pe.wait_ge(f_out, t + 1)
                    for n in range(2):
                        for k in range(KF):
                            mm = nc.tensor.matmul(psf[:, n * NB:(n + 1) * NB], y[:, b, k, :], w[:, k, n * NB:(n + 1) * NB],
                                                  start=(k == 0), stop=(k == KF - 1))
                    mm.then_inc(proj_f, 1)
                    pe.wait_ge(squared_y, t + 1)
                    pe.wait_ge(mixed, t + 1)
                    for k in range(KS):
                        mm = nc.tensor.matmul(psq[b][:, :], sq[:, b, k, :], ones[:, 0:1], start=(k == 0), stop=(k == KS - 1))
                    mm.then_inc(summed, 1)
                    for n in range(2):
                        for k in range(KS):
                            mm = nc.tensor.matmul(pss[b][:, n * NB:(n + 1) * NB], y[:, b, KF + k, :],
                                                  w[:, KF + k, n * NB:(n + 1) * NB], start=(k == 0), stop=(k == KS - 1))
                    mm.then_inc(proj, 1)

        @block.scalar
        def _(act):
            act.wait_ge(eps_set, 1)
            nc.scalar.preload_act_table(ACT.Sqrt)
            act.sem_inc(f_out, 1)
            with act.Fori(0, TILES // 2) as i:
                for b in range(2):
                    t = 2 * i + b
                    act.wait_ge(y_in[b], 16 * i + 16)
                    act.wait_ge(mixed, t + 1)
                    nc.scalar.activation(sq[:, b, :, :], y[:, b, KF:, :], ACT.Square).then_inc(squared_y, 1)
                    act.wait_ge(proj_f, t + 1)
                    nc.scalar.activation(h[:, b, :], psf[:, :], ACT.Copy).then_inc(f_out, 1)
                    act.wait_ge(summed, t + 1)
                    nc.scalar.activation(stat[:, b, 0:1], psq[b][:, :], ACT.Sqrt, scale=1.0 / SW, bias=eps[:, :]).then_inc(root_y, 1)
                    act.wait_ge(mixed, t + 3)
                    nc.scalar.activation(junk[:, :], h[:, b, :], ACT.Square, accum_out=stat[:, b, 2:3]).then_inc(squared, 1)
                    act.wait_ge(squared, t + 1)
                    nc.scalar.activation(stat[:, b, 3:4], stat[:, b, 2:3], ACT.Sqrt, scale=1.0 / D, bias=eps[:, :]).then_inc(rooted, 1)

        @block.vector
        def _(dve):
            nc.vector.memset(eps[:, :], EPS).then_inc(eps_set, 1)
            dve.wait_ge(w_in, 64)
            for k in range(KS):
                nc.vector.tensor_scalar(w[:, KF + k, :], w[:, KF + k, :], gs[:, k:k + 1], None, ALU.mult).then_inc(scaled_w, 1)
            nc.vector.tensor_tensor(gg[:, 0, :], gg[:, 0, :], gg[:, 1, :], ALU.mult).then_inc(scaled_w, 1)
            dve.wait_ge(scaled_w, KS + 1)
            dve.sem_inc(mixed, 2)
            dve.sem_inc(added, 2)
            with dve.Fori(0, TILES // 2) as i:
                for b in range(2):
                    t = 2 * i + b
                    dve.wait_ge(root_y, t + 1)
                    nc.vector.reciprocal(stat[:, b, 1:2], stat[:, b, 0:1]).then_inc(inv, 1)
                    dve.wait_ge(inv, 2 * t + 1)
                    dve.wait_ge(proj, t + 3)
                    dve.wait_ge(f_out, t + 2)
                    nc.vector.scalar_tensor_tensor(out=h[:, b, :], in0=pss[b][:, :], scalar=stat[:, b, 1:2], in1=h[:, b, :],
                                                   op0=ALU.mult, op1=ALU.add).then_inc(mixed, 1)
                    dve.wait_ge(rooted, t + 1)
                    nc.vector.reciprocal(stat[:, b, 4:5], stat[:, b, 3:4]).then_inc(inv, 1)
                    dve.wait_ge(inv, 2 * t + 2)
                    dve.wait_ge(free, t + 1)
                    nc.vector.scalar_tensor_tensor(out=o[:, b, :], in0=h[:, b, :], scalar=stat[:, b, 4:5], in1=gg[:, 0, :],
                                                   op0=ALU.mult, op1=ALU.mult).then_inc(normed, 1)
                    dve.wait_ge(normed, t + 1)
                    dve.wait_ge(x_in[b], 16 * i + 16)
                    nc.vector.tensor_tensor(o[:, b, :], o[:, b, :], xr[:, b, :], ALU.add).then_inc(added, 1)

        @block.gpsimd
        def _(pool):
            pool.sem_inc(free, 2)
            with pool.Fori(0, TILES // 2) as i:
                for b in range(2):
                    t = 2 * i + b
                    pool.wait_ge(added, t + 3)
                    pool.dma_start(rows_out[bass.ds(t, 1), :, :].rearrange("t p d -> p (t d)"), o[:, b, :]).then_inc(stored, 16)
                    pool.wait_ge(stored, 16 * t + 16)
                    pool.sem_inc(free, 1)


def feed_forward(nc, x3, g_pre, shift, scale, w_gate, w_up, w_down, g_post, gate, out, ident):
    RT = NB // P
    DH = D // 2
    NF = 2 * FT
    PIECES = 4
    with Mem(nc, "ff") as m:
        hraw = m.sb("hraw", P, KD, P)
        hb_lo, hb_hi = m.sb_r("hb_lo", P, KD, NB), m.sb_r("hb_hi", P, KD, NB)
        wg = m.sb("wg", P, 2, KD, P)
        wg_lo, wg_hi = m.sb_r("wg_lo", P, 2, 2, KD, P), m.sb_r("wg_hi", P, 2, 2, KD, P)
        wd = m.sb("wd", P, PIECES, DH)
        wd_lo, wd_hi = m.sb_r("wd_lo", P, PIECES, DH), m.sb_r("wd_hi", P, PIECES, DH)
        a_lo = m.sb_r("a_lo", P, PIECES, NB)
        a_hi = m.sb_r("a_hi", P, PIECES, NB)
        act_t = m.sb("act", P, FT, NB)
        sg = m.sb("sg", P, 2, NB)
        gg = m.sb("gg", P, D)
        xt = m.sb("xt", P, 2, D)
        xr = m.sb("xr", P, 2, D)
        h = m.sb("h", P, RT, D)
        ncol = m.sb("ncol", P, 3, KD)
        nstat = m.sb("nstat", P, 2, 4)
        stat = m.sb("stat", P, RT, 5)
        eps = m.sb("eps", P, 1)
        psg = [m.ps(f"psg{i}", P, 2, NB) for i in range(2)]
        psd = [m.ps(f"psd{i}", P, NB) for i in range(RT)]
        start, ready = m.sem("start"), m.sem("ready")
        loaded = [m.sem(f"loaded{i}") for i in range(2)]
        d_in = [m.sem(f"d_in{i}") for i in range(PIECES)]
        xt_in = [m.sem(f"xt_in{i}") for i in range(2)]
        (w_hi, w_lo, proj, gated, made, p_hi, p_lo, used, kept, squared, summed, rooted, inv, normed, added, stored) = (
            m.sem(n) for n in ("w_hi", "w_lo", "proj", "gated", "made", "p_hi", "p_lo", "used", "kept", "squared", "summed",
                               "rooted", "inv", "normed", "added", "stored"))
        x_in = [m.sem(f"x_in{i}") for i in range(2)]
        (n_sq, n_root, n_inv, n_scaled, n_turned, n_placed, n_shift, n_hi, n_lo) = (
            m.sem(n) for n in ("n_sq", "n_root", "n_inv", "n_scaled", "n_turned", "n_placed", "n_shift", "n_hi", "n_lo"))
        h_free, begun = m.sem("h_free"), m.sem("begun")
        block = m.block()
        gv, uv = (w.rearrange("(k p) c -> p k c", p=P) for w in (w_gate, w_up))
        dv = w_down.rearrange("(f p) d -> f p d", p=P)
        rows_in = x3.rearrange("(t p) d -> p t d", p=P)
        rows_out = out.rearrange("(t p) d -> p t d", p=P)
        LOAD_AT = (0, 0, 10, 16)
        SCALE_AT = (4, 8, 14, 20)
        TURN_AT = (8, 13, 19, 25)
        PLACE_AT = (9, 14, 20, 26)
        WEIGHTS_AT = (10, 33)
        SPLIT_AT = (26, 38)
        DEPTH_ = 3

        def blocks(eng, body):
            with eng.Fori(0, LB - 1) as n:
                body(n, False)
            body(LB - 1, True)

        def piece(j):
            return j // FT, j % FT, j % PIECES

        @block.sync
        def _(sp):
            sp.dma_start(gg[:, :], every_partition(g_post)).then_inc(start, 16)
            sp.dma_start(sg[:, :, :].rearrange("p a b -> p (a b)"), every_partition(gate)).then_inc(start, 16)
            for i, v in enumerate((g_pre, shift, scale)):
                sp.dma_start(ncol[:, i, :], columns(v, KD), allow_slow_non_contiguous=True).then_inc(start, 16)

            def load_rows(n, r):
                sp.wait_ge(n_turned, n * RT + r + 1)
                sp.dma_start(xt[:, r % 2, :], rows_in[:, bass.ds(n * RT + r, 1), :].rearrange("p t d -> p (t d)"))\
                  .then_inc(xt_in[r % 2], 16)

            def load_tile(n, t, b):
                for x, v in enumerate((gv, uv)):
                    sp.wait_ge(w_lo, n * (2 * FT) + 2 * t + x + 1)
                    sp.dma_start(wg[:, x, :, :], v[:, :, bass.ds(t * P, P)]).then_inc(loaded[x], 16)

            def load_piece(n, j):
                half, f, s = piece(j)
                sp.wait_ge(p_lo, n * (2 * NF) + 2 * j + 1)
                sp.dma_start(wd[:, s, :], dv[f, :, half * DH:(half + 1) * DH]).then_inc(d_in[s], 16)

            def body(n, last):
                with sp.Fori(0, FT // 2 - 1) as i:
                    for b in range(2):
                        load_tile(n, 2 * i + b + 2, b)
                for j in range(NF):
                    load_piece(n, j)
                    if not last:
                        for r in range(RT):
                            if LOAD_AT[r] == j:
                                load_rows(n + 1, r)
                        for b in range(2):
                            if WEIGHTS_AT[b] == j:
                                load_tile(n + 1, b, b)

            load_rows(0, 0)
            load_rows(0, 1)
            load_tile(0, 0, 0)
            load_rows(0, 2)
            load_rows(0, 3)
            load_tile(0, 1, 1)
            blocks(sp, body)

        @block.tensor
        def _(pe):
            pe.sem_inc(proj, 2)
            pe.sem_inc(used, 4)
            pe.sem_inc(n_turned, 2)

            def turn(n, r):
                pe.wait_ge(n_scaled, n * RT + r + 1)
                pe.wait_ge(n_placed, n * RT + r + 1)
                for k in range(KD):
                    x, c = k // 4, (k % 4) * P
                    t = nc.tensor.transpose(psg[r % 2][:, x, c:c + P], xt[:, r % 2, k * P:(k + 1) * P], ident[:, :])
                t.then_inc(n_turned, 1)

            def three(to, left, right, first, last):
                for p, (x, y) in enumerate(((0, 0), (0, 1), (1, 0))):
                    mm = nc.tensor.matmul(to, left[x], right[y], start=(first and p == 0), stop=(last and p == 2))
                return mm

            def body(n, last):
                pe.wait_ge(n_lo, (n + 1) * RT + 1)
                pe.wait_ge(n_placed, (n + 1) * RT + 2)
                pe.sem_inc(begun, 1)
                with pe.Fori(0, FT // 2) as i:
                    for b in range(2):
                        t = n * FT + 2 * i + b
                        pe.wait_ge(w_lo, n * (2 * FT) + 4 * i + 2 * b + 4)
                        pe.wait_ge(made, t + 1)
                        for x in range(2):
                            for k in range(KD):
                                mm = three(psg[b][:, x, :], (wg_hi[:, b, x, k, :], wg_lo[:, b, x, k, :]),
                                           (hb_hi[:, k, :], hb_lo[:, k, :]), k == 0, k == KD - 1)
                        mm.then_inc(proj, 1)
                pe.wait_ge(made, n * FT + FT + 2)
                for j in range(NF):
                    half, f, s = piece(j)
                    if f == 0:
                        pe.wait_ge(kept, 2 * n + half + 1)
                    pe.wait_ge(p_lo, n * (2 * NF) + 2 * j + 2 + 2 * PIECES)
                    for r in range(RT):
                        rs = slice(r * P, (r + 1) * P)
                        mm = three(psd[r][:, :], (a_hi[:, s, rs], a_lo[:, s, rs]),
                                   (wd_hi[:, s, :], wd_lo[:, s, :]), f == 0, f == FT - 1)
                    mm.then_inc(used, 1)
                    if not last:
                        for r in range(RT):
                            if TURN_AT[r] == j:
                                turn(n + 1, r)

            for r in range(RT):
                turn(0, r)
            blocks(pe, body)

        @block.scalar
        def _(act):
            act.wait_ge(ready, 3)
            act.sem_inc(kept, 1)

            def root(n, r):
                act.wait_ge(xt_in[r % 2], n * (RT // 2 * 16) + 16 * (r // 2) + 16)
                nc.scalar.activation(sg[:, :, :].rearrange("p a b -> p (a b)"), xt[:, r % 2, :], ACT.Square, accum_out=nstat[:, r % 2, 0:1]).then_inc(n_sq, 1)
                act.wait_ge(n_sq, n * RT + r + 1)
                nc.scalar.activation(nstat[:, r % 2, 1:2], nstat[:, r % 2, 0:1], ACT.Sqrt, scale=1.0 / D, bias=eps[:, :])\
                  .then_inc(n_root, 1)

            def tile_hi(n, i, b):
                t = n * FT + 2 * i + b
                act.wait_ge(proj, t + 1)
                for x in range(2):
                    act.wait_ge(loaded[x], 16 * t + 16)
                    nc.scalar.activation(wg_hi[:, b, x, :, :], wg[:, x, :, :], ACT.Copy).then_inc(w_hi, 1)

            def piece_hi(n, j):
                half, f, s = piece(j)
                act.wait_ge(used, n * NF + j + 1)
                act.wait_ge(d_in[s], n * (NF // PIECES * 16) + 16 * (j // PIECES) + 16)
                nc.scalar.activation(wd_hi[:, s, :], wd[:, s, :], ACT.Copy).then_inc(p_hi, 1)
                nc.scalar.activation(a_hi[:, s, :], act_t[:, f, :], ACT.Copy).then_inc(p_hi, 1)

            def body(n, last):
                nc.scalar.preload_act_table(ACT.Silu)

                def silu(i, b):
                    t = n * FT + 2 * i + b
                    act.wait_ge(proj, t + 3)
                    act.wait_ge(made, t + 1)
                    nc.scalar.activation(sg[:, b, :], psg[b][:, 0, :], ACT.Silu).then_inc(gated, 1)

                with act.Fori(0, FT // 2 - 1) as i:
                    for b in range(2):
                        silu(i, b)
                        tile_hi(n, i + 1, b)
                for b in range(2):
                    silu(FT // 2 - 1, b)
                act.wait_ge(made, n * FT + FT + 2)
                for j in range(DEPTH_):
                    piece_hi(n, j)
                for j in range(NF):
                    if j + DEPTH_ < NF:
                        piece_hi(n, j + DEPTH_)
                    if not last:
                        for r in range(RT):
                            if SCALE_AT[r] == j:
                                root(n + 1, r)
                        for b in range(2):
                            if SPLIT_AT[b] == j:
                                tile_hi(n + 1, 0, b)
                    if j % FT == FT - 1:
                        half = j // FT
                        act.wait_ge(used, n * NF + (half + 1) * FT + 4)
                        if half == 0:
                            act.wait_ge(h_free, n + 1)
                        cols = slice(half * DH, (half + 1) * DH)
                        for r in range(RT):
                            to = nc.scalar.activation(h[:, r, cols], psd[r][:, :], ACT.Copy)
                        to.then_inc(kept, 1)
                        act.wait_ge(kept, 2 * n + half + 2)
                        for r in range(RT):
                            nc.scalar.activation(sg[:, 0, :], h[:, r, cols], ACT.Square, accum_out=stat[:, r, half:half + 1])\
                              .then_inc(squared, 1)
                            act.wait_ge(squared, n * (2 * RT) + half * RT + r + 1)
                act.wait_ge(summed, n + 1)
                nc.scalar.activation(stat[:, :, 3:4], stat[:, :, 2:3], ACT.Sqrt, scale=1.0 / D, bias=eps[:, :]).then_inc(rooted, 1)

            for r in range(RT):
                root(0, r)
            tile_hi(0, 0, 0)
            tile_hi(0, 0, 1)
            blocks(act, body)

        @block.vector
        def _(dve):
            nc.vector.memset(eps[:, :], EPS).then_inc(ready, 1)
            dve.wait_ge(start, 80)
            nc.vector.tensor_tensor(gg[:, :], gg[:, :], sg[:, :, :].rearrange("p a b -> p (a b)"), ALU.mult).then_inc(ready, 1)
            nc.vector.scalar_tensor_tensor(out=ncol[:, 0, :], in0=ncol[:, 2, :], scalar=1.0, in1=ncol[:, 0, :],
                                           op0=ALU.add, op1=ALU.mult).then_inc(ready, 1)
            dve.wait_ge(ready, 3)
            dve.sem_inc(made, 2)
            dve.sem_inc(n_placed, 2)
            dve.sem_inc(h_free, 1)
            dve.sem_inc(n_lo, 1)
            dve.sem_inc(w_lo, 2)
            dve.sem_inc(p_lo, 2 * PIECES)

            def scaled_rows(n, r):
                dve.wait_ge(n_root, n * RT + r + 1)
                nc.vector.reciprocal(nstat[:, r % 2, 2:3], nstat[:, r % 2, 1:2]).then_inc(n_inv, 1)
                dve.wait_ge(n_inv, n * RT + r + 1)
                nc.vector.tensor_scalar(xt[:, r % 2, :], xt[:, r % 2, :], nstat[:, r % 2, 2:3], None, ALU.mult).then_inc(n_scaled, 1)

            def place(n, r):
                dve.wait_ge(n_turned, n * RT + r + 3)
                dve.wait_ge(n_lo, n * RT + r + 1)
                nc.vector.tensor_tensor(hraw[:, :, :],
                                        psg[r % 2][:, :, :].rearrange("p x (k l) -> p (x k) l", l=P),
                                        over(ncol[:, 0, :, None], (P, KD, P)), ALU.mult).then_inc(n_placed, 1)

            def tile_lo(n, t, b):
                for x in range(2):
                    dve.wait_ge(w_hi, n * (2 * FT) + 2 * t + x + 1)
                    nc.vector.tensor_tensor(wg_lo[:, b, x, :, :], wg[:, x, :, :], wg_hi[:, b, x, :, :].bitcast(F32),
                                            ALU.subtract).then_inc(w_lo, 1)

            def piece_lo(n, j):
                half, f, s = piece(j)
                dve.wait_ge(p_hi, n * (2 * NF) + 2 * j + 2)
                nc.vector.tensor_tensor(wd_lo[:, s, :], wd[:, s, :], wd_hi[:, s, :].bitcast(F32), ALU.subtract)\
                  .then_inc(p_lo, 1)
                nc.vector.tensor_tensor(a_lo[:, s, :], act_t[:, f, :], a_hi[:, s, :].bitcast(F32), ALU.subtract).then_inc(p_lo, 1)

            def body(n, last):
                def multiply(t, b):
                    dve.wait_ge(gated, n * FT + t + 1)
                    nc.vector.tensor_tensor(act_t[:, bass.ds(t, 1), :].rearrange("p f l -> p (f l)"),
                                            psg[b][:, 1, :], sg[:, b, :], ALU.mult).then_inc(made, 1)

                with dve.Fori(0, FT // 2 - 1) as i:
                    for b in range(2):
                        multiply(2 * i + b, b)
                        tile_lo(n, 2 * i + b + 2, b)
                for b in range(2):
                    multiply(FT - 2 + b, b)
                dve.wait_ge(made, n * FT + FT + 2)
                for j in range(DEPTH_):
                    piece_lo(n, j)
                for j in range(NF):
                    if j + DEPTH_ < NF:
                        piece_lo(n, j + DEPTH_)
                    if not last:
                        for r in range(RT):
                            if SCALE_AT[r] == j:
                                scaled_rows(n + 1, r)
                            if PLACE_AT[r] == j:
                                place(n + 1, r)
                        for b in range(2):
                            if SPLIT_AT[b] == j:
                                tile_lo(n + 1, b, b)
                dve.wait_ge(squared, (n + 1) * (2 * RT))
                nc.vector.tensor_tensor(stat[:, :, 2:3], stat[:, :, 0:1], stat[:, :, 1:2], ALU.add).then_inc(summed, 1)
                dve.wait_ge(rooted, n + 1)
                nc.vector.reciprocal(stat[:, :, 4:5], stat[:, :, 3:4]).then_inc(inv, 1)
                dve.wait_ge(inv, n + 1)
                for r in range(RT):
                    nc.vector.scalar_tensor_tensor(out=h[:, r, :], in0=h[:, r, :], scalar=stat[:, r, 4:5], in1=gg[:, :],
                                                   op0=ALU.mult, op1=ALU.mult).then_inc(normed, 1)

            for r in range(RT):
                scaled_rows(0, r)
                place(0, r)
            tile_lo(0, 0, 0)
            tile_lo(0, 1, 1)
            blocks(dve, body)

        @block.gpsimd
        def _(pool):
            pool.wait_ge(start, 80)

            def shift_and_split(n, r):
                cs = slice(r * P, (r + 1) * P)
                pool.wait_ge(n_placed, n * RT + r + 3)
                nc.gpsimd.tensor_tensor(hraw[:, :, :], hraw[:, :, :], over(ncol[:, 1, :, None], (P, KD, P)), ALU.add)\
                  .then_inc(n_shift, 1)
                pool.wait_ge(n_shift, n * RT + r + 1)
                pool.sem_inc(begun, 1)
                nc.gpsimd.tensor_copy(hb_hi[:, :, cs], hraw[:, :, :]).then_inc(n_hi, 1)
                pool.wait_ge(n_hi, n * RT + r + 1)
                nc.gpsimd.tensor_tensor(hb_lo[:, :, cs], hraw[:, :, :], hb_hi[:, :, cs].bitcast(F32), ALU.subtract)\
                    .then_inc(n_lo, 1)

            def load_residual(n, r):
                pool.dma_start(xr[:, r % 2, :], rows_in[:, bass.ds(n * RT + r, 1), :].rearrange("p t d -> p (t d)"))\
                    .then_inc(x_in[r % 2], 16)

            def body(n, last):
                load_residual(n, 0)
                load_residual(n, 1)
                if not last:
                    for r in range(RT):
                        shift_and_split(n + 1, r)
                for r in range(RT):
                    t = n * RT + r
                    pool.wait_ge(x_in[r % 2], n * (RT // 2 * 16) + 16 * (r // 2) + 16)
                    pool.wait_ge(normed, t + 1)
                    pool.sem_inc(begun, 1)
                    nc.gpsimd.tensor_tensor(h[:, r, :], h[:, r, :], xr[:, r % 2, :], ALU.add).then_inc(added, 1)
                    pool.wait_ge(added, t + 1)
                    pool.sem_inc(begun, 1)
                    pool.dma_start(rows_out[:, bass.ds(t, 1), :].rearrange("p t d -> p (t d)"), h[:, r, :]).then_inc(stored, 16)
                    if r + 2 < RT:
                        load_residual(n, r + 2)
                pool.wait_ge(stored, n * (16 * RT) + 16 * RT)
                pool.sem_inc(h_free, 1)

            for r in range(RT):
                shift_and_split(0, r)
            blocks(pool, body)


def program(nc, d):
    with Mem(nc, "all") as m:
        ident, ones = m.sb("ident", P, P), m.sb("ones", P, P)
        make_constants(nc, ident, ones)
        modulations(nc, d["c_2"][0], d["c_ctx_2"], d["w_ada_2"][0], d["b_ada_2"][0], d["s_mod"])

        w_in = d["w_in"][0]
        with Mem(nc, "m1") as m1:
            uc = m1.sb("uc", P, G1, NC8)
            with Mem(nc, "m1a") as m2:
                xn = m2.sb("xn", P, KD, L)
                norm_to_columns(nc, "n1", d["x"][0], TILES, xn, 0, ident, d["norm_gain"][0])
                silu_projection(nc, "z1", xn, w_in[:, SSM_W:2 * SSM_W], SSM_W // P, d["s_z1"])
                short_convolution(nc, xn, w_in, d["conv_w"][0], d["s_y1"])
                s5_inputs(nc, xn, w_in[:, 0:SSM_W], uc, ident)
            vw = m1.sb("vw", P, 2, QP, P)
            q = m1.sb("q", P, 2, QP, T8 + 1, H1)
            toeplitz = m1.sb("toeplitz", P, G1, P)
            a8 = m1.sb("a8", P, 2, QP)
            s5_weights(nc, d, vw, q, toeplitz, a8, ident, d["s_kernels"])
            st = m1.sb("st", P, 2, QP, NC8)
            s5_scan(nc, uc, vw, a8, st)
            yt = m1.sb("yt", P, SSM_W // P, L)
            s5_outputs(nc, uc, st, q, toeplitz, yt, ident)
            s5_gate(nc, yt, d["w_glu"][0], d["b_glu"][0], d["s_z1"], d["s_y1"])
        output_rows_1(nc, d["s_y1"], d["w_out"][0], d["x"][0], d["final_norm_gain"], d["s_x2"])

        w_in2 = d["w_in_2"][0]
        mod, modc = (lambda i: d["s_mod"][0, i * D:(i + 1) * D]), (lambda i: d["s_mod"][1, i * D:(i + 1) * D])
        with Mem(nc, "m3") as m3:
            ht = m3.sb("ht", P, KD, LT)
            norm_to_columns(nc, "n2", d["s_x2"], TILES, ht, 0, ident, d["g_pre_mix_2"][0], (mod(0), mod(1)))
            norm_to_columns(nc, "nc", d["ctx_2"][0], LC // P, ht, L, ident, d["g_pre_mix_2"][0], (modc(0), modc(1)))
            silu_projection(nc, "z2", ht, w_in2[:, FW:XBC], SW // P, d["s_z2"])
            convolved_projection(nc, ht, w_in2[:, XBC:XBC + CONV_DIM], d["conv_w_2"][0], d["conv_b_2"][0], d["s_xbc"])
            decays(nc, ht, w_in2[:, XBC + CONV_DIM:], d["dt_bias_2"][0], d["a_log_2"][0], d["s_decay_rows"],
                   d["s_totals"], d["s_decay_cols"], ident)
            fourier_mix(nc, ht, w_in2[:, 0:FW], d["t_over_b"], d["t_over_c"], d["t_over_a"], d["s_y2"])
        with Mem(nc, "m4") as m4:
            hf, hb = m4.sb("hf", P, HEADS, HD), m4.sb("hb", P, HEADS, HD)
            context_states(nc, d["s_xbc"], d["s_totals"], d["s_decay_cols"], hf[:, :, :], hb[:, :, :], ident)
            backward_states(nc, d["s_xbc"], d["s_totals"], d["s_decay_cols"], hb, d["s_hb"], ident)
            ssd_outputs(nc, d["s_xbc"], d["s_z2"], d["s_decay_rows"], d["s_totals"], d["s_decay_cols"], d["d_skip_2"][0],
                        hf, d["s_hb"], d["s_y2"], ident, ones)
        output_rows_2(nc, d["s_y2"], d["w_out_2"][0], d["g_ssd_2"][0], d["g_post_mix_2"][0], mod(2), d["s_x2"], d["s_x3"], ones)
        feed_forward(nc, d["s_x3"], d["g_pre_ffn_2"][0], mod(3), mod(4), d["w_gate_2"][0], d["w_up_2"][0], d["w_down_2"][0],
                     d["g_post_ffn_2"][0], mod(5), d["out"][0], ident)


SCRATCH = {
    "s_mod": (2, 6 * D),
    "s_z1": (SSM_W // P, P, L), "s_y1": (KD, P, L), "s_kernels": (H1, G1, 7 * H1 + P), "s_x2": (L, D),
    "s_z2": (SW // P, P, L), "s_xbc": (XT_, P, LT), "s_decay_rows": (LT // P, 2 * HEADS, P), "s_totals": (LT // P, 2 * HEADS),
    "s_decay_cols": (LT // P, P, 3 * 64), "s_hb": (NCH, P, HEADS * HD), "s_y2": (KD, P, L), "s_x3": (L, D),
}

_INS = ["x", "norm_gain", "w_in", "ssm_a_re", "ssm_a_im", "ssm_log_dt", "ssm_b_re", "ssm_b_im", "ssm_c_re", "ssm_c_im",
        "ssm_d", "w_glu", "b_glu", "conv_w", "w_out", "final_norm_gain", "c_2", "ctx_2", "c_ctx_2", "w_ada_2", "b_ada_2",
        "g_pre_mix_2", "g_post_mix_2", "g_pre_ffn_2", "g_post_ffn_2", "w_in_2", "conv_w_2", "conv_b_2", "dt_bias_2",
        "a_log_2", "d_skip_2", "g_ssd_2", "w_out_2", "w_gate_2", "w_up_2", "w_down_2"]


def kernel(**inputs):
    import concourse.bacc as _bacc
    from concourse.bass_utils import run_bass_kernel_spmd as _run

    nc = _bacc.Bacc("TRN2", target_bir_lowering=False, num_devices=1)
    arrays, d = {}, {}
    tables = dict(zip(("t_over_b", "t_over_c", "t_over_a"), fourier_tables()))
    for name, a in [(n, inputs[n]) for n in _INS] + list(tables.items()):
        a = np.ascontiguousarray(a)
        arrays[f"in_{name}_dram"] = a
        d[name] = nc.dram_tensor(f"in_{name}_dram", a.shape, mybir.dt.from_np(a.dtype), kind="ExternalInput").ap()
    for name, shape in SCRATCH.items():
        d[name] = nc.dram_tensor(name, shape, F32).ap()
    d["out"] = nc.dram_tensor("out_0_dram", (1, L, D), F32, kind="ExternalOutput").ap()
    program(nc, d)
    r = _run(nc, [arrays], core_ids=[0])
    return r.results[0]["out_0_dram"]
```

```python
from contextlib import ExitStack
import math

import numpy as np
import concourse.bass as bass
from concourse import mybir

F32 = mybir.dt.float32
F32R = mybir.dt.float32r
ALU = mybir.AluOpType
ACT = mybir.ActivationFunctionType

P = 128
D = 1024
KD = D // P
L = 2048
LC = 256
LT = L + LC
TILES = L // P
NB = 512
LB = L // NB
EPS = 1e-6

SSM_W = 512
CW = 512
G1, H1, S1 = 32, 16, 64
T8 = 8
NC8 = L // T8
QP = G1 // 2
HALF = NC8 // P
SB = 16
NSB = NC8 // SB

FW = 256
FG = 64
SW = 768
HEADS, HD, SG, ST = 12, 64, 4, 128
HR = HEADS // SG
CONV_DIM = SW + 2 * SG * ST
XT_ = CONV_DIM // P
KC = 7
ROWLEN = 64
XBC = FW + SW
NCH = L // P
CCH = LC // P
FF = 2816
FT = FF // P


class Mem:

    def __init__(self, nc, stage):
        self.nc, self.stage, self.stack, self.sems = nc, stage, ExitStack(), []

    def sb(self, name, *shape):
        return self.stack.enter_context(self.nc.sbuf_tensor(f"{self.stage}_{name}", list(shape), F32))

    def sb_r(self, name, *shape):
        return self.stack.enter_context(self.nc.sbuf_tensor(f"{self.stage}_{name}", list(shape), F32R))

    def ps(self, name, *shape):
        return self.stack.enter_context(self.nc.psum_tensor(f"{self.stage}_{name}", list(shape), F32))

    def sem(self, name):
        self.sems.append(self.nc.alloc_semaphore(f"{self.stage}_{name}"))
        return self.sems[-1]

    def block(self):
        return self.stack.enter_context(self.nc.Block())

    def __enter__(self):
        self.stack.__enter__()
        return self

    def __exit__(self, *e):
        self.stack.__exit__(*e)
        if self.sems and e[0] is None:
            self.nc.clear_and_free_semaphores(self.sems)
            self.nc.all_engine_barrier()


def over(ap, shape):
    return ap.broadcast_to(list(shape))


def columns(vec, tiles):
    return vec.rearrange("(k p) -> p k", p=P)


def every_partition(vec, n=P):
    return vec.partition_broadcast(n)


def make_constants(nc, ident, ones):
    with Mem(nc, "const") as m:
        zeroed, made = m.sem("zeroed"), m.sem("made")
        block = m.block()

        @block.gpsimd
        def _(pool):
            nc.gpsimd.memset(ident[:, :], 0.0).then_inc(zeroed, 1)
            nc.gpsimd.memset(ones[:, :], 1.0).then_inc(made, 1)
            pool.wait_ge(zeroed, 1)
            nc.gpsimd.affine_select(out=ident[:, :], in_=ident[:, :], compare_op=ALU.not_equal, fill=1.0,
                                    base=0, pattern=[[-1, P]], channel_multiplier=1).then_inc(made, 1)
            pool.wait_ge(made, 2)


def norm_to_columns(nc, stage, src, tiles, dst, col0, ident, gain, modulation=None):
    NX = 4
    with Mem(nc, stage) as m:
        x = m.sb("x", P, NX, D)
        xn = m.sb("xn", P, 2, D)
        junk = m.sb("junk", P, D)
        stat = m.sb("stat", P, 2, 4)
        a = m.sb("a", P, KD)
        b = m.sb("b", P, KD)
        s = m.sb("s", P, KD)
        eps = m.sb("eps", P, 1)
        ps = [m.ps(f"ps{i}", P, KD, P) for i in range(2)]
        vec = m.sem("vec")
        loaded = [m.sem(f"loaded{i}") for i in range(NX)]
        squared, rooted, inverted, scaled = m.sem("squared"), m.sem("rooted"), m.sem("inverted"), m.sem("scaled")
        turned, placed, shifted = m.sem("turned"), m.sem("placed"), m.sem("shifted")
        ab, eps_set = m.sem("ab"), m.sem("eps_set")
        block = m.block()
        rows = src.rearrange("(t p) d -> t p d", p=P)
        step = min(NX, tiles)

        @block.sync
        def _(sp):
            for t in range(min(NX, tiles)):
                sp.dma_start(x[:, t, :], rows[t, :, :]).then_inc(loaded[t], 16)
            sp.dma_start(a[:, :], columns(gain, KD), allow_slow_non_contiguous=True).then_inc(vec, 16)
            if modulation:
                sp.dma_start(b[:, :], columns(modulation[0], KD), allow_slow_non_contiguous=True).then_inc(vec, 16)
                sp.dma_start(s[:, :], columns(modulation[1], KD), allow_slow_non_contiguous=True).then_inc(vec, 16)
            if tiles > NX:
                with sp.Fori(0, tiles // NX - 1) as i:
                    for j in range(NX):
                        sp.wait_ge(scaled, NX * i + j + 1)
                        sp.dma_start(x[:, j, :], rows[bass.ds(NX * i + j + NX, 1), :, :].rearrange("t p d -> p (t d)"))\
                          .then_inc(loaded[j], 16)

        @block.scalar
        def _(act):
            act.wait_ge(eps_set, 1)
            nc.scalar.preload_act_table(ACT.Sqrt)
            act.sem_inc(turned, 2)
            with act.Fori(0, tiles // step) as i:
                for j in range(step):
                    t = step * i + j
                    act.wait_ge(loaded[j], 16 * i + 16)
                    act.wait_ge(inverted, t + 1)
                    nc.scalar.activation(junk[:, :], x[:, j, :], ACT.Square, accum_out=stat[:, j % 2, 0:1])\
                      .then_inc(squared, 1)
                    act.wait_ge(squared, t + 1)
                    nc.scalar.activation(stat[:, j % 2, 1:2], stat[:, j % 2, 0:1], ACT.Sqrt, scale=1.0 / D, bias=eps[:, :])\
                      .then_inc(rooted, 1)

        @block.vector
        def _(dve):
            nc.vector.memset(eps[:, :], EPS).then_inc(eps_set, 1)
            dve.sem_inc(inverted, 2)
            dve.sem_inc(placed, 2)

            def scale_rows(t, j):
                dve.wait_ge(rooted, t + 1)
                nc.vector.reciprocal(stat[:, j % 2, 2:3], stat[:, j % 2, 1:2]).then_inc(inverted, 1)
                dve.wait_ge(inverted, t + 3)
                dve.wait_ge(turned, t + 1)
                nc.vector.tensor_scalar(xn[:, j % 2, :], x[:, j, :], stat[:, j % 2, 2:3], None, ALU.mult).then_inc(scaled, 1)

            def place(t, j):
                dve.wait_ge(turned, t + 3)
                nc.vector.tensor_tensor(dst[:, :, bass.ds(col0 + t * P, P)], ps[j % 2][:, :, :], over(a[:, :, None], (P, KD, P)),
                                        ALU.mult).then_inc(placed, 1)

            scale_rows(0, 0)
            dve.wait_ge(vec, 48 if modulation else 16)
            if modulation:
                nc.vector.scalar_tensor_tensor(out=a[:, :], in0=s[:, :], scalar=1.0, in1=a[:, :],
                                               op0=ALU.add, op1=ALU.mult).then_inc(ab, 1)
                dve.wait_ge(ab, 1)
            if tiles > step:
                with dve.Fori(0, tiles // step - 1) as i:
                    for j in range(step):
                        scale_rows(step * i + j + 1, (j + 1) % step)
                        place(step * i + j, j)
            for j in range(step):
                if j + 1 < step:
                    scale_rows(tiles - step + j + 1, j + 1)
                place(tiles - step + j, j)

        @block.gpsimd
        def _(pool):
            if modulation:
                pool.wait_ge(vec, 48)
                with pool.Fori(0, tiles // 2) as i:
                    for j in range(2):
                        t = 2 * i + j
                        pool.wait_ge(placed, t + 3)
                        to = dst[:, :, bass.ds(col0 + t * P, P)]
                        nc.gpsimd.tensor_tensor(to, to, over(b[:, :, None], (P, KD, P)), ALU.add).then_inc(shifted, 1)

        @block.tensor
        def _(pe):
            with pe.Fori(0, tiles // 2) as i:
                for j in range(2):
                    pe.wait_ge(scaled, 2 * i + j + 1)
                    pe.wait_ge(placed, 2 * i + j + 1)
                    for k in range(KD):
                        t = nc.tensor.transpose(ps[j][:, k, :], xn[:, j, k * P:(k + 1) * P], ident[:, :])
                    t.then_inc(turned, 1)


def short_convolution(nc, xn, w_in, conv_w, out_t):
    with Mem(nc, "sc") as m:
        w = m.sb("w", P, 2, KD, 4, P)
        taps = m.sb("taps", P, 3, CW // P)
        v = m.sb("v", P, 2 + L)
        hs = m.sb("hs", P, NB)
        sz = m.sb("sz", P, 2, NB)
        y = m.sb("y", P, 2, L)
        ps = [[m.ps(f"ps{i}{s}", P, NB) for s in range(4)] for i in range(2)]
        taps_in, v_pad = m.sem("taps_in"), m.sem("v_pad")
        loaded = [m.sem(f"loaded{i}") for i in range(2)]
        stored, free = m.sem("stored"), m.sem("free")
        proj, h_out, z_out, drained, step, whole = (m.sem(n) for n in ("proj", "h_out", "z_out", "drained", "step", "whole"))
        block = m.block()
        H, B, C, Z = range(4)
        wv = w_in[:, 2 * SSM_W:].rearrange("(k p) (s c) -> p k s c", p=P, s=4)
        STEPS = 7

        @block.sync
        def _(sp):
            for k in range(3):
                sp.dma_start(taps[:, k, :], columns(conv_w[k, :], CW // P), allow_slow_non_contiguous=True)\
                  .then_inc(taps_in, 16)
            with sp.Fori(0, CW // P // 2) as i:
                for b in range(2):
                    sp.wait_ge(proj, (2 * i + b + 1) * LB)
                    for s in range(4):
                        sp.dma_start(w[:, b, :, s, :], wv[:, :, s, bass.ds((2 * i + b) * P, P)])\
                          .then_inc(loaded[b], 16)

        @block.tensor
        def _(pe):
            pe.sem_inc(proj, 2 * LB)
            with pe.Fori(0, CW // P // 2) as i:
                for b in range(2):
                    pe.wait_ge(loaded[b], 64 * i + 64)
                    for n in range(LB):
                        pe.wait_ge(drained, (2 * i + b) * LB + n + 1)
                        for s in range(4):
                            for k in range(KD):
                                mm = nc.tensor.matmul(ps[n % 2][s][:, :], w[:, b, k, s, :], xn[:, k, n * NB:(n + 1) * NB],
                                                      start=(k == 0), stop=(k == KD - 1))
                        mm.then_inc(proj, 1)

        @block.scalar
        def _(act):
            nc.scalar.preload_act_table(ACT.Sigmoid)
            with act.Fori(0, CW // P // 2) as i:
                for b in range(2):
                    for n in range(LB):
                        t = (2 * i + b) * LB + n
                        act.wait_ge(proj, t + 2 * LB + 1)
                        act.wait_ge(drained, t + 2)
                        nc.scalar.activation(hs[:, :], ps[n % 2][H][:, :], ACT.Copy).then_inc(h_out, 1)
                        nc.scalar.activation(sz[:, n % 2, :], ps[n % 2][Z][:, :], ACT.Sigmoid).then_inc(z_out, 1)

        @block.vector
        def _(dve):
            nc.vector.memset(v[:, 0:2], 0.0).then_inc(v_pad, 1)
            dve.wait_ge(taps_in, 48)
            dve.wait_ge(v_pad, 1)
            dve.sem_inc(drained, 2)
            with dve.Fori(0, CW // P // 2) as i:
                for b in range(2):
                    dve.wait_ge(free, 2 * i + b + 1)
                    for n in range(LB):
                        t = (2 * i + b) * LB + n
                        bank = ps[n % 2]
                        yn = y[:, b, n * NB:(n + 1) * NB]
                        tap = [taps[:, k, bass.ds(2 * i + b, 1)] for k in range(3)]
                        dve.wait_ge(h_out, t + 1)
                        nc.vector.tensor_tensor(v[:, 2 + n * NB:2 + (n + 1) * NB], bank[C][:, :], hs[:, :], ALU.mult)\
                          .then_inc(step, 1)
                        dve.wait_ge(step, STEPS * t + 1)
                        nc.vector.tensor_scalar(yn, v[:, n * NB:(n + 1) * NB], tap[0], None, ALU.mult).then_inc(step, 1)
                        for k in (1, 2):
                            dve.wait_ge(step, STEPS * t + 1 + k)
                            nc.vector.scalar_tensor_tensor(out=yn, in0=v[:, k + n * NB:k + (n + 1) * NB], scalar=tap[k],
                                                           in1=yn, op0=ALU.mult, op1=ALU.add).then_inc(step, 1)
                        dve.wait_ge(step, STEPS * t + 4)
                        nc.vector.tensor_tensor(yn, bank[B][:, :], yn, ALU.mult).then_inc(step, 1)
                        dve.wait_ge(step, STEPS * t + 5)
                        dve.wait_ge(z_out, t + 1)
                        nc.vector.tensor_tensor(yn, yn, sz[:, n % 2, :], ALU.mult).then_inc(step, 1)
                        dve.wait_ge(step, STEPS * t + 6)
                        nc.vector.tensor_tensor(yn, bank[Z][:, :], yn, ALU.mult).then_inc(step, 1)
                        dve.wait_ge(step, STEPS * t + 7)
                        dve.sem_inc(drained, 1)
                    dve.sem_inc(whole, 1)

        @block.gpsimd
        def _(pool):
            pool.sem_inc(free, 2)
            with pool.Fori(0, CW // P // 2) as i:
                for b in range(2):
                    pool.wait_ge(whole, 2 * i + b + 1)
                    pool.dma_start(out_t[bass.ds(SSM_W // P + 2 * i + b, 1), :, :].rearrange("k p l -> p (k l)"),
                                   y[:, b, :]).then_inc(stored, 16)
                    pool.wait_ge(stored, 16 * (2 * i + b) + 16)
                    pool.sem_inc(free, 1)


def silu_projection(nc, stage, xn, w, tiles, out_t):
    with Mem(nc, stage) as m:
        wt = m.sb("wt", P, 2, KD, P)
        sg = m.sb("sg", P, 2, NB)
        y = m.sb("y", P, 2, L)
        ps = [m.ps(f"ps{i}", P, NB) for i in range(2)]
        loaded = [m.sem(f"loaded{i}") for i in range(2)]
        stored, free = m.sem("stored"), m.sem("free")
        proj, gated, done = m.sem("proj"), m.sem("gated"), m.sem("done")
        block = m.block()
        wv = w.rearrange("(k p) c -> p k c", p=P)

        @block.sync
        def _(sp):
            with sp.Fori(0, tiles // 2) as i:
                for b in range(2):
                    sp.wait_ge(proj, (2 * i + b + 1) * LB)
                    sp.dma_start(wt[:, b, :, :], wv[:, :, bass.ds((2 * i + b) * P, P)]).then_inc(loaded[b], 16)

        @block.tensor
        def _(pe):
            pe.sem_inc(proj, 2 * LB)
            with pe.Fori(0, tiles // 2) as i:
                for b in range(2):
                    pe.wait_ge(loaded[b], 16 * i + 16)
                    for n in range(LB):
                        pe.wait_ge(done, (2 * i + b) * LB + n + 1)
                        for k in range(KD):
                            mm = nc.tensor.matmul(ps[n % 2][:, :], wt[:, b, k, :], xn[:, k, n * NB:(n + 1) * NB],
                                                  start=(k == 0), stop=(k == KD - 1))
                        mm.then_inc(proj, 1)

        @block.scalar
        def _(act):
            nc.scalar.preload_act_table(ACT.Sigmoid)
            with act.Fori(0, tiles // 2) as i:
                for b in range(2):
                    for n in range(LB):
                        t = (2 * i + b) * LB + n
                        act.wait_ge(proj, t + 2 * LB + 1)
                        act.wait_ge(done, t + 1)
                        nc.scalar.activation(sg[:, n % 2, :], ps[n % 2][:, :], ACT.Sigmoid).then_inc(gated, 1)

        @block.vector
        def _(dve):
            dve.sem_inc(done, 2)
            with dve.Fori(0, tiles // 2) as i:
                for b in range(2):
                    dve.wait_ge(free, 2 * i + b + 1)
                    for n in range(LB):
                        dve.wait_ge(gated, (2 * i + b) * LB + n + 1)
                        nc.vector.tensor_tensor(y[:, b, n * NB:(n + 1) * NB], ps[n % 2][:, :], sg[:, n % 2, :], ALU.mult)\
                          .then_inc(done, 1)

        @block.gpsimd
        def _(pool):
            pool.sem_inc(free, 2)
            with pool.Fori(0, tiles // 2) as i:
                for b in range(2):
                    pool.wait_ge(done, (2 * i + b + 1) * LB + 2)
                    pool.dma_start(out_t[bass.ds(2 * i + b, 1), :, :].rearrange("k p l -> p (k l)"),
                                   y[:, b, :]).then_inc(stored, 16)
                    pool.wait_ge(stored, 16 * (2 * i + b) + 16)
                    pool.sem_inc(free, 1)


def group_in(r, x):
    return 8 * (r // 2) + 2 * x + r % 2


def s5_weights(nc, d, vw, q, toeplitz, a8, ident, kernel_rows):
    TWO_PI = 2.0 * math.pi
    C1 = 6.28125
    C2 = float(np.float32(np.round((TWO_PI - C1) * 2.0 ** 22) / 2.0 ** 22))
    C3 = float(np.float32(TWO_PI - C1 - C2))
    ROUND = 1.5 * 2.0 ** 23
    HPI = float(np.float32(math.pi / 2))
    PI = float(np.nextafter(np.float32(math.pi), np.float32(0)))
    with Mem(nc, "s5w") as m:
        are, aim, dt = m.sb("are", P, QP), m.sb("aim", P, QP), m.sb("dt", P, QP)
        sc = m.sb("sc", P, 12, QP)
        pw = m.sb("pw", P, 2, T8 + 1, QP)
        rev = m.sb("rev", P, 2, T8, QP)
        tmp = m.sb("tmp", P, QP * (T8 + 1) * H1)
        tmp2 = m.sb("tmp2", P, QP * (T8 + 1) * H1)
        bin_ = m.sb("bin", P, 2, QP, H1)
        bb = m.sb("bb", P, 2, QP, H1)
        cc = m.sb("cc", P, 2, QP, H1)
        crow = m.sb("crow", P, 2, 4, 2, S1)
        w = m.sb("w", P, 2, QP, T8, H1)
        kp = m.sb("kp", H1, G1, 7 * H1 + P)
        dcol = m.sb("dcol", P, G1)
        pst = [m.ps(f"pst{i}", P, 4, P) for i in range(4)]
        psk = [m.ps(f"psk{i}", H1, 4, P) for i in range(4)]
        par, bld, cld, dld, chain_, act_done = (m.sem(n) for n in ("par", "bld", "cld", "dld", "chain", "act_done"))
        c_turned, w_turned, k_made, pe_free, w_ready, k_stored, t_loaded, k_pad = (
            m.sem(n) for n in ("c_turned", "w_turned", "k_made", "pe_free", "w_ready", "k_stored", "t_loaded", "k_pad"))
        b_ready, q_ready, k_ready, for_act = (m.sem(n) for n in ("b_ready", "q_ready", "k_ready", "for_act"))
        block = m.block()
        (DT, X, MAG, TH, N, R, SIN, COS, DEN, QR, QI, T) = range(12)

        @block.sync
        def _(sp):
            for g in range(2):
                half = slice(S1 * g, S1 * g + S1)
                for to, of in ((are, d["ssm_a_re"]), (aim, d["ssm_a_im"])):
                    sp.dma_start(to[half, :], of[0, g::2, :].rearrange("q p -> p q"), allow_slow_non_contiguous=True)\
                      .then_inc(par, 16)
                sp.dma_start(dt[half, :], d["ssm_log_dt"][0, g::2].partition_broadcast(S1), allow_slow_non_contiguous=True)\
                  .then_inc(par, 16)
            for g in range(2):
                half = slice(S1 * g, S1 * g + S1)
                for ri, of in ((0, d["ssm_b_re"]), (1, d["ssm_b_im"])):
                    sp.dma_start(bin_[half, ri, :, :], of[0, g::2, :, :].rearrange("q p h -> p q h")).then_inc(bld, 16)
            for ri, of in ((0, d["ssm_c_re"]), (1, d["ssm_c_im"])):
                for dup in range(2):
                    sp.dma_start(crow[:, ri, :, dup, :], of[0].rearrange("(r g) h p -> (g h) r p", r=4)).then_inc(cld, 16)
            for j in range(T8):
                sp.dma_start(dcol[j * H1:(j + 1) * H1, :], d["ssm_d"][0].rearrange("g h -> h g"),
                             allow_slow_non_contiguous=True).then_inc(dld, 16)
            sp.wait_ge(k_ready, 1)
            sp.dma_start(kernel_rows, kp[:, :, :]).then_inc(k_stored, 16)
            sp.wait_ge(k_stored, 16)
            for j in range(T8):
                at = (T8 - 1 - j) * H1
                sp.dma_start(toeplitz[j * H1:(j + 1) * H1, :, :], kernel_rows[:, :, at:at + P]).then_inc(t_loaded, 16)

        @block.scalar
        def _(act):
            act.wait_ge(par, 96)
            nc.scalar.activation(sc[:, DT, :], dt[:, :], ACT.Exp).then_inc(act_done, 1)
            act.wait_ge(for_act, 1)
            nc.scalar.activation(sc[:, MAG, :], sc[:, X, :], ACT.Exp).then_inc(act_done, 1)
            act.wait_ge(for_act, 2)
            nc.scalar.activation(sc[:, SIN, :], sc[:, R, :], ACT.Sin).then_inc(act_done, 1)
            nc.scalar.activation(sc[:, COS, :], sc[:, N, :], ACT.Sin).then_inc(act_done, 1)

        @block.gpsimd
        def _(pool):
            nc.gpsimd.memset(kp[:, :, :], 0.0).then_inc(k_pad, 1)

        @block.vector
        def _(dve):
            n = [0]

            def then(ins):
                n[0] += 1
                ins.then_inc(chain_, 1)
                dve.wait_ge(chain_, n[0])

            def s(i):
                return sc[:, i, :]

            def tt(o, a, b, op):
                then(nc.vector.tensor_tensor(o, a, b, op))

            def ts(o, a, s1, op1, s2=None, op2=None):
                if op2 is None:
                    then(nc.vector.tensor_scalar(o, a, s1, None, op1))
                else:
                    then(nc.vector.tensor_scalar(o, a, s1, s2, op1, op2))

            def complex_product(o, a, b, t, conj=False):
                tt(o[0], a[0], b[0], ALU.mult)
                tt(t, a[1], b[1], ALU.mult)
                tt(o[0], o[0], t, ALU.subtract)
                tt(o[1], a[0], b[1], ALU.mult)
                tt(t, a[1], b[0], ALU.mult)
                if conj:
                    ts(o[1], o[1], -1.0, ALU.mult)
                    tt(o[1], o[1], t, ALU.subtract)
                else:
                    tt(o[1], o[1], t, ALU.add)

            dve.wait_ge(act_done, 1)
            tt(s(X), are[:, :], s(DT), ALU.mult)
            dve.sem_inc(for_act, 1)
            tt(s(TH), aim[:, :], s(DT), ALU.mult)
            ts(s(N), s(TH), 1.0 / TWO_PI, ALU.mult, ROUND, ALU.add)
            ts(s(N), s(N), ROUND, ALU.subtract)
            then(nc.vector.scalar_tensor_tensor(out=s(R), in0=s(N), scalar=-C1, in1=s(TH), op0=ALU.mult, op1=ALU.add))
            then(nc.vector.scalar_tensor_tensor(out=s(R), in0=s(N), scalar=-C2, in1=s(R), op0=ALU.mult, op1=ALU.add))
            then(nc.vector.scalar_tensor_tensor(out=s(R), in0=s(N), scalar=-C3, in1=s(R), op0=ALU.mult, op1=ALU.add))
            ts(s(R), s(R), PI, ALU.min, -PI, ALU.max)
            ts(s(N), s(R), -1.0, ALU.mult)
            tt(s(N), s(N), s(R), ALU.max)
            ts(s(N), s(N), -1.0, ALU.mult, HPI, ALU.add)
            dve.sem_inc(for_act, 1)
            dve.wait_ge(act_done, 4)
            tt(pw[:, 0, 1, :], s(MAG), s(COS), ALU.mult)
            tt(pw[:, 1, 1, :], s(MAG), s(SIN), ALU.mult)
            then(nc.vector.memset(pw[:, 0, 0, :], 1.0))
            then(nc.vector.memset(pw[:, 1, 0, :], 0.0))
            tt(s(DEN), are[:, :], are[:, :], ALU.mult)
            tt(s(T), aim[:, :], aim[:, :], ALU.mult)
            tt(s(DEN), s(DEN), s(T), ALU.add)
            then(nc.vector.reciprocal(s(DEN), s(DEN)))
            ts(s(X), pw[:, 0, 1, :], 1.0, ALU.subtract)
            tt(s(QR), s(X), are[:, :], ALU.mult)
            tt(s(T), pw[:, 1, 1, :], aim[:, :], ALU.mult)
            tt(s(QR), s(QR), s(T), ALU.add)
            tt(s(QR), s(QR), s(DEN), ALU.mult)
            tt(s(QI), pw[:, 1, 1, :], are[:, :], ALU.mult)
            tt(s(T), s(X), aim[:, :], ALU.mult)
            tt(s(QI), s(QI), s(T), ALU.subtract)
            tt(s(QI), s(QI), s(DEN), ALU.mult)
            for have in (1, 2, 4):
                by = [over(pw[:, ri, have:have + 1, :], (P, have, QP)) for ri in range(2)]
                complex_product([pw[:, ri, have + 1:2 * have + 1, :] for ri in range(2)],
                                [pw[:, ri, 1:have + 1, :] for ri in range(2)], by,
                                tmp[:, 0:have * QP].rearrange("p (a b) -> p a b", a=have))
            for ri in range(2):
                then(nc.vector.tensor_copy(a8[:, ri, :], pw[:, ri, T8, :]))
                for j in range(T8):
                    then(nc.vector.tensor_copy(rev[:, ri, j, :], pw[:, ri, T8 - 1 - j, :]))
            dve.wait_ge(bld, 64)
            shape = (P, QP, H1)
            complex_product([bb[:, ri, :, :] for ri in range(2)], [over(s(x)[:, :, None], shape) for x in (QR, QI)],
                            [bin_[:, ri, :, :] for ri in range(2)],
                            tmp[:, 0:QP * H1].rearrange("p (a b) -> p a b", a=QP))
            shape = (P, QP, T8, H1)
            complex_product([w[:, ri, :, :, :] for ri in range(2)],
                            [over(rev[:, ri, :, :].rearrange("p j q -> p q j")[:, :, :, None], shape) for ri in range(2)],
                            [over(bb[:, ri, :, None, :], shape) for ri in range(2)],
                            tmp[:, 0:QP * T8 * H1].rearrange("p (a b c) -> p a b c", a=QP, b=T8))
            dve.sem_inc(w_ready, 1)
            for ri in range(2):
                dve.wait_ge(c_turned, ri + 1)
                for r in range(4):
                    for g in range(2):
                        half = slice(S1 * g, S1 * g + S1)
                        then(nc.vector.tensor_copy(
                            cc[half, ri, 4 * r:4 * r + 4, :],
                            pst[ri][half, r, :].rearrange("p (q g h) -> p q g h", g=2, h=H1)[:, :, g, :]))
            dve.sem_inc(pe_free, 1)
            shape = (P, QP, T8 + 1, H1)
            complex_product([q[:, ri, :, :, :] for ri in range(2)],
                            [over(pw[:, ri, :, :].rearrange("p t q -> p q t")[:, :, :, None], shape) for ri in range(2)],
                            [over(cc[:, ri, :, None, :], shape) for ri in range(2)],
                            tmp[:, :].rearrange("p (a b c) -> p a b c", a=QP, b=T8 + 1), conj=True)
            dve.sem_inc(q_ready, 1)
            for n8 in range(8):
                ri, r = n8 // 4, n8 % 4
                dve.wait_ge(w_turned, n8 + 1)
                then(nc.vector.tensor_copy(vw[:, ri, 4 * r:4 * r + 4, :], pst[2 + n8 % 2][:, :, :]))
                dve.sem_inc(pe_free, 1)
            dve.wait_ge(k_pad, 1)
            for r in range(8):
                dve.wait_ge(k_made, r + 1)
                g = group_in(r, 0)
                then(nc.vector.tensor_copy(kp[:, g:g + 7:2, 7 * H1:], psk[r % 4][:, :, :]))
                dve.sem_inc(pe_free, 1)
            dve.sem_inc(k_ready, 1)
            dve.wait_ge(t_loaded, 16 * T8)
            dve.wait_ge(dld, 16 * T8)
            diag = tmp[:, 0:8 * P].rearrange("p (g x) -> p g x", g=8)
            for r in range(4):
                gs = slice(8 * r, 8 * r + 8)
                tt(diag, over(ident[:, None, :], (P, 8, P)), over(dcol[:, gs, None], (P, 8, P)), ALU.mult)
                tt(toeplitz[:, gs, :], toeplitz[:, gs, :], diag, ALU.add)

        @block.tensor
        def _(pe):
            pe.wait_ge(cld, 64)
            for ri in range(2):
                for r in range(4):
                    t = nc.tensor.transpose(pst[ri][:, r, :], crow[:, ri, r, :, :].rearrange("p a b -> p (a b)"), ident[:, :])
                t.then_inc(c_turned, 1)
            pe.wait_ge(w_ready, 1)
            for n8 in range(8):
                ri, r = n8 // 4, n8 % 4
                if n8 >= 2:
                    pe.wait_ge(pe_free, n8)
                for x in range(4):
                    t = nc.tensor.transpose(pst[2 + n8 % 2][:, x, :],
                                            w[:, ri, 4 * r + x, :, :].rearrange("p a b -> p (a b)"), ident[:, :])
                t.then_inc(w_turned, 1)
            pe.wait_ge(q_ready, 1)
            for r in range(8):
                if r >= 4:
                    pe.wait_ge(pe_free, 9 + r - 3)
                for x in range(4):
                    g = group_in(r, x)
                    half = slice(S1 * (g % 2), S1 * (g % 2) + S1)
                    for ri in range(2):
                        mm = nc.tensor.matmul(psk[r % 4][:, x, :], bb[half, ri, g // 2, :],
                                              q[half, ri, g // 2, 0:T8, :].rearrange("p a b -> p (a b)"),
                                              start=(ri == 0), stop=(ri == 1))
                mm.then_inc(k_made, 1)


def s5_inputs(nc, xn, w_u, uc, ident):
    with Mem(nc, "s5u") as m:
        w = m.sb("w", P, KD, SSM_W)
        u = m.sb("u", P, G1, T8, H1)
        slab = m.sb("slab", P, 2, KD, P)
        ps = [m.ps(f"ps{i}", P, NB) for i in range(2)]
        pst = [m.ps(f"pst{i}", P, 4, P) for i in range(2)]
        loaded, cut, proj, kept, turned, placed = (m.sem(n) for n in ("loaded", "cut", "proj", "kept", "turned", "placed"))
        block = m.block()
        N = T8 // 2

        @block.sync
        def _(sp):
            sp.dma_start(w[:, :, :], w_u.rearrange("(k p) c -> p k c", p=P)).then_inc(loaded, 16)

        @block.vector
        def _(dve):
            dve.sem_inc(cut, 2)
            for half in range(HALF):
                with dve.Fori(0, N) as i:
                    for b in range(2):
                        dve.wait_ge(proj, half * T8 + 2 * i + b + 1)
                        src = xn[:, :, half * P * T8:(half + 1) * P * T8].rearrange("p k (c j) -> p k j c", j=T8)
                        nc.vector.tensor_copy(slab[:, b, :, :], src[:, :, bass.ds(2 * i + b, 1), :]
                                              .rearrange("p k j c -> p k (j c)")).then_inc(cut, 1)
                for r in range(8):
                    dve.wait_ge(turned, half * 8 + r + 1)
                    nc.vector.tensor_copy(uc[:, 4 * r:4 * r + 4, half * P:(half + 1) * P], pst[r % 2][:, :, :])\
                      .then_inc(placed, 1)

        @block.scalar
        def _(act):
            act.sem_inc(kept, 2)
            for half in range(HALF):
                if half:
                    act.wait_ge(turned, 8 * half)
                with act.Fori(0, N) as i:
                    for b in range(2):
                        act.wait_ge(proj, half * T8 + 2 * i + b + 3)
                        nc.scalar.activation(u[:, :, bass.ds(2 * i + b, 1), :].rearrange("p g j h -> p g (j h)"),
                                             ps[b][:, :].rearrange("p (g h) -> p g h", h=H1), ACT.Copy).then_inc(kept, 1)

        @block.tensor
        def _(pe):
            pe.sem_inc(proj, 2)
            pe.wait_ge(loaded, 16)
            for half in range(HALF):
                with pe.Fori(0, N) as i:
                    for b in range(2):
                        pe.wait_ge(cut, half * T8 + 2 * i + b + 3)
                        pe.wait_ge(kept, half * T8 + 2 * i + b + 1)
                        for k in range(KD):
                            mm = nc.tensor.matmul(ps[b][:, :], slab[:, b, k, :], w[:, k, :], start=(k == 0), stop=(k == KD - 1))
                        mm.then_inc(proj, 1)
                pe.wait_ge(kept, (half + 1) * T8 + 2)
                for r in range(8):
                    n = half * 8 + r
                    if n >= 2:
                        pe.wait_ge(placed, n - 1)
                    for x in range(4):
                        g = 4 * r + x
                        t = nc.tensor.transpose(pst[r % 2][:, x, :], u[:, g, :, :].rearrange("p j h -> p (j h)"), ident[:, :])
                    t.then_inc(turned, 1)


def s5_scan(nc, uc, vw, a8, st):
    with Mem(nc, "s5s") as m:
        ps = [m.ps(f"ps{i}", P, 2, NC8) for i in range(4)]
        a128 = m.sb("a128", P, 2, QP)
        carry = m.sb("carry", P, 2, QP, NSB)
        t1 = m.sb("t1", P, 2, QP, NSB)
        t2 = m.sb("t2", P, 2, QP, NSB)
        made, kept, link, zero = (m.sem(n) for n in ("made", "kept", "link", "zero"))
        block = m.block()

        @block.tensor
        def _(pe):
            for r in range(QP):
                if r >= 4:
                    pe.wait_ge(kept, r - 3)
                for ri in range(2):
                    for g in range(2):
                        mm = nc.tensor.matmul(ps[r % 4][S1 * g:S1 * g + S1, ri, :], vw[:, ri, r, S1 * g:S1 * g + S1],
                                              uc[:, 2 * r + g, :], start=True, stop=True)
                mm.then_inc(made, 1)

        @block.scalar
        def _(act):
            for r in range(QP):
                act.wait_ge(made, r + 1)
                nc.scalar.activation(st[:, :, r, 1:NC8], ps[r % 4][:, :, 0:NC8 - 1], ACT.Copy).then_inc(kept, 1)

        @block.vector
        def _(dve):
            n = [0]

            def then(ins):
                n[0] += 1
                ins.then_inc(link, 1)
                dve.wait_ge(link, n[0])

            def times(o, s, a, shape):
                x1, x2 = ([t[:, ri, :, 0:shape[2]] for ri in range(2)] for t in (t1, t2))
                for ri in range(2):
                    then(nc.vector.tensor_tensor(x1[ri], s[ri], over(a[:, 0, :, None], shape), ALU.mult))
                    then(nc.vector.tensor_tensor(x2[ri], s[ri], over(a[:, 1, :, None], shape), ALU.mult))
                then(nc.vector.tensor_tensor(o[0], x1[0], x2[1], ALU.subtract))
                then(nc.vector.tensor_tensor(o[1], x1[1], x2[0], ALU.add))

            then(nc.vector.memset(st[:, :, :, 0:1], 0.0))
            dve.wait_ge(kept, QP)
            blocks = [st[:, ri, :, :].rearrange("p q (b k) -> p q b k", k=SB) for ri in range(2)]
            shape = (P, QP, NSB)
            then(nc.vector.tensor_copy(a128[:, :, :], a8[:, :, :]))
            for _i in range(int(math.log2(SB))):
                x = [a128[:, ri, :] for ri in range(2)]
                then(nc.vector.tensor_tensor(t1[:, 0, :, 0], x[0], x[0], ALU.mult))
                then(nc.vector.tensor_tensor(t1[:, 1, :, 0], x[1], x[1], ALU.mult))
                then(nc.vector.tensor_tensor(t2[:, 0, :, 0], x[0], x[1], ALU.mult))
                then(nc.vector.tensor_tensor(x[0], t1[:, 0, :, 0], t1[:, 1, :, 0], ALU.subtract))
                then(nc.vector.tensor_scalar(x[1], t2[:, 0, :, 0], 2.0, None, ALU.mult))
            for k in range(1, SB):
                times([carry[:, ri, :, :] for ri in range(2)], [b[:, :, :, k - 1] for b in blocks], a8, shape)
                for ri in range(2):
                    then(nc.vector.tensor_tensor(blocks[ri][:, :, :, k], blocks[ri][:, :, :, k], carry[:, ri, :, :], ALU.add))
            for b in range(1, NSB):
                times([carry[:, ri, :, 0:1] for ri in range(2)], [x[:, :, b - 1:b, SB - 1] for x in blocks], a128, (P, QP, 1))
                for ri in range(2):
                    end = blocks[ri][:, :, b:b + 1, SB - 1]
                    then(nc.vector.tensor_tensor(end, end, carry[:, ri, :, 0:1], ALU.add))
            shape = (P, QP, NSB - 1)
            now = [carry[:, ri, :, 0:NSB - 1] for ri in range(2)]
            for k in range(SB - 1):
                times(now, [x[:, :, 0:NSB - 1, SB - 1] for x in blocks] if k == 0 else now, a8, shape)
                for ri in range(2):
                    to = blocks[ri][:, :, 1:NSB, k]
                    then(nc.vector.tensor_tensor(to, to, now[ri], ALU.add))


def s5_outputs(nc, uc, st, q, toeplitz, yt, ident):
    with Mem(nc, "s5y") as m:
        y = m.sb("y", P, T8, SSM_W)
        ps = [m.ps(f"ps{i}", P, 4, P) for i in range(2)]
        pst = [m.ps(f"pst{i}", P, 4, P) for i in range(2)]
        made, kept, turned, placed = (m.sem(n) for n in ("made", "kept", "turned", "placed"))
        block = m.block()

        @block.tensor
        def _(pe):
            for half in range(HALF):
                cs = slice(half * P, (half + 1) * P)
                for r in range(8):
                    n = half * 8 + r
                    if n >= 2:
                        pe.wait_ge(kept, n - 1)
                    for x in range(4):
                        g = group_in(r, x)
                        part = slice(S1 * (g % 2), S1 * (g % 2) + S1)
                        nc.tensor.matmul(ps[r % 2][:, x, :], uc[:, g, cs], toeplitz[:, g, :], start=True, stop=False)
                        for ri in range(2):
                            mm = nc.tensor.matmul(ps[r % 2][:, x, :], st[part, ri, g // 2, cs],
                                                  q[part, ri, g // 2, 1:, :].rearrange("p a b -> p (a b)"),
                                                  start=False, stop=(ri == 1))
                    mm.then_inc(made, 1)
                pe.wait_ge(kept, 8 * (half + 1))
                for j in range(T8):
                    n = half * T8 + j
                    if n >= 2:
                        pe.wait_ge(placed, n - 1)
                    for t in range(4):
                        tr = nc.tensor.transpose(pst[j % 2][:, t, :], y[:, j, t * P:(t + 1) * P], ident[:, :])
                    tr.then_inc(turned, 1)

        @block.scalar
        def _(act):
            nc.scalar.preload_act_table(ACT.Gelu_apprx_tanh)
            for half in range(HALF):
                if half:
                    act.wait_ge(turned, T8 * half)
                for r in range(8):
                    act.wait_ge(made, half * 8 + r + 1)
                    for x in range(4):
                        g = group_in(r, x)
                        a = nc.scalar.activation(y[:, :, g * H1:(g + 1) * H1],
                                                 ps[r % 2][:, x, :].rearrange("p (i h) -> p i h", h=H1), ACT.Gelu_apprx_tanh)
                    a.then_inc(kept, 1)

        @block.vector
        def _(dve):
            for half in range(HALF):
                to = yt[:, :, half * P * T8:(half + 1) * P * T8].rearrange("p t (c j) -> p t j c", j=T8)
                for j in range(T8):
                    dve.wait_ge(turned, half * T8 + j + 1)
                    nc.vector.tensor_copy(to[:, :, j, :], pst[j % 2][:, :, :]).then_inc(placed, 1)


def s5_gate(nc, yt, w_glu, b_glu, silu_z, out_t):
    KS = SSM_W // P
    with Mem(nc, "glu") as m:
        w = m.sb("w", P, KS, SSM_W)
        bias = m.sb("bias", P, KS)
        z = m.sb("z", P, 2, L)
        o = m.sb("o", P, 2, L)
        sg = m.sb("sg", P, 2, NB)
        ps = [m.ps(f"ps{i}", P, NB) for i in range(2)]
        loaded, biased = m.sem("loaded"), m.sem("biased")
        z_in = [m.sem(f"z_in{i}") for i in range(2)]
        stored = [m.sem(f"stored{i}") for i in range(2)]
        proj, gated, half_done, done = (m.sem(n) for n in ("proj", "gated", "half_done", "done"))
        block = m.block()

        @block.sync
        def _(sp):
            sp.dma_start(w[:, :, :], w_glu.rearrange("(k p) c -> p k c", p=P)).then_inc(loaded, 16)
            sp.dma_start(bias[:, :], columns(b_glu, KS), allow_slow_non_contiguous=True).then_inc(biased, 16)
            for e in range(KS):
                if e >= 2:
                    sp.wait_ge(done, LB * (e - 1))
                sp.dma_start(z[:, e % 2, :], silu_z[e, :, :]).then_inc(z_in[e % 2], 16)
            for e in range(KS):
                sp.wait_ge(done, LB * (e + 1))
                sp.dma_start(out_t[e, :, :], o[:, e % 2, :]).then_inc(stored[e % 2], 16)
            for b in range(2):
                sp.wait_ge(stored[b], 16 * KS // 2)

        @block.tensor
        def _(pe):
            pe.wait_ge(loaded, 16)
            for e in range(KS):
                for n in range(LB):
                    t = e * LB + n
                    if t >= 2:
                        pe.wait_ge(gated, t - 1)
                    for k in range(KS):
                        mm = nc.tensor.matmul(ps[n % 2][:, :], w[:, k, e * P:(e + 1) * P], yt[:, k, n * NB:(n + 1) * NB],
                                              start=(k == 0), stop=(k == KS - 1))
                    mm.then_inc(proj, 1)

        @block.scalar
        def _(act):
            act.wait_ge(biased, 16)
            for e in range(KS):
                for n in range(LB):
                    t = e * LB + n
                    act.wait_ge(proj, t + 1)
                    if t >= 2:
                        act.wait_ge(done, t - 1)
                    nc.scalar.activation(sg[:, n % 2, :], ps[n % 2][:, :], ACT.Sigmoid, bias=bias[:, e:e + 1]).then_inc(gated, 1)

        @block.vector
        def _(dve):
            for e in range(KS):
                dve.wait_ge(z_in[e % 2], 16 * (e // 2 + 1))
                if e >= 2:
                    dve.wait_ge(stored[e % 2], 16 * (e // 2))
                for n in range(LB):
                    t = e * LB + n
                    cols = slice(n * NB, (n + 1) * NB)
                    dve.wait_ge(gated, t + 1)
                    nc.vector.tensor_tensor(o[:, e % 2, cols], sg[:, n % 2, :], yt[:, e, cols], ALU.mult).then_inc(half_done, 1)
                    dve.wait_ge(half_done, t + 1)
                    nc.vector.tensor_tensor(o[:, e % 2, cols], o[:, e % 2, cols], z[:, e % 2, cols], ALU.mult).then_inc(done, 1)


def ahead(eng, n, prepare, finish):
    prepare(0, 0)
    with eng.Fori(0, n // 2 - 1) as i:
        for b in range(2):
            prepare(2 * i + b + 1, 1 - b)
            finish(2 * i + b, b)
    prepare(n - 1, 1)
    finish(n - 2, 0)
    finish(n - 1, 1)


def two_ahead(eng, n, first, second, finish, finish_first=False):
    first(0, 0)
    first(1, 1)
    second(0, 0)
    with eng.Fori(0, n // 2 - 1) as i:
        for b in range(2):
            t = 2 * i + b
            if finish_first:
                finish(t, b)
            first(t + 2, b)
            second(t + 1, 1 - b)
            if not finish_first:
                finish(t, b)
    if finish_first:
        finish(n - 2, 0)
        finish(n - 1, 1)
    second(n - 1, 1)
    if not finish_first:
        finish(n - 2, 0)
        finish(n - 1, 1)


def nothing(t, b):
    pass


def three_products(nc, to, left, right, first, last):
    for p, (x, y) in enumerate(((0, 0), (0, 1), (1, 0))):
        mm = nc.tensor.matmul(to, left[x], right[y], start=(first and p == 0), stop=(last and p == 2))
    return mm


def output_rows_1(nc, y_t, w_out, x, gain, x2):
    with Mem(nc, "or1") as m:
        w = m.sb("w", P, 2, D)
        w_hi, w_lo = m.sb_r("w_hi", P, KD, D), m.sb_r("w_lo", P, KD, D)
        g = m.sb("g", P, D)
        y = m.sb("y", P, 2, KD, P)
        y_hi, y_lo = m.sb_r("y_hi", P, 2, KD, P), m.sb_r("y_lo", P, 2, KD, P)
        xr = m.sb("xr", P, 2, D)
        h = m.sb("h", P, 2, D)
        o = m.sb("o", P, 2, D)
        junk = m.sb("junk", P, D)
        stat = m.sb("stat", P, 2, 4)
        eps = m.sb("eps", P, 1)
        ps = [m.ps(f"ps{i}", P, D) for i in range(2)]
        g_in, eps_set = m.sem("g_in"), m.sem("eps_set")
        w_in = [m.sem(f"w_in{i}") for i in range(2)]
        y_in = [m.sem(f"y_in{i}") for i in range(2)]
        x_in = [m.sem(f"x_in{i}") for i in range(2)]
        w_his, w_los, y_his, y_los, proj, added, squared, rooted, inverted, normed, stored, free = (
            m.sem(n) for n in ("w_his", "w_los", "y_his", "y_los", "proj", "added", "squared", "rooted", "inverted", "normed",
                               "stored", "free"))
        block = m.block()
        rows_in = x.rearrange("(t p) d -> t p d", p=P)
        rows_out = x2.rearrange("(t p) d -> t p d", p=P)

        @block.sync
        def _(sp):
            def load(t, b):
                sp.wait_ge(y_los, t + 1)
                sp.dma_start(y[:, b, :, :], y_t[:, :, bass.ds(t * P, P)].rearrange("k p l -> p k l")).then_inc(y_in[b], 16)

            def load_rows(t, b):
                sp.wait_ge(added, t + 1)
                sp.dma_start(xr[:, b, :], rows_in[bass.ds(t, 1), :, :].rearrange("t p d -> p (t d)")).then_inc(x_in[b], 16)

            load(0, 0)
            for k in range(KD):
                if k >= 2:
                    sp.wait_ge(w_los, k - 1)
                sp.dma_start(w[:, k % 2, :], w_out[k * P:(k + 1) * P, :]).then_inc(w_in[k % 2], 16)
            load(1, 1)
            load_rows(0, 0)
            sp.dma_start(g[:, :], every_partition(gain)).then_inc(g_in, 16)
            with sp.Fori(0, TILES // 2 - 1) as i:
                for b in range(2):
                    load(2 * i + b + 2, b)
                    load_rows(2 * i + b + 1, 1 - b)
            load_rows(TILES - 1, 1)

        @block.tensor
        def _(pe):
            pe.sem_inc(proj, 2)
            with pe.Fori(0, TILES // 2) as i:
                for b in range(2):
                    t = 2 * i + b
                    pe.wait_ge(w_los, KD)
                    pe.wait_ge(y_los, t + 3)
                    pe.wait_ge(added, t + 1)
                    for n in range(2):
                        cols = slice(n * NB, (n + 1) * NB)
                        for k in range(KD):
                            mm = three_products(nc, ps[b][:, cols], (y_hi[:, b, k, :], y_lo[:, b, k, :]),
                                                (w_hi[:, k, cols], w_lo[:, k, cols]), k == 0, k == KD - 1)
                    mm.then_inc(proj, 1)

        @block.scalar
        def _(act):
            for k in range(KD):
                act.wait_ge(w_in[k % 2], 16 * (k // 2) + 16)
                nc.scalar.activation(w_hi[:, k, :], w[:, k % 2, :], ACT.Copy).then_inc(w_his, 1)
            act.wait_ge(eps_set, 1)
            nc.scalar.preload_act_table(ACT.Sqrt)

            def prepare(t, b):
                act.wait_ge(y_in[b], 8 * (t - b) + 16)
                act.wait_ge(proj, t + 1)
                nc.scalar.activation(y_hi[:, b, :, :], y[:, b, :, :], ACT.Copy).then_inc(y_his, 1)

            def finish(t, b):
                act.wait_ge(added, t + 3)
                nc.scalar.activation(junk[:, :], h[:, b, :], ACT.Square, accum_out=stat[:, b, 0:1]).then_inc(squared, 1)
                act.wait_ge(squared, t + 1)
                nc.scalar.activation(stat[:, b, 1:2], stat[:, b, 0:1], ACT.Sqrt, scale=1.0 / D, bias=eps[:, :])\
                  .then_inc(rooted, 1)

            ahead(act, TILES, prepare, finish)

        @block.vector
        def _(dve):
            nc.vector.memset(eps[:, :], EPS).then_inc(eps_set, 1)
            dve.sem_inc(added, 2)
            dve.sem_inc(y_los, 2)
            for k in range(KD):
                dve.wait_ge(w_his, k + 1)
                nc.vector.tensor_tensor(w_lo[:, k, :], w[:, k % 2, :], w_hi[:, k, :].bitcast(F32), ALU.subtract).then_inc(w_los, 1)
            dve.wait_ge(g_in, 16)

            def prepare(t, b):
                dve.wait_ge(y_his, t + 1)
                nc.vector.tensor_tensor(y_lo[:, b, :, :], y[:, b, :, :], y_hi[:, b, :, :].bitcast(F32), ALU.subtract)\
                  .then_inc(y_los, 1)

            def finish(t, b):
                dve.wait_ge(x_in[b], 8 * (t - b) + 16)
                dve.wait_ge(proj, t + 3)
                nc.vector.tensor_tensor(h[:, b, :], ps[b][:, :], xr[:, b, :], ALU.add).then_inc(added, 1)
                dve.wait_ge(rooted, t + 1)
                nc.vector.reciprocal(stat[:, b, 2:3], stat[:, b, 1:2]).then_inc(inverted, 1)
                dve.wait_ge(inverted, t + 1)
                dve.wait_ge(free, t + 1)
                nc.vector.scalar_tensor_tensor(out=o[:, b, :], in0=h[:, b, :], scalar=stat[:, b, 2:3], in1=g[:, :],
                                               op0=ALU.mult, op1=ALU.mult).then_inc(normed, 1)

            ahead(dve, TILES, prepare, finish)

        @block.gpsimd
        def _(pool):
            pool.sem_inc(free, 2)
            with pool.Fori(0, TILES // 2) as i:
                for b in range(2):
                    t = 2 * i + b
                    pool.wait_ge(normed, t + 1)
                    pool.dma_start(rows_out[bass.ds(t, 1), :, :].rearrange("t p d -> p (t d)"), o[:, b, :]).then_inc(stored, 16)
                    pool.wait_ge(stored, 16 * t + 16)
                    pool.sem_inc(free, 1)


def modulations(nc, c, c_ctx, w_ada, b_ada, mod):
    NM = 6 * D
    with Mem(nc, "ada") as m:
        w = m.sb("w", P, 2, KD, NB)
        cc = m.sb("cc", P, KD, 2)
        sg = m.sb("sg", P, KD, 2)
        row = m.sb("row", 2, NM)
        bias = m.sb("bias", 2, NM)
        ps = [m.ps(f"ps{i}", 2, NB) for i in range(2)]
        c_in, b_in, gated, ready = (m.sem(n) for n in ("c_in", "b_in", "gated", "ready"))
        loaded = [m.sem(f"loaded{i}") for i in range(2)]
        proj, added, stored = m.sem("proj"), m.sem("added"), m.sem("stored")
        block = m.block()
        wv = w_ada.rearrange("(k p) n -> p k n", p=P)

        @block.sync
        def _(sp):
            for j, v in enumerate((c, c_ctx)):
                sp.dma_start(cc[:, :, j], columns(v, KD), allow_slow_non_contiguous=True).then_inc(c_in, 16)
            sp.dma_start(bias[:, :], every_partition(b_ada, 2)).then_inc(b_in, 16)
            with sp.Fori(0, NM // NB // 2) as i:
                for b in range(2):
                    sp.wait_ge(proj, 2 * i + b + 1)
                    sp.dma_start(w[:, b, :, :], wv[:, :, bass.ds((2 * i + b) * NB, NB)]).then_inc(loaded[b], 16)
            sp.wait_ge(added, NM // NB + 2)
            sp.dma_start(mod, row[:, :]).then_inc(stored, 16)
            sp.wait_ge(stored, 16)

        @block.scalar
        def _(act):
            act.wait_ge(c_in, 32)
            nc.scalar.activation(sg[:, :, :], cc[:, :, :], ACT.Sigmoid).then_inc(gated, 1)

        @block.vector
        def _(dve):
            dve.wait_ge(gated, 1)
            nc.vector.tensor_tensor(cc[:, :, :], cc[:, :, :], sg[:, :, :], ALU.mult).then_inc(ready, 1)
            dve.wait_ge(b_in, 16)
            dve.sem_inc(added, 2)
            with dve.Fori(0, NM // NB // 2) as i:
                for b in range(2):
                    dve.wait_ge(proj, 2 * i + b + 3)
                    cols = bass.ds((2 * i + b) * NB, NB)
                    nc.vector.tensor_tensor(row[:, cols], ps[b][:, :], bias[:, cols], ALU.add).then_inc(added, 1)

        @block.tensor
        def _(pe):
            pe.sem_inc(proj, 2)
            pe.wait_ge(ready, 1)
            with pe.Fori(0, NM // NB // 2) as i:
                for b in range(2):
                    pe.wait_ge(loaded[b], 16 * i + 16)
                    pe.wait_ge(added, 2 * i + b + 1)
                    for k in range(KD):
                        mm = nc.tensor.matmul(ps[b][:, :], cc[:, k, :], w[:, b, k, :], start=(k == 0), stop=(k == KD - 1))
                    mm.then_inc(proj, 1)


def convolved_projection(nc, h_t, w, conv_w, conv_b, xbc):
    with Mem(nc, "cp") as m:
        wt = m.sb("wt", P, 2, KD, P)
        taps = m.sb("taps", P, XT_, KC)
        bias = m.sb("bias", P, XT_)
        rows, half = L // ROWLEN, KC // 2
        pitch = ROWLEN + 2 * half
        XP = rows * pitch
        CP = LC + 2 * half
        pad = m.sb("pad", P, 2, XP + CP)
        acc = m.sb("acc", P, 2, LT)
        y = m.sb("y", P, 2, LT)
        blocks = [(n * NB, NB) for n in range(LB)] + [(L, LC)]
        ps = [m.ps(f"ps{n}", P, NB) for n in range(len(blocks))]
        taps_in, padded = m.sem("taps_in"), m.sem("padded")
        loaded = [m.sem(f"loaded{i}") for i in range(2)]
        proj, kept, tap, silu, stored, free = (m.sem(n) for n in ("proj", "kept", "tap", "silu", "stored", "free"))
        block = m.block()
        wv = w.rearrange("(k p) c -> p k c", p=P)
        NBL = len(blocks)

        @block.sync
        def _(sp):
            sp.dma_start(taps[:, :, :], conv_w.rearrange("(t p) k -> p t k", p=P)).then_inc(taps_in, 16)
            sp.dma_start(bias[:, :], columns(conv_b, XT_), allow_slow_non_contiguous=True).then_inc(taps_in, 16)
            with sp.Fori(0, XT_ // 2) as i:
                for b in range(2):
                    sp.wait_ge(proj, (2 * i + b + 1) * NBL)
                    sp.dma_start(wt[:, b, :, :], wv[:, :, bass.ds((2 * i + b) * P, P)]).then_inc(loaded[b], 16)

        @block.tensor
        def _(pe):
            pe.sem_inc(proj, 2 * NBL)
            with pe.Fori(0, XT_ // 2) as i:
                for b in range(2):
                    pe.wait_ge(loaded[b], 16 * i + 16)
                    for n, (at, size) in enumerate(blocks):
                        pe.wait_ge(kept, (2 * i + b) * NBL + n + 1)
                        for k in range(KD):
                            mm = nc.tensor.matmul(ps[n][:, 0:size], wt[:, b, k, :], h_t[:, k, at:at + size],
                                                  start=(k == 0), stop=(k == KD - 1))
                        mm.then_inc(proj, 1)

        @block.scalar
        def _(act):
            nc.scalar.preload_act_table(ACT.Silu)
            act.wait_ge(padded, 1)
            act.sem_inc(kept, NBL)
            act.sem_inc(silu, 2)

            def activate(t, b):
                act.wait_ge(tap, 2 * KC * (t + 1) + 2)
                act.wait_ge(free, t + 1)
                nc.scalar.activation(y[:, b, :], acc[:, b, :], ACT.Silu).then_inc(silu, 1)

            with act.Fori(0, XT_ // 2) as i:
                for b in range(2):
                    t = 2 * i + b
                    act.wait_ge(silu, t + 1)
                    for n, (at, size) in enumerate(blocks):
                        act.wait_ge(proj, t * NBL + n + 2 * NBL + 1)
                        if n < LB:
                            r = NB // ROWLEN
                            to = pad[:, b, n * r * pitch:(n + 1) * r * pitch].rearrange("p (r c) -> p r c", c=pitch)
                            nc.scalar.activation(to[:, :, half:half + ROWLEN], ps[n][:, :].rearrange("p (r c) -> p r c", c=ROWLEN),
                                                 ACT.Copy).then_inc(kept, 1)
                        else:
                            nc.scalar.activation(pad[:, b, XP + half:XP + half + LC], ps[n][:, 0:LC], ACT.Copy).then_inc(kept, 1)
                    activate(t, b)

        @block.vector
        def _(dve):
            nc.vector.memset(pad[:, :, :], 0.0).then_inc(padded, 1)
            dve.wait_ge(taps_in, 32)
            dve.sem_inc(tap, 2)
            with dve.Fori(0, XT_ // 2) as i:
                for b in range(2):
                    t = 2 * i + b
                    grid = pad[:, b, 0:XP].rearrange("p (r c) -> p r c", c=pitch)
                    parts = [(acc[:, b, 0:L].rearrange("p (r c) -> p r c", c=ROWLEN), lambda k: grid[:, :, k:k + ROWLEN]),
                             (acc[:, b, L:LT], lambda k: pad[:, b, XP + k:XP + k + LC])]
                    dve.wait_ge(kept, (t + 2) * NBL)
                    dve.wait_ge(silu, t + 1)
                    for k in range(KC):
                        for x, (to, src) in enumerate(parts):
                            one = taps[:, bass.ds(t, 1), k]
                            if k == 0:
                                nc.vector.tensor_scalar(to, src(0), one, bias[:, bass.ds(t, 1)], ALU.mult, ALU.add).then_inc(tap, 1)
                            else:
                                dve.wait_ge(tap, 2 * KC * t + 2 * (k - 1) + x + 3)
                                nc.vector.scalar_tensor_tensor(out=to, in0=src(k), scalar=one, in1=to, op0=ALU.mult,
                                                               op1=ALU.add).then_inc(tap, 1)

        @block.gpsimd
        def _(pool):
            pool.sem_inc(free, 2)
            with pool.Fori(0, XT_ // 2) as i:
                for b in range(2):
                    t = 2 * i + b
                    pool.wait_ge(silu, t + 3)
                    pool.dma_start(xbc[bass.ds(t, 1), :, :].rearrange("k p l -> p (k l)"), y[:, b, :]).then_inc(stored, 16)
                    pool.wait_ge(stored, 16 * t + 16)
                    pool.sem_inc(free, 1)


def decays(nc, h_t, w_dt, dt_bias, a_log, decay_rows, totals, decay_cols, ident):
    R2 = 64
    CH = LT // P
    with Mem(nc, "dec") as m:
        w = m.sb("w", P, KD, R2)
        bias, al = m.sb("bias", R2, 1), m.sb("al", R2, 1)
        v, n_, e, z, a, reset = (m.sb(n, R2, LT) for n in ("v", "n", "e", "z", "a", "reset"))
        dt_, wgt = m.sb("dt", R2, LT), m.sb("wgt", R2, LT)
        tot, etot = m.sb("tot", R2, CH), m.sb("etot", R2, CH)
        cols = m.sb("cols", P, CH, 3, R2)
        blocks = [(n * NB, NB) for n in range(LB)] + [(L, LC)]
        ps = [m.ps(f"ps{n}", R2, NB) for n in range(len(blocks))]
        pst = [m.ps(f"pst{n}", P, 3, R2) for n in range(2)]
        zeroed, loaded, proj, kept, link, exped, ready, turned, placed, stored = (
            m.sem(n) for n in ("zeroed", "loaded", "proj", "kept", "link", "exped", "ready", "turned", "placed", "stored"))
        block = m.block()
        halves = (slice(0, HEADS), slice(32, 32 + HEADS))

        @block.sync
        def _(sp):
            sp.wait_ge(zeroed, 3)
            for x in range(2):
                sp.dma_start(w[:, :, halves[x]], w_dt[:, x * HEADS:(x + 1) * HEADS].rearrange("(k p) h -> p k h", p=P))\
                  .then_inc(loaded, 16)
                sp.dma_start(bias[halves[x], :], dt_bias[x].rearrange("(h o) -> h o", o=1)).then_inc(loaded, 16)
                sp.dma_start(al[halves[x], :], a_log[x].rearrange("(h o) -> h o", o=1)).then_inc(loaded, 16)
            sp.wait_ge(ready, 1)
            for x in range(2):
                hs = slice(x * HEADS, (x + 1) * HEADS)
                sp.dma_start(decay_rows[:, hs, :].rearrange("c h l -> h c l"),
                             a[halves[x], :].rearrange("h (c l) -> h c l", l=P)).then_inc(stored, 16)
            sp.wait_ge(exped, 5)
            for x in range(2):
                hs = slice(x * HEADS, (x + 1) * HEADS)
                sp.dma_start(totals[:, hs].rearrange("c h -> h c"), etot[halves[x], :], allow_slow_non_contiguous=True)\
                  .then_inc(stored, 16)
            sp.wait_ge(placed, CH)
            sp.dma_start(decay_cols.rearrange("c p x -> p c x"), cols[:, :, :, :].rearrange("p c a b -> p c (a b)"))\
              .then_inc(stored, 16)
            sp.wait_ge(stored, 80)

        @block.gpsimd
        def _(pool):
            nc.gpsimd.memset(w[:, :, :], 0.0).then_inc(zeroed, 1)
            nc.gpsimd.memset(bias[:, :], 0.0).then_inc(zeroed, 1)
            nc.gpsimd.memset(al[:, :], 0.0).then_inc(zeroed, 1)

        @block.tensor
        def _(pe):
            pe.wait_ge(loaded, 96)
            for n, (at, size) in enumerate(blocks):
                for k in range(KD):
                    mm = nc.tensor.matmul(ps[n][:, 0:size], w[:, k, :], h_t[:, k, at:at + size], start=(k == 0), stop=(k == KD - 1))
                mm.then_inc(proj, 1)
            pe.wait_ge(ready, 2)
            for c in range(CH):
                if c >= 2:
                    pe.wait_ge(placed, c - 1)
                for x, of in enumerate((dt_, a, wgt)):
                    t = nc.tensor.transpose(pst[c % 2][:, x, :], of[:, c * P:(c + 1) * P], ident[0:R2, 0:R2])
                t.then_inc(turned, 1)

        @block.scalar
        def _(act):
            act.wait_ge(loaded, 96)
            nc.scalar.activation(al[:, :], al[:, :], ACT.Exp).then_inc(exped, 1)
            act.wait_ge(kept, 1)
            nc.scalar.activation(e[:, :], n_[:, :], ACT.Exp).then_inc(exped, 1)
            act.wait_ge(kept, 2)
            nc.scalar.activation(wgt[:, :], wgt[:, :], ACT.Exp).then_inc(exped, 1)
            nc.scalar.activation(etot[:, :], tot[:, :], ACT.Exp).then_inc(exped, 2)

        @block.vector
        def _(dve):
            n = [0]

            def then(ins):
                n[0] += 1
                ins.then_inc(link, 1)
                dve.wait_ge(link, n[0])

            chunks = [t[:, :].rearrange("h (c l) -> h c l", l=P) for t in (a, wgt, dt_, z)]
            then(nc.vector.memset(reset[:, :], 1.0))
            then(nc.vector.memset(reset[:, 0:LT:P], 0.0))
            dve.wait_ge(loaded, 96)
            for k, (at, size) in enumerate(blocks):
                dve.wait_ge(proj, k + 1)
                then(nc.vector.tensor_scalar(v[:, at:at + size], ps[k][:, 0:size], bias[:, :], None, ALU.add))
            then(nc.vector.tensor_scalar(n_[:, :], v[:, :], -1.0, None, ALU.mult))
            then(nc.vector.tensor_tensor(n_[:, :], n_[:, :], v[:, :], ALU.min))
            dve.sem_inc(kept, 1)
            then(nc.vector.tensor_scalar(v[:, :], v[:, :], 0.0, None, ALU.max))
            dve.wait_ge(exped, 2)
            then(nc.vector.tensor_scalar(n_[:, :], e[:, :], 2.0, None, ALU.add))
            then(nc.vector.reciprocal(n_[:, :], n_[:, :]))
            then(nc.vector.tensor_tensor(z[:, :], e[:, :], n_[:, :], ALU.mult))
            then(nc.vector.tensor_tensor(n_[:, :], z[:, :], z[:, :], ALU.mult))
            then(nc.vector.tensor_scalar(e[:, :], n_[:, :], 1.0 / 15, None, ALU.mult))
            for k in range(13, 1, -2):
                then(nc.vector.scalar_tensor_tensor(out=e[:, :], in0=e[:, :], scalar=1.0 / k, in1=n_[:, :], op0=ALU.add, op1=ALU.mult))
            then(nc.vector.scalar_tensor_tensor(out=e[:, :], in0=e[:, :], scalar=1.0, in1=z[:, :], op0=ALU.add, op1=ALU.mult))
            then(nc.vector.scalar_tensor_tensor(out=dt_[:, :], in0=e[:, :], scalar=2.0, in1=v[:, :], op0=ALU.mult, op1=ALU.add))
            then(nc.vector.tensor_scalar(al[:, :], al[:, :], -1.0, None, ALU.mult))
            then(nc.vector.tensor_scalar(z[:, :], dt_[:, :], al[:, :], None, ALU.mult))
            then(nc.vector.tensor_tensor_scan(out=a[:, :], data0=reset[:, :], data1=z[:, :], initial=0.0, op0=ALU.mult, op1=ALU.add))
            then(nc.vector.tensor_copy(tot[:, :], a[:, P - 1:LT:P]))
            b = slice(32, R2)
            whole = over(tot[:, :, None], (R2, CH, P))
            then(nc.vector.tensor_tensor(chunks[0][b], whole[b], chunks[0][b], ALU.subtract))
            then(nc.vector.tensor_tensor(chunks[0][b], chunks[0][b], chunks[3][b], ALU.add))
            then(nc.vector.tensor_tensor(chunks[1], whole, chunks[0], ALU.subtract))
            dve.sem_inc(ready, 1)
            dve.sem_inc(kept, 1)
            dve.wait_ge(exped, 5)
            then(nc.vector.tensor_tensor(wgt[:, :], wgt[:, :], dt_[:, :], ALU.mult))
            dve.sem_inc(ready, 1)
            for c in range(CH):
                dve.wait_ge(turned, c + 1)
                nc.vector.tensor_copy(cols[:, c, :, :], pst[c % 2][:, :, :]).then_inc(placed, 1)


def turn_chunk(nc, xc, pst, tiles, ident):
    for k in range(tiles):
        t = nc.tensor.transpose(pst[:, k, :], xc[:, k, :], ident[:, :])
    return t


def chunk_states(nc, rows, xw, pss):
    XR = SW // P
    for g in range(SG):
        mm = nc.tensor.matmul(pss[:, g // 2, (g % 2) * HR * HD:(g % 2 + 1) * HR * HD], rows[:, XR + g, :],
                              xw[:, g * HR:(g + 1) * HR, :].rearrange("p h d -> p (h d)"), start=True, stop=True)
    return mm


def states_view(h):
    return h.rearrange("p (b x) d -> p b (x d)", b=2)


def context_states(nc, xbc, totals, decay_cols, hf, hb, ident):
    XR, TS = SW // P, SW // P + SG
    with Mem(nc, "cst") as m:
        xc = m.sb("xc", P, CCH, TS, P)
        dc = m.sb("dc", P, CCH, 3, 64)
        dec = m.sb("dec", P, LT // P, 2 * HEADS)
        rows = m.sb("rows", P, TS, P)
        xw = m.sb("xw", P, HEADS, HD)
        pst = m.ps("pst", P, 12, P)
        pss = m.ps("pss", P, 2, NB)
        loaded, turned, kept, weighted, made, link = (m.sem(n) for n in ("loaded", "turned", "kept", "weighted", "made", "link"))
        block = m.block()
        work = [(0, 0, hf, True), (0, 1, hb, True), (1, 0, hf, False), (1, 1, hb, False)]

        @block.sync
        def _(sp):
            for c in range(CCH):
                sp.dma_start(xc[:, c, :, :], xbc[0:TS, :, L + c * P:L + (c + 1) * P].rearrange("k p l -> p k l")).then_inc(loaded, 16)
                sp.dma_start(dc[:, c, :, :].rearrange("p a b -> p (a b)"), decay_cols[NCH + c, :, :]).then_inc(loaded, 16)
            sp.dma_start(dec[:, :, :].rearrange("p c h -> p (c h)"), every_partition(totals.rearrange("c h -> (c h)")))\
              .then_inc(loaded, 16)

        @block.tensor
        def _(pe):
            pe.wait_ge(loaded, 80)
            for c in range(CCH):
                if c:
                    pe.wait_ge(kept, c)
                turn_chunk(nc, xc[:, c, :, :], pst, TS, ident).then_inc(turned, 1)
                for x in range(2):
                    pe.wait_ge(weighted, 2 * c + x + 1)
                    chunk_states(nc, rows, xw, pss).then_inc(made, 1)

        @block.scalar
        def _(act):
            for c in range(CCH):
                act.wait_ge(turned, c + 1)
                if c:
                    act.wait_ge(made, 2 * c)
                nc.scalar.activation(rows[:, :, :], pst[:, 0:TS, :], ACT.Copy).then_inc(kept, 1)

        @block.vector
        def _(dve):
            n = [0]

            def then(ins):
                n[0] += 1
                ins.then_inc(link, 1)
                dve.wait_ge(link, n[0])

            dve.wait_ge(loaded, 80)
            for w, (c, x, h, first) in enumerate(work):
                dve.wait_ge(kept, c + 1)
                if w:
                    dve.wait_ge(made, w)
                nc.vector.tensor_tensor(xw[:, :, :], rows[:, 0:XR, :].rearrange("p k (h d) -> p (k h) d", d=HD),
                                        over(dc[:, c, 2, 32 * x:32 * x + HEADS, None], (P, HEADS, HD)), ALU.mult).then_inc(weighted, 1)
                dve.wait_ge(made, w + 1)
                sts = pss[:, :, 0:2 * HR * HD]
                if first:
                    then(nc.vector.tensor_copy(states_view(h), sts))
                elif x == 0:
                    then(nc.vector.tensor_tensor(h, h, over(dec[:, NCH + 1, 0:HEADS, None], (P, HEADS, HD)), ALU.mult))
                    then(nc.vector.tensor_tensor(states_view(h), states_view(h), sts, ALU.add))
                else:
                    t = xw[:, :, :]
                    then(nc.vector.tensor_copy(states_view(t), sts))
                    then(nc.vector.tensor_tensor(t, t, over(dec[:, NCH, HEADS:2 * HEADS, None], (P, HEADS, HD)), ALU.mult))
                    then(nc.vector.tensor_tensor(h, h, t, ALU.add))


def backward_states(nc, xbc, totals, decay_cols, hb, hb_in, ident):
    XR, TS = SW // P, SW // P + SG
    with Mem(nc, "bst") as m:
        xc = m.sb("xc", P, 2, TS, P)
        dc = m.sb("dc", P, 2, 3 * 64)
        dec = m.sb("dec", P, LT // P, 2 * HEADS)
        rows = m.sb("rows", P, 2, TS, P)
        xw = m.sb("xw", P, 2, HEADS, HD)
        h = m.sb("h", P, 2, HEADS, HD)
        pst = [m.ps(f"pst{i}", P, 12, P) for i in range(2)]
        pss = m.ps("pss", P, 2, NB)
        start, turned, kept, weighted, made, decayed, ahead, stored, free, begun = (
            m.sem(n) for n in ("start", "turned", "kept", "weighted", "made", "decayed", "ahead", "stored", "free", "begun"))
        loaded = [m.sem(f"loaded{i}") for i in range(2)]
        block = m.block()

        @block.sync
        def _(sp):
            sp.dma_start(dec[:, :, :].rearrange("p c h -> p (c h)"), every_partition(totals.rearrange("c h -> (c h)")))\
              .then_inc(start, 16)
            chunk = sp.alloc_register("back_sp")
            sp.reg_mov(chunk, NCH + 1)
            with sp.Fori(0, NCH // 2) as i:
                sp.reg_sub(chunk, chunk, 2)
                last = sp.snap(chunk, min_val=1, max_val=NCH - 1)
                for b in range(2):
                    t = 2 * i + b
                    sp.wait_ge(turned, t + 1)
                    sp.wait_ge(weighted, t + 1)
                    c = last - b
                    sp.dma_start(xc[:, b, :, :], xbc[0:TS, :, bass.ds(c * P, P)].rearrange("k p l -> p k l")).then_inc(loaded[b], 16)
                    sp.dma_start(dc[:, b, :], decay_cols[bass.ds(c, 1), :, :].rearrange("c p x -> p (c x)")).then_inc(loaded[b], 16)

        @block.tensor
        def _(pe):
            pe.sem_inc(turned, 2)
            pe.sem_inc(made, 2)
            with pe.Fori(0, NCH // 2) as i:
                for b in range(2):
                    t = 2 * i + b
                    pe.wait_ge(loaded[b], 32 * i + 32)
                    pe.wait_ge(kept, t + 1)
                    turn_chunk(nc, xc[:, b, :, :], pst[b], TS, ident).then_inc(turned, 1)
                    pe.wait_ge(weighted, t + 3)
                    pe.wait_ge(ahead, t + 1)
                    chunk_states(nc, rows[:, b, :, :], xw[:, b, :, :], pss).then_inc(made, 1)

        @block.scalar
        def _(act):
            act.sem_inc(kept, 2)
            with act.Fori(0, NCH // 2) as i:
                for b in range(2):
                    t = 2 * i + b
                    act.wait_ge(turned, t + 3)
                    act.wait_ge(made, t + 1)
                    nc.scalar.activation(rows[:, b, :, :], pst[b][:, 0:TS, :], ACT.Copy).then_inc(kept, 1)

        @block.vector
        def _(dve):
            dve.sem_inc(weighted, 2)
            dve.sem_inc(ahead, 1)
            dve.wait_ge(start, 16)
            nc.vector.tensor_copy(h[:, 0, :, :], hb[:, :, :]).then_inc(begun, 1)
            dve.wait_ge(begun, 1)
            chunk = dve.alloc_register("back_dve")
            dve.reg_mov(chunk, NCH + 1)
            with dve.Fori(0, NCH // 2) as i:
                dve.reg_sub(chunk, chunk, 2)
                last = dve.snap(chunk, min_val=1, max_val=NCH - 1)
                for b in range(2):
                    t = 2 * i + b
                    dve.wait_ge(kept, t + 3)
                    nc.vector.tensor_tensor(xw[:, b, :, :], rows[:, b, 0:XR, :].rearrange("p k (h d) -> p (k h) d", d=HD),
                                            over(dc[:, b, 128 + 32:128 + 32 + HEADS, None], (P, HEADS, HD)), ALU.mult)\
                      .then_inc(weighted, 1)
                    dve.wait_ge(free, t + 1)
                    nc.vector.tensor_tensor(h[:, 1 - b, :, :], h[:, b, :, :],
                                            over(dec[:, bass.ds(last - b, 1), HEADS:2 * HEADS].rearrange("p c h -> p (c h)")[:, :, None],
                                                 (P, HEADS, HD)), ALU.mult).then_inc(decayed, 1)
                    dve.wait_ge(decayed, t + 1)
                    dve.wait_ge(made, t + 3)
                    nc.vector.tensor_tensor(states_view(h[:, 1 - b, :, :]), states_view(h[:, 1 - b, :, :]),
                                            pss[:, :, 0:2 * HR * HD], ALU.add).then_inc(ahead, 1)
                    dve.wait_ge(ahead, t + 2)

        @block.gpsimd
        def _(pool):
            pool.sem_inc(free, 1)
            pool.wait_ge(begun, 1)
            chunk = pool.alloc_register("back_pool")
            pool.reg_mov(chunk, NCH + 1)
            with pool.Fori(0, NCH // 2) as i:
                pool.reg_sub(chunk, chunk, 2)
                last = pool.snap(chunk, min_val=1, max_val=NCH - 1)
                for b in range(2):
                    t = 2 * i + b
                    pool.wait_ge(ahead, t + 1)
                    pool.dma_start(hb_in[bass.ds(last - b, 1), :, :].rearrange("c p x -> p (c x)"),
                                   h[:, b, :, :].rearrange("p h d -> p (h d)")).then_inc(stored, 16)
                    pool.wait_ge(stored, 16 * t + 16)
                    pool.sem_inc(free, 1)


def ssd_outputs(nc, xbc, silu_z, decay_rows, totals, decay_cols, d_skip, hf, hb_in, y_t, ident, ones):
    XR = SW // P
    TS = XR + SG
    H2 = 2 * HEADS
    IN = 4
    with Mem(nc, "so") as m:
        xc = m.sb("xc", P, IN, XT_, P)
        dc = m.sb("dc", P, IN, 3 * 64)
        decay = m.sb("decay", P, 2, H2, P)
        z = m.sb("z", P, IN, XR, P)
        hb = m.sb("hb", P, IN, HEADS, HD)
        h = m.sb("h", P, 2, HEADS, HD)
        dec = m.sb("dec", P, LT // P, H2)
        skip = m.sb("skip", P, XR)
        mask = m.sb("mask", P, 2, P)
        seg = m.sb("seg", P, 2, H2, P)
        cs = m.sb("cs", P, 2, H2, P)
        sm = m.sb("sm", P, 2, 2, SG, P)
        rows = m.sb("rows", P, 2, TS, P)
        xw = m.sb("xw", P, 2, HEADS, HD)
        xd = m.sb("xd", P, 2, 2, HEADS, HD)
        y = m.sb("y", P, 2, XR, P)
        pst = m.ps("pst", P, 12, P)
        psc = m.ps("psc", P, SG, P)
        psy = m.ps("psy", P, 8, P)
        pss = m.ps("pss", P, 2, NB)
        start, masks, begun = m.sem("start"), m.sem("masks"), m.sem("begun")
        loaded = [m.sem(f"loaded{i}") for i in range(IN)]
        decay_in = [m.sem(f"decay_in{i}") for i in range(2)]
        stored = [m.sem(f"stored{i}") for i in range(2)]
        (turned, scored, made_s, made_y, kept, seg_exp, grown, seg_max, weighted, masked, cs_f, cs_b, mix_f, mix_b,
         skipped, gated, decayed, ahead) = (m.sem(n) for n in (
            "turned", "scored", "made_s", "made_y", "kept", "seg_exp", "grown", "seg_max", "weighted", "masked", "cs_f",
            "cs_b", "mix_f", "mix_b", "skipped", "gated", "decayed", "ahead"))
        x_dt = m.sem("x_dt")
        block = m.block()
        A, DT, W = 64, 0, 128
        heads = [(x, hh, x * HEADS + hh) for x in range(2) for hh in range(HEADS)]
        by_group = "p (g r) q -> p g r q"

        def chunks(eng, prepare, finish):
            prepare(0, 0, 0)
            with eng.Fori(0, NCH // IN - 1) as i:
                for s in range(IN):
                    prepare(IN * i + s + 1, (s + 1) % IN, i + (s + 1) // IN)
                    finish(IN * i + s, s, i)
            for s in range(IN):
                if s + 1 < IN:
                    prepare(NCH - IN + s + 1, s + 1, NCH // IN - 1)
                finish(NCH - IN + s, s, NCH // IN - 1)

        def load_decay(eng, c, b):
            eng.dma_start(decay[:, b, :, :].rearrange("p h l -> p (h l)"),
                          decay_rows[bass.ds(c, 1), :, :].rearrange("c h l -> (c h l)").partition_broadcast(P))\
               .then_inc(decay_in[b], 16)

        def load(sp, c, s):
            at = bass.ds(c * P, P)
            one = bass.ds(c, 1)
            sp.dma_start(xc[:, s, :, :], xbc[:, :, at].rearrange("k p l -> p k l")).then_inc(loaded[s], 16)
            sp.dma_start(dc[:, s, :], decay_cols[one, :, :].rearrange("c p x -> p (c x)")).then_inc(loaded[s], 16)
            sp.dma_start(z[:, s, :, :], silu_z[:, :, at].rearrange("k p l -> p k l")).then_inc(loaded[s], 16)
            sp.dma_start(hb[:, s, :, :].rearrange("p h d -> p (h d)"), hb_in[one, :, :].rearrange("c p x -> p (c x)"))\
              .then_inc(loaded[s], 16)

        def store(sp, c, b):
            sp.dma_start(y_t[FW // P:, :, bass.ds(c * P, P)].rearrange("k p l -> p k l"), y[:, b, :, :]).then_inc(stored[b], 16)

        @block.sync
        def _(sp):
            sp.dma_start(dec[:, :, :].rearrange("p c h -> p (c h)"), every_partition(totals.rearrange("c h -> (c h)")))\
              .then_inc(start, 16)
            for g in range(2):
                sp.dma_start(skip[HD * g:HD * g + HD, :], d_skip[g::2].partition_broadcast(HD),
                             allow_slow_non_contiguous=True).then_inc(start, 16)
            for s in range(IN):
                load(sp, s, s)
            with sp.Fori(0, NCH // IN - 1) as i:
                for s in range(IN):
                    sp.wait_ge(gated, IN * i + s + 1)
                    store(sp, IN * i + s, s % 2)
                    load(sp, IN * i + s + IN, s)
            for s in range(IN):
                sp.wait_ge(gated, NCH - IN + s + 1)
                store(sp, NCH - IN + s, s % 2)
            for b in range(2):
                sp.wait_ge(stored[b], 16 * (NCH // 2) + 16)

        @block.tensor
        def _(pe):
            def prepare(c, s, i):
                b = s % 2
                pe.wait_ge(loaded[s], 64 * i + 64)
                pe.wait_ge(kept, c + 1)
                turn_chunk(nc, xc[:, s, :, :], pst, TS, ident).then_inc(turned, 1)
                pe.wait_ge(masked, c + 1)
                for g in range(SG):
                    mm = nc.tensor.matmul(psc[:, g, :], xc[:, s, XR + g, :], xc[:, s, TS + g, :], start=True, stop=True)
                mm.then_inc(scored, 1)

            def finish(c, s, i):
                b = s % 2
                pe.wait_ge(weighted, c + 1)
                pe.wait_ge(ahead, c + 1)
                chunk_states(nc, rows[:, b, :, :], xw[:, b, :, :], pss).then_inc(made_s, 1)
                pe.wait_ge(skipped, c + 1)
                pe.wait_ge(cs_f, c + 1)
                pe.wait_ge(mix_f, c + 1)
                pe.wait_ge(cs_b, c + 1)
                pe.wait_ge(mix_b, c + 1)
                pe.wait_ge(x_dt, 2 * c + 2)
                for hh in range(HEADS):
                    to = psy[HD * (hh % 2):HD * (hh % 2) + HD, hh // 2, :]
                    nc.tensor.matmul(to, xd[:, b, 0, hh, :], seg[:, b, hh, :], start=True, stop=False)
                    nc.tensor.matmul(to, h[:, b, hh, :], cs[:, b, hh, :], start=False, stop=False)
                    nc.tensor.matmul(to, xd[:, b, 1, hh, :], seg[:, b, HEADS + hh, :], start=False, stop=False)
                    mm = nc.tensor.matmul(to, hb[:, s, hh, :], cs[:, b, HEADS + hh, :], start=False, stop=True)
                mm.then_inc(made_y, 1)

            chunks(pe, prepare, finish)

        @block.scalar
        def _(act):
            nc.scalar.preload_act_table(ACT.Exp)
            act.sem_inc(kept, 1)
            for b in range(2):
                load_decay(act, b, b)

            def prepare(c, s, i):
                b = s % 2
                act.wait_ge(loaded[s], 64 * i + 64)
                act.wait_ge(decay_in[b], IN // 2 * 16 * i + 16 * (s // 2) + 16)
                act.wait_ge(made_y, c + 1)
                nc.scalar.activation(cs[:, b, :, :], decay[:, b, :, :], ACT.Exp).then_inc(grown, 1)
                for x, hh, n in heads:
                    last = nc.scalar.activation(seg[:, b, n, :], decay[:, b, n, :], ACT.Relu, scale=-1.0,
                                                bias=dc[:, s, A + 32 * x + hh:A + 32 * x + hh + 1])
                last.then_inc(seg_max, 1)
                act.wait_ge(turned, c + 1)
                nc.scalar.activation(rows[:, b, :, :], pst[:, 0:TS, :], ACT.Copy).then_inc(kept, 1)
                act.wait_ge(seg_max, c + 1)
                if not (isinstance(c, int) and c >= NCH - 2):
                    act.wait_ge(grown, c + 1)
                    load_decay(act, c + 2, b)
                nc.scalar.activation(seg[:, b, :, :], seg[:, b, :, :], ACT.Exp, scale=-1.0).then_inc(seg_exp, 1)

            chunks(act, prepare, lambda c, s, i: None)

        @block.vector
        def _(dve):
            dve.wait_ge(start, 48)
            dve.sem_inc(masked, 1)
            dve.sem_inc(ahead, 1)
            dve.sem_inc(skipped, 1)
            for b in range(2):
                dve.sem_inc(stored[b], 16)
            dve.sem_inc(made_y, 2)
            nc.vector.tensor_copy(h[:, 0, :, :], hf[:, :, :]).then_inc(begun, 1)
            dve.wait_ge(begun, 1)
            dve.wait_ge(masks, 4)

            def prepare(c, s, i):
                b = s % 2
                dve.wait_ge(grown, c + 1)
                dve.wait_ge(scored, c + 1)
                for x in range(2):
                    last = nc.vector.tensor_tensor(sm[:, b, x, :, :], psc[:, :, :], over(mask[:, x, None, :], (P, SG, P)), ALU.mult)
                last.then_inc(masked, 1)
                half = cs[:, b, 0:HEADS, :].rearrange(by_group, r=HR)
                nc.vector.tensor_tensor(half, half, over(xc[:, s, TS:, None, :], (P, SG, HR, P)), ALU.mult).then_inc(cs_f, 1)
                dve.wait_ge(kept, c + 2)
                nc.vector.tensor_tensor(xw[:, b, :, :], rows[:, b, 0:XR, :].rearrange("p k (h d) -> p (k h) d", d=HD),
                                        over(dc[:, s, W:W + HEADS, None], (P, HEADS, HD)), ALU.mult).then_inc(weighted, 1)
                nc.vector.tensor_tensor(xd[:, b, 0, :, :], rows[:, b, 0:XR, :].rearrange("p k (h d) -> p (k h) d", d=HD),
                                        over(dc[:, s, DT:DT + HEADS, None], (P, HEADS, HD)), ALU.mult).then_inc(x_dt, 1)
                dve.wait_ge(masked, c + 2)
                dve.wait_ge(seg_exp, c + 1)
                half = seg[:, b, 0:HEADS, :].rearrange(by_group, r=HR)
                nc.vector.tensor_tensor(half, half, over(sm[:, b, 0, :, None, :], (P, SG, HR, P)), ALU.mult).then_inc(mix_f, 1)

            def finish(c, s, i):
                b = s % 2
                dve.wait_ge(made_y, c + 2)
                nc.vector.tensor_tensor(h[:, 1 - b, :, :], h[:, b, :, :],
                                        over(dec[:, bass.ds(c, 1), 0:HEADS].rearrange("p c h -> p (c h)")[:, :, None],
                                             (P, HEADS, HD)), ALU.mult).then_inc(decayed, 1)
                dve.wait_ge(decayed, c + 1)
                dve.wait_ge(made_s, c + 1)
                nc.vector.tensor_tensor(states_view(h[:, 1 - b, :, :]), states_view(h[:, 1 - b, :, :]),
                                        pss[:, :, 0:2 * HR * HD], ALU.add).then_inc(ahead, 1)
                dve.wait_ge(stored[b], IN // 2 * 16 * i + 16 * (s // 2) + 16)
                dve.wait_ge(made_y, c + 3)
                for k in range(XR):
                    last = nc.vector.scalar_tensor_tensor(out=y[:, b, k, :], in0=xc[:, s, k, :], scalar=skip[:, k:k + 1],
                                                          in1=psy[:, k, :], op0=ALU.mult, op1=ALU.add)
                last.then_inc(skipped, 1)
                dve.wait_ge(skipped, c + 2)
                nc.vector.tensor_tensor(y[:, b, :, :], y[:, b, :, :], z[:, s, :, :], ALU.mult).then_inc(gated, 1)

            chunks(dve, prepare, finish)

        @block.gpsimd
        def _(pool):
            nc.gpsimd.memset(mask[:, :, :], 1.0).then_inc(masks, 1)
            pool.wait_ge(masks, 1)
            for x, sign in ((0, 1), (1, -1)):
                nc.gpsimd.affine_select(out=mask[:, x, :], in_=mask[:, x, :], compare_op=ALU.is_ge, fill=0.0, base=0,
                                        pattern=[[sign, P]], channel_multiplier=-sign).then_inc(masks, 1)
            pool.sem_inc(masks, 1)
            pool.wait_ge(masks, 4)

            def prepare(c, s, i):
                b = s % 2
                pool.wait_ge(grown, c + 1)
                half = cs[:, b, HEADS:, :].rearrange(by_group, r=HR)
                nc.gpsimd.tensor_tensor(half, half, over(xc[:, s, TS:, None, :], (P, SG, HR, P)), ALU.mult).then_inc(cs_b, 1)
                pool.wait_ge(kept, c + 2)
                nc.gpsimd.tensor_tensor(xd[:, b, 1, :, :], rows[:, b, 0:XR, :].rearrange("p k (h d) -> p (k h) d", d=HD),
                                        over(dc[:, s, DT + 32:DT + 32 + HEADS, None], (P, HEADS, HD)), ALU.mult).then_inc(x_dt, 1)
                pool.wait_ge(masked, c + 2)
                pool.wait_ge(seg_exp, c + 1)
                half = seg[:, b, HEADS:, :].rearrange(by_group, r=HR)
                nc.gpsimd.tensor_tensor(half, half, over(sm[:, b, 1, :, None, :], (P, SG, HR, P)), ALU.mult).then_inc(mix_b, 1)

            chunks(pool, prepare, lambda c, s, i: None)


def fourier_tables():
    B, A8 = L // P, 8
    kb = np.outer(np.arange(B), np.arange(B)) * (2 * np.pi / B)
    eye = np.eye(A8)
    over_b = np.stack([np.kron(np.cos(kb), eye), -np.kron(np.sin(kb), eye)], 1)
    kc = np.outer(np.arange(FG), np.arange(FG)) * (2 * np.pi / FG)
    two = np.eye(P // FG)
    c, s = np.kron(two, np.cos(kc)), np.kron(two, np.sin(kc))
    over_c = np.stack([np.concatenate([c, -s], 1), np.concatenate([s, c], 1)], 1)
    k = (B * np.arange(P)[None, :] + np.arange(B)[:, None]).reshape(-1)
    ka = (np.arange(P)[:, None] * k[None, :] % L) * (2 * np.pi / L)
    over_a = np.stack([np.cos(ka), np.sin(ka)], 1)
    return [np.ascontiguousarray(t, np.float32) for t in (over_b, over_c, over_a)]


def fourier_mix(nc, h_t, w_u, over_b, over_c, over_a, y_t):
    B, A8 = L // P, 8
    NA = P // A8
    FT2 = FW // P
    SCALE = 1.0 / math.sqrt(L * FG)
    with Mem(nc, "fo") as m:
        w = m.sb("w", P, KD, FW)
        tb = m.sb("tb", P, 2 * P)
        tc = m.sb("tc", P, 2, 2 * P)
        ta = m.sb("ta", P, 2, L)
        slab = m.sb("slab", P, 2, KD, P)
        u = m.sb("u", P, 2, FW)
        g = m.sb("g", P, FT2, 2 * B, P)
        gs = m.sb("gs", P, 2, FT2 * 2, P)
        hs = m.sb("hs", P, 2, FT2, 2, P)
        y = m.sb("y", P, FT2, L)
        psu = [m.ps(f"psu{i}", P, FW) for i in range(2)]
        psg = [m.ps(f"psg{i}", P, FT2, 2 * P) for i in range(2)]
        psh = [m.ps(f"psh{i}", P, FT2, 2 * P) for i in range(2)]
        psy = [m.ps(f"psy{i}", P, FT2, P) for i in range(2)]
        (loaded, cut, proj, kept_u, made_g, kept_g, cut_g, made_h, kept_h, made_y, kept_y, stored) = (m.sem(n) for n in (
            "loaded", "cut", "proj", "kept_u", "made_g", "kept_g", "cut_g", "made_h", "kept_h", "made_y", "kept_y", "stored"))
        block = m.block()

        @block.sync
        def _(sp):
            sp.dma_start(w[:, :, :], w_u.rearrange("(k p) c -> p k c", p=P)).then_inc(loaded, 16)
            sp.dma_start(tb[:, :], over_b.rearrange("p r c -> p (r c)")).then_inc(loaded, 16)
            sp.dma_start(tc[:, :, :], over_c).then_inc(loaded, 16)
            sp.dma_start(ta[:, :, :], over_a).then_inc(loaded, 16)
            sp.wait_ge(kept_y, B + 2)
            for k in range(FT2):
                sp.dma_start(y_t[k, :, :], y[:, k, :]).then_inc(stored, 16)
            sp.wait_ge(stored, 16 * FT2)

        @block.scalar
        def _(act):
            act.sem_inc(cut, 2)
            with act.Fori(0, NA // 2) as i:
                for b in range(2):
                    t = 2 * i + b
                    act.wait_ge(proj, t + 1)
                    src = h_t[:, :, 0:L].rearrange("p k (b a) -> p k b a", b=B)[:, :, :, bass.ds(t * A8, A8)]
                    nc.scalar.activation(slab[:, b, :, :].rearrange("p k (b a) -> p k b a", b=B), src, ACT.Copy).then_inc(cut, 1)
            act.wait_ge(kept_g, NA + 2)
            with act.Fori(0, B // 2) as i:
                for b in range(2):
                    t = 2 * i + b
                    act.wait_ge(made_h, t + 1)
                    nc.scalar.activation(gs[:, b, :, :].rearrange("p (t r) a -> p t r a", r=2),
                                         g[:, :, :, :].rearrange("p t (r k) a -> p t r k a", r=2)[:, :, :, bass.ds(t, 1), :]
                                         .rearrange("p t r k a -> p t r (k a)"), ACT.Copy).then_inc(cut_g, 1)

        @block.vector
        def _(dve):
            dve.sem_inc(kept_u, 2)
            dve.sem_inc(kept_g, 2)
            dve.sem_inc(kept_h, 2)
            dve.sem_inc(kept_y, 2)
            with dve.Fori(0, NA // 2) as i:
                for b in range(2):
                    t = 2 * i + b
                    dve.wait_ge(proj, t + 3)
                    nc.vector.tensor_copy(u[:, b, :], psu[b][:, :]).then_inc(kept_u, 1)
                    dve.wait_ge(made_g, t + 3)
                    nc.vector.tensor_copy(g[:, :, :, bass.ds(t * A8, A8)], psg[b][:, :, :].rearrange("p t (k a) -> p t k a", a=A8))\
                      .then_inc(kept_g, 1)
            with dve.Fori(0, B // 2) as i:
                for b in range(2):
                    t = 2 * i + b
                    dve.wait_ge(made_h, t + 3)
                    nc.vector.tensor_copy(hs[:, b, :, :, :].rearrange("p t r c -> p t (r c)"), psh[b][:, :, :]).then_inc(kept_h, 1)
                    dve.wait_ge(made_y, t + 1)
                    to = y[:, :, :].rearrange("p t (k1 k2) -> p t k1 k2", k2=B)[:, :, :, bass.ds(t, 1)].rearrange("p t a b -> p t (a b)")
                    nc.vector.tensor_scalar(to, psy[b][:, :, :], SCALE, None, ALU.mult).then_inc(kept_y, 1)

        @block.tensor
        def _(pe):
            pe.sem_inc(proj, 2)
            pe.sem_inc(made_g, 2)
            pe.sem_inc(made_h, 2)
            pe.wait_ge(loaded, 64)
            with pe.Fori(0, NA // 2) as i:
                for b in range(2):
                    t = 2 * i + b
                    pe.wait_ge(cut, t + 3)
                    pe.wait_ge(kept_u, t + 1)
                    for k in range(KD):
                        mm = nc.tensor.matmul(psu[b][:, :], slab[:, b, k, :], w[:, k, :], start=(k == 0), stop=(k == KD - 1))
                    mm.then_inc(proj, 1)
                    pe.wait_ge(kept_u, t + 3)
                    pe.wait_ge(kept_g, t + 1)
                    for x in range(FT2):
                        mm = nc.tensor.matmul(psg[b][:, x, :], u[:, b, x * P:(x + 1) * P], tb[:, :], start=True, stop=True)
                    mm.then_inc(made_g, 1)
            with pe.Fori(0, B // 2) as i:
                for b in range(2):
                    t = 2 * i + b
                    pe.wait_ge(cut_g, t + 1)
                    pe.wait_ge(kept_h, t + 1)
                    for x in range(FT2):
                        for ri in range(2):
                            mm = nc.tensor.matmul(psh[b][:, x, :], gs[:, b, 2 * x + ri, :], tc[:, ri, :], start=(ri == 0), stop=(ri == 1))
                    mm.then_inc(made_h, 1)
                    pe.wait_ge(kept_h, t + 3)
                    pe.wait_ge(kept_y, t + 1)
                    for x in range(FT2):
                        for ri in range(2):
                            mm = nc.tensor.matmul(psy[b][:, x, :], hs[:, b, x, ri, :], ta[:, ri, bass.ds(t * P, P)],
                                                  start=(ri == 0), stop=(ri == 1))
                    mm.then_inc(made_y, 1)


def output_rows_2(nc, y_t, w_out, g_ssd, g_post, gate, x2, x3, ones):
    KF = FW // P
    KS = SW // P
    with Mem(nc, "or2") as m:
        w = m.sb("w", P, 2, D)
        w_hi, w_lo = m.sb_r("w_hi", P, KD, D), m.sb_r("w_lo", P, KD, D)
        gs = m.sb("gs", P, KS)
        gg = m.sb("gg", P, 2, D)
        y = m.sb("y", P, 2, KD, P)
        y_hi, y_lo = m.sb_r("y_hi", P, 2, KD, P), m.sb_r("y_lo", P, 2, KD, P)
        sq = m.sb("sq", P, 2, KS, P)
        ry = m.sb("ry", P, 2, 2, P)
        xr = m.sb("xr", P, 2, D)
        o = m.sb("o", P, 2, D)
        junk = m.sb("junk", P, D)
        stat = m.sb("stat", P, 2, 4)
        eps = m.sb("eps", P, 1)
        ps = [m.ps(f"ps{i}", P, D) for i in range(2)]
        psq = [m.ps(f"psq{i}", P, P) for i in range(2)]
        vec_in, eps_set, scaled_w = m.sem("vec_in"), m.sem("eps_set"), m.sem("scaled_w")
        w_in = [m.sem(f"w_in{i}") for i in range(2)]
        y_in = [m.sem(f"y_in{i}") for i in range(2)]
        x_in = [m.sem(f"x_in{i}") for i in range(2)]
        (w_his, w_los, squared_y, summed, root_y, inv_y, scaled_y, y_his, y_los, proj, squared, rooted, inv, normed, added,
         stored, free) = (m.sem(n) for n in (
            "w_his", "w_los", "squared_y", "summed", "root_y", "inv_y", "scaled_y", "y_his", "y_los", "proj", "squared",
            "rooted", "inv", "normed", "added", "stored", "free"))
        block = m.block()
        rows_in = x2.rearrange("(t p) d -> t p d", p=P)
        rows_out = x3.rearrange("(t p) d -> t p d", p=P)

        @block.sync
        def _(sp):
            def load(t, b):
                sp.wait_ge(y_los, t + 1)
                sp.dma_start(y[:, b, :, :], y_t[:, :, bass.ds(t * P, P)].rearrange("k p l -> p k l")).then_inc(y_in[b], 16)

            def load_rows(t, b):
                sp.wait_ge(added, t + 1)
                sp.dma_start(xr[:, b, :], rows_in[bass.ds(t, 1), :, :].rearrange("t p d -> p (t d)")).then_inc(x_in[b], 16)

            sp.dma_start(gs[:, :], columns(g_ssd, KS), allow_slow_non_contiguous=True).then_inc(vec_in, 16)
            load(0, 0)
            for k in range(KD):
                if k >= 2:
                    sp.wait_ge(w_los, k - 1)
                sp.dma_start(w[:, k % 2, :], w_out[k * P:(k + 1) * P, :]).then_inc(w_in[k % 2], 16)
            load(1, 1)
            load_rows(0, 0)
            sp.dma_start(gg[:, 0, :], every_partition(g_post)).then_inc(vec_in, 16)
            sp.dma_start(gg[:, 1, :], every_partition(gate)).then_inc(vec_in, 16)
            with sp.Fori(0, TILES // 2 - 1) as i:
                for b in range(2):
                    load(2 * i + b + 2, b)
                    load_rows(2 * i + b + 1, 1 - b)
            load_rows(TILES - 1, 1)

        @block.tensor
        def _(pe):
            pe.sem_inc(proj, 2)

            def first(t, b):
                pe.wait_ge(squared_y, t + 1)
                pe.wait_ge(inv_y, t + 1)
                for k in range(KS):
                    mm = nc.tensor.matmul(psq[b][:, :], ones[:, :], sq[:, b, k, :], start=(k == 0), stop=(k == KS - 1))
                mm.then_inc(summed, 1)

            def finish(t, b):
                pe.wait_ge(w_los, KD)
                pe.wait_ge(y_los, t + 3)
                pe.wait_ge(normed, t + 1)
                for n in range(2):
                    cols = slice(n * NB, (n + 1) * NB)
                    for k in range(KD):
                        mm = three_products(nc, ps[b][:, cols], (y_hi[:, b, k, :], y_lo[:, b, k, :]),
                                            (w_hi[:, k, cols], w_lo[:, k, cols]), k == 0, k == KD - 1)
                mm.then_inc(proj, 1)

            two_ahead(pe, TILES, first, nothing, finish, finish_first=True)

        @block.scalar
        def _(act):
            for k in range(KD):
                if k >= KF:
                    act.wait_ge(scaled_w, k - KF + 1)
                else:
                    act.wait_ge(w_in[k % 2], 16 * (k // 2) + 16)
                nc.scalar.activation(w_hi[:, k, :], w[:, k % 2, :], ACT.Copy).then_inc(w_his, 1)
            act.wait_ge(eps_set, 1)
            nc.scalar.preload_act_table(ACT.Sqrt)

            def first(t, b):
                act.wait_ge(y_in[b], 8 * (t - b) + 16)
                act.wait_ge(summed, t + 1)
                nc.scalar.activation(sq[:, b, :, :], y[:, b, KF:, :], ACT.Square).then_inc(squared_y, 1)

            def second(t, b):
                act.wait_ge(summed, t + 3)
                nc.scalar.activation(ry[:, b, 0, :], psq[b][:, :], ACT.Sqrt, scale=1.0 / SW, bias=eps[:, :]).then_inc(root_y, 1)
                act.wait_ge(proj, t + 1)
                act.wait_ge(scaled_y, t + 1)
                nc.scalar.activation(y_hi[:, b, :, :], y[:, b, :, :], ACT.Copy).then_inc(y_his, 1)

            def finish(t, b):
                act.wait_ge(proj, t + 3)
                nc.scalar.activation(junk[:, :], ps[b][:, :], ACT.Square, accum_out=stat[:, b, 0:1]).then_inc(squared, 1)
                act.wait_ge(squared, t + 1)
                nc.scalar.activation(stat[:, b, 1:2], stat[:, b, 0:1], ACT.Sqrt, scale=1.0 / D, bias=eps[:, :]).then_inc(rooted, 1)

            two_ahead(act, TILES, first, second, finish)

        @block.vector
        def _(dve):
            nc.vector.memset(eps[:, :], EPS).then_inc(eps_set, 1)
            dve.sem_inc(y_los, 2)
            dve.sem_inc(added, 2)
            dve.sem_inc(summed, 2)
            dve.sem_inc(inv_y, 2)
            dve.sem_inc(normed, 2)
            dve.wait_ge(vec_in, 16)
            for k in range(KD):
                if k >= KF:
                    dve.wait_ge(w_in[k % 2], 16 * (k // 2) + 16)
                    nc.vector.tensor_scalar(w[:, k % 2, :], w[:, k % 2, :], gs[:, k - KF:k - KF + 1], None, ALU.mult)\
                      .then_inc(scaled_w, 1)
                dve.wait_ge(w_his, k + 1)
                nc.vector.tensor_tensor(w_lo[:, k, :], w[:, k % 2, :], w_hi[:, k, :].bitcast(F32), ALU.subtract).then_inc(w_los, 1)
            dve.wait_ge(vec_in, 48)
            nc.vector.tensor_tensor(gg[:, 0, :], gg[:, 0, :], gg[:, 1, :], ALU.mult).then_inc(scaled_w, 1)
            dve.wait_ge(scaled_w, KS + 1)

            def prepare(t, b):
                dve.wait_ge(root_y, t + 1)
                nc.vector.reciprocal(ry[:, b, 1, :], ry[:, b, 0, :]).then_inc(inv_y, 1)
                dve.wait_ge(inv_y, t + 3)
                nc.vector.tensor_tensor(y[:, b, KF:, :], y[:, b, KF:, :], over(ry[:, b, 1:2, :], (P, KS, P)), ALU.mult)\
                  .then_inc(scaled_y, 1)
                dve.wait_ge(y_his, t + 1)
                nc.vector.tensor_tensor(y_lo[:, b, :, :], y[:, b, :, :], y_hi[:, b, :, :].bitcast(F32), ALU.subtract)\
                  .then_inc(y_los, 1)

            def finish(t, b):
                dve.wait_ge(rooted, t + 1)
                nc.vector.reciprocal(stat[:, b, 2:3], stat[:, b, 1:2]).then_inc(inv, 1)
                dve.wait_ge(inv, t + 1)
                dve.wait_ge(free, t + 1)
                nc.vector.scalar_tensor_tensor(out=o[:, b, :], in0=ps[b][:, :], scalar=stat[:, b, 2:3], in1=gg[:, 0, :],
                                               op0=ALU.mult, op1=ALU.mult).then_inc(normed, 1)
                dve.wait_ge(normed, t + 3)
                dve.wait_ge(x_in[b], 8 * (t - b) + 16)
                nc.vector.tensor_tensor(o[:, b, :], o[:, b, :], xr[:, b, :], ALU.add).then_inc(added, 1)

            ahead(dve, TILES, prepare, finish)

        @block.gpsimd
        def _(pool):
            pool.sem_inc(free, 2)
            with pool.Fori(0, TILES // 2) as i:
                for b in range(2):
                    t = 2 * i + b
                    pool.wait_ge(added, t + 3)
                    pool.dma_start(rows_out[bass.ds(t, 1), :, :].rearrange("t p d -> p (t d)"), o[:, b, :]).then_inc(stored, 16)
                    pool.wait_ge(stored, 16 * t + 16)
                    pool.sem_inc(free, 1)


def feed_forward(nc, x3, g_pre, shift, scale, w_gate, w_up, w_down, g_post, gate, out, ident):
    RT = NB // P
    DH = D // 2
    NF = 2 * FT
    PIECES = 4
    with Mem(nc, "ff") as m:
        hraw = m.sb("hraw", P, KD, P)
        hb_lo, hb_hi = m.sb_r("hb_lo", P, KD, NB), m.sb_r("hb_hi", P, KD, NB)
        wg = m.sb("wg", P, 2, KD, P)
        wg_lo, wg_hi = m.sb_r("wg_lo", P, 2, 2, KD, P), m.sb_r("wg_hi", P, 2, 2, KD, P)
        wd = m.sb("wd", P, PIECES, DH)
        wd_lo, wd_hi = m.sb_r("wd_lo", P, PIECES, DH), m.sb_r("wd_hi", P, PIECES, DH)
        a_lo = m.sb_r("a_lo", P, PIECES, NB)
        a_hi = m.sb_r("a_hi", P, PIECES, NB)
        act_t = m.sb("act", P, FT, NB)
        sg = m.sb("sg", P, 2, NB)
        gg = m.sb("gg", P, D)
        xt = m.sb("xt", P, 2, D)
        xr = m.sb("xr", P, 2, D)
        h = m.sb("h", P, RT, D)
        ncol = m.sb("ncol", P, 3, KD)
        nstat = m.sb("nstat", P, 2, 4)
        stat = m.sb("stat", P, RT, 5)
        eps = m.sb("eps", P, 1)
        psg = [m.ps(f"psg{i}", P, 2, NB) for i in range(2)]
        psd = [m.ps(f"psd{i}", P, NB) for i in range(RT)]
        start, ready = m.sem("start"), m.sem("ready")
        loaded = [m.sem(f"loaded{i}") for i in range(2)]
        d_in = [m.sem(f"d_in{i}") for i in range(PIECES)]
        xt_in = [m.sem(f"xt_in{i}") for i in range(2)]
        (w_hi, w_lo, proj, gated, made, p_hi, p_lo, used, kept, squared, summed, rooted, inv, normed, added, stored) = (
            m.sem(n) for n in ("w_hi", "w_lo", "proj", "gated", "made", "p_hi", "p_lo", "used", "kept", "squared", "summed",
                               "rooted", "inv", "normed", "added", "stored"))
        x_in = [m.sem(f"x_in{i}") for i in range(2)]
        (n_sq, n_root, n_inv, n_scaled, n_turned, n_placed, n_shift, n_hi, n_lo) = (
            m.sem(n) for n in ("n_sq", "n_root", "n_inv", "n_scaled", "n_turned", "n_placed", "n_shift", "n_hi", "n_lo"))
        h_free, begun = m.sem("h_free"), m.sem("begun")
        block = m.block()
        gv, uv = (w.rearrange("(k p) c -> p k c", p=P) for w in (w_gate, w_up))
        dv = w_down.rearrange("(f p) d -> f p d", p=P)
        rows_in = x3.rearrange("(t p) d -> p t d", p=P)
        rows_out = out.rearrange("(t p) d -> p t d", p=P)
        LOAD_AT = (0, 0, 10, 16)
        SCALE_AT = (4, 8, 14, 20)
        TURN_AT = (8, 13, 19, 25)
        PLACE_AT = (9, 14, 20, 26)
        WEIGHTS_AT = (10, 33)
        SPLIT_AT = (26, 38)
        DEPTH_ = 3

        def blocks(eng, body):
            with eng.Fori(0, LB - 1) as n:
                body(n, False)
            body(LB - 1, True)

        def piece(j):
            return j // FT, j % FT, j % PIECES

        @block.sync
        def _(sp):
            sp.dma_start(gg[:, :], every_partition(g_post)).then_inc(start, 16)
            sp.dma_start(sg[:, :, :].rearrange("p a b -> p (a b)"), every_partition(gate)).then_inc(start, 16)
            for i, v in enumerate((g_pre, shift, scale)):
                sp.dma_start(ncol[:, i, :], columns(v, KD), allow_slow_non_contiguous=True).then_inc(start, 16)

            def load_rows(n, r):
                sp.wait_ge(n_turned, n * RT + r + 1)
                sp.dma_start(xt[:, r % 2, :], rows_in[:, bass.ds(n * RT + r, 1), :].rearrange("p t d -> p (t d)"))\
                  .then_inc(xt_in[r % 2], 16)

            def load_tile(n, t, b):
                for x, v in enumerate((gv, uv)):
                    sp.wait_ge(w_lo, n * (2 * FT) + 2 * t + x + 1)
                    sp.dma_start(wg[:, x, :, :], v[:, :, bass.ds(t * P, P)]).then_inc(loaded[x], 16)

            def load_piece(n, j):
                half, f, s = piece(j)
                sp.wait_ge(p_lo, n * (2 * NF) + 2 * j + 1)
                sp.dma_start(wd[:, s, :], dv[f, :, half * DH:(half + 1) * DH]).then_inc(d_in[s], 16)

            def body(n, last):
                with sp.Fori(0, FT // 2 - 1) as i:
                    for b in range(2):
                        load_tile(n, 2 * i + b + 2, b)
                for j in range(NF):
                    load_piece(n, j)
                    if not last:
                        for r in range(RT):
                            if LOAD_AT[r] == j:
                                load_rows(n + 1, r)
                        for b in range(2):
                            if WEIGHTS_AT[b] == j:
                                load_tile(n + 1, b, b)

            load_rows(0, 0)
            load_rows(0, 1)
            load_tile(0, 0, 0)
            load_rows(0, 2)
            load_rows(0, 3)
            load_tile(0, 1, 1)
            blocks(sp, body)

        @block.tensor
        def _(pe):
            pe.sem_inc(proj, 2)
            pe.sem_inc(used, 4)
            pe.sem_inc(n_turned, 2)

            def turn(n, r):
                pe.wait_ge(n_scaled, n * RT + r + 1)
                pe.wait_ge(n_placed, n * RT + r + 1)
                for k in range(KD):
                    x, c = k // 4, (k % 4) * P
                    t = nc.tensor.transpose(psg[r % 2][:, x, c:c + P], xt[:, r % 2, k * P:(k + 1) * P], ident[:, :])
                t.then_inc(n_turned, 1)

            def three(to, left, right, first, last):
                for p, (x, y) in enumerate(((0, 0), (0, 1), (1, 0))):
                    mm = nc.tensor.matmul(to, left[x], right[y], start=(first and p == 0), stop=(last and p == 2))
                return mm

            def body(n, last):
                pe.wait_ge(n_lo, (n + 1) * RT + 1)
                pe.wait_ge(n_placed, (n + 1) * RT + 2)
                pe.sem_inc(begun, 1)
                with pe.Fori(0, FT // 2) as i:
                    for b in range(2):
                        t = n * FT + 2 * i + b
                        pe.wait_ge(w_lo, n * (2 * FT) + 4 * i + 2 * b + 4)
                        pe.wait_ge(made, t + 1)
                        for x in range(2):
                            for k in range(KD):
                                mm = three(psg[b][:, x, :], (wg_hi[:, b, x, k, :], wg_lo[:, b, x, k, :]),
                                           (hb_hi[:, k, :], hb_lo[:, k, :]), k == 0, k == KD - 1)
                        mm.then_inc(proj, 1)
                pe.wait_ge(made, n * FT + FT + 2)
                for j in range(NF):
                    half, f, s = piece(j)
                    if f == 0:
                        pe.wait_ge(kept, 2 * n + half + 1)
                    pe.wait_ge(p_lo, n * (2 * NF) + 2 * j + 2 + 2 * PIECES)
                    for r in range(RT):
                        rs = slice(r * P, (r + 1) * P)
                        mm = three(psd[r][:, :], (a_hi[:, s, rs], a_lo[:, s, rs]),
                                   (wd_hi[:, s, :], wd_lo[:, s, :]), f == 0, f == FT - 1)
                    mm.then_inc(used, 1)
                    if not last:
                        for r in range(RT):
                            if TURN_AT[r] == j:
                                turn(n + 1, r)

            for r in range(RT):
                turn(0, r)
            blocks(pe, body)

        @block.scalar
        def _(act):
            act.wait_ge(ready, 3)
            act.sem_inc(kept, 1)

            def root(n, r):
                act.wait_ge(xt_in[r % 2], n * (RT // 2 * 16) + 16 * (r // 2) + 16)
                nc.scalar.activation(sg[:, :, :].rearrange("p a b -> p (a b)"), xt[:, r % 2, :], ACT.Square, accum_out=nstat[:, r % 2, 0:1]).then_inc(n_sq, 1)
                act.wait_ge(n_sq, n * RT + r + 1)
                nc.scalar.activation(nstat[:, r % 2, 1:2], nstat[:, r % 2, 0:1], ACT.Sqrt, scale=1.0 / D, bias=eps[:, :])\
                  .then_inc(n_root, 1)

            def tile_hi(n, i, b):
                t = n * FT + 2 * i + b
                act.wait_ge(proj, t + 1)
                for x in range(2):
                    act.wait_ge(loaded[x], 16 * t + 16)
                    nc.scalar.activation(wg_hi[:, b, x, :, :], wg[:, x, :, :], ACT.Copy).then_inc(w_hi, 1)

            def piece_hi(n, j):
                half, f, s = piece(j)
                act.wait_ge(used, n * NF + j + 1)
                act.wait_ge(d_in[s], n * (NF // PIECES * 16) + 16 * (j // PIECES) + 16)
                nc.scalar.activation(wd_hi[:, s, :], wd[:, s, :], ACT.Copy).then_inc(p_hi, 1)
                nc.scalar.activation(a_hi[:, s, :], act_t[:, f, :], ACT.Copy).then_inc(p_hi, 1)

            def body(n, last):
                nc.scalar.preload_act_table(ACT.Silu)

                def silu(i, b):
                    t = n * FT + 2 * i + b
                    act.wait_ge(proj, t + 3)
                    act.wait_ge(made, t + 1)
                    nc.scalar.activation(sg[:, b, :], psg[b][:, 0, :], ACT.Silu).then_inc(gated, 1)

                with act.Fori(0, FT // 2 - 1) as i:
                    for b in range(2):
                        silu(i, b)
                        tile_hi(n, i + 1, b)
                for b in range(2):
                    silu(FT // 2 - 1, b)
                act.wait_ge(made, n * FT + FT + 2)
                for j in range(DEPTH_):
                    piece_hi(n, j)
                for j in range(NF):
                    if j + DEPTH_ < NF:
                        piece_hi(n, j + DEPTH_)
                    if not last:
                        for r in range(RT):
                            if SCALE_AT[r] == j:
                                root(n + 1, r)
                        for b in range(2):
                            if SPLIT_AT[b] == j:
                                tile_hi(n + 1, 0, b)
                    if j % FT == FT - 1:
                        half = j // FT
                        act.wait_ge(used, n * NF + (half + 1) * FT + 4)
                        if half == 0:
                            act.wait_ge(h_free, n + 1)
                        cols = slice(half * DH, (half + 1) * DH)
                        for r in range(RT):
                            to = nc.scalar.activation(h[:, r, cols], psd[r][:, :], ACT.Copy)
                        to.then_inc(kept, 1)
                        act.wait_ge(kept, 2 * n + half + 2)
                        for r in range(RT):
                            nc.scalar.activation(sg[:, 0, :], h[:, r, cols], ACT.Square, accum_out=stat[:, r, half:half + 1])\
                              .then_inc(squared, 1)
                            act.wait_ge(squared, n * (2 * RT) + half * RT + r + 1)
                act.wait_ge(summed, n + 1)
                nc.scalar.activation(stat[:, :, 3:4], stat[:, :, 2:3], ACT.Sqrt, scale=1.0 / D, bias=eps[:, :]).then_inc(rooted, 1)

            for r in range(RT):
                root(0, r)
            tile_hi(0, 0, 0)
            tile_hi(0, 0, 1)
            blocks(act, body)

        @block.vector
        def _(dve):
            nc.vector.memset(eps[:, :], EPS).then_inc(ready, 1)
            dve.wait_ge(start, 80)
            nc.vector.tensor_tensor(gg[:, :], gg[:, :], sg[:, :, :].rearrange("p a b -> p (a b)"), ALU.mult).then_inc(ready, 1)
            nc.vector.scalar_tensor_tensor(out=ncol[:, 0, :], in0=ncol[:, 2, :], scalar=1.0, in1=ncol[:, 0, :],
                                           op0=ALU.add, op1=ALU.mult).then_inc(ready, 1)
            dve.wait_ge(ready, 3)
            dve.sem_inc(made, 2)
            dve.sem_inc(n_placed, 2)
            dve.sem_inc(h_free, 1)
            dve.sem_inc(n_lo, 1)
            dve.sem_inc(w_lo, 2)
            dve.sem_inc(p_lo, 2 * PIECES)

            def scaled_rows(n, r):
                dve.wait_ge(n_root, n * RT + r + 1)
                nc.vector.reciprocal(nstat[:, r % 2, 2:3], nstat[:, r % 2, 1:2]).then_inc(n_inv, 1)
                dve.wait_ge(n_inv, n * RT + r + 1)
                nc.vector.tensor_scalar(xt[:, r % 2, :], xt[:, r % 2, :], nstat[:, r % 2, 2:3], None, ALU.mult).then_inc(n_scaled, 1)

            def place(n, r):
                dve.wait_ge(n_turned, n * RT + r + 3)
                dve.wait_ge(n_lo, n * RT + r + 1)
                nc.vector.tensor_tensor(hraw[:, :, :],
                                        psg[r % 2][:, :, :].rearrange("p x (k l) -> p (x k) l", l=P),
                                        over(ncol[:, 0, :, None], (P, KD, P)), ALU.mult).then_inc(n_placed, 1)

            def tile_lo(n, t, b):
                for x in range(2):
                    dve.wait_ge(w_hi, n * (2 * FT) + 2 * t + x + 1)
                    nc.vector.tensor_tensor(wg_lo[:, b, x, :, :], wg[:, x, :, :], wg_hi[:, b, x, :, :].bitcast(F32),
                                            ALU.subtract).then_inc(w_lo, 1)

            def piece_lo(n, j):
                half, f, s = piece(j)
                dve.wait_ge(p_hi, n * (2 * NF) + 2 * j + 2)
                nc.vector.tensor_tensor(wd_lo[:, s, :], wd[:, s, :], wd_hi[:, s, :].bitcast(F32), ALU.subtract)\
                  .then_inc(p_lo, 1)
                nc.vector.tensor_tensor(a_lo[:, s, :], act_t[:, f, :], a_hi[:, s, :].bitcast(F32), ALU.subtract).then_inc(p_lo, 1)

            def body(n, last):
                def multiply(t, b):
                    dve.wait_ge(gated, n * FT + t + 1)
                    nc.vector.tensor_tensor(act_t[:, bass.ds(t, 1), :].rearrange("p f l -> p (f l)"),
                                            psg[b][:, 1, :], sg[:, b, :], ALU.mult).then_inc(made, 1)

                with dve.Fori(0, FT // 2 - 1) as i:
                    for b in range(2):
                        multiply(2 * i + b, b)
                        tile_lo(n, 2 * i + b + 2, b)
                for b in range(2):
                    multiply(FT - 2 + b, b)
                dve.wait_ge(made, n * FT + FT + 2)
                for j in range(DEPTH_):
                    piece_lo(n, j)
                for j in range(NF):
                    if j + DEPTH_ < NF:
                        piece_lo(n, j + DEPTH_)
                    if not last:
                        for r in range(RT):
                            if SCALE_AT[r] == j:
                                scaled_rows(n + 1, r)
                            if PLACE_AT[r] == j:
                                place(n + 1, r)
                        for b in range(2):
                            if SPLIT_AT[b] == j:
                                tile_lo(n + 1, b, b)
                dve.wait_ge(squared, (n + 1) * (2 * RT))
                nc.vector.tensor_tensor(stat[:, :, 2:3], stat[:, :, 0:1], stat[:, :, 1:2], ALU.add).then_inc(summed, 1)
                dve.wait_ge(rooted, n + 1)
                nc.vector.reciprocal(stat[:, :, 4:5], stat[:, :, 3:4]).then_inc(inv, 1)
                dve.wait_ge(inv, n + 1)
                for r in range(RT):
                    nc.vector.scalar_tensor_tensor(out=h[:, r, :], in0=h[:, r, :], scalar=stat[:, r, 4:5], in1=gg[:, :],
                                                   op0=ALU.mult, op1=ALU.mult).then_inc(normed, 1)

            for r in range(RT):
                scaled_rows(0, r)
                place(0, r)
            tile_lo(0, 0, 0)
            tile_lo(0, 1, 1)
            blocks(dve, body)

        @block.gpsimd
        def _(pool):
            pool.wait_ge(start, 80)

            def shift_and_split(n, r):
                cs = slice(r * P, (r + 1) * P)
                pool.wait_ge(n_placed, n * RT + r + 3)
                nc.gpsimd.tensor_tensor(hraw[:, :, :], hraw[:, :, :], over(ncol[:, 1, :, None], (P, KD, P)), ALU.add)\
                  .then_inc(n_shift, 1)
                pool.wait_ge(n_shift, n * RT + r + 1)
                pool.sem_inc(begun, 1)
                nc.gpsimd.tensor_copy(hb_hi[:, :, cs], hraw[:, :, :]).then_inc(n_hi, 1)
                pool.wait_ge(n_hi, n * RT + r + 1)
                nc.gpsimd.tensor_tensor(hb_lo[:, :, cs], hraw[:, :, :], hb_hi[:, :, cs].bitcast(F32), ALU.subtract)\
                    .then_inc(n_lo, 1)

            def load_residual(n, r):
                pool.dma_start(xr[:, r % 2, :], rows_in[:, bass.ds(n * RT + r, 1), :].rearrange("p t d -> p (t d)"))\
                    .then_inc(x_in[r % 2], 16)

            def body(n, last):
                load_residual(n, 0)
                load_residual(n, 1)
                if not last:
                    for r in range(RT):
                        shift_and_split(n + 1, r)
                for r in range(RT):
                    t = n * RT + r
                    pool.wait_ge(x_in[r % 2], n * (RT // 2 * 16) + 16 * (r // 2) + 16)
                    pool.wait_ge(normed, t + 1)
                    pool.sem_inc(begun, 1)
                    nc.gpsimd.tensor_tensor(h[:, r, :], h[:, r, :], xr[:, r % 2, :], ALU.add).then_inc(added, 1)
                    pool.wait_ge(added, t + 1)
                    pool.sem_inc(begun, 1)
                    pool.dma_start(rows_out[:, bass.ds(t, 1), :].rearrange("p t d -> p (t d)"), h[:, r, :]).then_inc(stored, 16)
                    if r + 2 < RT:
                        load_residual(n, r + 2)
                pool.wait_ge(stored, n * (16 * RT) + 16 * RT)
                pool.sem_inc(h_free, 1)

            for r in range(RT):
                shift_and_split(0, r)
            blocks(pool, body)


def program(nc, d):
    with Mem(nc, "all") as m:
        ident, ones = m.sb("ident", P, P), m.sb("ones", P, P)
        make_constants(nc, ident, ones)
        modulations(nc, d["c_2"][0], d["c_ctx_2"], d["w_ada_2"][0], d["b_ada_2"][0], d["s_mod"])

        w_in = d["w_in"][0]
        with Mem(nc, "m1") as m1:
            uc = m1.sb("uc", P, G1, NC8)
            with Mem(nc, "m1a") as m2:
                xn = m2.sb("xn", P, KD, L)
                norm_to_columns(nc, "n1", d["x"][0], TILES, xn, 0, ident, d["norm_gain"][0])
                silu_projection(nc, "z1", xn, w_in[:, SSM_W:2 * SSM_W], SSM_W // P, d["s_z1"])
                short_convolution(nc, xn, w_in, d["conv_w"][0], d["s_y1"])
                s5_inputs(nc, xn, w_in[:, 0:SSM_W], uc, ident)
            vw = m1.sb("vw", P, 2, QP, P)
            q = m1.sb("q", P, 2, QP, T8 + 1, H1)
            toeplitz = m1.sb("toeplitz", P, G1, P)
            a8 = m1.sb("a8", P, 2, QP)
            s5_weights(nc, d, vw, q, toeplitz, a8, ident, d["s_kernels"])
            st = m1.sb("st", P, 2, QP, NC8)
            s5_scan(nc, uc, vw, a8, st)
            yt = m1.sb("yt", P, SSM_W // P, L)
            s5_outputs(nc, uc, st, q, toeplitz, yt, ident)
            s5_gate(nc, yt, d["w_glu"][0], d["b_glu"][0], d["s_z1"], d["s_y1"])
        output_rows_1(nc, d["s_y1"], d["w_out"][0], d["x"][0], d["final_norm_gain"], d["s_x2"])

        w_in2 = d["w_in_2"][0]
        mod, modc = (lambda i: d["s_mod"][0, i * D:(i + 1) * D]), (lambda i: d["s_mod"][1, i * D:(i + 1) * D])
        with Mem(nc, "m3") as m3:
            ht = m3.sb("ht", P, KD, LT)
            norm_to_columns(nc, "n2", d["s_x2"], TILES, ht, 0, ident, d["g_pre_mix_2"][0], (mod(0), mod(1)))
            norm_to_columns(nc, "nc", d["ctx_2"][0], LC // P, ht, L, ident, d["g_pre_mix_2"][0], (modc(0), modc(1)))
            silu_projection(nc, "z2", ht, w_in2[:, FW:XBC], SW // P, d["s_z2"])
            convolved_projection(nc, ht, w_in2[:, XBC:XBC + CONV_DIM], d["conv_w_2"][0], d["conv_b_2"][0], d["s_xbc"])
            decays(nc, ht, w_in2[:, XBC + CONV_DIM:], d["dt_bias_2"][0], d["a_log_2"][0], d["s_decay_rows"],
                   d["s_totals"], d["s_decay_cols"], ident)
            fourier_mix(nc, ht, w_in2[:, 0:FW], d["t_over_b"], d["t_over_c"], d["t_over_a"], d["s_y2"])
        with Mem(nc, "m4") as m4:
            hf, hb = m4.sb("hf", P, HEADS, HD), m4.sb("hb", P, HEADS, HD)
            context_states(nc, d["s_xbc"], d["s_totals"], d["s_decay_cols"], hf[:, :, :], hb[:, :, :], ident)
            backward_states(nc, d["s_xbc"], d["s_totals"], d["s_decay_cols"], hb, d["s_hb"], ident)
            ssd_outputs(nc, d["s_xbc"], d["s_z2"], d["s_decay_rows"], d["s_totals"], d["s_decay_cols"], d["d_skip_2"][0],
                        hf, d["s_hb"], d["s_y2"], ident, ones)
        output_rows_2(nc, d["s_y2"], d["w_out_2"][0], d["g_ssd_2"][0], d["g_post_mix_2"][0], mod(2), d["s_x2"], d["s_x3"], ones)
        feed_forward(nc, d["s_x3"], d["g_pre_ffn_2"][0], mod(3), mod(4), d["w_gate_2"][0], d["w_up_2"][0], d["w_down_2"][0],
                     d["g_post_ffn_2"][0], mod(5), d["out"][0], ident)


SCRATCH = {
    "s_mod": (2, 6 * D),
    "s_z1": (SSM_W // P, P, L), "s_y1": (KD, P, L), "s_kernels": (H1, G1, 7 * H1 + P), "s_x2": (L, D),
    "s_z2": (SW // P, P, L), "s_xbc": (XT_, P, LT), "s_decay_rows": (LT // P, 2 * HEADS, P), "s_totals": (LT // P, 2 * HEADS),
    "s_decay_cols": (LT // P, P, 3 * 64), "s_hb": (NCH, P, HEADS * HD), "s_y2": (KD, P, L), "s_x3": (L, D),
}

_INS = ["x", "norm_gain", "w_in", "ssm_a_re", "ssm_a_im", "ssm_log_dt", "ssm_b_re", "ssm_b_im", "ssm_c_re", "ssm_c_im",
        "ssm_d", "w_glu", "b_glu", "conv_w", "w_out", "final_norm_gain", "c_2", "ctx_2", "c_ctx_2", "w_ada_2", "b_ada_2",
        "g_pre_mix_2", "g_post_mix_2", "g_pre_ffn_2", "g_post_ffn_2", "w_in_2", "conv_w_2", "conv_b_2", "dt_bias_2",
        "a_log_2", "d_skip_2", "g_ssd_2", "w_out_2", "w_gate_2", "w_up_2", "w_down_2"]


def kernel(**inputs):
    import concourse.bacc as _bacc
    from concourse.bass_utils import run_bass_kernel_spmd as _run

    nc = _bacc.Bacc("TRN2", target_bir_lowering=False, num_devices=1)
    arrays, d = {}, {}
    tables = dict(zip(("t_over_b", "t_over_c", "t_over_a"), fourier_tables()))
    for name, a in [(n, inputs[n]) for n in _INS] + list(tables.items()):
        a = np.ascontiguousarray(a)
        arrays[f"in_{name}_dram"] = a
        d[name] = nc.dram_tensor(f"in_{name}_dram", a.shape, mybir.dt.from_np(a.dtype), kind="ExternalInput").ap()
    for name, shape in SCRATCH.items():
        d[name] = nc.dram_tensor(name, shape, F32).ap()
    d["out"] = nc.dram_tensor("out_0_dram", (1, L, D), F32, kind="ExternalOutput").ap()
    program(nc, d)
    r = _run(nc, [arrays], core_ids=[0])
    return r.results[0]["out_0_dram"]
```

```python
from contextlib import ExitStack
import math

import numpy as np
import concourse.bass as bass
from concourse import mybir

F32 = mybir.dt.float32
F32R = mybir.dt.float32r
ALU = mybir.AluOpType
ACT = mybir.ActivationFunctionType

P = 128
D = 1024
KD = D // P
L = 2048
LC = 256
LT = L + LC
TILES = L // P
NB = 512
LB = L // NB
EPS = 1e-6

WR = 4

SSM_W = 512
CW = 512
G1, H1, S1 = 32, 16, 64
T8 = 8
NC8 = L // T8
QP = G1 // 2
HALF = NC8 // P
SB = 16
NSB = NC8 // SB

FW = 256
FG = 64
SW = 768
HEADS, HD, SG, ST = 12, 64, 4, 128
HR = HEADS // SG
CONV_DIM = SW + 2 * SG * ST
XT_ = CONV_DIM // P
KC = 7
ROWLEN = 64
XBC = FW + SW
NCH = L // P
CCH = LC // P
FF = 2816
FT = FF // P


class Mem:

    def __init__(self, nc, stage):
        self.nc, self.stage, self.stack, self.sems = nc, stage, ExitStack(), []

    def sb(self, name, *shape):
        return self.stack.enter_context(self.nc.sbuf_tensor(f"{self.stage}_{name}", list(shape), F32))

    def sb_r(self, name, *shape):
        return self.stack.enter_context(self.nc.sbuf_tensor(f"{self.stage}_{name}", list(shape), F32R))

    def ps(self, name, *shape):
        return self.stack.enter_context(self.nc.psum_tensor(f"{self.stage}_{name}", list(shape), F32))

    def sem(self, name):
        self.sems.append(self.nc.alloc_semaphore(f"{self.stage}_{name}"))
        return self.sems[-1]

    def block(self):
        return self.stack.enter_context(self.nc.Block())

    def __enter__(self):
        self.stack.__enter__()
        return self

    def __exit__(self, *e):
        self.stack.__exit__(*e)
        if self.sems and e[0] is None:
            self.nc.clear_and_free_semaphores(self.sems)
            self.nc.all_engine_barrier()


def over(ap, shape):
    return ap.broadcast_to(list(shape))


def columns(vec, tiles):
    return vec.rearrange("(k p) -> p k", p=P)


def every_partition(vec, n=P):
    return vec.partition_broadcast(n)


def ahead(eng, n, prepare, finish, once=None):
    prepare(0, 0)
    if once:
        once()
    with eng.Fori(0, n // 2 - 1) as i:
        for b in range(2):
            prepare(2 * i + b + 1, 1 - b)
            finish(2 * i + b, b)
    prepare(n - 1, 1)
    finish(n - 2, 0)
    finish(n - 1, 1)


def two_ahead(eng, n, first, second, finish, finish_first=False, once=None):
    first(0, 0)
    first(1, 1)
    second(0, 0)
    if once:
        once()
    with eng.Fori(0, n // 2 - 1) as i:
        for b in range(2):
            t = 2 * i + b
            if finish_first:
                finish(t, b)
            first(t + 2, b)
            second(t + 1, 1 - b)
            if not finish_first:
                finish(t, b)
    if finish_first:
        finish(n - 2, 0)
        finish(n - 1, 1)
    second(n - 1, 1)
    if not finish_first:
        finish(n - 2, 0)
        finish(n - 1, 1)


def nothing(t, b):
    pass


def three_products(nc, to, left, right, first, last):
    for p, (x, y) in enumerate(((0, 0), (0, 1), (1, 0))):
        mm = nc.tensor.matmul(to, left[x], right[y], start=(first and p == 0), stop=(last and p == 2))
    return mm


def minus_hi(nc, lo, x, hi):
    return nc.vector.tensor_tensor(lo, x, hi.bitcast(F32), ALU.subtract)


def make_constants(nc, ident, ones):
    with Mem(nc, "const") as m:
        zeroed, made = m.sem("zeroed"), m.sem("made")
        block = m.block()

        @block.gpsimd
        def _(pool):
            nc.gpsimd.memset(ident[:, :], 0.0).then_inc(zeroed, 1)
            nc.gpsimd.memset(ones[:, :], 1.0).then_inc(made, 1)
            pool.wait_ge(zeroed, 1)
            nc.gpsimd.affine_select(out=ident[:, :], in_=ident[:, :], compare_op=ALU.not_equal, fill=1.0,
                                    base=0, pattern=[[-1, P]], channel_multiplier=1).then_inc(made, 1)
            pool.wait_ge(made, 2)


def norm_to_columns(nc, stage, src, tiles, hi, lo, col0, ident, gain, modulation=None):
    NX = 4
    with Mem(nc, stage) as m:
        x = m.sb("x", P, NX, D)
        xn = m.sb("xn", P, 2, D)
        junk = m.sb("junk", P, D)
        raw = m.sb("raw", P, 2, KD, P)
        stat = m.sb("stat", P, 2, 4)
        a = m.sb("a", P, KD)
        b = m.sb("b", P, KD)
        s = m.sb("s", P, KD)
        eps = m.sb("eps", P, 1)
        ps = [m.ps(f"ps{i}", P, KD, P) for i in range(2)]
        vec = m.sem("vec")
        loaded = [m.sem(f"loaded{i}") for i in range(NX)]
        squared, rooted, inverted, scaled = m.sem("squared"), m.sem("rooted"), m.sem("inverted"), m.sem("scaled")
        turned, placed, shifted = m.sem("turned"), m.sem("placed"), m.sem("shifted")
        his, los = m.sem("his"), m.sem("los")
        ab, eps_set = m.sem("ab"), m.sem("eps_set")
        block = m.block()
        rows = src.rearrange("(t p) d -> t p d", p=P)
        step = min(NX, tiles)

        @block.sync
        def _(sp):
            for t in range(min(NX, tiles)):
                sp.dma_start(x[:, t, :], rows[t, :, :]).then_inc(loaded[t], 16)
            sp.dma_start(a[:, :], columns(gain, KD), allow_slow_non_contiguous=True).then_inc(vec, 16)
            if modulation:
                sp.dma_start(b[:, :], columns(modulation[0], KD), allow_slow_non_contiguous=True).then_inc(vec, 16)
                sp.dma_start(s[:, :], columns(modulation[1], KD), allow_slow_non_contiguous=True).then_inc(vec, 16)
            if tiles > NX:
                with sp.Fori(0, tiles // NX - 1) as i:
                    for j in range(NX):
                        sp.wait_ge(scaled, NX * i + j + 1)
                        sp.dma_start(x[:, j, :], rows[bass.ds(NX * i + j + NX, 1), :, :].rearrange("t p d -> p (t d)"))\
                          .then_inc(loaded[j], 16)

        @block.scalar
        def _(act):
            act.wait_ge(eps_set, 1)
            nc.scalar.preload_act_table(ACT.Sqrt)
            act.sem_inc(turned, 2)

            def part(t, j, round_):
                act.wait_ge(loaded[j], 16 * round_ + 16)
                act.wait_ge(inverted, t + 1)
                nc.scalar.activation(junk[:, :], x[:, j, :], ACT.Square, accum_out=stat[:, j % 2, 0:1])\
                  .then_inc(squared, 1)
                act.wait_ge(squared, t + 1)
                nc.scalar.activation(stat[:, j % 2, 1:2], stat[:, j % 2, 0:1], ACT.Sqrt, scale=1.0 / D, bias=eps[:, :])\
                  .then_inc(rooted, 1)

            def round_off(t, j):
                act.wait_ge(shifted if modulation else placed, t + (1 if modulation else 3))
                nc.scalar.activation(hi[:, :, bass.ds(col0 + t * P, P)], raw[:, j % 2, :, :], ACT.Copy).then_inc(his, 1)

            part(0, 0, 0)
            part(1, 1, 0)
            if tiles > step:
                with act.Fori(0, tiles // step - 1) as i:
                    for j in range(step):
                        part(step * i + j + 2, (j + 2) % step, i + (j + 2) // step)
                        round_off(step * i + j, j)
            for j in range(step):
                if j + 2 < step:
                    part(tiles - step + j + 2, j + 2, tiles // step - 1)
                round_off(tiles - step + j, j)

        @block.vector
        def _(dve):
            nc.vector.memset(eps[:, :], EPS).then_inc(eps_set, 1)
            dve.sem_inc(inverted, 2)
            dve.sem_inc(placed, 2)
            dve.sem_inc(los, 2)

            def scale_rows(t, j):
                dve.wait_ge(rooted, t + 1)
                nc.vector.reciprocal(stat[:, j % 2, 2:3], stat[:, j % 2, 1:2]).then_inc(inverted, 1)
                dve.wait_ge(inverted, t + 3)
                dve.wait_ge(turned, t + 1)
                nc.vector.tensor_scalar(xn[:, j % 2, :], x[:, j, :], stat[:, j % 2, 2:3], None, ALU.mult).then_inc(scaled, 1)

            def place(t, j):
                dve.wait_ge(turned, t + 3)
                dve.wait_ge(los, t + 1)
                nc.vector.tensor_tensor(raw[:, j % 2, :, :], ps[j % 2][:, :, :], over(a[:, :, None], (P, KD, P)),
                                        ALU.mult).then_inc(placed, 1)

            def rest(t, j):
                dve.wait_ge(his, t + 1)
                cols = bass.ds(col0 + t * P, P)
                minus_hi(nc, lo[:, :, cols], raw[:, j % 2, :, :], hi[:, :, cols]).then_inc(los, 1)

            scale_rows(0, 0)
            dve.wait_ge(vec, 48 if modulation else 16)
            if modulation:
                nc.vector.scalar_tensor_tensor(out=a[:, :], in0=s[:, :], scalar=1.0, in1=a[:, :],
                                               op0=ALU.add, op1=ALU.mult).then_inc(ab, 1)
                dve.wait_ge(ab, 1)
            scale_rows(1, 1)
            place(0, 0)
            if tiles > step:
                with dve.Fori(0, tiles // step - 1) as i:
                    for j in range(step):
                        scale_rows(step * i + j + 2, (j + 2) % step)
                        place(step * i + j + 1, (j + 1) % step)
                        rest(step * i + j, j)
            for j in range(step):
                if j + 2 < step:
                    scale_rows(tiles - step + j + 2, j + 2)
                if j + 1 < step:
                    place(tiles - step + j + 1, j + 1)
                rest(tiles - step + j, j)

        @block.gpsimd
        def _(pool):
            if modulation:
                pool.wait_ge(vec, 48)
                with pool.Fori(0, tiles // 2) as i:
                    for j in range(2):
                        t = 2 * i + j
                        pool.wait_ge(placed, t + 3)
                        nc.gpsimd.tensor_tensor(raw[:, j, :, :], raw[:, j, :, :], over(b[:, :, None], (P, KD, P)), ALU.add)\
                          .then_inc(shifted, 1)

        @block.tensor
        def _(pe):
            with pe.Fori(0, tiles // 2) as i:
                for j in range(2):
                    pe.wait_ge(scaled, 2 * i + j + 1)
                    pe.wait_ge(placed, 2 * i + j + 1)
                    for k in range(KD):
                        t = nc.tensor.transpose(ps[j][:, k, :], xn[:, j, k * P:(k + 1) * P], ident[:, :])
                    t.then_inc(turned, 1)


def short_convolution(nc, x_hi, x_lo, w_in, conv_w, out_t):
    with Mem(nc, "sc") as m:
        w = m.sb("w", P, 2, KD, P)
        w_hi, w_lo = m.sb_r("w_hi", P, 2, KD, P), m.sb_r("w_lo", P, 2, KD, P)
        taps = m.sb("taps", P, 3, CW // P)
        v = m.sb("v", P, 2 + L)
        hs = m.sb("hs", P, L)
        sz = m.sb("sz", P, 2, NB)
        y = m.sb("y", P, L)
        ps = [[m.ps(f"ps{i}{n}", P, NB) for n in range(LB)] for i in range(2)]
        taps_in, v_pad = m.sem("taps_in"), m.sem("v_pad")
        loaded = [m.sem(f"loaded{i}") for i in range(2)]
        (stored, free, his, los, proj, h_out, z_out, c_used, tap, b_used, half_z, z_used) = (m.sem(n) for n in (
            "stored", "free", "his", "los", "proj", "h_out", "z_out", "c_used", "tap", "b_used", "half_z", "z_used"))
        block = m.block()
        TILES_C = CW // P
        PARTS = 4
        H, C, B, Z = range(PARTS)
        PART_AT = (0, 2, 1, 3)
        wv = w_in[:, 2 * SSM_W:].rearrange("(k p) (s c) -> p k s c", p=P, s=PARTS)

        def cols(n):
            return slice(n * NB, (n + 1) * NB)

        def stream(eng, split, work):
            split(0, 0)

            def tile(j, last):
                for part in range(PARTS):
                    if part + 1 < PARTS:
                        split(j, part + 1)
                    elif not last:
                        split(j + 1, 0)
                    work(j, part)

            with eng.Fori(0, TILES_C - 1) as j:
                tile(j, False)
            tile(TILES_C - 1, True)

        @block.sync
        def _(sp):
            for k in range(3):
                sp.dma_start(taps[:, k, :], columns(conv_w[k, :], CW // P), allow_slow_non_contiguous=True)\
                  .then_inc(taps_in, 16)
            with sp.Fori(0, TILES_C) as j:
                for part in range(PARTS):
                    sp.wait_ge(los, PARTS * j + part + 1)
                    sp.dma_start(w[:, part % 2, :, :], wv[:, :, PART_AT[part], bass.ds(j * P, P)]).then_inc(loaded[part % 2], 16)

        @block.tensor
        def _(pe):
            pe.sem_inc(proj, 2 * LB)
            with pe.Fori(0, TILES_C) as j:
                for part in range(PARTS):
                    pe.wait_ge(los, PARTS * j + part + 3)
                    for n in range(LB):
                        if part == H:
                            pe.wait_ge(b_used, LB * j + n + 1)
                        elif part == C:
                            pe.wait_ge(z_used, LB * j + n + 1)
                        elif part == B:
                            pe.wait_ge(h_out, LB * j + n + 1)
                        else:
                            pe.wait_ge(c_used, LB * j + n + 1 + LB)
                        for k in range(KD):
                            mm = three_products(nc, ps[part % 2][n][:, :], (w_hi[:, part % 2, k, :], w_lo[:, part % 2, k, :]),
                                                (x_hi[:, k, cols(n)], x_lo[:, k, cols(n)]), k == 0, k == KD - 1)
                        mm.then_inc(proj, 1)

        def made(j, part, n):
            return PARTS * LB * j + part * LB + n + 1 + 2 * LB

        @block.scalar
        def _(act):
            nc.scalar.preload_act_table(ACT.Sigmoid)

            def split(j, part):
                act.wait_ge(loaded[part % 2], PARTS // 2 * 16 * j + 16 * (part // 2) + 16)
                act.wait_ge(proj, PARTS * LB * j + (part + 1) * LB)
                nc.scalar.activation(w_hi[:, part % 2, :, :], w[:, part % 2, :, :], ACT.Copy).then_inc(his, 1)

            def work(j, part):
                for n in range(LB):
                    if part == H:
                        act.wait_ge(proj, made(j, H, n))
                        act.wait_ge(c_used, LB * j + n + 1)
                        nc.scalar.activation(hs[:, cols(n)], ps[0][n][:, :], ACT.Copy).then_inc(h_out, 1)
                    elif part == Z:
                        act.wait_ge(proj, made(j, Z, n))
                        act.wait_ge(z_used, LB * j + n + 3)
                        nc.scalar.activation(sz[:, n % 2, :], ps[1][n][:, :], ACT.Sigmoid).then_inc(z_out, 1)

            stream(act, split, work)

        @block.vector
        def _(dve):
            nc.vector.memset(v[:, 0:2], 0.0).then_inc(v_pad, 1)
            dve.wait_ge(taps_in, 48)
            dve.wait_ge(v_pad, 1)
            dve.sem_inc(los, 2)
            dve.sem_inc(b_used, LB)
            dve.sem_inc(z_used, LB)
            dve.sem_inc(c_used, LB)

            def split(j, part):
                dve.wait_ge(his, PARTS * j + part + 1)
                minus_hi(nc, w_lo[:, part % 2, :, :], w[:, part % 2, :, :], w_hi[:, part % 2, :, :]).then_inc(los, 1)

            def work(j, part):
                for n in range(LB):
                    yn = y[:, cols(n)]
                    if part == C:
                        one = [taps[:, k, bass.ds(j, 1)] for k in range(3)]
                        if n == 0:
                            dve.wait_ge(free, j + 1)
                        dve.wait_ge(h_out, LB * j + n + 1)
                        dve.wait_ge(proj, made(j, C, n))
                        nc.vector.tensor_tensor(v[:, 2 + n * NB:2 + (n + 1) * NB], ps[1][n][:, :], hs[:, cols(n)], ALU.mult)\
                          .then_inc(c_used, 1)
                        dve.wait_ge(c_used, LB * j + n + 1 + LB)
                        nc.vector.tensor_scalar(yn, v[:, cols(n)], one[0], None, ALU.mult).then_inc(tap, 1)
                        for k in (1, 2):
                            dve.wait_ge(tap, 3 * LB * j + 3 * n + k)
                            nc.vector.scalar_tensor_tensor(out=yn, in0=v[:, k + n * NB:k + (n + 1) * NB], scalar=one[k],
                                                           in1=yn, op0=ALU.mult, op1=ALU.add).then_inc(tap, 1)
                    elif part == B:
                        dve.wait_ge(tap, 3 * LB * j + 3 * n + 3)
                        dve.wait_ge(proj, made(j, B, n))
                        nc.vector.tensor_tensor(yn, ps[0][n][:, :], yn, ALU.mult).then_inc(b_used, 1)
                    elif part == Z:
                        dve.wait_ge(b_used, LB * j + n + 1 + LB)
                        dve.wait_ge(z_out, LB * j + n + 1)
                        nc.vector.tensor_tensor(yn, yn, sz[:, n % 2, :], ALU.mult).then_inc(half_z, 1)
                        dve.wait_ge(half_z, LB * j + n + 1)
                        nc.vector.tensor_tensor(yn, ps[1][n][:, :], yn, ALU.mult).then_inc(z_used, 1)

            stream(dve, split, work)

        @block.gpsimd
        def _(pool):
            pool.sem_inc(free, 1)
            with pool.Fori(0, TILES_C) as j:
                pool.wait_ge(z_used, LB * j + 2 * LB)
                pool.dma_start(out_t[bass.ds(SSM_W // P + j, 1), :, :].rearrange("k p l -> p (k l)"), y[:, :]).then_inc(stored, 16)
                pool.wait_ge(stored, 16 * j + 16)
                pool.sem_inc(free, 1)


def silu_projection(nc, stage, x_hi, x_lo, w, tiles, out_t):
    with Mem(nc, stage) as m:
        wt = m.sb("wt", P, 2, KD, P)
        w_hi, w_lo = m.sb_r("w_hi", P, 2, KD, P), m.sb_r("w_lo", P, 2, KD, P)
        sg = m.sb("sg", P, 2, NB)
        y = m.sb("y", P, 2, L)
        ps = [m.ps(f"ps{i}", P, NB) for i in range(2)]
        loaded = [m.sem(f"loaded{i}") for i in range(2)]
        stored, free = m.sem("stored"), m.sem("free")
        his, los, proj, gated, done = (m.sem(n) for n in ("his", "los", "proj", "gated", "done"))
        block = m.block()
        wv = w.rearrange("(k p) c -> p k c", p=P)

        @block.sync
        def _(sp):
            with sp.Fori(0, tiles // 2) as i:
                for b in range(2):
                    sp.wait_ge(los, 2 * i + b + 1)
                    sp.dma_start(wt[:, b, :, :], wv[:, :, bass.ds((2 * i + b) * P, P)]).then_inc(loaded[b], 16)

        @block.tensor
        def _(pe):
            pe.sem_inc(proj, 2 * LB)
            with pe.Fori(0, tiles // 2) as i:
                for b in range(2):
                    pe.wait_ge(los, 2 * i + b + 3)
                    for n in range(LB):
                        cols = slice(n * NB, (n + 1) * NB)
                        pe.wait_ge(done, (2 * i + b) * LB + n + 1)
                        for k in range(KD):
                            mm = three_products(nc, ps[n % 2][:, :], (w_hi[:, b, k, :], w_lo[:, b, k, :]),
                                                (x_hi[:, k, cols], x_lo[:, k, cols]), k == 0, k == KD - 1)
                        mm.then_inc(proj, 1)

        @block.scalar
        def _(act):
            nc.scalar.preload_act_table(ACT.Sigmoid)

            def prepare(e, b):
                act.wait_ge(loaded[b], 8 * (e - b) + 16)
                act.wait_ge(proj, (e + 1) * LB)
                nc.scalar.activation(w_hi[:, b, :, :], wt[:, b, :, :], ACT.Copy).then_inc(his, 1)

            def finish(e, b):
                for n in range(LB):
                    t = e * LB + n
                    act.wait_ge(proj, t + 2 * LB + 1)
                    act.wait_ge(done, t + 1)
                    nc.scalar.activation(sg[:, n % 2, :], ps[n % 2][:, :], ACT.Sigmoid).then_inc(gated, 1)

            ahead(act, tiles, prepare, finish)

        @block.vector
        def _(dve):
            dve.sem_inc(done, 2)
            dve.sem_inc(los, 2)

            def prepare(e, b):
                dve.wait_ge(his, e + 1)
                minus_hi(nc, w_lo[:, b, :, :], wt[:, b, :, :], w_hi[:, b, :, :]).then_inc(los, 1)

            def finish(e, b):
                dve.wait_ge(free, e + 1)
                for n in range(LB):
                    dve.wait_ge(gated, e * LB + n + 1)
                    nc.vector.tensor_tensor(y[:, b, n * NB:(n + 1) * NB], ps[n % 2][:, :], sg[:, n % 2, :], ALU.mult)\
                      .then_inc(done, 1)

            ahead(dve, tiles, prepare, finish)

        @block.gpsimd
        def _(pool):
            pool.sem_inc(free, 2)
            with pool.Fori(0, tiles // 2) as i:
                for b in range(2):
                    pool.wait_ge(done, (2 * i + b + 1) * LB + 2)
                    pool.dma_start(out_t[bass.ds(2 * i + b, 1), :, :].rearrange("k p l -> p (k l)"),
                                   y[:, b, :]).then_inc(stored, 16)
                    pool.wait_ge(stored, 16 * (2 * i + b) + 16)
                    pool.sem_inc(free, 1)


def group_in(r, x):
    return 8 * (r // 2) + 2 * x + r % 2


def s5_weights(nc, d, vw, q, toeplitz, a8, ident, kernel_rows, uc, uc_in):
    TWO_PI = 2.0 * math.pi
    C1 = 6.28125
    C2 = float(np.float32(np.round((TWO_PI - C1) * 2.0 ** 22) / 2.0 ** 22))
    C3 = float(np.float32(TWO_PI - C1 - C2))
    ROUND = 1.5 * 2.0 ** 23
    HPI = float(np.float32(math.pi / 2))
    PI = float(np.nextafter(np.float32(math.pi), np.float32(0)))
    with Mem(nc, "s5w") as m:
        are, aim, dt = m.sb("are", P, QP), m.sb("aim", P, QP), m.sb("dt", P, QP)
        sc = m.sb("sc", P, 12, QP)
        pw = m.sb("pw", P, 2, T8 + 1, QP)
        rev = m.sb("rev", P, 2, T8, QP)
        tmp = m.sb("tmp", P, QP * (T8 + 1) * H1)
        bin_ = m.sb("bin", P, 2, QP, H1)
        bb = m.sb("bb", P, 2, QP, H1)
        cc = m.sb("cc", P, 2, QP, H1)
        crow = m.sb("crow", P, 2, 4, 2, S1)
        w = m.sb("w", P, 2, QP, T8, H1)
        kp = m.sb("kp", H1, G1, 7 * H1 + P)
        dcol = m.sb("dcol", P, G1)
        pst = [m.ps(f"pst{i}", P, 4, P) for i in range(4)]
        psk = [m.ps(f"psk{i}", H1, 4, P) for i in range(4)]
        par, bld, cld, dld, chain_, act_done = (m.sem(n) for n in ("par", "bld", "cld", "dld", "chain", "act_done"))
        c_turned, w_turned, k_made, pe_free, w_ready, k_stored, t_loaded, k_pad = (
            m.sem(n) for n in ("c_turned", "w_turned", "k_made", "pe_free", "w_ready", "k_stored", "t_loaded", "k_pad"))
        uc_loaded = m.sem("uc_loaded")
        b_ready, q_ready, k_ready, for_act = (m.sem(n) for n in ("b_ready", "q_ready", "k_ready", "for_act"))
        block = m.block()
        (DT, X, MAG, TH, N, R, SIN, COS, DEN, QR, QI, T) = range(12)

        @block.sync
        def _(sp):
            for g in range(2):
                half = slice(S1 * g, S1 * g + S1)
                for to, of in ((are, d["ssm_a_re"]), (aim, d["ssm_a_im"])):
                    sp.dma_start(to[half, :], of[0, g::2, :].rearrange("q p -> p q"), allow_slow_non_contiguous=True)\
                      .then_inc(par, 16)
                sp.dma_start(dt[half, :], d["ssm_log_dt"][0, g::2].partition_broadcast(S1), allow_slow_non_contiguous=True)\
                  .then_inc(par, 16)
            for g in range(2):
                half = slice(S1 * g, S1 * g + S1)
                for ri, of in ((0, d["ssm_b_re"]), (1, d["ssm_b_im"])):
                    sp.dma_start(bin_[half, ri, :, :], of[0, g::2, :, :].rearrange("q p h -> p q h")).then_inc(bld, 16)
            for ri, of in ((0, d["ssm_c_re"]), (1, d["ssm_c_im"])):
                for dup in range(2):
                    sp.dma_start(crow[:, ri, :, dup, :], of[0].rearrange("(r g) h p -> (g h) r p", r=4)).then_inc(cld, 16)
            for j in range(T8):
                sp.dma_start(dcol[j * H1:(j + 1) * H1, :], d["ssm_d"][0].rearrange("g h -> h g"),
                             allow_slow_non_contiguous=True).then_inc(dld, 16)
            for half in range(HALF):
                sp.dma_start(uc[:, :, half * P:(half + 1) * P], uc_in[half, :, :, :]).then_inc(uc_loaded, 16)
            sp.wait_ge(k_ready, 1)
            sp.dma_start(kernel_rows, kp[:, :, :]).then_inc(k_stored, 16)
            sp.wait_ge(k_stored, 16)
            for j in range(T8):
                at = (T8 - 1 - j) * H1
                sp.dma_start(toeplitz[j * H1:(j + 1) * H1, :, :], kernel_rows[:, :, at:at + P]).then_inc(t_loaded, 16)
            sp.wait_ge(uc_loaded, 16 * HALF)

        @block.scalar
        def _(act):
            act.wait_ge(par, 96)
            nc.scalar.activation(sc[:, DT, :], dt[:, :], ACT.Exp).then_inc(act_done, 1)
            act.wait_ge(for_act, 1)
            nc.scalar.activation(sc[:, MAG, :], sc[:, X, :], ACT.Exp).then_inc(act_done, 1)
            act.wait_ge(for_act, 2)
            nc.scalar.activation(sc[:, SIN, :], sc[:, R, :], ACT.Sin).then_inc(act_done, 1)
            nc.scalar.activation(sc[:, COS, :], sc[:, N, :], ACT.Sin).then_inc(act_done, 1)

        @block.gpsimd
        def _(pool):
            nc.gpsimd.memset(kp[:, :, :], 0.0).then_inc(k_pad, 1)

        @block.vector
        def _(dve):
            n = [0]

            def then(ins):
                n[0] += 1
                ins.then_inc(chain_, 1)
                dve.wait_ge(chain_, n[0])

            def s(i):
                return sc[:, i, :]

            def tt(o, a, b, op):
                then(nc.vector.tensor_tensor(o, a, b, op))

            def ts(o, a, s1, op1, s2=None, op2=None):
                if op2 is None:
                    then(nc.vector.tensor_scalar(o, a, s1, None, op1))
                else:
                    then(nc.vector.tensor_scalar(o, a, s1, s2, op1, op2))

            def complex_product(o, a, b, t, conj=False):
                tt(o[0], a[0], b[0], ALU.mult)
                tt(t, a[1], b[1], ALU.mult)
                tt(o[0], o[0], t, ALU.subtract)
                tt(o[1], a[0], b[1], ALU.mult)
                tt(t, a[1], b[0], ALU.mult)
                if conj:
                    ts(o[1], o[1], -1.0, ALU.mult)
                    tt(o[1], o[1], t, ALU.subtract)
                else:
                    tt(o[1], o[1], t, ALU.add)

            dve.wait_ge(act_done, 1)
            tt(s(X), are[:, :], s(DT), ALU.mult)
            dve.sem_inc(for_act, 1)
            tt(s(TH), aim[:, :], s(DT), ALU.mult)
            ts(s(N), s(TH), 1.0 / TWO_PI, ALU.mult, ROUND, ALU.add)
            ts(s(N), s(N), ROUND, ALU.subtract)
            then(nc.vector.scalar_tensor_tensor(out=s(R), in0=s(N), scalar=-C1, in1=s(TH), op0=ALU.mult, op1=ALU.add))
            then(nc.vector.scalar_tensor_tensor(out=s(R), in0=s(N), scalar=-C2, in1=s(R), op0=ALU.mult, op1=ALU.add))
            then(nc.vector.scalar_tensor_tensor(out=s(R), in0=s(N), scalar=-C3, in1=s(R), op0=ALU.mult, op1=ALU.add))
            ts(s(R), s(R), PI, ALU.min, -PI, ALU.max)
            ts(s(N), s(R), -1.0, ALU.mult)
            tt(s(N), s(N), s(R), ALU.max)
            ts(s(N), s(N), -1.0, ALU.mult, HPI, ALU.add)
            dve.sem_inc(for_act, 1)
            dve.wait_ge(act_done, 4)
            tt(pw[:, 0, 1, :], s(MAG), s(COS), ALU.mult)
            tt(pw[:, 1, 1, :], s(MAG), s(SIN), ALU.mult)
            then(nc.vector.memset(pw[:, 0, 0, :], 1.0))
            then(nc.vector.memset(pw[:, 1, 0, :], 0.0))
            tt(s(DEN), are[:, :], are[:, :], ALU.mult)
            tt(s(T), aim[:, :], aim[:, :], ALU.mult)
            tt(s(DEN), s(DEN), s(T), ALU.add)
            then(nc.vector.reciprocal(s(DEN), s(DEN)))
            ts(s(X), pw[:, 0, 1, :], 1.0, ALU.subtract)
            tt(s(QR), s(X), are[:, :], ALU.mult)
            tt(s(T), pw[:, 1, 1, :], aim[:, :], ALU.mult)
            tt(s(QR), s(QR), s(T), ALU.add)
            tt(s(QR), s(QR), s(DEN), ALU.mult)
            tt(s(QI), pw[:, 1, 1, :], are[:, :], ALU.mult)
            tt(s(T), s(X), aim[:, :], ALU.mult)
            tt(s(QI), s(QI), s(T), ALU.subtract)
            tt(s(QI), s(QI), s(DEN), ALU.mult)
            for have in (1, 2, 4):
                by = [over(pw[:, ri, have:have + 1, :], (P, have, QP)) for ri in range(2)]
                complex_product([pw[:, ri, have + 1:2 * have + 1, :] for ri in range(2)],
                                [pw[:, ri, 1:have + 1, :] for ri in range(2)], by,
                                tmp[:, 0:have * QP].rearrange("p (a b) -> p a b", a=have))
            for ri in range(2):
                then(nc.vector.tensor_copy(a8[:, ri, :], pw[:, ri, T8, :]))
                for j in range(T8):
                    then(nc.vector.tensor_copy(rev[:, ri, j, :], pw[:, ri, T8 - 1 - j, :]))
            dve.wait_ge(bld, 64)
            shape = (P, QP, H1)
            complex_product([bb[:, ri, :, :] for ri in range(2)], [over(s(x)[:, :, None], shape) for x in (QR, QI)],
                            [bin_[:, ri, :, :] for ri in range(2)],
                            tmp[:, 0:QP * H1].rearrange("p (a b) -> p a b", a=QP))
            shape = (P, QP, T8, H1)
            complex_product([w[:, ri, :, :, :] for ri in range(2)],
                            [over(rev[:, ri, :, :].rearrange("p j q -> p q j")[:, :, :, None], shape) for ri in range(2)],
                            [over(bb[:, ri, :, None, :], shape) for ri in range(2)],
                            tmp[:, 0:QP * T8 * H1].rearrange("p (a b c) -> p a b c", a=QP, b=T8))
            dve.sem_inc(w_ready, 1)
            for ri in range(2):
                dve.wait_ge(c_turned, ri + 1)
                for r in range(4):
                    for g in range(2):
                        half = slice(S1 * g, S1 * g + S1)
                        then(nc.vector.tensor_copy(
                            cc[half, ri, 4 * r:4 * r + 4, :],
                            pst[ri][half, r, :].rearrange("p (q g h) -> p q g h", g=2, h=H1)[:, :, g, :]))
            dve.sem_inc(pe_free, 1)
            shape = (P, QP, T8 + 1, H1)
            complex_product([q[:, ri, :, :, :] for ri in range(2)],
                            [over(pw[:, ri, :, :].rearrange("p t q -> p q t")[:, :, :, None], shape) for ri in range(2)],
                            [over(cc[:, ri, :, None, :], shape) for ri in range(2)],
                            tmp[:, :].rearrange("p (a b c) -> p a b c", a=QP, b=T8 + 1), conj=True)
            dve.sem_inc(q_ready, 1)
            for n8 in range(8):
                ri, r = n8 // 4, n8 % 4
                dve.wait_ge(w_turned, n8 + 1)
                then(nc.vector.tensor_copy(vw[:, ri, 4 * r:4 * r + 4, :], pst[2 + n8 % 2][:, :, :]))
                dve.sem_inc(pe_free, 1)
            dve.wait_ge(k_pad, 1)
            for r in range(8):
                dve.wait_ge(k_made, r + 1)
                g = group_in(r, 0)
                then(nc.vector.tensor_copy(kp[:, g:g + 7:2, 7 * H1:], psk[r % 4][:, :, :]))
                dve.sem_inc(pe_free, 1)
            dve.sem_inc(k_ready, 1)
            dve.wait_ge(t_loaded, 16 * T8)
            dve.wait_ge(dld, 16 * T8)
            diag = tmp[:, 0:8 * P].rearrange("p (g x) -> p g x", g=8)
            for r in range(4):
                gs = slice(8 * r, 8 * r + 8)
                tt(diag, over(ident[:, None, :], (P, 8, P)), over(dcol[:, gs, None], (P, 8, P)), ALU.mult)
                tt(toeplitz[:, gs, :], toeplitz[:, gs, :], diag, ALU.add)

        @block.tensor
        def _(pe):
            pe.wait_ge(cld, 64)
            for ri in range(2):
                for r in range(4):
                    t = nc.tensor.transpose(pst[ri][:, r, :], crow[:, ri, r, :, :].rearrange("p a b -> p (a b)"), ident[:, :])
                t.then_inc(c_turned, 1)
            pe.wait_ge(w_ready, 1)
            for n8 in range(8):
                ri, r = n8 // 4, n8 % 4
                if n8 >= 2:
                    pe.wait_ge(pe_free, n8)
                for x in range(4):
                    t = nc.tensor.transpose(pst[2 + n8 % 2][:, x, :],
                                            w[:, ri, 4 * r + x, :, :].rearrange("p a b -> p (a b)"), ident[:, :])
                t.then_inc(w_turned, 1)
            pe.wait_ge(q_ready, 1)
            for r in range(8):
                if r >= 4:
                    pe.wait_ge(pe_free, 9 + r - 3)
                for x in range(4):
                    g = group_in(r, x)
                    half = slice(S1 * (g % 2), S1 * (g % 2) + S1)
                    for ri in range(2):
                        mm = nc.tensor.matmul(psk[r % 4][:, x, :], bb[half, ri, g // 2, :],
                                              q[half, ri, g // 2, 0:T8, :].rearrange("p a b -> p (a b)"),
                                              start=(ri == 0), stop=(ri == 1))
                mm.then_inc(k_made, 1)


def s5_inputs(nc, x_hi, x_lo, w_u, uc_out, ident):
    with Mem(nc, "s5u") as m:
        w = m.sb("w", P, WR, SSM_W)
        w_hi, w_lo = m.sb_r("w_hi", P, KD, SSM_W), m.sb_r("w_lo", P, KD, SSM_W)
        u = m.sb("u", P, G1, T8, H1)
        s_hi, s_lo = m.sb_r("s_hi", P, 2, KD, P), m.sb_r("s_lo", P, 2, KD, P)
        uc = m.sb("uc", P, 2, 4, P)
        ps = [m.ps(f"ps{i}", P, NB) for i in range(2)]
        pst = [m.ps(f"pst{i}", P, 4, P) for i in range(2)]
        w_in = [m.sem(f"w_in{i}") for i in range(WR)]
        stored = [m.sem(f"stored{i}") for i in range(2)]
        w_his, w_los, cut, cut_lo, proj, kept, turned, placed = (m.sem(n) for n in (
            "w_his", "w_los", "cut", "cut_lo", "proj", "kept", "turned", "placed"))
        block = m.block()
        N = T8 // 2

        def slab_of(x, half, t):
            return x[:, :, half * P * T8:(half + 1) * P * T8].rearrange("p k (c j) -> p k j c", j=T8)[:, :, bass.ds(t, 1), :]\
                .rearrange("p k j c -> p k (j c)")

        @block.sync
        def _(sp):
            for k in range(KD):
                if k >= WR:
                    sp.wait_ge(w_los, k - WR + 1)
                sp.dma_start(w[:, k % WR, :], w_u[k * P:(k + 1) * P, :]).then_inc(w_in[k % WR], 16)
            for n in range(HALF * 8):
                half, r = n // 8, n % 8
                sp.wait_ge(placed, n + 1)
                sp.dma_start(uc_out[half, :, 4 * r:4 * r + 4, :], uc[:, n % 2, :, :]).then_inc(stored[n % 2], 16)
            for b in range(2):
                sp.wait_ge(stored[b], 16 * (HALF * 4))

        @block.vector
        def _(dve):
            for k in range(KD):
                dve.wait_ge(w_his, k + 1)
                minus_hi(nc, w_lo[:, k, :], w[:, k % WR, :], w_hi[:, k, :]).then_inc(w_los, 1)
            dve.sem_inc(cut, 2)
            for half in range(HALF):
                with dve.Fori(0, N) as i:
                    for b in range(2):
                        dve.wait_ge(proj, half * T8 + 2 * i + b + 1)
                        nc.vector.tensor_copy(s_hi[:, b, :, :], slab_of(x_hi, half, 2 * i + b)).then_inc(cut, 1)
                for r in range(8):
                    n = half * 8 + r
                    dve.wait_ge(turned, n + 1)
                    if n >= 2:
                        dve.wait_ge(stored[n % 2], 16 * (n // 2))
                    nc.vector.tensor_copy(uc[:, n % 2, :, :], pst[r % 2][:, :, :]).then_inc(placed, 1)

        @block.scalar
        def _(act):
            act.sem_inc(kept, 2)
            for k in range(KD):
                act.wait_ge(w_in[k % WR], 16 * (k // WR) + 16)
                nc.scalar.activation(w_hi[:, k, :], w[:, k % WR, :], ACT.Copy).then_inc(w_his, 1)
            for half in range(HALF):
                def cut_off(t, b):
                    act.wait_ge(proj, half * T8 + t + 1)
                    nc.scalar.activation(s_lo[:, b, :, :], slab_of(x_lo, half, t), ACT.Copy).then_inc(cut_lo, 1)

                def keep(t, b):
                    act.wait_ge(proj, half * T8 + t + 3)
                    nc.scalar.activation(u[:, :, bass.ds(t, 1), :].rearrange("p g j h -> p g (j h)"),
                                         ps[b][:, :].rearrange("p (g h) -> p g h", h=H1), ACT.Copy).then_inc(kept, 1)

                if half:
                    act.wait_ge(turned, 8 * half)
                ahead(act, T8, cut_off, keep)

        @block.tensor
        def _(pe):
            pe.sem_inc(proj, 2)
            for half in range(HALF):
                with pe.Fori(0, N) as i:
                    for b in range(2):
                        t = half * T8 + 2 * i + b
                        pe.wait_ge(cut, t + 3)
                        pe.wait_ge(cut_lo, t + 1)
                        pe.wait_ge(kept, t + 1)
                        for k in range(KD):
                            pe.wait_ge(w_los, k + 1)
                            mm = three_products(nc, ps[b][:, :], (s_hi[:, b, k, :], s_lo[:, b, k, :]),
                                                (w_hi[:, k, :], w_lo[:, k, :]), k == 0, k == KD - 1)
                        mm.then_inc(proj, 1)
                pe.wait_ge(kept, (half + 1) * T8 + 2)
                for r in range(8):
                    n = half * 8 + r
                    if n >= 2:
                        pe.wait_ge(placed, n - 1)
                    for x in range(4):
                        g = 4 * r + x
                        t = nc.tensor.transpose(pst[r % 2][:, x, :], u[:, g, :, :].rearrange("p j h -> p (j h)"), ident[:, :])
                    t.then_inc(turned, 1)


def s5_scan_and_modulations(nc, uc, vw, a8, st, c, c_ctx, w_ada, b_ada, mod):
    with Mem(nc, "s5s") as m:
        ps = [m.ps(f"ps{i}", P, 2, NC8) for i in range(4)]
        a128 = m.sb("a128", P, 2, QP)
        carry = m.sb("carry", P, 2, QP, NSB)
        t1 = m.sb("t1", P, 2, QP, NSB)
        t2 = m.sb("t2", P, 2, QP, NSB)
        made, kept = m.sem("made"), m.sem("kept")
        links = [m.sem(f"link{i}") for i in range(2)]
        QV = 11
        NM = 6 * D
        w = m.sb("w", P, 2, KD, NB)
        cc = m.sb("cc", P, KD, 2)
        sg = m.sb("sg", P, KD, 2)
        row = m.sb("row", 2, NM)
        bias = m.sb("bias", 2, NM)
        psm = [m.ps(f"psm{i}", 2, NB) for i in range(2)]
        c_in, b_in, gated, ready = (m.sem(n) for n in ("c_in", "b_in", "gated", "ready"))
        loaded = [m.sem(f"loaded{i}") for i in range(2)]
        proj, copied, biased, stored = m.sem("proj"), m.sem("copied"), m.sem("biased"), m.sem("stored")
        block = m.block()
        wv = w_ada.rearrange("(k p) n -> p k n", p=P)

        @block.sync
        def _(sp):
            for j, vec in enumerate((c, c_ctx)):
                sp.dma_start(cc[:, :, j], columns(vec, KD), allow_slow_non_contiguous=True).then_inc(c_in, 16)
            sp.dma_start(bias[:, :], every_partition(b_ada, 2)).then_inc(b_in, 16)
            with sp.Fori(0, NM // NB // 2) as i:
                for b in range(2):
                    sp.wait_ge(proj, 2 * i + b + 1)
                    sp.dma_start(w[:, b, :, :], wv[:, :, bass.ds((2 * i + b) * NB, NB)]).then_inc(loaded[b], 16)
            sp.wait_ge(biased, 4)
            sp.dma_start(mod, row[:, :]).then_inc(stored, 16)
            sp.wait_ge(stored, 16)

        def recurrence(eng, ops, link, qs):
            n = [0]
            nq = qs.stop - qs.start

            def count(ins):
                n[0] += 1
                ins.then_inc(link, 1)

            def settled():
                eng.wait_ge(link, n[0])

            def times(o, s, a, width):
                shape = (P, 2, nq, width)
                x1, x2 = (t[:, :, qs, 0:width] for t in (t1, t2))
                count(ops.tensor_tensor(x1, s, over(a[:, 0:1, qs, None], shape), ALU.mult))
                count(ops.tensor_tensor(x2, s, over(a[:, 1:2, qs, None], shape), ALU.mult))
                settled()
                count(ops.tensor_tensor(o[:, 0, :, :], x1[:, 0, :, :], x2[:, 1, :, :], ALU.subtract))
                count(ops.tensor_tensor(o[:, 1, :, :], x1[:, 1, :, :], x2[:, 0, :, :], ALU.add))
                settled()

            def add(to, x):
                count(ops.tensor_tensor(to, to, x, ALU.add))
                settled()

            count(ops.memset(st[:, :, qs, 0:1], 0.0))
            count(ops.tensor_copy(a128[:, :, qs], a8[:, :, qs]))
            settled()
            for _i in range(int(math.log2(SB))):
                x = [a128[:, ri, qs] for ri in range(2)]
                count(ops.tensor_tensor(t1[:, 0, qs, 0], x[0], x[0], ALU.mult))
                count(ops.tensor_tensor(t1[:, 1, qs, 0], x[1], x[1], ALU.mult))
                count(ops.tensor_tensor(t2[:, 0, qs, 0], x[0], x[1], ALU.mult))
                settled()
                count(ops.tensor_tensor(x[0], t1[:, 0, qs, 0], t1[:, 1, qs, 0], ALU.subtract))
                count(ops.tensor_scalar(x[1], t2[:, 0, qs, 0], 2.0, None, ALU.mult))
                settled()
            eng.wait_ge(kept, QP)
            blocks = [st[:, :, qs, k:NC8:SB] for k in range(SB)]
            now = carry[:, :, qs, :]
            for k in range(1, SB):
                times(now, blocks[k - 1], a8, NSB)
                add(blocks[k], now)
            ends = blocks[SB - 1]
            for b in range(1, NSB):
                times(now[:, :, :, 0:1], ends[:, :, :, b - 1:b], a128, 1)
                add(ends[:, :, :, b:b + 1], now[:, :, :, 0:1])
            now = now[:, :, :, 0:NSB - 1]
            for k in range(SB - 1):
                times(now, ends[:, :, :, 0:NSB - 1] if k == 0 else now, a8, NSB - 1)
                add(blocks[k][:, :, :, 1:NSB], now)

        @block.gpsimd
        def _(pool):
            pool.wait_ge(gated, 1)
            nc.gpsimd.tensor_tensor(cc[:, :, :], cc[:, :, :], sg[:, :, :], ALU.mult).then_inc(ready, 1)
            recurrence(pool, nc.gpsimd, links[1], slice(QV, QP))

        @block.tensor
        def _(pe):
            pe.sem_inc(proj, 2)
            for r in range(QP):
                if r >= 4:
                    pe.wait_ge(kept, r - 3)
                for ri in range(2):
                    for g in range(2):
                        mm = nc.tensor.matmul(ps[r % 4][S1 * g:S1 * g + S1, ri, :], vw[:, ri, r, S1 * g:S1 * g + S1],
                                              uc[:, 2 * r + g, :], start=True, stop=True)
                mm.then_inc(made, 1)
            pe.wait_ge(ready, 1)
            with pe.Fori(0, NM // NB // 2) as i:
                for b in range(2):
                    pe.wait_ge(loaded[b], 16 * i + 16)
                    pe.wait_ge(copied, 2 * i + b + 1)
                    for k in range(KD):
                        mm = nc.tensor.matmul(psm[b][:, :], cc[:, k, :], w[:, b, k, :], start=(k == 0), stop=(k == KD - 1))
                    mm.then_inc(proj, 1)

        @block.scalar
        def _(act):
            act.wait_ge(c_in, 32)
            nc.scalar.activation(sg[:, :, :], cc[:, :, :], ACT.Sigmoid).then_inc(gated, 1)
            for r in range(QP):
                act.wait_ge(made, r + 1)
                nc.scalar.activation(st[:, :, r, 1:NC8], ps[r % 4][:, :, 0:NC8 - 1], ACT.Copy).then_inc(kept, 1)
            act.sem_inc(copied, 2)
            with act.Fori(0, NM // NB // 2) as i:
                for b in range(2):
                    act.wait_ge(proj, 2 * i + b + 3)
                    nc.scalar.activation(row[:, bass.ds((2 * i + b) * NB, NB)], psm[b][:, :], ACT.Copy).then_inc(copied, 1)

        @block.vector
        def _(dve):
            recurrence(dve, nc.vector, links[0], slice(0, QV))
            dve.wait_ge(b_in, 16)
            for part in range(4):
                cols = slice(part * (NM // 4), (part + 1) * (NM // 4))
                dve.wait_ge(copied, (part + 1) * (NM // NB // 4) + 2)
                nc.vector.tensor_tensor(row[:, cols], row[:, cols], bias[:, cols], ALU.add).then_inc(biased, 1)


def s5_outputs(nc, uc, st, q, toeplitz, yt, ident):
    with Mem(nc, "s5y") as m:
        y = m.sb("y", P, T8, SSM_W)
        ps = [m.ps(f"ps{i}", P, 4, P) for i in range(2)]
        pst = [m.ps(f"pst{i}", P, 4, P) for i in range(2)]
        made, kept, turned, placed = (m.sem(n) for n in ("made", "kept", "turned", "placed"))
        block = m.block()

        @block.tensor
        def _(pe):
            for half in range(HALF):
                cs = slice(half * P, (half + 1) * P)
                for r in range(8):
                    n = half * 8 + r
                    if n >= 2:
                        pe.wait_ge(kept, n - 1)
                    for x in range(4):
                        g = group_in(r, x)
                        part = slice(S1 * (g % 2), S1 * (g % 2) + S1)
                        nc.tensor.matmul(ps[r % 2][:, x, :], uc[:, g, cs], toeplitz[:, g, :], start=True, stop=False)
                        for ri in range(2):
                            mm = nc.tensor.matmul(ps[r % 2][:, x, :], st[part, ri, g // 2, cs],
                                                  q[part, ri, g // 2, 1:, :].rearrange("p a b -> p (a b)"),
                                                  start=False, stop=(ri == 1))
                    mm.then_inc(made, 1)
                pe.wait_ge(kept, 8 * (half + 1))
                for j in range(T8):
                    n = half * T8 + j
                    if n >= 2:
                        pe.wait_ge(placed, n - 1)
                    for t in range(4):
                        tr = nc.tensor.transpose(pst[j % 2][:, t, :], y[:, j, t * P:(t + 1) * P], ident[:, :])
                    tr.then_inc(turned, 1)

        @block.scalar
        def _(act):
            nc.scalar.preload_act_table(ACT.Gelu_apprx_tanh)
            for half in range(HALF):
                if half:
                    act.wait_ge(turned, T8 * half)
                for r in range(8):
                    act.wait_ge(made, half * 8 + r + 1)
                    for x in range(4):
                        g = group_in(r, x)
                        a = nc.scalar.activation(y[:, :, g * H1:(g + 1) * H1],
                                                 ps[r % 2][:, x, :].rearrange("p (i h) -> p i h", h=H1), ACT.Gelu_apprx_tanh)
                    a.then_inc(kept, 1)

        @block.vector
        def _(dve):
            for half in range(HALF):
                to = yt[:, :, half * P * T8:(half + 1) * P * T8].rearrange("p t (c j) -> p t j c", j=T8)
                for j in range(T8):
                    dve.wait_ge(turned, half * T8 + j + 1)
                    nc.vector.tensor_copy(to[:, :, j, :], pst[j % 2][:, :, :]).then_inc(placed, 1)


def s5_gate(nc, yt, w_glu, b_glu, silu_z, out_t):
    KS = SSM_W // P
    with Mem(nc, "glu") as m:
        w = m.sb("w", P, KS, SSM_W)
        bias = m.sb("bias", P, KS)
        z = m.sb("z", P, 2, L)
        o = m.sb("o", P, 2, L)
        sg = m.sb("sg", P, 2, NB)
        ps = [m.ps(f"ps{i}", P, NB) for i in range(2)]
        loaded, biased = m.sem("loaded"), m.sem("biased")
        z_in = [m.sem(f"z_in{i}") for i in range(2)]
        stored = [m.sem(f"stored{i}") for i in range(2)]
        proj, gated, half_done, done = (m.sem(n) for n in ("proj", "gated", "half_done", "done"))
        block = m.block()

        @block.sync
        def _(sp):
            sp.dma_start(w[:, :, :], w_glu.rearrange("(k p) c -> p k c", p=P)).then_inc(loaded, 16)
            sp.dma_start(bias[:, :], columns(b_glu, KS), allow_slow_non_contiguous=True).then_inc(biased, 16)
            for e in range(KS):
                if e >= 2:
                    sp.wait_ge(done, LB * (e - 1))
                sp.dma_start(z[:, e % 2, :], silu_z[e, :, :]).then_inc(z_in[e % 2], 16)
            for e in range(KS):
                sp.wait_ge(done, LB * (e + 1))
                sp.dma_start(out_t[e, :, :], o[:, e % 2, :]).then_inc(stored[e % 2], 16)
            for b in range(2):
                sp.wait_ge(stored[b], 16 * KS // 2)

        @block.tensor
        def _(pe):
            pe.wait_ge(loaded, 16)
            for e in range(KS):
                for n in range(LB):
                    t = e * LB + n
                    if t >= 2:
                        pe.wait_ge(gated, t - 1)
                    for k in range(KS):
                        mm = nc.tensor.matmul(ps[n % 2][:, :], w[:, k, e * P:(e + 1) * P], yt[:, k, n * NB:(n + 1) * NB],
                                              start=(k == 0), stop=(k == KS - 1))
                    mm.then_inc(proj, 1)

        @block.scalar
        def _(act):
            act.wait_ge(biased, 16)
            for e in range(KS):
                for n in range(LB):
                    t = e * LB + n
                    act.wait_ge(proj, t + 1)
                    if t >= 2:
                        act.wait_ge(done, t - 1)
                    nc.scalar.activation(sg[:, n % 2, :], ps[n % 2][:, :], ACT.Sigmoid, bias=bias[:, e:e + 1]).then_inc(gated, 1)

        @block.vector
        def _(dve):
            for e in range(KS):
                dve.wait_ge(z_in[e % 2], 16 * (e // 2 + 1))
                if e >= 2:
                    dve.wait_ge(stored[e % 2], 16 * (e // 2))
                for n in range(LB):
                    t = e * LB + n
                    cols = slice(n * NB, (n + 1) * NB)
                    dve.wait_ge(gated, t + 1)
                    nc.vector.tensor_tensor(o[:, e % 2, cols], sg[:, n % 2, :], yt[:, e, cols], ALU.mult).then_inc(half_done, 1)
                    dve.wait_ge(half_done, t + 1)
                    nc.vector.tensor_tensor(o[:, e % 2, cols], o[:, e % 2, cols], z[:, e % 2, cols], ALU.mult).then_inc(done, 1)


def output_rows_1(nc, y_t, w_out, x, gain, x2):
    with Mem(nc, "or1") as m:
        w = m.sb("w", P, WR, D)
        w_hi, w_lo = m.sb_r("w_hi", P, KD, D), m.sb_r("w_lo", P, KD, D)
        g = m.sb("g", P, D)
        y = m.sb("y", P, 2, KD, P)
        y_hi, y_lo = m.sb_r("y_hi", P, 2, KD, P), m.sb_r("y_lo", P, 2, KD, P)
        xr = m.sb("xr", P, 2, D)
        h = m.sb("h", P, 2, D)
        o = m.sb("o", P, 2, D)
        junk = m.sb("junk", P, D)
        stat = m.sb("stat", P, 2, 4)
        eps = m.sb("eps", P, 1)
        ps = [m.ps(f"ps{i}", P, D) for i in range(2)]
        g_in, eps_set = m.sem("g_in"), m.sem("eps_set")
        w_in = [m.sem(f"w_in{i}") for i in range(WR)]
        y_in = [m.sem(f"y_in{i}") for i in range(2)]
        x_in = [m.sem(f"x_in{i}") for i in range(2)]
        w_his, w_los, y_his, y_los, proj, added, squared, rooted, inverted, normed, stored, free = (
            m.sem(n) for n in ("w_his", "w_los", "y_his", "y_los", "proj", "added", "squared", "rooted", "inverted", "normed",
                               "stored", "free"))
        block = m.block()
        rows_in = x.rearrange("(t p) d -> t p d", p=P)
        rows_out = x2.rearrange("(t p) d -> t p d", p=P)

        @block.sync
        def _(sp):
            def load(t, b):
                sp.wait_ge(y_los, t + 1)
                sp.dma_start(y[:, b, :, :], y_t[:, :, bass.ds(t * P, P)].rearrange("k p l -> p k l")).then_inc(y_in[b], 16)

            def load_rows(t, b):
                sp.wait_ge(added, t + 1)
                sp.dma_start(xr[:, b, :], rows_in[bass.ds(t, 1), :, :].rearrange("t p d -> p (t d)")).then_inc(x_in[b], 16)

            load(0, 0)
            for k in range(KD):
                if k >= WR:
                    sp.wait_ge(w_los, k - WR + 1)
                sp.dma_start(w[:, k % WR, :], w_out[k * P:(k + 1) * P, :]).then_inc(w_in[k % WR], 16)
            load(1, 1)
            load_rows(0, 0)
            sp.dma_start(g[:, :], every_partition(gain)).then_inc(g_in, 16)
            with sp.Fori(0, TILES // 2 - 1) as i:
                for b in range(2):
                    load(2 * i + b + 2, b)
                    load_rows(2 * i + b + 1, 1 - b)
            load_rows(TILES - 1, 1)

        @block.tensor
        def _(pe):
            pe.sem_inc(proj, 2)
            with pe.Fori(0, TILES // 2) as i:
                for b in range(2):
                    t = 2 * i + b
                    pe.wait_ge(y_los, t + 3)
                    pe.wait_ge(added, t + 1)
                    for k in range(KD):
                        pe.wait_ge(w_los, k + 1)
                        for n in range(2):
                            cols = slice(n * NB, (n + 1) * NB)
                            mm = three_products(nc, ps[b][:, cols], (y_hi[:, b, k, :], y_lo[:, b, k, :]),
                                                (w_hi[:, k, cols], w_lo[:, k, cols]), k == 0, k == KD - 1)
                    mm.then_inc(proj, 1)

        @block.scalar
        def _(act):
            act.wait_ge(eps_set, 1)
            nc.scalar.preload_act_table(ACT.Sqrt)

            def prepare(t, b):
                act.wait_ge(y_in[b], 8 * (t - b) + 16)
                act.wait_ge(proj, t + 1)
                nc.scalar.activation(y_hi[:, b, :, :], y[:, b, :, :], ACT.Copy).then_inc(y_his, 1)

            def finish(t, b):
                act.wait_ge(added, t + 3)
                nc.scalar.activation(junk[:, :], h[:, b, :], ACT.Square, accum_out=stat[:, b, 0:1]).then_inc(squared, 1)
                act.wait_ge(squared, t + 1)
                nc.scalar.activation(stat[:, b, 1:2], stat[:, b, 0:1], ACT.Sqrt, scale=1.0 / D, bias=eps[:, :])\
                  .then_inc(rooted, 1)

            def weights():
                for k in range(KD):
                    act.wait_ge(w_in[k % WR], 16 * (k // WR) + 16)
                    nc.scalar.activation(w_hi[:, k, :], w[:, k % WR, :], ACT.Copy).then_inc(w_his, 1)

            ahead(act, TILES, prepare, finish, weights)

        @block.vector
        def _(dve):
            nc.vector.memset(eps[:, :], EPS).then_inc(eps_set, 1)
            dve.sem_inc(added, 2)
            dve.sem_inc(y_los, 2)

            def prepare(t, b):
                dve.wait_ge(y_his, t + 1)
                nc.vector.tensor_tensor(y_lo[:, b, :, :], y[:, b, :, :], y_hi[:, b, :, :].bitcast(F32), ALU.subtract)\
                  .then_inc(y_los, 1)

            def finish(t, b):
                dve.wait_ge(x_in[b], 8 * (t - b) + 16)
                dve.wait_ge(proj, t + 3)
                nc.vector.tensor_tensor(h[:, b, :], ps[b][:, :], xr[:, b, :], ALU.add).then_inc(added, 1)
                dve.wait_ge(rooted, t + 1)
                nc.vector.reciprocal(stat[:, b, 2:3], stat[:, b, 1:2]).then_inc(inverted, 1)
                dve.wait_ge(inverted, t + 1)
                dve.wait_ge(free, t + 1)
                nc.vector.scalar_tensor_tensor(out=o[:, b, :], in0=h[:, b, :], scalar=stat[:, b, 2:3], in1=g[:, :],
                                               op0=ALU.mult, op1=ALU.mult).then_inc(normed, 1)

            def weights():
                for k in range(KD):
                    dve.wait_ge(w_his, k + 1)
                    minus_hi(nc, w_lo[:, k, :], w[:, k % WR, :], w_hi[:, k, :]).then_inc(w_los, 1)
                dve.wait_ge(g_in, 16)

            ahead(dve, TILES, prepare, finish, weights)

        @block.gpsimd
        def _(pool):
            pool.sem_inc(free, 2)
            with pool.Fori(0, TILES // 2) as i:
                for b in range(2):
                    t = 2 * i + b
                    pool.wait_ge(normed, t + 1)
                    pool.dma_start(rows_out[bass.ds(t, 1), :, :].rearrange("t p d -> p (t d)"), o[:, b, :]).then_inc(stored, 16)
                    pool.wait_ge(stored, 16 * t + 16)
                    pool.sem_inc(free, 1)


def convolved_projection(nc, h_hi, h_lo, w, conv_w, conv_b, xbc):
    with Mem(nc, "cp") as m:
        wt = m.sb("wt", P, KD, P)
        w_hi, w_lo = m.sb_r("w_hi", P, 2, KD, P), m.sb_r("w_lo", P, 2, KD, P)
        taps = m.sb("taps", P, XT_, KC)
        bias = m.sb("bias", P, XT_)
        rows, half = L // ROWLEN, KC // 2
        pitch = ROWLEN + 2 * half
        XP = rows * pitch
        CP = LC + 2 * half
        pad = m.sb("pad", P, 2, XP + CP)
        acc = m.sb("acc", P, 2, LT)
        blocks = [(n * NB, NB) for n in range(LB)] + [(L, LC)]
        ps = [m.ps(f"ps{n}", P, NB) for n in range(len(blocks))]
        taps_in, padded = m.sem("taps_in"), m.sem("padded")
        loaded, his, los = m.sem("loaded"), m.sem("his"), m.sem("los")
        proj, kept, tap, silu, stored, free = (m.sem(n) for n in ("proj", "kept", "tap", "silu", "stored", "free"))
        block = m.block()
        wv = w.rearrange("(k p) c -> p k c", p=P)
        NBL = len(blocks)

        @block.sync
        def _(sp):
            sp.dma_start(taps[:, :, :], conv_w.rearrange("(t p) k -> p t k", p=P)).then_inc(taps_in, 16)
            sp.dma_start(bias[:, :], columns(conv_b, XT_), allow_slow_non_contiguous=True).then_inc(taps_in, 16)
            with sp.Fori(0, XT_) as t:
                sp.wait_ge(los, t + 1)
                sp.dma_start(wt[:, :, :], wv[:, :, bass.ds(t * P, P)]).then_inc(loaded, 16)

        @block.tensor
        def _(pe):
            pe.sem_inc(proj, 2 * NBL)
            with pe.Fori(0, XT_ // 2) as i:
                for b in range(2):
                    pe.wait_ge(los, 2 * i + b + 2)
                    for n, (at, size) in enumerate(blocks):
                        pe.wait_ge(kept, (2 * i + b) * NBL + n + 1)
                        for k in range(KD):
                            mm = three_products(nc, ps[n][:, 0:size], (w_hi[:, b, k, :], w_lo[:, b, k, :]),
                                                (h_hi[:, k, at:at + size], h_lo[:, k, at:at + size]), k == 0, k == KD - 1)
                        mm.then_inc(proj, 1)

        @block.scalar
        def _(act):
            nc.scalar.preload_act_table(ACT.Silu)
            act.wait_ge(padded, 1)
            act.sem_inc(kept, NBL)
            act.sem_inc(silu, 2)

            def prepare(t, b):
                act.wait_ge(loaded, 16 * t + 16)
                act.wait_ge(proj, (t + 1) * NBL)
                nc.scalar.activation(w_hi[:, b, :, :], wt[:, :, :], ACT.Copy).then_inc(his, 1)

            def finish(t, b):
                act.wait_ge(silu, t + 1)
                for n, (at, size) in enumerate(blocks):
                    act.wait_ge(proj, t * NBL + n + 2 * NBL + 1)
                    if n < LB:
                        r = NB // ROWLEN
                        to = pad[:, b, n * r * pitch:(n + 1) * r * pitch].rearrange("p (r c) -> p r c", c=pitch)
                        nc.scalar.activation(to[:, :, half:half + ROWLEN], ps[n][:, :].rearrange("p (r c) -> p r c", c=ROWLEN),
                                             ACT.Copy).then_inc(kept, 1)
                    else:
                        nc.scalar.activation(pad[:, b, XP + half:XP + half + LC], ps[n][:, 0:LC], ACT.Copy).then_inc(kept, 1)
                act.wait_ge(tap, 2 * KC * (t + 1) + 2)
                nc.scalar.activation(acc[:, b, :], acc[:, b, :], ACT.Silu).then_inc(silu, 1)

            ahead(act, XT_, prepare, finish)

        @block.vector
        def _(dve):
            nc.vector.memset(pad[:, :, :], 0.0).then_inc(padded, 1)
            dve.wait_ge(taps_in, 32)
            dve.sem_inc(tap, 2)
            dve.sem_inc(los, 1)

            def prepare(t, b):
                dve.wait_ge(his, t + 1)
                minus_hi(nc, w_lo[:, b, :, :], wt[:, :, :], w_hi[:, b, :, :]).then_inc(los, 1)

            def finish(t, b):
                grid = pad[:, b, 0:XP].rearrange("p (r c) -> p r c", c=pitch)
                parts = [(acc[:, b, 0:L].rearrange("p (r c) -> p r c", c=ROWLEN), lambda k: grid[:, :, k:k + ROWLEN]),
                         (acc[:, b, L:LT], lambda k: pad[:, b, XP + k:XP + k + LC])]
                dve.wait_ge(kept, (t + 2) * NBL)
                dve.wait_ge(free, t + 1)
                for k in range(KC):
                    for x, (to, src) in enumerate(parts):
                        one = taps[:, bass.ds(t, 1), k]
                        if k == 0:
                            nc.vector.tensor_scalar(to, src(0), one, bias[:, bass.ds(t, 1)], ALU.mult, ALU.add).then_inc(tap, 1)
                        else:
                            dve.wait_ge(tap, 2 * KC * t + 2 * (k - 1) + x + 3)
                            nc.vector.scalar_tensor_tensor(out=to, in0=src(k), scalar=one, in1=to, op0=ALU.mult,
                                                           op1=ALU.add).then_inc(tap, 1)

            ahead(dve, XT_, prepare, finish)

        @block.gpsimd
        def _(pool):
            pool.sem_inc(free, 2)
            with pool.Fori(0, XT_ // 2) as i:
                for b in range(2):
                    t = 2 * i + b
                    pool.wait_ge(silu, t + 3)
                    pool.dma_start(xbc[bass.ds(t, 1), :, :].rearrange("k p l -> p (k l)"), acc[:, b, :]).then_inc(stored, 16)
                    pool.wait_ge(stored, 16 * t + 16)
                    pool.sem_inc(free, 1)


def decays(nc, h_hi, h_lo, w_dt, dt_bias, a_log, decay_rows, totals, decay_cols, ident, ones):
    CH = LT // P
    H2 = 2 * HEADS
    GROUP = P // H2
    groups = [(c, min(GROUP, CH - c)) for c in range(0, CH, GROUP)]
    with Mem(nc, "dec") as m:
        w = m.sb("w", P, KD, H2)
        w_hi, w_lo = m.sb_r("w_hi", P, KD, H2), m.sb_r("w_lo", P, KD, H2)
        bias, al, A = m.sb("bias", P, H2), m.sb("al", P, H2), m.sb("A", P, H2)
        raw = m.sb("raw", H2, LT)
        v, n_, e, z, x, a, dt_, etot = (m.sb(n, P, CH, H2) for n in ("v", "n", "e", "z", "x", "a", "dt", "etot"))
        tri = m.sb("tri", P, 4, P)
        rows = m.sb("rows", P, len(groups), P)
        cols = m.sb("cols", P, CH, 3, 64)
        ps = m.ps("ps", P, CH, H2)
        psa = m.ps("psa", P, CH, H2)
        psx = m.ps("psx", P, CH, H2)
        psw = m.ps("psw", P, CH, H2)
        psr = [m.ps(f"psr{i}", H2, NB) for i in range(2)]
        pst = m.ps("pst", P, len(groups), P)
        raw_made, raw_kept = m.sem("raw_made"), m.sem("raw_kept")
        blocks = [(n * NB, NB) for n in range(LB)] + [(L, LC)]
        filled, loaded, w_split, proj, for_act, link, exped, ready, summed, turned, stored = (
            m.sem(n) for n in ("filled", "loaded", "w_split", "proj", "for_act", "link", "exped", "ready", "summed", "turned",
                               "stored"))
        block = m.block()

        @block.sync
        def _(sp):
            sp.dma_start(w[:, :, :], w_dt.rearrange("(k p) h -> p k h", p=P)).then_inc(loaded, 16)
            sp.dma_start(bias[:, :], every_partition(dt_bias.rearrange("x h -> (x h)"))).then_inc(loaded, 16)
            sp.dma_start(al[:, :], every_partition(a_log.rearrange("x h -> (x h)"))).then_inc(loaded, 16)
            sp.wait_ge(ready, 3)
            for i, (c, size) in enumerate(groups):
                sp.dma_start(decay_rows[c:c + size, :, :].rearrange("c h l -> (c h) l"), rows[0:size * H2, i, :]).then_inc(stored, 16)
            sp.wait_ge(exped, 4)
            sp.dma_start(totals.rearrange("c h -> (c h)").rearrange("(o x) -> o x", o=1),
                         etot[0:1, :, :].rearrange("p c h -> p (c h)")).then_inc(stored, 16)
            sp.wait_ge(ready, 4)
            sp.dma_start(decay_cols.rearrange("c p x -> p c x"), cols[:, :, :, :].rearrange("p c a b -> p c (a b)"))\
              .then_inc(stored, 16)
            sp.wait_ge(stored, 16 * (len(groups) + 2))

        @block.gpsimd
        def _(pool):
            nc.gpsimd.memset(tri[:, :, :], 1.0).then_inc(filled, 1)
            nc.gpsimd.memset(cols[:, :, :, :], 0.0).then_inc(filled, 1)
            pool.wait_ge(filled, 2)
            for i, (sign, base) in enumerate(((1, 0), (-1, 0), (-1, -1), (1, -1))):
                nc.gpsimd.affine_select(out=tri[:, i, :], in_=tri[:, i, :], compare_op=ALU.is_ge, fill=0.0, base=base,
                                        pattern=[[sign, P]], channel_multiplier=-sign).then_inc(filled, 1)

        @block.tensor
        def _(pe):
            pe.wait_ge(w_split, 2)
            for n, (at, size) in enumerate(blocks):
                if n >= 2:
                    pe.wait_ge(raw_kept, n - 1)
                for k in range(KD):
                    mm = three_products(nc, psr[n % 2][:, 0:size], (w_hi[:, k, :], w_lo[:, k, :]),
                                        (h_hi[:, k, at:at + size], h_lo[:, k, at:at + size]), k == 0, k == KD - 1)
                mm.then_inc(raw_made, 1)
            pe.wait_ge(raw_kept, len(blocks))
            for c in range(CH):
                t = nc.tensor.transpose(ps[:, c, :], raw[:, c * P:(c + 1) * P], ident[0:H2, 0:H2])
            t.then_inc(proj, 1)
            pe.wait_ge(filled, 6)
            pe.wait_ge(ready, 1)
            for to, of in ((psa, 0), (psx, 2)):
                for d in range(2):
                    hs = slice(d * HEADS, (d + 1) * HEADS)
                    nc.tensor.matmul(to[:, :, hs], tri[:, of + d, :], z[:, :, hs], start=True, stop=True)
            nc.tensor.matmul(psw[:, :, :], ones[:, :], z[:, :, :], start=True, stop=True).then_inc(summed, 1)
            pe.wait_ge(ready, 2)
            for i, (c, size) in enumerate(groups):
                t = nc.tensor.transpose(pst[0:size * H2, i, :], a[:, c:c + size, :].rearrange("p c h -> p (c h)"), ident[:, :])
            t.then_inc(turned, 1)

        @block.scalar
        def _(act):
            act.wait_ge(loaded, 48)
            nc.scalar.activation(al[:, :], al[:, :], ACT.Exp).then_inc(exped, 1)
            for n, (at, size) in enumerate(blocks):
                act.wait_ge(raw_made, n + 1)
                nc.scalar.activation(raw[:, at:at + size], psr[n % 2][:, 0:size], ACT.Copy).then_inc(raw_kept, 1)
            act.wait_ge(for_act, 1)
            nc.scalar.activation(e[:, :, :], n_[:, :, :], ACT.Exp).then_inc(exped, 1)
            act.wait_ge(summed, 1)
            nc.scalar.activation(x[:, :, :], psx[:, :, :], ACT.Exp).then_inc(exped, 1)
            nc.scalar.activation(etot[:, :, :], psw[:, :, :], ACT.Exp).then_inc(exped, 1)

        @block.vector
        def _(dve):
            n = [0]

            def then(ins):
                n[0] += 1
                ins.then_inc(link, 1)
                dve.wait_ge(link, n[0])

            def tt(o, p, q, op):
                then(nc.vector.tensor_tensor(o[:, :, :], p[:, :, :], q, op))

            shape = (P, CH, H2)
            dve.wait_ge(loaded, 48)
            nc.vector.tensor_copy(w_hi[:, :, :], w[:, :, :]).then_inc(w_split, 1)
            dve.wait_ge(w_split, 1)
            minus_hi(nc, w_lo[:, :, :], w[:, :, :], w_hi[:, :, :]).then_inc(w_split, 1)
            dve.wait_ge(exped, 1)
            then(nc.vector.tensor_scalar(A[:, :], al[:, :], -1.0, None, ALU.mult))
            dve.wait_ge(proj, 1)
            tt(v, ps, over(bias[:, None, :], shape), ALU.add)
            then(nc.vector.tensor_scalar(n_[:, :, :], v[:, :, :], -1.0, None, ALU.mult))
            tt(n_, n_, v[:, :, :], ALU.min)
            dve.sem_inc(for_act, 1)
            then(nc.vector.tensor_scalar(v[:, :, :], v[:, :, :], 0.0, None, ALU.max))
            dve.wait_ge(exped, 2)
            then(nc.vector.tensor_scalar(n_[:, :, :], e[:, :, :], 2.0, None, ALU.add))
            then(nc.vector.reciprocal(n_[:, :, :], n_[:, :, :]))
            tt(z, e, n_[:, :, :], ALU.mult)
            tt(n_, z, z[:, :, :], ALU.mult)
            then(nc.vector.tensor_scalar(e[:, :, :], n_[:, :, :], 1.0 / 15, None, ALU.mult))
            for k in range(13, 1, -2):
                then(nc.vector.scalar_tensor_tensor(out=e[:, :, :], in0=e[:, :, :], scalar=1.0 / k, in1=n_[:, :, :],
                                                    op0=ALU.add, op1=ALU.mult))
            then(nc.vector.scalar_tensor_tensor(out=e[:, :, :], in0=e[:, :, :], scalar=1.0, in1=z[:, :, :], op0=ALU.add, op1=ALU.mult))
            then(nc.vector.scalar_tensor_tensor(out=dt_[:, :, :], in0=e[:, :, :], scalar=2.0, in1=v[:, :, :], op0=ALU.mult, op1=ALU.add))
            tt(z, dt_, over(A[:, None, :], shape), ALU.mult)
            dve.sem_inc(ready, 1)
            dve.wait_ge(summed, 1)
            then(nc.vector.tensor_copy(a[:, :, :], psa[:, :, :]))
            dve.sem_inc(ready, 1)
            dve.wait_ge(filled, 6)
            for d in range(2):
                hs, to = slice(d * HEADS, (d + 1) * HEADS), slice(32 * d, 32 * d + HEADS)
                then(nc.vector.tensor_copy(cols[:, :, 0, to], dt_[:, :, hs]))
                then(nc.vector.tensor_copy(cols[:, :, 1, to], a[:, :, hs]))
            dve.wait_ge(turned, 1)
            for i, (c, size) in enumerate(groups):
                then(nc.vector.tensor_copy(rows[0:size * H2, i, :], pst[0:size * H2, i, :]))
            dve.sem_inc(ready, 1)
            dve.wait_ge(exped, 3)
            for d in range(2):
                hs, to = slice(d * HEADS, (d + 1) * HEADS), slice(32 * d, 32 * d + HEADS)
                then(nc.vector.tensor_tensor(cols[:, :, 2, to], x[:, :, hs], dt_[:, :, hs], ALU.mult))
            dve.sem_inc(ready, 1)


def turn_chunk(nc, xc, pst, tiles, ident):
    for k in range(tiles):
        t = nc.tensor.transpose(pst[:, k, :], xc[:, k, :], ident[:, :])
    return t


def chunk_states(nc, rows, xw, pss):
    XR = SW // P
    for g in range(SG):
        mm = nc.tensor.matmul(pss[:, g // 2, (g % 2) * HR * HD:(g % 2 + 1) * HR * HD], rows[:, XR + g, :],
                              xw[:, g * HR:(g + 1) * HR, :].rearrange("p h d -> p (h d)"), start=True, stop=True)
    return mm


def states_view(h):
    return h.rearrange("p (b x) d -> p b (x d)", b=2)


def context_states(nc, m, block, xbc, totals, decay_cols, hf, hb, ident):
    XR, TS = SW // P, SW // P + SG
    xc = m.sb("c_xc", P, CCH, TS, P)
    dc = m.sb("c_dc", P, CCH, 3, 64)
    dec = m.sb("c_dec", P, LT // P, 2 * HEADS)
    rows = m.sb("c_rows", P, TS, P)
    xw = m.sb("c_xw", P, HEADS, HD)
    pst = m.ps("c_pst", P, 12, P)
    pss = pst[:, 0:8, :].rearrange("p (b x) q -> p b (x q)", b=2)
    taken = m.sem("c_taken")
    loaded, turned, kept, weighted, made, link = (m.sem(n) for n in ("c_loaded", "c_turned", "c_kept", "c_weighted", "c_made", "c_link"))
    work = [(0, 0, hf, True), (0, 1, hb, True), (1, 0, hf, False), (1, 1, hb, False)]

    @block.sync
    def _(sp):
        for c in range(CCH):
            sp.dma_start(xc[:, c, :, :], xbc[0:TS, :, L + c * P:L + (c + 1) * P].rearrange("k p l -> p k l")).then_inc(loaded, 16)
            sp.dma_start(dc[:, c, :, :].rearrange("p a b -> p (a b)"), decay_cols[NCH + c, :, :]).then_inc(loaded, 16)
        sp.dma_start(dec[:, :, :].rearrange("p c h -> p (c h)"), every_partition(totals.rearrange("c h -> (c h)")))\
          .then_inc(loaded, 16)

    @block.tensor
    def _(pe):
        pe.wait_ge(loaded, 80)
        for c in range(CCH):
            if c:
                pe.wait_ge(taken, 2 * c)
            turn_chunk(nc, xc[:, c, :, :], pst, TS, ident).then_inc(turned, 1)
            for x in range(2):
                pe.wait_ge(weighted, 2 * c + x + 1)
                chunk_states(nc, rows, xw, pss).then_inc(made, 1)

    @block.scalar
    def _(act):
        for c in range(CCH):
            act.wait_ge(turned, c + 1)
            if c:
                act.wait_ge(made, 2 * c)
            nc.scalar.activation(rows[:, :, :], pst[:, 0:TS, :], ACT.Copy).then_inc(kept, 1)

    @block.vector
    def _(dve):
        n = [0]

        def then(ins):
            n[0] += 1
            ins.then_inc(link, 1)
            dve.wait_ge(link, n[0])

        dve.wait_ge(loaded, 80)
        for w, (c, x, h, first) in enumerate(work):
            dve.wait_ge(kept, c + 1)
            if w:
                dve.wait_ge(made, w)
            nc.vector.tensor_tensor(xw[:, :, :], rows[:, 0:XR, :].rearrange("p k (h d) -> p (k h) d", d=HD),
                                    over(dc[:, c, 2, 32 * x:32 * x + HEADS, None], (P, HEADS, HD)), ALU.mult).then_inc(weighted, 1)
            dve.wait_ge(made, w + 1)
            sts = pss[:, :, 0:2 * HR * HD]
            if first:
                then(nc.vector.tensor_copy(states_view(h), sts))
            elif x == 0:
                then(nc.vector.tensor_tensor(h, h, over(dec[:, NCH + 1, 0:HEADS, None], (P, HEADS, HD)), ALU.mult))
                then(nc.vector.tensor_tensor(states_view(h), states_view(h), sts, ALU.add))
            else:
                t = xw[:, :, :]
                then(nc.vector.tensor_copy(states_view(t), sts))
                then(nc.vector.tensor_tensor(t, t, over(dec[:, NCH, HEADS:2 * HEADS, None], (P, HEADS, HD)), ALU.mult))
                then(nc.vector.tensor_tensor(h, h, t, ALU.add))
            dve.sem_inc(taken, 1)


def backward_states(nc, xbc, totals, decay_cols, hb, hb_in, ident):
    XR, TS = SW // P, SW // P + SG
    with Mem(nc, "bst") as m:
        xc = m.sb("xc", P, 2, TS, P)
        dc = m.sb("dc", P, 2, 3 * 64)
        dec = m.sb("dec", P, LT // P, 2 * HEADS)
        rows = m.sb("rows", P, 2, TS, P)
        xw = m.sb("xw", P, 2, HEADS, HD)
        h = m.sb("h", P, 2, HEADS, HD)
        pst = [m.ps(f"pst{i}", P, 12, P) for i in range(2)]
        pss = m.ps("pss", P, 2, NB)
        start, turned, kept, weighted, made, decayed, ahead_s, stored, free, begun = (
            m.sem(n) for n in ("start", "turned", "kept", "weighted", "made", "decayed", "ahead", "stored", "free", "begun"))
        loaded = [m.sem(f"loaded{i}") for i in range(2)]
        block = m.block()

        @block.sync
        def _(sp):
            sp.dma_start(dec[:, :, :].rearrange("p c h -> p (c h)"), every_partition(totals.rearrange("c h -> (c h)")))\
              .then_inc(start, 16)
            chunk = sp.alloc_register("back_sp")
            sp.reg_mov(chunk, NCH + 1)
            with sp.Fori(0, NCH // 2) as i:
                sp.reg_sub(chunk, chunk, 2)
                last = sp.snap(chunk, min_val=1, max_val=NCH - 1)
                for b in range(2):
                    t = 2 * i + b
                    sp.wait_ge(turned, t + 1)
                    sp.wait_ge(weighted, t + 1)
                    c = last - b
                    sp.dma_start(xc[:, b, :, :], xbc[0:TS, :, bass.ds(c * P, P)].rearrange("k p l -> p k l")).then_inc(loaded[b], 16)
                    sp.dma_start(dc[:, b, :], decay_cols[bass.ds(c, 1), :, :].rearrange("c p x -> p (c x)")).then_inc(loaded[b], 16)

        @block.tensor
        def _(pe):
            pe.sem_inc(turned, 2)
            pe.sem_inc(made, 2)

            def turn(t, b):
                pe.wait_ge(loaded[b], 16 * (t - b) + 32)
                pe.wait_ge(kept, t + 1)
                turn_chunk(nc, xc[:, b, :, :], pst[b], TS, ident).then_inc(turned, 1)

            def states(t, b):
                pe.wait_ge(weighted, t + 3)
                pe.wait_ge(ahead_s, t + 1)
                chunk_states(nc, rows[:, b, :, :], xw[:, b, :, :], pss).then_inc(made, 1)

            ahead(pe, NCH, turn, states)

        @block.scalar
        def _(act):
            act.sem_inc(kept, 2)
            with act.Fori(0, NCH // 2) as i:
                for b in range(2):
                    t = 2 * i + b
                    act.wait_ge(turned, t + 3)
                    act.wait_ge(made, t + 1)
                    nc.scalar.activation(rows[:, b, :, :], pst[b][:, 0:TS, :], ACT.Copy).then_inc(kept, 1)

        @block.vector
        def _(dve):
            dve.sem_inc(weighted, 2)
            dve.sem_inc(ahead_s, 1)
            dve.wait_ge(start, 16)
            nc.vector.tensor_copy(h[:, 0, :, :], hb[:, :, :]).then_inc(begun, 1)
            dve.wait_ge(begun, 1)
            def weigh(t, b):
                dve.wait_ge(kept, t + 3)
                nc.vector.tensor_tensor(xw[:, b, :, :], rows[:, b, 0:XR, :].rearrange("p k (h d) -> p (k h) d", d=HD),
                                        over(dc[:, b, 128 + 32:128 + 32 + HEADS, None], (P, HEADS, HD)), ALU.mult)\
                  .then_inc(weighted, 1)

            def advance(t, b, c):
                dve.wait_ge(free, t + 1)
                nc.vector.tensor_tensor(h[:, 1 - b, :, :], h[:, b, :, :],
                                        over(dec[:, bass.ds(c, 1), HEADS:2 * HEADS].rearrange("p c h -> p (c h)")[:, :, None],
                                             (P, HEADS, HD)), ALU.mult).then_inc(decayed, 1)
                dve.wait_ge(decayed, t + 1)
                dve.wait_ge(made, t + 3)
                nc.vector.tensor_tensor(states_view(h[:, 1 - b, :, :]), states_view(h[:, 1 - b, :, :]),
                                        pss[:, :, 0:2 * HR * HD], ALU.add).then_inc(ahead_s, 1)
                dve.wait_ge(ahead_s, t + 2)

            weigh(0, 0)
            chunk = dve.alloc_register("back_dve")
            dve.reg_mov(chunk, NCH + 1)
            with dve.Fori(0, NCH // 2 - 1) as i:
                dve.reg_sub(chunk, chunk, 2)
                last = dve.snap(chunk, min_val=1, max_val=NCH - 1)
                for b in range(2):
                    weigh(2 * i + b + 1, 1 - b)
                    advance(2 * i + b, b, last - b)
            weigh(NCH - 1, 1)
            for b in range(2):
                advance(NCH - 2 + b, b, 1 - b)

        @block.gpsimd
        def _(pool):
            pool.sem_inc(free, 1)
            pool.wait_ge(begun, 1)
            chunk = pool.alloc_register("back_pool")
            pool.reg_mov(chunk, NCH + 1)
            with pool.Fori(0, NCH // 2) as i:
                pool.reg_sub(chunk, chunk, 2)
                last = pool.snap(chunk, min_val=1, max_val=NCH - 1)
                for b in range(2):
                    t = 2 * i + b
                    pool.wait_ge(ahead_s, t + 1)
                    pool.dma_start(hb_in[bass.ds(last - b, 1), :, :].rearrange("c p x -> p (c x)"),
                                   h[:, b, :, :].rearrange("p h d -> p (h d)")).then_inc(stored, 16)
                    pool.wait_ge(stored, 16 * t + 16)
                    pool.sem_inc(free, 1)


def ssd_outputs(nc, xbc, silu_z, decay_rows, totals, decay_cols, d_skip, hf, hb_in, y_t, ident, ones):
    XR = SW // P
    TS = XR + SG
    H2 = 2 * HEADS
    IN = 4
    with Mem(nc, "so") as m:
        xc = m.sb("xc", P, IN, XT_, P)
        dc = m.sb("dc", P, IN, 3 * 64)
        decay = m.sb("decay", P, 2, H2, P)
        z = m.sb("z", P, IN, XR, P)
        hb = m.sb("hb", P, IN, HEADS, HD)
        h = m.sb("h", P, 2, HEADS, HD)
        dec = m.sb("dec", P, LT // P, H2)
        skip = m.sb("skip", P, XR)
        mask = m.sb("mask", P, 2, P)
        seg = m.sb("seg", P, 2, H2, P)
        cs = m.sb("cs", P, 2, H2, P)
        sm = m.sb("sm", P, 2, 2, SG, P)
        rows = m.sb("rows", P, 2, TS, P)
        xw = m.sb("xw", P, 2, HEADS, HD)
        xd = m.sb("xd", P, 2, 2, HEADS, HD)
        y = m.sb("y", P, 2, XR, P)
        pst = m.ps("pst", P, 12, P)
        psc = m.ps("psc", P, SG, P)
        psy = m.ps("psy", P, 8, P)
        pss = m.ps("pss", P, 2, NB)
        start, masks, begun = m.sem("start"), m.sem("masks"), m.sem("begun")
        loaded = [m.sem(f"loaded{i}") for i in range(IN)]
        decay_in = [m.sem(f"decay_in{i}") for i in range(2)]
        stored = [m.sem(f"stored{i}") for i in range(2)]
        (turned, scored, made_s, made_y, kept, seg_exp, grown, seg_max, weighted, masked, cs_f, cs_b, mix_f, mix_b,
         skipped, gated, decayed, ahead) = (m.sem(n) for n in (
            "turned", "scored", "made_s", "made_y", "kept", "seg_exp", "grown", "seg_max", "weighted", "masked", "cs_f",
            "cs_b", "mix_f", "mix_b", "skipped", "gated", "decayed", "ahead"))
        x_dt, seg_f, first_y, first_skipped = (m.sem(n) for n in ("x_dt", "seg_f", "first_y", "first_skipped"))
        BANK = 4
        block = m.block()
        A, DT, W = 64, 0, 128
        heads = [(x, hh, x * HEADS + hh) for x in range(2) for hh in range(HEADS)]
        by_group = "p (g r) q -> p g r q"

        def chunks(eng, prepare, finish):
            prepare(0, 0, 0)
            with eng.Fori(0, NCH // IN - 1) as i:
                for s in range(IN):
                    prepare(IN * i + s + 1, (s + 1) % IN, i + (s + 1) // IN)
                    finish(IN * i + s, s, i)
            for s in range(IN):
                if s + 1 < IN:
                    prepare(NCH - IN + s + 1, s + 1, NCH // IN - 1)
                finish(NCH - IN + s, s, NCH // IN - 1)

        def load_decay(eng, c, b):
            eng.dma_start(decay[:, b, :, :].rearrange("p h l -> p (h l)"),
                          decay_rows[bass.ds(c, 1), :, :].rearrange("c h l -> (c h l)").partition_broadcast(P))\
               .then_inc(decay_in[b], 16)

        def load(sp, c, s):
            at = bass.ds(c * P, P)
            one = bass.ds(c, 1)
            sp.dma_start(xc[:, s, :, :], xbc[:, :, at].rearrange("k p l -> p k l")).then_inc(loaded[s], 16)
            sp.dma_start(dc[:, s, :], decay_cols[one, :, :].rearrange("c p x -> p (c x)")).then_inc(loaded[s], 16)
            sp.dma_start(z[:, s, :, :], silu_z[:, :, at].rearrange("k p l -> p k l")).then_inc(loaded[s], 16)
            sp.dma_start(hb[:, s, :, :].rearrange("p h d -> p (h d)"), hb_in[one, :, :].rearrange("c p x -> p (c x)"))\
              .then_inc(loaded[s], 16)

        def store(sp, c, b):
            sp.dma_start(y_t[FW // P:, :, bass.ds(c * P, P)].rearrange("k p l -> p k l"), y[:, b, :, :]).then_inc(stored[b], 16)

        @block.sync
        def _(sp):
            sp.dma_start(dec[:, :, :].rearrange("p c h -> p (c h)"), every_partition(totals.rearrange("c h -> (c h)")))\
              .then_inc(start, 16)
            for g in range(2):
                sp.dma_start(skip[HD * g:HD * g + HD, :], d_skip[g::2].partition_broadcast(HD),
                             allow_slow_non_contiguous=True).then_inc(start, 16)
            for s in range(IN):
                load(sp, s, s)
            with sp.Fori(0, NCH // IN - 1) as i:
                for s in range(IN):
                    sp.wait_ge(gated, IN * i + s + 1)
                    store(sp, IN * i + s, s % 2)
                    load(sp, IN * i + s + IN, s)
            for s in range(IN):
                sp.wait_ge(gated, NCH - IN + s + 1)
                store(sp, NCH - IN + s, s % 2)
            for b in range(2):
                sp.wait_ge(stored[b], 16 * (NCH // 2) + 16)

        @block.tensor
        def _(pe):
            def prepare(c, s, i):
                b = s % 2
                pe.wait_ge(loaded[s], 64 * i + 64)
                pe.wait_ge(kept, c + 1)
                turn_chunk(nc, xc[:, s, :, :], pst, TS, ident).then_inc(turned, 1)
                pe.wait_ge(masked, c + 1)
                for g in range(SG):
                    mm = nc.tensor.matmul(psc[:, g, :], xc[:, s, XR + g, :], xc[:, s, TS + g, :], start=True, stop=True)
                mm.then_inc(scored, 1)

            def finish(c, s, i):
                b = s % 2
                pe.wait_ge(weighted, c + 1)
                pe.wait_ge(ahead, c + 1)
                chunk_states(nc, rows[:, b, :, :], xw[:, b, :, :], pss).then_inc(made_s, 1)
                pe.wait_ge(first_skipped, c + 1)
                pe.wait_ge(cs_f, c + 1)
                pe.wait_ge(mix_f, c + 1)
                pe.wait_ge(cs_b, c + 1)
                pe.wait_ge(mix_b, c + 1)
                pe.wait_ge(x_dt, 2 * c + 2)
                for hh in range(HEADS):
                    if hh == 2 * BANK:
                        pe.wait_ge(skipped, c + 1)
                    to = psy[HD * (hh % 2):HD * (hh % 2) + HD, hh // 2, :]
                    nc.tensor.matmul(to, xd[:, b, 0, hh, :], seg[:, b, hh, :], start=True, stop=False)
                    nc.tensor.matmul(to, h[:, b, hh, :], cs[:, b, hh, :], start=False, stop=False)
                    nc.tensor.matmul(to, xd[:, b, 1, hh, :], seg[:, b, HEADS + hh, :], start=False, stop=False)
                    mm = nc.tensor.matmul(to, hb[:, s, hh, :], cs[:, b, HEADS + hh, :], start=False, stop=True)
                    if hh == 2 * BANK - 1:
                        mm.then_inc(first_y, 1)
                mm.then_inc(made_y, 1)

            chunks(pe, prepare, finish)

        @block.scalar
        def _(act):
            nc.scalar.preload_act_table(ACT.Exp)
            act.sem_inc(kept, 1)
            for b in range(2):
                load_decay(act, b, b)

            def prepare(c, s, i):
                b = s % 2
                act.wait_ge(loaded[s], 64 * i + 64)
                act.wait_ge(decay_in[b], IN // 2 * 16 * i + 16 * (s // 2) + 16)
                act.wait_ge(made_y, c + 1)
                nc.scalar.activation(cs[:, b, :, :], decay[:, b, :, :], ACT.Exp).then_inc(grown, 1)
                for x, hh, n in heads[HEADS:]:
                    last = nc.scalar.activation(seg[:, b, n, :], decay[:, b, n, :], ACT.Relu, scale=-1.0,
                                                bias=dc[:, s, A + 32 * x + hh:A + 32 * x + hh + 1])
                last.then_inc(seg_max, 1)
                act.wait_ge(seg_f, c + 1)
                nc.scalar.activation(seg[:, b, 0:HEADS, :], seg[:, b, 0:HEADS, :], ACT.Relu).then_inc(seg_max, 1)
                act.wait_ge(turned, c + 1)
                nc.scalar.activation(rows[:, b, :, :], pst[:, 0:TS, :], ACT.Copy).then_inc(kept, 1)
                act.wait_ge(seg_max, 2 * c + 2)
                if not (isinstance(c, int) and c >= NCH - 2):
                    act.wait_ge(grown, c + 1)
                    load_decay(act, c + 2, b)
                nc.scalar.activation(seg[:, b, :, :], seg[:, b, :, :], ACT.Exp, scale=-1.0).then_inc(seg_exp, 1)

            chunks(act, prepare, lambda c, s, i: None)

        @block.vector
        def _(dve):
            dve.wait_ge(start, 48)
            dve.sem_inc(masked, 1)
            dve.sem_inc(ahead, 1)
            dve.sem_inc(skipped, 1)
            dve.sem_inc(first_skipped, 1)
            for b in range(2):
                dve.sem_inc(stored[b], 16)
            dve.sem_inc(made_y, 2)
            nc.vector.tensor_copy(h[:, 0, :, :], hf[:, :, :]).then_inc(begun, 1)
            dve.wait_ge(begun, 1)
            dve.wait_ge(masks, 4)

            def prepare(c, s, i):
                b = s % 2
                dve.wait_ge(made_y, c + 1)
                dve.wait_ge(loaded[s], 64 * i + 64)
                dve.wait_ge(decay_in[b], IN // 2 * 16 * i + 16 * (s // 2) + 16)
                nc.vector.tensor_tensor(seg[:, b, 0:HEADS, :], over(dc[:, s, A:A + HEADS, None], (P, HEADS, P)),
                                        decay[:, b, 0:HEADS, :], ALU.subtract).then_inc(seg_f, 1)
                dve.wait_ge(grown, c + 1)
                dve.wait_ge(scored, c + 1)
                for x in range(2):
                    last = nc.vector.tensor_tensor(sm[:, b, x, :, :], psc[:, :, :], over(mask[:, x, None, :], (P, SG, P)), ALU.mult)
                last.then_inc(masked, 1)
                half = cs[:, b, 0:HEADS, :].rearrange(by_group, r=HR)
                nc.vector.tensor_tensor(half, half, over(xc[:, s, TS:, None, :], (P, SG, HR, P)), ALU.mult).then_inc(cs_f, 1)
                dve.wait_ge(kept, c + 2)
                nc.vector.tensor_tensor(xd[:, b, 0, :, :], rows[:, b, 0:XR, :].rearrange("p k (h d) -> p (k h) d", d=HD),
                                        over(dc[:, s, DT:DT + HEADS, None], (P, HEADS, HD)), ALU.mult).then_inc(x_dt, 1)
                dve.wait_ge(masked, c + 2)
                dve.wait_ge(seg_exp, c + 1)
                half = seg[:, b, 0:HEADS, :].rearrange(by_group, r=HR)
                nc.vector.tensor_tensor(half, half, over(sm[:, b, 0, :, None, :], (P, SG, HR, P)), ALU.mult).then_inc(mix_f, 1)

            def finish(c, s, i):
                b = s % 2
                dve.wait_ge(made_y, c + 2)
                nc.vector.tensor_tensor(h[:, 1 - b, :, :], h[:, b, :, :],
                                        over(dec[:, bass.ds(c, 1), 0:HEADS].rearrange("p c h -> p (c h)")[:, :, None],
                                             (P, HEADS, HD)), ALU.mult).then_inc(decayed, 1)
                dve.wait_ge(decayed, c + 1)
                dve.wait_ge(made_s, c + 1)
                nc.vector.tensor_tensor(states_view(h[:, 1 - b, :, :]), states_view(h[:, 1 - b, :, :]),
                                        pss[:, :, 0:2 * HR * HD], ALU.add).then_inc(ahead, 1)
                dve.wait_ge(stored[b], IN // 2 * 16 * i + 16 * (s // 2) + 16)
                dve.wait_ge(first_y, c + 1)
                for k in range(XR):
                    if k == BANK:
                        last.then_inc(first_skipped, 1)
                        dve.wait_ge(made_y, c + 3)
                    last = nc.vector.scalar_tensor_tensor(out=y[:, b, k, :], in0=xc[:, s, k, :], scalar=skip[:, k:k + 1],
                                                          in1=psy[:, k, :], op0=ALU.mult, op1=ALU.add)
                last.then_inc(skipped, 1)
                dve.wait_ge(first_skipped, c + 2)
                dve.wait_ge(skipped, c + 2)
                nc.vector.tensor_tensor(y[:, b, :, :], y[:, b, :, :], z[:, s, :, :], ALU.mult).then_inc(gated, 1)

            chunks(dve, prepare, finish)

        @block.gpsimd
        def _(pool):
            nc.gpsimd.memset(mask[:, :, :], 1.0).then_inc(masks, 1)
            pool.wait_ge(masks, 1)
            for x, sign in ((0, 1), (1, -1)):
                nc.gpsimd.affine_select(out=mask[:, x, :], in_=mask[:, x, :], compare_op=ALU.is_ge, fill=0.0, base=0,
                                        pattern=[[sign, P]], channel_multiplier=-sign).then_inc(masks, 1)
            pool.sem_inc(masks, 1)
            pool.wait_ge(masks, 4)

            def prepare(c, s, i):
                b = s % 2
                pool.wait_ge(grown, c + 1)
                half = cs[:, b, HEADS:, :].rearrange(by_group, r=HR)
                nc.gpsimd.tensor_tensor(half, half, over(xc[:, s, TS:, None, :], (P, SG, HR, P)), ALU.mult).then_inc(cs_b, 1)
                pool.wait_ge(kept, c + 2)
                nc.gpsimd.tensor_tensor(xw[:, b, :, :], rows[:, b, 0:XR, :].rearrange("p k (h d) -> p (k h) d", d=HD),
                                        over(dc[:, s, W:W + HEADS, None], (P, HEADS, HD)), ALU.mult).then_inc(weighted, 1)
                nc.gpsimd.tensor_tensor(xd[:, b, 1, :, :], rows[:, b, 0:XR, :].rearrange("p k (h d) -> p (k h) d", d=HD),
                                        over(dc[:, s, DT + 32:DT + 32 + HEADS, None], (P, HEADS, HD)), ALU.mult).then_inc(x_dt, 1)
                pool.wait_ge(masked, c + 2)
                pool.wait_ge(seg_exp, c + 1)
                half = seg[:, b, HEADS:, :].rearrange(by_group, r=HR)
                nc.gpsimd.tensor_tensor(half, half, over(sm[:, b, 1, :, None, :], (P, SG, HR, P)), ALU.mult).then_inc(mix_b, 1)

            chunks(pool, prepare, lambda c, s, i: None)


def fourier_tables():
    B, A8 = L // P, 8
    kb = np.outer(np.arange(B), np.arange(B)) * (2 * np.pi / B)
    eye = np.eye(A8)
    over_b = np.stack([np.kron(np.cos(kb), eye), -np.kron(np.sin(kb), eye)], 1)
    kc = np.outer(np.arange(FG), np.arange(FG)) * (2 * np.pi / FG)
    two = np.eye(P // FG)
    c, s = np.kron(two, np.cos(kc)), np.kron(two, np.sin(kc))
    over_c = np.stack([np.concatenate([c, -s], 1), np.concatenate([s, c], 1)], 1)
    k = (B * np.arange(P)[None, :] + np.arange(B)[:, None]).reshape(-1)
    ka = (np.arange(P)[:, None] * k[None, :] % L) * (2 * np.pi / L)
    over_a = np.stack([np.cos(ka), np.sin(ka)], 1)
    return [np.ascontiguousarray(t, np.float32) for t in (over_b, over_c, over_a)]


def fourier_over_b(nc, h_hi, h_lo, w_u, over_b, g_out):
    B, A8 = L // P, 8
    NA = P // A8
    FT2 = FW // P
    with Mem(nc, "fb") as m:
        w = m.sb("w", P, KD, FW)
        w_hi, w_lo = m.sb_r("w_hi", P, KD, FW), m.sb_r("w_lo", P, KD, FW)
        tb = m.sb("tb", P, 2 * P)
        s_hi, s_lo = m.sb_r("s_hi", P, 2, KD, P), m.sb_r("s_lo", P, 2, KD, P)
        u = m.sb("u", P, 2, FW)
        g = m.sb("g", P, 2, FT2, 2 * P)
        psu = [m.ps(f"psu{i}", P, FW) for i in range(2)]
        psg = [m.ps(f"psg{i}", P, FT2, 2 * P) for i in range(2)]
        w_in, tb_in, w_split, cut, cut_lo, proj, kept_u, made_g, kept_g, stored, free = (m.sem(n) for n in (
            "w_in", "tb_in", "w_split", "cut", "cut_lo", "proj", "kept_u", "made_g", "kept_g", "stored", "free"))
        block = m.block()

        def slab_of(h, t):
            return h[:, :, 0:L].rearrange("p k (b a) -> p k b a", b=B)[:, :, :, bass.ds(t * A8, A8)]

        @block.sync
        def _(sp):
            sp.dma_start(w[:, :, :], w_u.rearrange("(k p) c -> p k c", p=P)).then_inc(w_in, 16)
            sp.dma_start(tb[:, :], over_b.rearrange("p r c -> p (r c)")).then_inc(tb_in, 16)

        @block.scalar
        def _(act):
            act.sem_inc(cut, 2)
            act.wait_ge(w_in, 16)
            nc.scalar.activation(w_hi[:, :, :], w[:, :, :], ACT.Copy).then_inc(w_split, 1)
            with act.Fori(0, NA // 2) as i:
                for b in range(2):
                    t = 2 * i + b
                    act.wait_ge(proj, t + 1)
                    nc.scalar.activation(s_hi[:, b, :, :].rearrange("p k (b a) -> p k b a", b=B), slab_of(h_hi, t), ACT.Copy)\
                      .then_inc(cut, 1)

        @block.vector
        def _(dve):
            dve.sem_inc(kept_u, 2)
            dve.sem_inc(kept_g, 2)
            dve.wait_ge(w_split, 1)
            minus_hi(nc, w_lo[:, :, :], w[:, :, :], w_hi[:, :, :]).then_inc(w_split, 1)

            def cut_low(t, b):
                dve.wait_ge(proj, t + 1)
                nc.vector.tensor_copy(s_lo[:, b, :, :].rearrange("p k (b a) -> p k b a", b=B), slab_of(h_lo, t)).then_inc(cut_lo, 1)

            def keep_u(t, b):
                dve.wait_ge(proj, t + 3)
                nc.vector.tensor_copy(u[:, b, :], psu[b][:, :]).then_inc(kept_u, 1)

            def keep_g(t, b):
                dve.wait_ge(made_g, t + 3)
                dve.wait_ge(free, t + 1)
                nc.vector.tensor_copy(g[:, b, :, :], psg[b][:, :, :]).then_inc(kept_g, 1)

            cut_low(0, 0)
            cut_low(1, 1)
            with dve.Fori(0, NA // 2 - 1) as i:
                for b in range(2):
                    keep_u(2 * i + b, b)
                    cut_low(2 * i + b + 2, b)
                    keep_g(2 * i + b, b)
            for b in range(2):
                keep_u(NA - 2 + b, b)
                keep_g(NA - 2 + b, b)

        @block.gpsimd
        def _(pool):
            pool.sem_inc(free, 2)
            with pool.Fori(0, NA // 2) as i:
                for b in range(2):
                    t = 2 * i + b
                    pool.wait_ge(kept_g, t + 3)
                    pool.dma_start(g_out[bass.ds(t, 1), :, :].rearrange("t p x -> p (t x)"),
                                   g[:, b, :, :].rearrange("p a b -> p (a b)")).then_inc(stored, 16)
                    pool.wait_ge(stored, 16 * t + 16)
                    pool.sem_inc(free, 1)

        @block.tensor
        def _(pe):
            pe.sem_inc(proj, 2)
            pe.sem_inc(made_g, 2)
            pe.wait_ge(tb_in, 16)
            pe.wait_ge(w_split, 2)

            def prepare(t, b):
                pe.wait_ge(cut, t + 3)
                pe.wait_ge(cut_lo, t + 1)
                pe.wait_ge(kept_u, t + 1)
                for k in range(KD):
                    mm = three_products(nc, psu[b][:, :], (s_hi[:, b, k, :], s_lo[:, b, k, :]), (w_hi[:, k, :], w_lo[:, k, :]),
                                        k == 0, k == KD - 1)
                mm.then_inc(proj, 1)

            def finish(t, b):
                pe.wait_ge(kept_u, t + 3)
                pe.wait_ge(kept_g, t + 1)
                for x in range(FT2):
                    mm = nc.tensor.matmul(psg[b][:, x, :], u[:, b, x * P:(x + 1) * P], tb[:, :], start=True, stop=True)
                mm.then_inc(made_g, 1)

            ahead(pe, NA, prepare, finish)


def fourier_rest(nc, m, block, g_in, over_c, over_a, y_t):
    B, A8 = L // P, 8
    NA = P // A8
    FT2 = FW // P
    SCALE = 1.0 / math.sqrt(L * FG)
    tc = m.sb("tc", P, 2, 2 * P)
    ta = m.sb("ta", P, 2, L)
    g = m.sb("g", P, NA, FT2 * 2, B, A8)
    gs = m.sb("gs", P, 2, FT2 * 2, P)
    hs = m.sb("hs", P, 2, FT2, 2, P)
    y = m.sb("y", P, FT2, L)
    psh = [m.ps(f"psh{i}", P, FT2, 2 * P) for i in range(2)]
    psy = [m.ps(f"psy{i}", P, FT2, P) for i in range(2)]
    (loaded, g_loaded, cut_g, made_h, kept_h, made_y, kept_y, stored) = (m.sem(n) for n in (
        "loaded", "g_loaded", "cut_g", "made_h", "kept_h", "made_y", "kept_y", "stored"))

    @block.sync
    def _(sp):
        for t in range(0, NA, 4):
            sp.dma_start(g[:, t:t + 4, :, :, :].rearrange("p t x k a -> p t (x k a)"), g_in[t:t + 4, :, :].rearrange("t p x -> p t x"))\
              .then_inc(g_loaded, 16)
        sp.dma_start(tc[:, :, :], over_c).then_inc(loaded, 16)
        sp.dma_start(ta[:, :, :], over_a).then_inc(loaded, 16)
        sp.wait_ge(kept_y, B + 2)
        for k in range(FT2):
            sp.dma_start(y_t[k, :, :], y[:, k, :]).then_inc(stored, 16)
        sp.wait_ge(stored, 16 * FT2)

    @block.scalar
    def _(act):
        act.wait_ge(g_loaded, NA // 4 * 16)
        with act.Fori(0, B // 2) as i:
            for b in range(2):
                t = 2 * i + b
                act.wait_ge(made_h, t + 1)
                nc.scalar.activation(gs[:, b, :, :].rearrange("p x (t a) -> p x t a", a=A8),
                                     g[:, :, :, bass.ds(t, 1), :].rearrange("p t x k a -> p x t (k a)"), ACT.Copy).then_inc(cut_g, 1)

    @block.vector
    def _(dve):
        dve.sem_inc(kept_h, 2)
        dve.sem_inc(kept_y, 2)
        dve.sem_inc(made_y, 1)

        def prepare(t, b):
            dve.wait_ge(made_h, t + 3)
            nc.vector.tensor_copy(hs[:, b, :, :, :].rearrange("p t r c -> p t (r c)"), psh[b][:, :, :]).then_inc(kept_h, 1)

        def finish(t, b):
            dve.wait_ge(made_y, t + 2)
            to = y[:, :, :].rearrange("p t (k1 k2) -> p t k1 k2", k2=B)[:, :, :, bass.ds(t, 1)].rearrange("p t a b -> p t (a b)")
            nc.vector.tensor_scalar(to, psy[b][:, :, :], SCALE, None, ALU.mult).then_inc(kept_y, 1)

        ahead(dve, B, prepare, finish)

    @block.tensor
    def _(pe):
        pe.sem_inc(made_h, 2)
        pe.wait_ge(loaded, 32)

        def prepare(t, b):
            pe.wait_ge(cut_g, t + 1)
            pe.wait_ge(kept_h, t + 1)
            for x in range(FT2):
                for ri in range(2):
                    mm = nc.tensor.matmul(psh[b][:, x, :], gs[:, b, 2 * x + ri, :], tc[:, ri, :], start=(ri == 0), stop=(ri == 1))
            mm.then_inc(made_h, 1)

        def finish(t, b):
            pe.wait_ge(kept_h, t + 3)
            pe.wait_ge(kept_y, t + 1)
            for x in range(FT2):
                for ri in range(2):
                    mm = nc.tensor.matmul(psy[b][:, x, :], hs[:, b, x, ri, :], ta[:, ri, bass.ds(t * P, P)],
                                          start=(ri == 0), stop=(ri == 1))
            mm.then_inc(made_y, 1)

        ahead(pe, B, prepare, finish)


def output_rows_2(nc, y_t, w_out, g_ssd, g_post, gate, x2, x3, ones):
    KF = FW // P
    KS = SW // P
    with Mem(nc, "or2") as m:
        w = m.sb("w", P, WR, D)
        w_hi, w_lo = m.sb_r("w_hi", P, KD, D), m.sb_r("w_lo", P, KD, D)
        gs = m.sb("gs", P, KS)
        gg = m.sb("gg", P, 2, D)
        y = m.sb("y", P, 2, KD, P)
        y_hi, y_lo = m.sb_r("y_hi", P, 2, KD, P), m.sb_r("y_lo", P, 2, KD, P)
        sq = m.sb("sq", P, 2, KS, P)
        ry = m.sb("ry", P, 2, 2, P)
        xr = m.sb("xr", P, 2, D)
        o = m.sb("o", P, 2, D)
        junk = m.sb("junk", P, D)
        stat = m.sb("stat", P, 2, 4)
        eps = m.sb("eps", P, 1)
        ps = [m.ps(f"ps{i}", P, D) for i in range(2)]
        psq = [m.ps(f"psq{i}", P, P) for i in range(2)]
        vec_in, eps_set, scaled_w = m.sem("vec_in"), m.sem("eps_set"), m.sem("scaled_w")
        w_in = [m.sem(f"w_in{i}") for i in range(WR)]
        y_in = [m.sem(f"y_in{i}") for i in range(2)]
        x_in = [m.sem(f"x_in{i}") for i in range(2)]
        (w_his, w_los, squared_y, summed, root_y, inv_y, scaled_y, y_his, y_los, proj, squared, rooted, inv, normed, added,
         stored, free) = (m.sem(n) for n in (
            "w_his", "w_los", "squared_y", "summed", "root_y", "inv_y", "scaled_y", "y_his", "y_los", "proj", "squared",
            "rooted", "inv", "normed", "added", "stored", "free"))
        block = m.block()
        rows_in = x2.rearrange("(t p) d -> t p d", p=P)
        rows_out = x3.rearrange("(t p) d -> t p d", p=P)

        @block.sync
        def _(sp):
            def load(t, b):
                sp.wait_ge(y_los, t + 1)
                sp.dma_start(y[:, b, :, :], y_t[:, :, bass.ds(t * P, P)].rearrange("k p l -> p k l")).then_inc(y_in[b], 16)

            def load_rows(t, b):
                sp.wait_ge(added, t + 1)
                sp.dma_start(xr[:, b, :], rows_in[bass.ds(t, 1), :, :].rearrange("t p d -> p (t d)")).then_inc(x_in[b], 16)

            sp.dma_start(gs[:, :], columns(g_ssd, KS), allow_slow_non_contiguous=True).then_inc(vec_in, 16)
            load(0, 0)
            load(1, 1)
            for k in range(KD):
                if k >= WR:
                    sp.wait_ge(w_los, k - WR + 1)
                sp.dma_start(w[:, k % WR, :], w_out[k * P:(k + 1) * P, :]).then_inc(w_in[k % WR], 16)
            load_rows(0, 0)
            sp.dma_start(gg[:, 0, :], every_partition(g_post)).then_inc(vec_in, 16)
            sp.dma_start(gg[:, 1, :], every_partition(gate)).then_inc(vec_in, 16)
            with sp.Fori(0, TILES // 2 - 1) as i:
                for b in range(2):
                    load(2 * i + b + 2, b)
                    load_rows(2 * i + b + 1, 1 - b)
            load_rows(TILES - 1, 1)

        @block.tensor
        def _(pe):
            pe.sem_inc(proj, 2)

            def first(t, b):
                pe.wait_ge(squared_y, t + 1)
                pe.wait_ge(inv_y, t + 1)
                for k in range(KS):
                    mm = nc.tensor.matmul(psq[b][:, :], ones[:, :], sq[:, b, k, :], start=(k == 0), stop=(k == KS - 1))
                mm.then_inc(summed, 1)

            def finish(t, b):
                pe.wait_ge(y_los, t + 3)
                pe.wait_ge(normed, t + 1)
                for k in range(KD):
                    pe.wait_ge(w_los, k + 1)
                    for n in range(2):
                        cols = slice(n * NB, (n + 1) * NB)
                        mm = three_products(nc, ps[b][:, cols], (y_hi[:, b, k, :], y_lo[:, b, k, :]),
                                            (w_hi[:, k, cols], w_lo[:, k, cols]), k == 0, k == KD - 1)
                mm.then_inc(proj, 1)

            two_ahead(pe, TILES, first, nothing, finish, finish_first=True)

        @block.scalar
        def _(act):
            act.wait_ge(eps_set, 1)
            nc.scalar.preload_act_table(ACT.Sqrt)

            def first(t, b):
                act.wait_ge(y_in[b], 8 * (t - b) + 16)
                act.wait_ge(summed, t + 1)
                nc.scalar.activation(sq[:, b, :, :], y[:, b, KF:, :], ACT.Square).then_inc(squared_y, 1)

            def second(t, b):
                act.wait_ge(summed, t + 3)
                nc.scalar.activation(ry[:, b, 0, :], psq[b][:, :], ACT.Sqrt, scale=1.0 / SW, bias=eps[:, :]).then_inc(root_y, 1)
                act.wait_ge(proj, t + 1)
                act.wait_ge(scaled_y, t + 1)
                nc.scalar.activation(y_hi[:, b, :, :], y[:, b, :, :], ACT.Copy).then_inc(y_his, 1)

            def finish(t, b):
                act.wait_ge(proj, t + 3)
                nc.scalar.activation(junk[:, :], ps[b][:, :], ACT.Square, accum_out=stat[:, b, 0:1]).then_inc(squared, 1)
                act.wait_ge(squared, t + 1)
                nc.scalar.activation(stat[:, b, 1:2], stat[:, b, 0:1], ACT.Sqrt, scale=1.0 / D, bias=eps[:, :]).then_inc(rooted, 1)

            def weights():
                for k in range(KD):
                    if k >= KF:
                        act.wait_ge(scaled_w, k - KF + 1)
                    else:
                        act.wait_ge(w_in[k % WR], 16 * (k // WR) + 16)
                    nc.scalar.activation(w_hi[:, k, :], w[:, k % WR, :], ACT.Copy).then_inc(w_his, 1)

            two_ahead(act, TILES, first, second, finish, once=weights)

        @block.vector
        def _(dve):
            nc.vector.memset(eps[:, :], EPS).then_inc(eps_set, 1)
            dve.sem_inc(y_los, 2)
            dve.sem_inc(added, 2)
            dve.sem_inc(summed, 2)
            dve.sem_inc(inv_y, 2)
            dve.sem_inc(normed, 2)
            def weights():
                dve.wait_ge(vec_in, 16)
                for k in range(KD):
                    if k >= KF:
                        dve.wait_ge(w_in[k % WR], 16 * (k // WR) + 16)
                        nc.vector.tensor_scalar(w[:, k % WR, :], w[:, k % WR, :], gs[:, k - KF:k - KF + 1], None, ALU.mult)\
                          .then_inc(scaled_w, 1)
                    dve.wait_ge(w_his, k + 1)
                    minus_hi(nc, w_lo[:, k, :], w[:, k % WR, :], w_hi[:, k, :]).then_inc(w_los, 1)
                dve.wait_ge(vec_in, 48)
                nc.vector.tensor_tensor(gg[:, 0, :], gg[:, 0, :], gg[:, 1, :], ALU.mult).then_inc(scaled_w, 1)
                dve.wait_ge(scaled_w, KS + 1)

            def prepare(t, b):
                dve.wait_ge(root_y, t + 1)
                nc.vector.reciprocal(ry[:, b, 1, :], ry[:, b, 0, :]).then_inc(inv_y, 1)
                dve.wait_ge(inv_y, t + 3)
                nc.vector.tensor_tensor(y[:, b, KF:, :], y[:, b, KF:, :], over(ry[:, b, 1:2, :], (P, KS, P)), ALU.mult)\
                  .then_inc(scaled_y, 1)
                dve.wait_ge(y_his, t + 1)
                nc.vector.tensor_tensor(y_lo[:, b, :, :], y[:, b, :, :], y_hi[:, b, :, :].bitcast(F32), ALU.subtract)\
                  .then_inc(y_los, 1)

            def finish(t, b):
                dve.wait_ge(rooted, t + 1)
                nc.vector.reciprocal(stat[:, b, 2:3], stat[:, b, 1:2]).then_inc(inv, 1)
                dve.wait_ge(inv, t + 1)
                dve.wait_ge(free, t + 1)
                nc.vector.scalar_tensor_tensor(out=o[:, b, :], in0=ps[b][:, :], scalar=stat[:, b, 2:3], in1=gg[:, 0, :],
                                               op0=ALU.mult, op1=ALU.mult).then_inc(normed, 1)
                dve.wait_ge(normed, t + 3)
                dve.wait_ge(x_in[b], 8 * (t - b) + 16)
                nc.vector.tensor_tensor(o[:, b, :], o[:, b, :], xr[:, b, :], ALU.add).then_inc(added, 1)

            ahead(dve, TILES, prepare, finish, weights)

        @block.gpsimd
        def _(pool):
            pool.sem_inc(free, 2)
            with pool.Fori(0, TILES // 2) as i:
                for b in range(2):
                    t = 2 * i + b
                    pool.wait_ge(added, t + 3)
                    pool.dma_start(rows_out[bass.ds(t, 1), :, :].rearrange("t p d -> p (t d)"), o[:, b, :]).then_inc(stored, 16)
                    pool.wait_ge(stored, 16 * t + 16)
                    pool.sem_inc(free, 1)


def feed_forward(nc, x3, g_pre, shift, scale, w_gate, w_up, w_down, g_post, gate, out, ident):
    RT = NB // P
    DH = D // 2
    NF = 2 * FT
    PIECES = 4
    with Mem(nc, "ff") as m:
        hraw = m.sb("hraw", P, KD, P)
        hb_lo, hb_hi = m.sb_r("hb_lo", P, KD, NB), m.sb_r("hb_hi", P, KD, NB)
        wg = m.sb("wg", P, 2, KD, P)
        wg_lo, wg_hi = m.sb_r("wg_lo", P, 2, 2, KD, P), m.sb_r("wg_hi", P, 2, 2, KD, P)
        wd = m.sb("wd", P, PIECES, DH)
        wd_lo, wd_hi = m.sb_r("wd_lo", P, PIECES, DH), m.sb_r("wd_hi", P, PIECES, DH)
        a_lo = m.sb_r("a_lo", P, PIECES, NB)
        a_hi = m.sb_r("a_hi", P, PIECES, NB)
        act_t = m.sb("act", P, FT, NB)
        sg = m.sb("sg", P, 2, NB)
        gg = m.sb("gg", P, D)
        xt = m.sb("xt", P, 2, D)
        xr = m.sb("xr", P, 2, D)
        h = m.sb("h", P, RT, D)
        ncol = m.sb("ncol", P, 3, KD)
        nstat = m.sb("nstat", P, 2, 4)
        stat = m.sb("stat", P, RT, 5)
        eps = m.sb("eps", P, 1)
        psg = [m.ps(f"psg{i}", P, 2, NB) for i in range(2)]
        psd = [m.ps(f"psd{i}", P, NB) for i in range(RT)]
        start, ready = m.sem("start"), m.sem("ready")
        loaded = [m.sem(f"loaded{i}") for i in range(2)]
        d_in = [m.sem(f"d_in{i}") for i in range(PIECES)]
        xt_in = [m.sem(f"xt_in{i}") for i in range(2)]
        (w_hi, w_lo, proj, gated, made, p_hi, p_lo, used, kept, squared, summed, rooted, inv, normed, added, stored) = (
            m.sem(n) for n in ("w_hi", "w_lo", "proj", "gated", "made", "p_hi", "p_lo", "used", "kept", "squared", "summed",
                               "rooted", "inv", "normed", "added", "stored"))
        x_in = [m.sem(f"x_in{i}") for i in range(2)]
        (n_sq, n_root, n_inv, n_scaled, n_turned, n_placed, n_shift, n_hi, n_lo) = (
            m.sem(n) for n in ("n_sq", "n_root", "n_inv", "n_scaled", "n_turned", "n_placed", "n_shift", "n_hi", "n_lo"))
        h_free, begun, begun_act = m.sem("h_free"), m.sem("begun"), m.sem("begun_act")
        block = m.block()
        gv, uv = (w.rearrange("(k p) c -> p k c", p=P) for w in (w_gate, w_up))
        dv = w_down.rearrange("(f p) d -> f p d", p=P)
        rows_in = x3.rearrange("(t p) d -> p t d", p=P)
        rows_out = out.rearrange("(t p) d -> p t d", p=P)
        LOAD_AT = (0, 0, 13, 18)
        SCALE_AT = (4, 8, 14, 20)
        TURN_AT = (8, 13, 19, 25)
        PLACE_AT = (9, 14, 20, 26)
        WEIGHTS_AT = ((21, 24), (32, 36))
        SPLIT_AT = (26, 38)
        DEPTH_ = 3

        def blocks(eng, body):
            with eng.Fori(0, LB - 1) as n:
                body(n, False)
            body(LB - 1, True)

        def piece(j):
            return j // FT, j % FT, j % PIECES

        @block.sync
        def _(sp):
            sp.dma_start(gg[:, :], every_partition(g_post)).then_inc(start, 16)
            sp.dma_start(sg[:, :, :].rearrange("p a b -> p (a b)"), every_partition(gate)).then_inc(start, 16)
            for i, v in enumerate((g_pre, shift, scale)):
                sp.dma_start(ncol[:, i, :], columns(v, KD), allow_slow_non_contiguous=True).then_inc(start, 16)

            def load_rows(n, r):
                sp.wait_ge(n_turned, n * RT + r + 1)
                sp.dma_start(xt[:, r % 2, :], rows_in[:, bass.ds(n * RT + r, 1), :].rearrange("p t d -> p (t d)"))\
                  .then_inc(xt_in[r % 2], 16)

            def load_tile(n, t, parts=(0, 1)):
                for x in parts:
                    v = (gv, uv)[x]
                    sp.wait_ge(w_lo, n * (2 * FT) + 2 * t + x + 1)
                    sp.dma_start(wg[:, x, :, :], v[:, :, bass.ds(t * P, P)]).then_inc(loaded[x], 16)

            def load_piece(n, j):
                half, f, s = piece(j)
                sp.wait_ge(p_lo, n * (2 * NF) + 2 * j + 1)
                sp.dma_start(wd[:, s, :], dv[f, :, half * DH:(half + 1) * DH]).then_inc(d_in[s], 16)

            def body(n, last):
                with sp.Fori(0, FT // 2 - 1) as i:
                    for b in range(2):
                        load_tile(n, 2 * i + b + 2)
                for j in range(NF):
                    load_piece(n, j)
                    if not last:
                        for r in range(RT):
                            if LOAD_AT[r] == j:
                                load_rows(n + 1, r)
                        for t in range(2):
                            for x in range(2):
                                if WEIGHTS_AT[t][x] == j:
                                    load_tile(n + 1, t, (x,))

            load_rows(0, 0)
            load_rows(0, 1)
            load_tile(0, 0)
            load_rows(0, 2)
            load_rows(0, 3)
            load_tile(0, 1)
            blocks(sp, body)

        @block.tensor
        def _(pe):
            pe.sem_inc(proj, 2)
            pe.sem_inc(used, 4)
            pe.sem_inc(n_turned, 2)

            def turn(n, r):
                pe.wait_ge(n_scaled, n * RT + r + 1)
                pe.wait_ge(n_placed, n * RT + r + 1)
                for k in range(KD):
                    x, c = k // 4, (k % 4) * P
                    t = nc.tensor.transpose(psg[r % 2][:, x, c:c + P], xt[:, r % 2, k * P:(k + 1) * P], ident[:, :])
                t.then_inc(n_turned, 1)

            def three(to, left, right, first, last):
                for p, (x, y) in enumerate(((0, 0), (0, 1), (1, 0))):
                    mm = nc.tensor.matmul(to, left[x], right[y], start=(first and p == 0), stop=(last and p == 2))
                return mm

            def body(n, last):
                pe.wait_ge(n_lo, (n + 1) * RT + 1)
                pe.wait_ge(n_placed, (n + 1) * RT + 2)
                pe.sem_inc(begun, 1)
                with pe.Fori(0, FT // 2) as i:
                    for b in range(2):
                        t = n * FT + 2 * i + b
                        pe.wait_ge(w_lo, n * (2 * FT) + 4 * i + 2 * b + 4)
                        pe.wait_ge(made, t + 1)
                        for x in range(2):
                            for k in range(KD):
                                mm = three(psg[b][:, x, :], (wg_hi[:, b, x, k, :], wg_lo[:, b, x, k, :]),
                                           (hb_hi[:, k, :], hb_lo[:, k, :]), k == 0, k == KD - 1)
                        mm.then_inc(proj, 1)
                for j in range(NF):
                    half, f, s = piece(j)
                    pe.wait_ge(p_lo, n * (2 * NF) + 2 * j + 2 + 2 * PIECES)
                    for r in range(RT):
                        rs = slice(r * P, (r + 1) * P)
                        if f == 0:
                            pe.wait_ge(kept, (2 * n + half) * RT + r + 1)
                        mm = three(psd[r][:, :], (a_hi[:, s, rs], a_lo[:, s, rs]),
                                   (wd_hi[:, s, :], wd_lo[:, s, :]), f == 0, f == FT - 1)
                    mm.then_inc(used, 1)
                    if not last:
                        for r in range(RT):
                            if TURN_AT[r] == j:
                                if r == 0:
                                    pe.wait_ge(made, n * FT + FT + 2)
                                turn(n + 1, r)

            for r in range(RT):
                turn(0, r)
            blocks(pe, body)

        @block.scalar
        def _(act):
            act.wait_ge(ready, 3)
            act.sem_inc(kept, RT)

            def root(n, r):
                act.wait_ge(xt_in[r % 2], n * (RT // 2 * 16) + 16 * (r // 2) + 16)
                nc.scalar.activation(sg[:, :, :].rearrange("p a b -> p (a b)"), xt[:, r % 2, :], ACT.Square, accum_out=nstat[:, r % 2, 0:1]).then_inc(n_sq, 1)
                act.wait_ge(n_sq, n * RT + r + 1)
                nc.scalar.activation(nstat[:, r % 2, 1:2], nstat[:, r % 2, 0:1], ACT.Sqrt, scale=1.0 / D, bias=eps[:, :])\
                  .then_inc(n_root, 1)

            def first_hi(r):
                act.wait_ge(n_shift, r + 1)
                nc.scalar.activation(hb_hi[:, :, r * P:(r + 1) * P], hraw[:, :, :], ACT.Copy).then_inc(n_hi, 1)

            def tile_hi(n, i, b):
                t = n * FT + 2 * i + b
                act.wait_ge(proj, t + 1)
                for x in range(2):
                    act.wait_ge(loaded[x], 16 * t + 16)
                    nc.scalar.activation(wg_hi[:, b, x, :, :], wg[:, x, :, :], ACT.Copy).then_inc(w_hi, 1)

            def piece_hi(n, j):
                half, f, s = piece(j)
                act.wait_ge(used, n * NF + j + 1)
                act.wait_ge(d_in[s], n * (NF // PIECES * 16) + 16 * (j // PIECES) + 16)
                nc.scalar.activation(wd_hi[:, s, :], wd[:, s, :], ACT.Copy).then_inc(p_hi, 1)
                nc.scalar.activation(a_hi[:, s, :], act_t[:, f, :], ACT.Copy).then_inc(p_hi, 1)

            def body(n, last):
                nc.scalar.preload_act_table(ACT.Silu)

                def silu(i, b):
                    t = n * FT + 2 * i + b
                    act.wait_ge(proj, t + 3)
                    act.wait_ge(made, t + 1)
                    nc.scalar.activation(sg[:, b, :], psg[b][:, 0, :], ACT.Silu).then_inc(gated, 1)

                with act.Fori(0, FT // 2 - 1) as i:
                    for b in range(2):
                        silu(i, b)
                        tile_hi(n, i + 1, b)
                silu(FT // 2 - 1, 0)
                act.wait_ge(made, n * FT + DEPTH_ + 2)
                act.sem_inc(begun_act, 1)
                for j in range(DEPTH_):
                    piece_hi(n, j)
                silu(FT // 2 - 1, 1)
                act.wait_ge(made, n * FT + FT + 2)
                for j in range(NF):
                    if j + DEPTH_ < NF:
                        piece_hi(n, j + DEPTH_)
                    if not last:
                        for r in range(RT):
                            if SCALE_AT[r] == j:
                                root(n + 1, r)
                        for b in range(2):
                            if SPLIT_AT[b] == j:
                                tile_hi(n + 1, 0, b)
                    if j % FT == FT - 1:
                        half = j // FT
                        act.wait_ge(used, n * NF + (half + 1) * FT + 4)
                        if half == 0:
                            act.wait_ge(h_free, n + 1)
                        cols = slice(half * DH, (half + 1) * DH)
                        for r in range(RT):
                            nc.scalar.activation(h[:, r, cols], psd[r][:, :], ACT.Copy).then_inc(kept, 1)
                        act.wait_ge(kept, (2 * n + half + 2) * RT)
                        for r in range(RT):
                            nc.scalar.activation(sg[:, 0, :], h[:, r, cols], ACT.Square, accum_out=stat[:, r, half:half + 1])\
                              .then_inc(squared, 1)
                            act.wait_ge(squared, n * (2 * RT) + half * RT + r + 1)
                act.wait_ge(summed, n + 1)
                nc.scalar.activation(stat[:, :, 3:4], stat[:, :, 2:3], ACT.Sqrt, scale=1.0 / D, bias=eps[:, :]).then_inc(rooted, 1)

            for r in range(RT):
                root(0, r)
                if r:
                    first_hi(r - 1)
            first_hi(RT - 1)
            tile_hi(0, 0, 0)
            tile_hi(0, 0, 1)
            blocks(act, body)

        @block.vector
        def _(dve):
            nc.vector.memset(eps[:, :], EPS).then_inc(ready, 1)
            dve.wait_ge(start, 80)
            nc.vector.tensor_tensor(gg[:, :], gg[:, :], sg[:, :, :].rearrange("p a b -> p (a b)"), ALU.mult).then_inc(ready, 1)
            nc.vector.scalar_tensor_tensor(out=ncol[:, 0, :], in0=ncol[:, 2, :], scalar=1.0, in1=ncol[:, 0, :],
                                           op0=ALU.add, op1=ALU.mult).then_inc(ready, 1)
            dve.wait_ge(ready, 3)
            dve.sem_inc(made, 2)
            dve.sem_inc(n_placed, 2)
            dve.sem_inc(h_free, 1)
            dve.sem_inc(n_lo, 1)
            dve.sem_inc(w_lo, 2)
            dve.sem_inc(p_lo, 2 * PIECES)

            def scaled_rows(n, r):
                dve.wait_ge(n_root, n * RT + r + 1)
                nc.vector.reciprocal(nstat[:, r % 2, 2:3], nstat[:, r % 2, 1:2]).then_inc(n_inv, 1)
                dve.wait_ge(n_inv, n * RT + r + 1)
                nc.vector.tensor_scalar(xt[:, r % 2, :], xt[:, r % 2, :], nstat[:, r % 2, 2:3], None, ALU.mult).then_inc(n_scaled, 1)

            def place(n, r):
                dve.wait_ge(n_turned, n * RT + r + 3)
                dve.wait_ge(n_lo, n * RT + r + 1)
                nc.vector.tensor_tensor(hraw[:, :, :],
                                        psg[r % 2][:, :, :].rearrange("p x (k l) -> p (x k) l", l=P),
                                        over(ncol[:, 0, :, None], (P, KD, P)), ALU.mult).then_inc(n_placed, 1)

            def tile_lo(n, t, b):
                for x in range(2):
                    dve.wait_ge(w_hi, n * (2 * FT) + 2 * t + x + 1)
                    nc.vector.tensor_tensor(wg_lo[:, b, x, :, :], wg[:, x, :, :], wg_hi[:, b, x, :, :].bitcast(F32),
                                            ALU.subtract).then_inc(w_lo, 1)

            def piece_lo(n, j):
                half, f, s = piece(j)
                dve.wait_ge(p_hi, n * (2 * NF) + 2 * j + 2)
                nc.vector.tensor_tensor(wd_lo[:, s, :], wd[:, s, :], wd_hi[:, s, :].bitcast(F32), ALU.subtract)\
                  .then_inc(p_lo, 1)
                nc.vector.tensor_tensor(a_lo[:, s, :], act_t[:, f, :], a_hi[:, s, :].bitcast(F32), ALU.subtract).then_inc(p_lo, 1)

            def body(n, last):
                def multiply(t, b):
                    dve.wait_ge(gated, n * FT + t + 1)
                    nc.vector.tensor_tensor(act_t[:, bass.ds(t, 1), :].rearrange("p f l -> p (f l)"),
                                            psg[b][:, 1, :], sg[:, b, :], ALU.mult).then_inc(made, 1)

                with dve.Fori(0, FT // 2 - 1) as i:
                    for b in range(2):
                        multiply(2 * i + b, b)
                        tile_lo(n, 2 * i + b + 2, b)
                multiply(FT - 2, 0)
                dve.wait_ge(made, n * FT + DEPTH_ + 2)
                for j in range(DEPTH_):
                    piece_lo(n, j)
                multiply(FT - 1, 1)
                dve.wait_ge(made, n * FT + FT + 2)
                for j in range(NF):
                    if j + DEPTH_ < NF:
                        piece_lo(n, j + DEPTH_)
                    if not last:
                        for r in range(RT):
                            if SCALE_AT[r] == j:
                                scaled_rows(n + 1, r)
                            if PLACE_AT[r] == j:
                                place(n + 1, r)
                        for b in range(2):
                            if SPLIT_AT[b] == j:
                                tile_lo(n + 1, b, b)
                dve.wait_ge(squared, (n + 1) * (2 * RT))
                nc.vector.tensor_tensor(stat[:, :, 2:3], stat[:, :, 0:1], stat[:, :, 1:2], ALU.add).then_inc(summed, 1)
                dve.wait_ge(rooted, n + 1)
                nc.vector.reciprocal(stat[:, :, 4:5], stat[:, :, 3:4]).then_inc(inv, 1)
                dve.wait_ge(inv, n + 1)
                for r in range(RT):
                    nc.vector.scalar_tensor_tensor(out=h[:, r, :], in0=h[:, r, :], scalar=stat[:, r, 4:5], in1=gg[:, :],
                                                   op0=ALU.mult, op1=ALU.mult).then_inc(normed, 1)

            scaled_rows(0, 0)
            for r in range(RT):
                place(0, r)
                if r + 1 < RT:
                    scaled_rows(0, r + 1)
                dve.wait_ge(n_hi, r + 1)
                minus_hi(nc, hb_lo[:, :, r * P:(r + 1) * P], hraw[:, :, :], hb_hi[:, :, r * P:(r + 1) * P]).then_inc(n_lo, 1)
            tile_lo(0, 0, 0)
            tile_lo(0, 1, 1)
            blocks(dve, body)

        @block.gpsimd
        def _(pool):
            pool.wait_ge(start, 80)

            def shifted(n, r):
                pool.wait_ge(n_placed, n * RT + r + 3)
                nc.gpsimd.tensor_tensor(hraw[:, :, :], hraw[:, :, :], over(ncol[:, 1, :, None], (P, KD, P)), ALU.add)\
                  .then_inc(n_shift, 1)

            def shift_and_split(n, r):
                cs = slice(r * P, (r + 1) * P)
                shifted(n, r)
                pool.wait_ge(n_shift, n * RT + r + 1)
                pool.sem_inc(begun, 1)
                nc.gpsimd.tensor_copy(hb_hi[:, :, cs], hraw[:, :, :]).then_inc(n_hi, 1)
                pool.wait_ge(n_hi, n * RT + r + 1)
                nc.gpsimd.tensor_tensor(hb_lo[:, :, cs], hraw[:, :, :], hb_hi[:, :, cs].bitcast(F32), ALU.subtract)\
                    .then_inc(n_lo, 1)

            def load_residual(n, r):
                pool.dma_start(xr[:, r % 2, :], rows_in[:, bass.ds(n * RT + r, 1), :].rearrange("p t d -> p (t d)"))\
                    .then_inc(x_in[r % 2], 16)

            def body(n, last):
                load_residual(n, 0)
                load_residual(n, 1)
                if not last:
                    for r in range(RT):
                        shift_and_split(n + 1, r)
                for r in range(RT):
                    t = n * RT + r
                    pool.wait_ge(x_in[r % 2], n * (RT // 2 * 16) + 16 * (r // 2) + 16)
                    pool.wait_ge(normed, t + 1)
                    pool.sem_inc(begun, 1)
                    nc.gpsimd.tensor_tensor(h[:, r, :], h[:, r, :], xr[:, r % 2, :], ALU.add).then_inc(added, 1)
                    pool.wait_ge(added, t + 1)
                    pool.sem_inc(begun, 1)
                    pool.dma_start(rows_out[:, bass.ds(t, 1), :].rearrange("p t d -> p (t d)"), h[:, r, :]).then_inc(stored, 16)
                    if r + 2 < RT:
                        load_residual(n, r + 2)
                pool.wait_ge(stored, n * (16 * RT) + 16 * RT)
                pool.sem_inc(h_free, 1)

            for r in range(RT):
                shifted(0, r)
            blocks(pool, body)


def program(nc, d):
    with Mem(nc, "all") as m:
        ident, ones = m.sb("ident", P, P), m.sb("ones", P, P)
        make_constants(nc, ident, ones)

        w_in = d["w_in"][0]
        with Mem(nc, "m1") as m1:
            with Mem(nc, "m1a") as m2:
                x_hi, x_lo = m2.sb_r("x_hi", P, KD, L), m2.sb_r("x_lo", P, KD, L)
                norm_to_columns(nc, "n1", d["x"][0], TILES, x_hi, x_lo, 0, ident, d["norm_gain"][0])
                silu_projection(nc, "z1", x_hi, x_lo, w_in[:, SSM_W:2 * SSM_W], SSM_W // P, d["s_z1"])
                s5_inputs(nc, x_hi, x_lo, w_in[:, 0:SSM_W], d["s_uc"], ident)
                short_convolution(nc, x_hi, x_lo, w_in, d["conv_w"][0], d["s_y1"])
            uc = m1.sb("uc", P, G1, NC8)
            vw = m1.sb("vw", P, 2, QP, P)
            q = m1.sb("q", P, 2, QP, T8 + 1, H1)
            toeplitz = m1.sb("toeplitz", P, G1, P)
            a8 = m1.sb("a8", P, 2, QP)
            s5_weights(nc, d, vw, q, toeplitz, a8, ident, d["s_kernels"], uc, d["s_uc"])
            st = m1.sb("st", P, 2, QP, NC8)
            s5_scan_and_modulations(nc, uc, vw, a8, st, d["c_2"][0], d["c_ctx_2"], d["w_ada_2"][0], d["b_ada_2"][0],
                                    d["s_mod"])
            yt = m1.sb("yt", P, SSM_W // P, L)
            s5_outputs(nc, uc, st, q, toeplitz, yt, ident)
            s5_gate(nc, yt, d["w_glu"][0], d["b_glu"][0], d["s_z1"], d["s_y1"])
        output_rows_1(nc, d["s_y1"], d["w_out"][0], d["x"][0], d["final_norm_gain"], d["s_x2"])

        w_in2 = d["w_in_2"][0]
        mod, modc = (lambda i: d["s_mod"][0, i * D:(i + 1) * D]), (lambda i: d["s_mod"][1, i * D:(i + 1) * D])
        with Mem(nc, "m3") as m3:
            h_hi, h_lo = m3.sb_r("h_hi", P, KD, LT), m3.sb_r("h_lo", P, KD, LT)
            gain = d["g_pre_mix_2"][0]
            norm_to_columns(nc, "nc", d["ctx_2"][0], LC // P, h_hi, h_lo, L, ident, gain, (modc(0), modc(1)))
            norm_to_columns(nc, "n2", d["s_x2"], TILES, h_hi, h_lo, 0, ident, gain, (mod(0), mod(1)))
            silu_projection(nc, "z2", h_hi, h_lo, w_in2[:, FW:XBC], SW // P, d["s_z2"])
            convolved_projection(nc, h_hi, h_lo, w_in2[:, XBC:XBC + CONV_DIM], d["conv_w_2"][0], d["conv_b_2"][0], d["s_xbc"])
            decays(nc, h_hi, h_lo, w_in2[:, XBC + CONV_DIM:], d["dt_bias_2"][0], d["a_log_2"][0], d["s_decay_rows"],
                   d["s_totals"], d["s_decay_cols"], ident, ones)
            fourier_over_b(nc, h_hi, h_lo, w_in2[:, 0:FW], d["t_over_b"], d["s_g"])
        with Mem(nc, "m4") as m4:
            hf, hb = m4.sb("hf", P, HEADS, HD), m4.sb("hb", P, HEADS, HD)
            with Mem(nc, "cf") as m5:
                block = m5.block()
                context_states(nc, m5, block, d["s_xbc"], d["s_totals"], d["s_decay_cols"], hf[:, :, :], hb[:, :, :], ident)
                fourier_rest(nc, m5, block, d["s_g"], d["t_over_c"], d["t_over_a"], d["s_y2"])
            backward_states(nc, d["s_xbc"], d["s_totals"], d["s_decay_cols"], hb, d["s_hb"], ident)
            ssd_outputs(nc, d["s_xbc"], d["s_z2"], d["s_decay_rows"], d["s_totals"], d["s_decay_cols"], d["d_skip_2"][0],
                        hf, d["s_hb"], d["s_y2"], ident, ones)
        output_rows_2(nc, d["s_y2"], d["w_out_2"][0], d["g_ssd_2"][0], d["g_post_mix_2"][0], mod(2), d["s_x2"], d["s_x3"], ones)
        feed_forward(nc, d["s_x3"], d["g_pre_ffn_2"][0], mod(3), mod(4), d["w_gate_2"][0], d["w_up_2"][0], d["w_down_2"][0],
                     d["g_post_ffn_2"][0], mod(5), d["out"][0], ident)


SCRATCH = {
    "s_mod": (2, 6 * D),
    "s_uc": (HALF, P, G1, P), "s_z1": (SSM_W // P, P, L), "s_y1": (KD, P, L), "s_kernels": (H1, G1, 7 * H1 + P), "s_x2": (L, D),
    "s_g": (P // 8, P, FW // P * 2 * P), "s_z2": (SW // P, P, L), "s_xbc": (XT_, P, LT), "s_decay_rows": (LT // P, 2 * HEADS, P), "s_totals": (LT // P, 2 * HEADS),
    "s_decay_cols": (LT // P, P, 3 * 64), "s_hb": (NCH, P, HEADS * HD), "s_y2": (KD, P, L), "s_x3": (L, D),
}

_INS = ["x", "norm_gain", "w_in", "ssm_a_re", "ssm_a_im", "ssm_log_dt", "ssm_b_re", "ssm_b_im", "ssm_c_re", "ssm_c_im",
        "ssm_d", "w_glu", "b_glu", "conv_w", "w_out", "final_norm_gain", "c_2", "ctx_2", "c_ctx_2", "w_ada_2", "b_ada_2",
        "g_pre_mix_2", "g_post_mix_2", "g_pre_ffn_2", "g_post_ffn_2", "w_in_2", "conv_w_2", "conv_b_2", "dt_bias_2",
        "a_log_2", "d_skip_2", "g_ssd_2", "w_out_2", "w_gate_2", "w_up_2", "w_down_2"]


def kernel(**inputs):
    import concourse.bacc as _bacc
    from concourse.bass_utils import run_bass_kernel_spmd as _run

    nc = _bacc.Bacc("TRN2", target_bir_lowering=False, num_devices=1)
    arrays, d = {}, {}
    tables = dict(zip(("t_over_b", "t_over_c", "t_over_a"), fourier_tables()))
    for name, a in [(n, inputs[n]) for n in _INS] + list(tables.items()):
        a = np.ascontiguousarray(a)
        arrays[f"in_{name}_dram"] = a
        d[name] = nc.dram_tensor(f"in_{name}_dram", a.shape, mybir.dt.from_np(a.dtype), kind="ExternalInput").ap()
    for name, shape in SCRATCH.items():
        d[name] = nc.dram_tensor(name, shape, F32).ap()
    d["out"] = nc.dram_tensor("out_0_dram", (1, L, D), F32, kind="ExternalOutput").ap()
    program(nc, d)
    r = _run(nc, [arrays], core_ids=[0])
    return r.results[0]["out_0_dram"]
```
